# Optimizing a Trainium2 kernel written in Bass

```python
import math
import jax, jax.numpy as jnp
from jax import lax
import numpy as np

D_MODEL = 1024
BATCH = 1
SEQ = 256
DEPTH = 4

GRID_W = 64
CTX_LEN = 256
N_MIXERS = 3
N_A = (DEPTH + 2) // 3
N_B = (DEPTH + 1) // 3
N_C = DEPTH // 3
NORM_EPS = 1e-6
ROPE_BASE = 10000.0
Q_BLOCK = 128
NEG_INF = -1e30
MOD_GAIN = 0.5

A_HEADS = 8
A_Q_RANK = 512
A_KV_RANK = 256
A_NOPE = 128
A_ROPE = 64
A_VDIM = 128
A_WIDTH = A_HEADS * A_VDIM
A_IN = A_Q_RANK + A_KV_RANK + A_ROPE + A_WIDTH

B_HEADS = 16
B_KV_HEADS = 4
B_GROUP = B_HEADS // B_KV_HEADS
B_HDIM = 64
B_WINDOW = 128
B_BLOCK = 128
B_WIDTH = B_HEADS * B_HDIM
B_KVW = B_KV_HEADS * B_HDIM
B_IN = B_WIDTH + 2 * B_KVW + B_WIDTH

C_WIDTH = D_MODEL
C_ORDER = 2
C_SHORT = 3
C_BANDS = 16
C_EMB = 1 + 2 * C_BANDS
C_FFN = 64
C_TARGET = 1e-2
C_FAST = 0.3
C_SLOW = 1.5
C_MIN_DECAY = math.log(C_TARGET) / C_SLOW
C_MAX_DECAY = math.log(C_TARGET) / C_FAST
C_FILTER_GAIN = 0.1
C_IN = (C_ORDER + 1) * C_WIDTH + C_WIDTH


def rmsnorm(x, g):
    xf = x.astype(jnp.float32)
    y = xf * lax.rsqrt(jnp.mean(xf * xf, axis=-1, keepdims=True) + NORM_EPS)
    return (y * g.astype(jnp.float32)).astype(x.dtype)

def axial_rope(n, rot_dim):
    rows = n // GRID_W
    row = jnp.repeat(jnp.arange(rows, dtype=jnp.float32), GRID_W)
    col = jnp.tile(jnp.arange(GRID_W, dtype=jnp.float32), rows)
    per_axis = rot_dim // 2
    inv = ROPE_BASE ** (-jnp.arange(0, per_axis, 2, dtype=jnp.float32) / per_axis)
    ang = jnp.concatenate([row[:, None] * inv, col[:, None] * inv], axis=-1)
    return jnp.cos(ang), jnp.sin(ang)

def apply_rope(x, cos, sin):
    half = x.shape[-1] // 2
    x1 = x[..., :half].astype(jnp.float32)
    x2 = x[..., half:].astype(jnp.float32)
    return jnp.concatenate([x1 * cos - x2 * sin, x1 * sin + x2 * cos], axis=-1).astype(x.dtype)

def dense_attend(q, k, v, scale):
    s = jnp.einsum('bqhd,bkhd->bhqk', q, k).astype(jnp.float32) * scale
    p = jax.nn.softmax(s, axis=-1).astype(v.dtype)
    return jnp.einsum('bhqk,bkhd->bqhd', p, v)

def blockwise_attend(q, k, v, scale):
    b, n, h, d = q.shape
    qb = q.reshape(b, n // Q_BLOCK, Q_BLOCK, h, d).swapaxes(0, 1)
    ob = lax.map(lambda qi: dense_attend(qi, k, v, scale), qb)
    return ob.swapaxes(0, 1).reshape(b, n, h, v.shape[-1])

def sink_attend(scores, values, sink_l):
    sink_col = jnp.broadcast_to(sink_l[None, :, :, None, None], scores[0].shape[:-1] + (1,))
    p = jax.nn.softmax(jnp.concatenate(scores + [sink_col], axis=-1), axis=-1)
    offset = 0
    parts = []
    for s, v in zip(scores, values):
        kk = s.shape[-1]
        parts.append(jnp.einsum('bhgqk,bkhd->bqhgd', p[..., offset:offset + kk].astype(v.dtype), v))
        offset += kk
    out = parts[0]
    for part in parts[1:]:
        out = out + part
    return out

def mla_mixer(hx, hc, w_in, g_q, w_q, g_kv, w_kv, w_out, with_ctx_out):
    b, n, _ = hx.shape
    cos, sin = axial_rope(n, A_ROPE)
    split_at = [A_Q_RANK, A_Q_RANK + A_KV_RANK, A_Q_RANK + A_KV_RANK + A_ROPE]
    scale = (A_NOPE + A_ROPE) ** -0.5

    def queries(cq, rope):
        bb, m, _ = cq.shape
        q = (rmsnorm(cq, g_q) @ w_q).reshape(bb, m, A_HEADS, A_NOPE + A_ROPE)
        if rope:
            q = jnp.concatenate([q[..., :A_NOPE], apply_rope(q[..., A_NOPE:], cos[:, None, :], sin[:, None, :])], axis=-1)
        return q

    def keys_values(ckv, kr, rope):
        bb, m, _ = ckv.shape
        kv = (rmsnorm(ckv, g_kv) @ w_kv).reshape(bb, m, A_HEADS, A_NOPE + A_VDIM)
        if rope:
            kr = apply_rope(kr, cos, sin)
        kr = jnp.broadcast_to(kr[:, :, None, :], (bb, m, A_HEADS, A_ROPE))
        return jnp.concatenate([kv[..., :A_NOPE], kr], axis=-1), kv[..., A_NOPE:]

    cq_x, ckv_x, kr_x, gate_x = jnp.split(hx @ w_in, split_at, axis=-1)
    q_x = queries(cq_x, True)
    k_x, v_x = keys_values(ckv_x, kr_x, True)
    if with_ctx_out:
        cq_c, ckv_c, kr_c, gate_c = jnp.split(hc @ w_in, split_at, axis=-1)
    else:
        ckv_c, kr_c = jnp.split(hc @ w_in[:, split_at[0]:split_at[2]], [A_KV_RANK], axis=-1)
    k_c, v_c = keys_values(ckv_c, kr_c, False)

    k_all = jnp.concatenate([k_c, k_x], axis=1)
    v_all = jnp.concatenate([v_c, v_x], axis=1)
    o_x = blockwise_attend(q_x, k_all, v_all, scale)
    y_x = (o_x.reshape(b, n, A_WIDTH) * jax.nn.silu(gate_x)) @ w_out
    if not with_ctx_out:
        return y_x, None
    q_c = queries(cq_c, False)
    o_c = dense_attend(q_c, k_c, v_c, scale)
    y_c = (o_c.reshape(b, hc.shape[1], A_WIDTH) * jax.nn.silu(gate_c)) @ w_out
    return y_x, y_c

def swa_mixer(hx, hc, w_in, sink, w_out, with_ctx_out):
    b, n, _ = hx.shape
    cos, sin = axial_rope(n, B_HDIM)
    scale = B_HDIM ** -0.5
    sink_l = sink.astype(jnp.float32).reshape(B_KV_HEADS, B_GROUP)

    def project(h):
        m = h.shape[1]
        q, k, v, gate = jnp.split(h @ w_in, [B_WIDTH, B_WIDTH + B_KVW, B_WIDTH + 2 * B_KVW], axis=-1)
        return (q.reshape(b, m, B_KV_HEADS, B_GROUP, B_HDIM), k.reshape(b, m, B_KV_HEADS, B_HDIM),
                v.reshape(b, m, B_KV_HEADS, B_HDIM), gate)

    q_x, k_x, v_x, gate_x = project(hx)
    q_c, k_c, v_c, gate_c = project(hc)
    q_x = apply_rope(q_x, cos[:, None, None, :], sin[:, None, None, :])
    k_x = apply_rope(k_x, cos[:, None, :], sin[:, None, :])

    pad = ((0, 0), (B_BLOCK, B_BLOCK), (0, 0), (0, 0))
    kp = jnp.pad(k_x, pad)
    vp = jnp.pad(v_x, pad)
    n_blocks = n // B_BLOCK
    qb = q_x.reshape(b, n_blocks, B_BLOCK, B_KV_HEADS, B_GROUP, B_HDIM).swapaxes(0, 1)

    def band_block(args):
        i, qi = args
        start = i * B_BLOCK
        kb = lax.dynamic_slice_in_dim(kp, start, 3 * B_BLOCK, axis=1)
        vb = lax.dynamic_slice_in_dim(vp, start, 3 * B_BLOCK, axis=1)
        qpos = start + jnp.arange(B_BLOCK)
        kpos = start - B_BLOCK + jnp.arange(3 * B_BLOCK)
        mask = (jnp.abs(qpos[:, None] - kpos[None, :]) <= B_WINDOW) & (kpos[None, :] >= 0) & (kpos[None, :] < n)
        s_band = jnp.einsum('bqhgd,bkhd->bhgqk', qi, kb).astype(jnp.float32) * scale
        s_band = jnp.where(mask, s_band, NEG_INF)
        s_ctx = jnp.einsum('bqhgd,bkhd->bhgqk', qi, k_c).astype(jnp.float32) * scale
        return sink_attend([s_ctx, s_band], [v_c, vb], sink_l)

    ob = lax.map(band_block, (jnp.arange(n_blocks), qb))
    o_x = ob.swapaxes(0, 1).reshape(b, n, B_WIDTH)
    y_x = (o_x * jax.nn.silu(gate_x)) @ w_out
    if not with_ctx_out:
        return y_x, None
    s_cc = jnp.einsum('bqhgd,bkhd->bhgqk', q_c, k_c).astype(jnp.float32) * scale
    o_c = sink_attend([s_cc], [v_c], sink_l).reshape(b, hc.shape[1], B_WIDTH)
    y_c = (o_c * jax.nn.silu(gate_c)) @ w_out
    return y_x, y_c

def short_conv(u, w, bias):
    n = u.shape[1]
    p = C_SHORT // 2
    up = jnp.pad(u, ((0, 0), (p, p), (0, 0)))
    y = bias
    for j in range(C_SHORT):
        y = y + up[:, j:j + n] * w[j]
    return y

def hyena_filters(n, f_w1, f_b1, f_freq, f_w2, f_b2, f_w3):
    t = jnp.linspace(0.0, 1.0, n, dtype=jnp.float32)[:, None]
    w = (2.0 * math.pi / n) * jnp.arange(n, dtype=jnp.float32)[:, None]
    bands = jnp.linspace(1e-4, C_BANDS - 1, C_BANDS, dtype=jnp.float32)[None, :]
    z = jnp.concatenate([t, jnp.cos(bands * w), -jnp.sin(bands * w)], axis=-1)
    freq = f_freq.astype(jnp.float32)
    h = jnp.sin(freq * (z @ f_w1 + f_b1))
    h = jnp.sin(freq * (h @ f_w2 + f_b2))
    h = (h @ f_w3).astype(jnp.float32).reshape(n, 2, C_ORDER, C_WIDTH)
    deltas = jnp.abs(jnp.linspace(C_MIN_DECAY, C_MAX_DECAY, C_WIDTH, dtype=jnp.float32))
    return h * jnp.exp(-t[:, :, None, None] * deltas)

def bidir_long_conv(u, h_fwd, h_bwd, bias):
    n = u.shape[1]
    lag0 = h_fwd[:1] + h_bwd[:1]
    k = jnp.concatenate([lag0, h_fwd[1:], jnp.zeros((1, C_WIDTH), jnp.float32), h_bwd[:0:-1]], axis=0)
    uf = jnp.fft.rfft(u.astype(jnp.float32), n=2 * n, axis=1)
    kf = jnp.fft.rfft(k, axis=0)
    y = jnp.fft.irfft(uf * kf[None], n=2 * n, axis=1)[:, :n]
    return (y + u.astype(jnp.float32) * bias.astype(jnp.float32)).astype(u.dtype)

def hyena_mixer(hx, hc, w_in, conv_w, conv_b, f_w1, f_b1, f_freq, f_w2, f_b2, f_w3, filt_bias, w_out, with_ctx_out):
    def run(h):
        n = h.shape[1]
        p = h @ w_in
        u = short_conv(p[..., :(C_ORDER + 1) * C_WIDTH], conv_w, conv_b)
        gate = p[..., (C_ORDER + 1) * C_WIDTH:]
        v, *gx = jnp.split(u, C_ORDER + 1, axis=-1)
        filt = hyena_filters(n, f_w1, f_b1, f_freq, f_w2, f_b2, f_w3)
        z = v
        for o in range(C_ORDER):
            z = gx[o] * bidir_long_conv(z, filt[:, 0, o], filt[:, 1, o], filt_bias[o])
        return (z * jax.nn.silu(gate)) @ w_out
    y_x = run(hx)
    y_c = run(hc) if with_ctx_out else None
    return y_x, y_c

def first_inputs(seed: int = 0) -> dict:
    key = jax.random.key(seed)
    ks = iter(jax.random.split(key, 40))
    f32 = jnp.float32

    def nrm(shape, fan_in, gain=1.0):
        return jax.random.normal(next(ks), shape, f32) * (gain * fan_in ** -0.5)

    def gains(shape):
        return 1.0 + 0.01 * jax.random.normal(next(ks), shape, f32)

    def small(shape, s=0.01):
        return s * jax.random.normal(next(ks), shape, f32)

    D = D_MODEL
    return {
        'x': jax.random.normal(next(ks), (BATCH, SEQ, D), f32),
        'c': jax.random.normal(next(ks), (BATCH, D), f32),
        'ctx': jax.random.normal(next(ks), (BATCH, CTX_LEN, D), f32),
        'c_ctx': jax.random.normal(next(ks), (D,), f32),
        'w_mod': nrm((DEPTH, D, 3 * D), D, MOD_GAIN),
        'b_mod': small((DEPTH, 3 * D)),
        'g_pre': gains((DEPTH, D)),
        'g_post': gains((DEPTH, D)),
        'a_w_in': nrm((N_A, D, A_IN), D),
        'a_g_q': gains((N_A, A_Q_RANK)),
        'a_w_q': nrm((N_A, A_Q_RANK, A_HEADS * (A_NOPE + A_ROPE)), A_Q_RANK),
        'a_g_kv': gains((N_A, A_KV_RANK)),
        'a_w_kv': nrm((N_A, A_KV_RANK, A_HEADS * (A_NOPE + A_VDIM)), A_KV_RANK),
        'a_w_out': nrm((N_A, A_WIDTH, D), A_WIDTH),
        'b_w_in': nrm((N_B, D, B_IN), D),
        'b_sink': small((N_B, B_HEADS), 0.5),
        'b_w_out': nrm((N_B, B_WIDTH, D), B_WIDTH),
        'c_w_in': nrm((N_C, D, C_IN), D),
        'c_conv_w': nrm((N_C, C_SHORT, (C_ORDER + 1) * C_WIDTH), C_SHORT),
        'c_conv_b': small((N_C, (C_ORDER + 1) * C_WIDTH)),
        'c_f_w1': nrm((N_C, C_EMB, C_FFN), C_EMB),
        'c_f_b1': small((N_C, C_FFN), 0.1),
        'c_f_freq': gains((N_C, C_FFN)),
        'c_f_w2': nrm((N_C, C_FFN, C_FFN), C_FFN),
        'c_f_b2': small((N_C, C_FFN), 0.1),
        'c_f_w3': nrm((N_C, C_FFN, 2 * C_ORDER * C_WIDTH), C_FFN, C_FILTER_GAIN),
        'c_filt_bias': small((N_C, C_ORDER, C_WIDTH), 0.1),
        'c_w_out': nrm((N_C, C_WIDTH, D), C_WIDTH),
    }

def first_block(x, c, ctx, c_ctx, w_mod, b_mod, g_pre, g_post,
              a_w_in, a_g_q, a_w_q, a_g_kv, a_w_kv, a_w_out,
              b_w_in, b_sink, b_w_out,
              c_w_in, c_conv_w, c_conv_b, c_f_w1, c_f_b1, c_f_freq, c_f_w2, c_f_b2, c_f_w3, c_filt_bias, c_w_out):
    cond_x = jax.nn.silu(c)
    cond_c = jax.nn.silu(c_ctx)
    for layer in range(DEPTH):
        kind = layer % N_MIXERS
        j = layer // N_MIXERS
        with_ctx_out = layer < DEPTH - 1
        mx = cond_x @ w_mod[layer] + b_mod[layer]
        mc = cond_c @ w_mod[layer] + b_mod[layer]
        shift_x, scale_x, gate_x = jnp.split(mx[:, None, :], 3, axis=-1)
        shift_c, scale_c, gate_c = jnp.split(mc, 3, axis=-1)
        hx = rmsnorm(x, g_pre[layer]) * (1.0 + scale_x) + shift_x
        hc = rmsnorm(ctx, g_pre[layer]) * (1.0 + scale_c) + shift_c
        if kind == 0:
            yx, yc = mla_mixer(hx, hc, a_w_in[j], a_g_q[j], a_w_q[j], a_g_kv[j], a_w_kv[j], a_w_out[j], with_ctx_out)
        elif kind == 1:
            yx, yc = swa_mixer(hx, hc, b_w_in[j], b_sink[j], b_w_out[j], with_ctx_out)
        else:
            yx, yc = hyena_mixer(hx, hc, c_w_in[j], c_conv_w[j], c_conv_b[j], c_f_w1[j], c_f_b1[j], c_f_freq[j],
                                 c_f_w2[j], c_f_b2[j], c_f_w3[j], c_filt_bias[j], c_w_out[j], with_ctx_out)
        x = x + gate_x * rmsnorm(yx, g_post[layer])
        if with_ctx_out:
            ctx = ctx + gate_c * rmsnorm(yc, g_post[layer])
    return x


DEPTH_2 = 1

CHUNK = 64
D_POOL = D_MODEL // 2
POOL_WINDOWS = (2, 4, 8, 16)
POOL_GROUPS = len(POOL_WINDOWS)
POOL_GC = D_POOL // POOL_GROUPS
D_MLSTM = D_MODEL // 2
N_HEADS = 4
HEAD_DIM = D_MLSTM // N_HEADS
CONV_K = 4
N_GROUPS = 4
EXPERTS_PER_GROUP = 8
N_EXPERTS = N_GROUPS * EXPERTS_PER_GROUP
TOP_K = 2
D_EXPERT = D_MODEL // 2
MOE_BLOCK = 128
EPS = 1e-6
SPLIT_SIZES = (D_POOL, D_MLSTM, D_MLSTM, D_MLSTM, D_MLSTM, N_HEADS, N_HEADS, D_MODEL, D_MODEL)
N_IN = sum(SPLIT_SIZES)


def rmsnorm_2(x, g):
    xf = x.astype(jnp.float32)
    y = xf * lax.rsqrt(jnp.mean(xf * xf, axis=-1, keepdims=True) + EPS) * g.astype(jnp.float32)
    return y.astype(x.dtype)

def pool_mixer(u, w_pool, pool_scale):
    B, S, _ = u.shape
    uf = u.astype(jnp.float32)
    cs = jnp.pad(jnp.cumsum(uf, axis=1), ((0, 0), (1, 0), (0, 0)))
    t = jnp.arange(S)
    outs = []
    for g, w in enumerate(POOL_WINDOWS):
        sl = slice(g * POOL_GC, (g + 1) * POOL_GC)
        start = jnp.maximum(t + 1 - w, 0)
        win_sum = cs[:, 1:, sl] - cs[:, start, sl]
        cnt = (t + 1 - start).astype(jnp.float32)
        outs.append(win_sum / cnt[None, :, None] - uf[:, :, sl])
    d = jnp.stack(outs, axis=2)
    y = jnp.einsum('bsgc,gcd->bsgd', d, w_pool.astype(jnp.float32)).reshape(B, S, D_POOL)
    return (y * pool_scale.astype(jnp.float32)).astype(u.dtype)

def causal_conv(u, w):
    S = u.shape[1]
    up = jnp.pad(u, ((0, 0), (CONV_K - 1, 0), (0, 0)))
    return sum(up[:, j:j + S, :] * w[j] for j in range(CONV_K))

def mlstm_chunkwise(q, k, v, i_pre, f_pre):
    B, S, H, Dh = q.shape
    NC, L = S // CHUNK, CHUNK

    def to_chunks(a):
        a = a.astype(jnp.float32).reshape((B, NC, L, H) + a.shape[3:])
        return jnp.moveaxis(a, 3, 1)

    q = to_chunks(q)
    k = to_chunks(k) * (Dh ** -0.5)
    v = to_chunks(v)
    ig = to_chunks(i_pre)
    lf = jax.nn.log_sigmoid(to_chunks(f_pre))
    b = jnp.cumsum(lf, axis=-1)
    b_last = b[..., -1]

    a_log = b_last[..., None] - b + ig
    a_max = jnp.max(a_log, axis=-1)
    w_loc = jnp.exp(a_log - a_max[..., None])
    C_loc = jnp.einsum('bhcld,bhcle->bhcde', w_loc[..., None] * k, v)
    n_loc = jnp.einsum('bhcl,bhcld->bhcd', w_loc, k)

    def step(carry, inp):
        C, n, m = carry
        bl, am, Cl, nl = inp
        m_new = jnp.maximum(bl + m, am)
        s_prev = jnp.exp(bl + m - m_new)
        s_loc = jnp.exp(am - m_new)
        C_new = s_prev[..., None, None] * C + s_loc[..., None, None] * Cl
        n_new = s_prev[..., None] * n + s_loc[..., None] * nl
        return (C_new, n_new, m_new), (C, n, m)

    init = (jnp.zeros((B, H, Dh, Dh), jnp.float32), jnp.zeros((B, H, Dh), jnp.float32),
            jnp.zeros((B, H), jnp.float32))
    xs = (jnp.moveaxis(b_last, 2, 0), jnp.moveaxis(a_max, 2, 0),
          jnp.moveaxis(C_loc, 2, 0), jnp.moveaxis(n_loc, 2, 0))
    _, (C_prev, n_prev, m_prev) = lax.scan(step, init, xs)
    C_prev = jnp.moveaxis(C_prev, 0, 2)
    n_prev = jnp.moveaxis(n_prev, 0, 2)
    m_prev = jnp.moveaxis(m_prev, 0, 2)

    inter_log = b + m_prev[..., None]
    causal = jnp.tril(jnp.ones((L, L), dtype=bool))
    D = b[..., :, None] - b[..., None, :] + ig[..., None, :]
    D = jnp.where(causal, D, -jnp.inf)
    m_t = jnp.maximum(inter_log, jnp.max(D, axis=-1))
    w_inter = jnp.exp(inter_log - m_t)
    s = jnp.einsum('bhctd,bhcsd->bhcts', q, k) * jnp.exp(D - m_t[..., None])
    num = (w_inter[..., None] * jnp.einsum('bhctd,bhcde->bhcte', q, C_prev)
           + jnp.einsum('bhcts,bhcse->bhcte', s, v))
    nq = w_inter * jnp.einsum('bhctd,bhcd->bhct', q, n_prev) + jnp.sum(s, axis=-1)
    den = jnp.maximum(jnp.abs(nq), jnp.exp(-m_t))
    h = num / den[..., None]
    return jnp.moveaxis(h, 1, 3).reshape(B, S, H, Dh)

def head_layernorm(h, g):
    B, S, H, Dh = h.shape
    mu = jnp.mean(h, axis=-1, keepdims=True)
    var = jnp.mean(jnp.square(h - mu), axis=-1, keepdims=True)
    hn = (h - mu) * lax.rsqrt(var + EPS)
    return hn * g.astype(jnp.float32).reshape(H, Dh)

def hybrid_mixer(h, w_in, b_if, conv_q, conv_k, g_head, w_pool, pool_scale, w_br_a, w_br_b, w_out):
    B, S, _ = h.shape
    z = h @ w_in
    idx = [int(c) for c in np.cumsum(SPLIT_SIZES)[:-1]]
    u_pool, q, k, v, o, i_pre, f_pre, ga, gb = jnp.split(z, idx, axis=-1)
    y_a = pool_mixer(u_pool, w_pool, pool_scale) @ w_br_a
    q = jax.nn.silu(causal_conv(q, conv_q)).reshape(B, S, N_HEADS, HEAD_DIM)
    k = jax.nn.silu(causal_conv(k, conv_k)).reshape(B, S, N_HEADS, HEAD_DIM)
    v = v.reshape(B, S, N_HEADS, HEAD_DIM)
    i_pre = i_pre.astype(jnp.float32) + b_if[:N_HEADS].astype(jnp.float32)
    f_pre = f_pre.astype(jnp.float32) + b_if[N_HEADS:].astype(jnp.float32)
    hm = mlstm_chunkwise(q, k, v, i_pre, f_pre)
    hm = head_layernorm(hm, g_head).reshape(B, S, D_MLSTM)
    hm = (jax.nn.sigmoid(o.astype(jnp.float32)) * hm).astype(h.dtype)
    y_b = hm @ w_br_b
    merged = jax.nn.sigmoid(ga) * y_a + jax.nn.sigmoid(gb) * y_b
    return merged @ w_out

def hier_moe(h, w_rg, b_rg, w_re, b_re, w_gate, w_up, w_down):
    B, S, D = h.shape
    T = B * S
    xt = h.reshape(T, D)
    g_logits = (xt @ w_rg).astype(jnp.float32) + b_rg.astype(jnp.float32)
    g_prob = jax.nn.softmax(g_logits, axis=-1)
    g_sel = jnp.argmax(g_logits, axis=-1)
    p_g = jnp.take_along_axis(g_prob, g_sel[:, None], axis=-1)
    e_logits = ((xt @ w_re).astype(jnp.float32) + b_re.astype(jnp.float32)).reshape(
        T, N_GROUPS, EXPERTS_PER_GROUP)
    e_sel = jnp.take_along_axis(e_logits, g_sel[:, None, None], axis=1)[:, 0]
    top_p, top_i = lax.top_k(jax.nn.softmax(e_sel, axis=-1), TOP_K)
    gate = p_g * top_p / jnp.sum(top_p, axis=-1, keepdims=True)
    expert_id = g_sel[:, None] * EXPERTS_PER_GROUP + top_i

    A = T * TOP_K
    flat_e = expert_id.reshape(A)
    flat_tok = jnp.repeat(jnp.arange(T), TOP_K)
    flat_w = gate.reshape(A)
    order = jnp.argsort(flat_e)
    e_s, tok_s, w_s = flat_e[order], flat_tok[order], flat_w[order]
    counts = jnp.bincount(flat_e, length=N_EXPERTS)
    padded = (counts + MOE_BLOCK - 1) // MOE_BLOCK * MOE_BLOCK
    off = jnp.cumsum(counts) - counts
    pend = jnp.cumsum(padded)
    poff = pend - padded
    dest = poff[e_s] + jnp.arange(A) - off[e_s]
    n_rows = A + N_EXPERTS * MOE_BLOCK
    n_blocks = n_rows // MOE_BLOCK
    buf = jnp.zeros((n_rows, D), h.dtype).at[dest].set(xt[tok_s])
    block_e = jnp.clip(jnp.searchsorted(pend, jnp.arange(n_blocks) * MOE_BLOCK, side='right'),
                       0, N_EXPERTS - 1)

    def run_block(args):
        xb, e = args
        hid = jax.nn.silu(xb @ w_gate[e]) * (xb @ w_up[e])
        return hid @ w_down[e]

    yb = lax.map(run_block, (buf.reshape(n_blocks, MOE_BLOCK, D), block_e)).reshape(n_rows, D)
    y = jnp.zeros((T, D), jnp.float32).at[tok_s].add(yb[dest].astype(jnp.float32) * w_s[:, None])
    return y.reshape(B, S, D).astype(h.dtype)

def second_inputs(seed: int = 0) -> dict:
    key = jax.random.key(seed)
    ks = jax.random.split(key, 24)
    nrm = jax.random.normal
    f32 = jnp.float32
    x = nrm(ks[0], (BATCH, SEQ, D_MODEL), f32)
    g_mix = 1.0 + 0.1 * nrm(ks[1], (DEPTH_2, D_MODEL), f32)
    w_in = nrm(ks[2], (DEPTH_2, D_MODEL, N_IN), f32) * D_MODEL ** -0.5
    b_i = 0.1 * nrm(ks[3], (DEPTH_2, N_HEADS), f32)
    b_f = jnp.linspace(3.0, 6.0, N_HEADS, dtype=f32)[None] + 0.1 * nrm(ks[4], (DEPTH_2, N_HEADS), f32)
    b_if = jnp.concatenate([b_i, b_f], axis=-1)
    conv_q = nrm(ks[5], (DEPTH_2, CONV_K, D_MLSTM), f32) * CONV_K ** -0.5
    conv_k = nrm(ks[6], (DEPTH_2, CONV_K, D_MLSTM), f32) * CONV_K ** -0.5
    g_head = 1.0 + 0.1 * nrm(ks[7], (DEPTH_2, D_MLSTM), f32)
    w_pool = nrm(ks[8], (DEPTH_2, POOL_GROUPS, POOL_GC, POOL_GC), f32) * POOL_GC ** -0.5
    pool_scale = 1.0 + 0.1 * nrm(ks[9], (DEPTH_2, D_POOL), f32)
    w_br_a = nrm(ks[10], (DEPTH_2, D_POOL, D_MODEL), f32) * D_POOL ** -0.5
    w_br_b = nrm(ks[11], (DEPTH_2, D_MLSTM, D_MODEL), f32) * D_MLSTM ** -0.5
    w_out = nrm(ks[12], (DEPTH_2, D_MODEL, D_MODEL), f32) * D_MODEL ** -0.5
    g_ffn = 1.0 + 0.1 * nrm(ks[13], (DEPTH_2, D_MODEL), f32)
    w_rg = nrm(ks[14], (DEPTH_2, D_MODEL, N_GROUPS), f32) * D_MODEL ** -0.5
    b_rg = 0.01 * nrm(ks[15], (DEPTH_2, N_GROUPS), f32)
    w_re = nrm(ks[16], (DEPTH_2, D_MODEL, N_EXPERTS), f32) * D_MODEL ** -0.5
    b_re = 0.01 * nrm(ks[17], (DEPTH_2, N_EXPERTS), f32)
    w_e_gate = nrm(ks[18], (DEPTH_2, N_EXPERTS, D_MODEL, D_EXPERT), f32) * D_MODEL ** -0.5
    w_e_up = nrm(ks[19], (DEPTH_2, N_EXPERTS, D_MODEL, D_EXPERT), f32) * D_MODEL ** -0.5
    w_e_down = nrm(ks[20], (DEPTH_2, N_EXPERTS, D_EXPERT, D_MODEL), f32) * D_EXPERT ** -0.5
    g_final = 1.0 + 0.1 * nrm(ks[21], (D_MODEL,), f32)
    return {"x": x, "g_mix": g_mix, "w_in": w_in, "b_if": b_if, "conv_q": conv_q,
            "conv_k": conv_k, "g_head": g_head, "w_pool": w_pool, "pool_scale": pool_scale,
            "w_br_a": w_br_a, "w_br_b": w_br_b, "w_out": w_out, "g_ffn": g_ffn,
            "w_rg": w_rg, "b_rg": b_rg, "w_re": w_re, "b_re": b_re, "w_e_gate": w_e_gate,
            "w_e_up": w_e_up, "w_e_down": w_e_down, "g_final": g_final}

def second_block(x, g_mix, w_in, b_if, conv_q, conv_k, g_head, w_pool, pool_scale, w_br_a, w_br_b,
              w_out, g_ffn, w_rg, b_rg, w_re, b_re, w_e_gate, w_e_up, w_e_down, g_final):
    for l in range(DEPTH_2):
        x = x + hybrid_mixer(rmsnorm_2(x, g_mix[l]), w_in[l], b_if[l], conv_q[l], conv_k[l],
                             g_head[l], w_pool[l], pool_scale[l], w_br_a[l], w_br_b[l], w_out[l])
        x = x + hier_moe(rmsnorm_2(x, g_ffn[l]), w_rg[l], b_rg[l], w_re[l], b_re[l],
                         w_e_gate[l], w_e_up[l], w_e_down[l])
    return rmsnorm_2(x, g_final)


def setup_inputs(seed=0):
    out = dict(first_inputs(seed))
    for name, value in second_inputs(seed + 1).items():
        if name != "x":
            out[name + "_2"] = value
    return out


def reference(
    x, c, ctx, c_ctx, w_mod, b_mod, g_pre, g_post, a_w_in, a_g_q, a_w_q, a_g_kv, a_w_kv,
    a_w_out, b_w_in, b_sink, b_w_out, c_w_in, c_conv_w, c_conv_b, c_f_w1, c_f_b1, c_f_freq,
    c_f_w2, c_f_b2, c_f_w3, c_filt_bias, c_w_out, g_mix_2, w_in_2, b_if_2, conv_q_2, conv_k_2,
    g_head_2, w_pool_2, pool_scale_2, w_br_a_2, w_br_b_2, w_out_2, g_ffn_2, w_rg_2, b_rg_2,
    w_re_2, b_re_2, w_e_gate_2, w_e_up_2, w_e_down_2, g_final_2,
):
    x = first_block(
        x, c, ctx, c_ctx, w_mod, b_mod, g_pre, g_post, a_w_in, a_g_q, a_w_q, a_g_kv, a_w_kv,
        a_w_out, b_w_in, b_sink, b_w_out, c_w_in, c_conv_w, c_conv_b, c_f_w1, c_f_b1, c_f_freq,
        c_f_w2, c_f_b2, c_f_w3, c_filt_bias, c_w_out,
    )
    return second_block(
        x, g_mix_2, w_in_2, b_if_2, conv_q_2, conv_k_2, g_head_2, w_pool_2, pool_scale_2,
        w_br_a_2, w_br_b_2, w_out_2, g_ffn_2, w_rg_2, b_rg_2, w_re_2, b_re_2, w_e_gate_2,
        w_e_up_2, w_e_down_2, g_final_2,
    )


_drawn_inputs = setup_inputs


def setup_inputs(seed=0):
    import zlib

    import numpy as np

    out = dict(_drawn_inputs(seed))
    spreads = {}
    factors = {'g_pre': 4.435,
     'g_post': 3.992,
     'a_g_q': 8.0,
     'a_g_kv': 3.86,
     'b_sink': 8.0,
     'c_conv_b': 3.661,
     'c_f_freq': 8.0,
     'b_rg_2': 15.549,
     'b_re_2': 41.656,
     'g_head_2': 4.256,
     'pool_scale_2': 3.17}
    for name, (base, spread) in spreads.items():
        noise = np.random.default_rng([zlib.crc32(name.encode()), seed]).standard_normal(out[name].shape)
        drawn = base * np.exp(spread * noise) if base else spread * noise
        out[name] = __import__('jax').numpy.asarray(drawn.astype(out[name].dtype))
    for name, factor in factors.items():
        out[name] = (out[name] * factor).astype(out[name].dtype)
    return out
```

```python
import math
from contextlib import ExitStack, contextmanager

import numpy as np

import concourse.bass as bass
from concourse import mybir

F32 = mybir.dt.float32
U32 = mybir.dt.uint32
ALU = mybir.AluOpType
ACT = mybir.ActivationFunctionType
AX = mybir.AxisListType.X

P = 128
D = 1024
KD = D // P
N = 256
NX = N // P
NT = 2 * NX
DEPTH = 4
EPS = 1e-6
GRID_W = 64
ROPE_BASE = 10000.0
MASKED = -1e30

A_H, A_QR, A_KVR, A_NOPE, A_ROPE, A_V = 8, 512, 256, 128, 64, 128
B_H, B_KVH, B_HD, B_WINDOW = 16, 4, 64, 128
C_BANDS = 16
C_EMB = 1 + 2 * C_BANDS
C_FFN = 64
C_MIN_DECAY = math.log(1e-2) / 1.5
C_MAX_DECAY = math.log(1e-2) / 0.3

POOL_WINDOWS = (2, 4, 8, 16)
POOL_PAD = 16
M_H, M_HD = 4, 128
CONV_K = 4
N_GROUPS, PER_GROUP = 4, 8
N_EXP = N_GROUPS * PER_GROUP
D_EXP = 512
N_ROUTE = N_GROUPS + N_EXP

SLOT = 4096
RING = 4
MOE_RING = 6


def columns(fields):
    at, out = 0, {}
    for name, width in fields:
        out[name] = (at, at + width)
        at += width
    out["width"] = at
    return out


VEC = columns([
    ("g_pre", DEPTH * KD), ("a_g_q", 2 * 4), ("a_g_kv", 2 * 2), ("conv_w", 3 * 24), ("conv_b", 24),
    ("f_b1", 1), ("f_freq", 1), ("f_b2", 1), ("f_w1", C_FFN), ("f_w2", C_FFN),
    ("g_mix", KD), ("g_ffn", KD), ("g_head", 4), ("pool_scale", 4), ("conv_q", 4 * 4), ("conv_k", 4 * 4),
    ("cond", 2 * KD), ("w_if", KD * 8), ("w_route", KD * N_ROUTE),
])
ROW = columns([("sink", B_H), ("b_route", N_ROUTE), ("b_if", 8), ("iota", N_EXP)])
CST = columns([("ident", P), ("cos", NX * 32), ("sin", NX * 32), ("sel", 4 * P)])


def panel_plan():
    plan = []
    for layer in range(DEPTH):
        plan += [(f"mod{layer}.{n}", SLOT) for n in range(6)]
        if layer % 3 == 0:
            plan += [(f"a_cq{layer}", SLOT), (f"a_ckv{layer}", 8 * (A_KVR + A_ROPE))]
            plan += [(f"a_gate{layer}.{n}", SLOT) for n in range(2)]
            plan += [(f"a_q{layer}.{n}", 4 * 768) for n in range(2)]
            plan += [(f"a_kv{layer}", SLOT)]
            plan += [(f"a_out{layer}.{n}", SLOT) for n in range(2)]
        elif layer % 3 == 1:
            plan += [(f"b_in.{n}", SLOT) for n in range(5)]
            plan += [(f"b_out.{n}", SLOT) for n in range(2)]
        else:
            plan += [(f"c_in.{n}", SLOT) for n in range(8)]
            plan += [("c_decay", SLOT), ("c_w3", SLOT)]
            plan += [(f"c_out.{n}", SLOT) for n in range(2)]
    plan += [(f"s_in.{n}", SLOT) for n in range(9)]
    plan += [("s_pool", 512), ("s_br_a", SLOT), ("s_br_b", SLOT)]
    plan += [(f"s_out.{n}", SLOT) for n in range(2)]
    return plan


N_DENSE = len(panel_plan())


def slot_of(i):
    return i % RING if i < N_DENSE else (i - N_DENSE) % MOE_RING


class Signal:

    def __init__(self, sem):
        self.sem, self.total, self.base = sem, 0, 0

    def one(self):
        self.total += 1
        return 1

    def sixteen(self):
        self.total += 16
        return 16

    def at(self, n):
        return self.base + n


class Core:

    def __init__(self, nc, stack, dram):
        self.nc, self.stack, self.dram = nc, stack, dram
        self.signals, self.names = {}, {}
        self.plan = panel_plan()
        self.next_panel = 0
        self.ps = [stack.enter_context(nc.psum_tensor(f"bank{i}", [P, 512], F32)) for i in range(8)]

    def sb(self, name, shape, stack=None, dt=F32):
        again = self.names[name] = self.names.get(name, 0) + 1
        name = name if again == 1 else f"{name}_{again}"
        return (stack or self.stack).enter_context(self.nc.sbuf_tensor(name, shape, dt))

    def sig(self, name):
        if name not in self.signals:
            self.signals[name] = Signal(self.stack.enter_context(self.nc.semaphore(name)))
        return self.signals[name]

    @contextmanager
    def step(self):
        for s in self.signals.values():
            s.base = s.total
        with self.nc.Block(no_gpsimd_drain=True) as block:
            yield block

    def slot(self, i):
        return self.slots[slot_of(i)]

    def loaded(self, i):
        s = slot_of(i)
        before = sum(1 for j in range(i + 1) if slot_of(j) == s)
        return self.sig(f"slot{s}_loaded").sem, 16 * before

    def issue(self, sp, i):
        width = self.plan[i][1] if i < N_DENSE else SLOT
        g = self.sig(f"slot{slot_of(i)}_loaded")
        sp.dma_start(self.slot(i)[:, 0:width], self.dram["panels"][i, :, 0:width]).then_inc(g.sem, g.sixteen())

    def followers(self, i):
        s = slot_of(i)
        return [j for j in range(i + 1, min(i + 1 + 2 * MOE_RING, N_DENSE + MOE_RING)) if slot_of(j) == s][:1]

    def take(self, n, *names):
        got = list(range(self.next_panel, self.next_panel + n))
        self.next_panel += n
        for i, name in zip(got, names):
            assert self.plan[i][0].startswith(name), (self.plan[i], name)
        return got

    def load_next(self, sp, i):
        for j in self.followers(i):
            self.issue(sp, j)

    def vec(self, name, a=0, b=None):
        lo, hi = VEC[name]
        return self.vecs[:, lo + a:(hi if b is None else lo + b)]


def after(eng, ins, signal):
    ins.then_inc(signal.sem, signal.one())
    eng.wait_ge(signal.sem, signal.total)


def variance(m, dve, v, sums, inv_n):
    m.nc.vector.tensor_scalar(v, sums, inv_n, EPS, ALU.mult, ALU.add) \
        .then_inc(m.sig("variance_ready").sem, m.sig("variance_ready").one())


def rough_rstd(m, act, v, y, nth=1):
    s, rough = m.sig("act_chain"), m.sig("rough_rstd_ready")
    act.wait_ge(m.sig("variance_ready").sem, m.sig("variance_ready").at(nth))
    after(act, m.nc.scalar.activation(y, v, ACT.Ln), s)
    m.nc.scalar.activation(y, y, ACT.Exp, scale=-0.5).then_inc(rough.sem, rough.one())


def fine_rstd(m, dve, v, y, tmp, nth=1):
    s = m.sig("dve_chain")
    dve.wait_ge(m.sig("rough_rstd_ready").sem, m.sig("rough_rstd_ready").at(nth))
    after(dve, m.nc.vector.tensor_tensor(tmp, y, y, ALU.mult), s)
    after(dve, m.nc.vector.tensor_tensor(tmp, tmp, v, ALU.mult), s)
    after(dve, m.nc.vector.tensor_scalar(tmp, tmp, -0.5, 1.5, ALU.mult, ALU.add), s)
    after(dve, m.nc.vector.tensor_tensor(y, y, tmp, ALU.mult), s)


def load_constants(m):
    nc = m.nc
    with m.step() as block:
        landed = m.sig("constants_landed")

        @block.sync
        def _(sp):
            for dst, src in ((m.vecs, "vecs"), (m.cst, "cst")):
                sp.dma_start(dst[:], m.dram[src]).then_inc(landed.sem, landed.sixteen())
            for t in range(NT):
                sp.dma_start(m.x[:, t, :], m.dram["tokens"][t * P:(t + 1) * P, :]) \
                    .then_inc(landed.sem, landed.sixteen())
            sp.dma_start(m.rows[:], m.dram["rows"]).then_inc(landed.sem, landed.sixteen())
            for i in range(RING):
                m.issue(sp, i)

        @block.scalar
        def _(act):
            act.wait_ge(landed.sem, landed.at(16 * (3 + NT)))
            nc.scalar.activation(m.cond[:], m.vec("cond"), ACT.Exp, scale=-1.0) \
                .then_inc(m.sig("act_chain").sem, m.sig("act_chain").one())

        @block.vector
        def _(dve):
            s = m.sig("dve_chain")
            dve.wait_ge(m.sig("act_chain").sem, m.sig("act_chain").at(1))
            after(dve, nc.vector.tensor_scalar(m.cond[:], m.cond[:], 1.0, None, ALU.add), s)
            after(dve, nc.vector.reciprocal(m.cond[:], m.cond[:]), s)
            after(dve, nc.vector.tensor_tensor(m.cond[:], m.cond[:], m.vec("cond"), ALU.mult), s)


def modulation(m, layer):
    nc, ps = m.nc, m.ps
    panels = m.take(6, *[f"mod{layer}.{n}" for n in range(6)])
    with ExitStack() as own:
        given = m.sb("mod_given", [2, 4 * D], own)
        row = m.sb("mod_row", [2, 3 * D], own)
        cond = m.cond[:].rearrange("p (s k) -> p k s", s=2)
        with m.step() as block:
            landed, chunk, chunk_read = m.sig("mod_given_landed"), m.sig("mod_chunk_in_psum"), m.sig("mod_chunk_read")
            cols, gates = m.sig("mod_columns_in_psum"), m.sig("mod_gate_in_psum")

            @block.sync
            def _(sp):
                sp.dma_start(given[:], m.dram["mod_rows"][layer]).then_inc(landed.sem, landed.sixteen())
                for n, i in enumerate(panels):
                    sp.wait_ge(chunk.sem, chunk.at(n + 1))
                    m.load_next(sp, i)
                sp.wait_ge(landed.sem, landed.at(16))

            @block.tensor
            def _(pe):
                for n, i in enumerate(panels):
                    pe.wait_ge(*m.loaded(i))
                    if n >= 2:
                        pe.wait_ge(chunk_read.sem, chunk_read.at(n - 1))
                    for k in range(KD):
                        last = nc.tensor.matmul(ps[n % 2][0:2, :], cond[:, k, :], m.slot(i)[:, k * 512:(k + 1) * 512],
                                                start=k == 0, stop=k == KD - 1)
                    last.then_inc(chunk.sem, chunk.one())
                pe.wait_ge(chunk_read.sem, chunk_read.at(6))
                for j in range(2 * KD):
                    last = nc.tensor.matmul(ps[2][:, 2 * j:2 * j + 2], row[0:2, j * P:(j + 1) * P], m.ident[0:2, 0:2],
                                            start=True, stop=True)
                last.then_inc(cols.sem, cols.one())
                for s in range(2):
                    for n in range(2):
                        nc.tensor.matmul(ps[4 + 2 * s + n][:, :], m.sel[0:2, s, :],
                                         row[0:2, 2 * D + n * 512:2 * D + (n + 1) * 512], start=True, stop=True) \
                            .then_inc(gates.sem, gates.one())

            @block.vector
            def _(dve):
                chain = m.sig("dve_chain")
                dve.wait_ge(landed.sem, landed.at(16))
                for n in range(6):
                    dve.wait_ge(chunk.sem, chunk.at(n + 1))
                    part = row[:, n * 512:(n + 1) * 512]
                    add = nc.vector.tensor_tensor(part, ps[n % 2][0:2, :], given[:, n * 512:(n + 1) * 512], ALU.add)
                    if n >= 4:
                        after(dve, add, chain)
                        add = nc.vector.tensor_tensor(part, part, given[:, 3 * D + (n - 4) * 512:3 * D + (n - 3) * 512],
                                                      ALU.mult)
                    add.then_inc(chunk_read.sem, chunk_read.one())
                dve.wait_ge(cols.sem, cols.at(1))
                both = ps[2][:, 0:4 * KD].rearrange("p (w k s) -> p w s k", w=2, s=2)
                nc.vector.tensor_copy(m.shift[:], both[:, 0])
                for s in range(2):
                    nc.vector.scalar_tensor_tensor(out=m.scale1[:, s, :], in0=both[:, 1, s, :], scalar=1.0,
                                                   in1=m.vec("g_pre", layer * KD, (layer + 1) * KD),
                                                   op0=ALU.add, op1=ALU.mult)

            @block.scalar
            def _(act):
                for s in range(2):
                    for n in range(2):
                        act.wait_ge(gates.sem, gates.at(2 * s + n + 1))
                        nc.scalar.activation(m.gate[:, s, n * 512:(n + 1) * 512], ps[4 + 2 * s + n][:, :], ACT.Copy)


def norm_to_channels(m, tiles, out, scale, shift):
    nc, ps = m.nc, m.ps
    with m.step() as block:
        squares, normed, turned = m.sig("squares_summed"), m.sig("normed_ready"), m.sig("turned_in_psum")
        taken = {0: m.sig("turned_taken_by_dve"), 1: m.sig("turned_taken_by_act")}

        @block.scalar
        def _(act):
            for t in range(tiles):
                after(act, nc.scalar.activation(m.scratch[:, t % 2, :], m.x[:, t, :], ACT.Square,
                                                accum_out=m.sums[:, t:t + 1]), m.sig("act_chain"))
            nc.scalar.nop().then_inc(squares.sem, squares.one())
            rough_rstd(m, act, m.var[:, 0:tiles], m.rstd[:, 0:tiles])
            for t in range(tiles):
                act.wait_ge(turned.sem, turned.at(2 * t + 2))
                for k in range(4, 8):
                    last = nc.scalar.activation(out[:, k, t * P:(t + 1) * P], ps[(2 * t + 1) % 4][:, (k - 4) * P:(k - 3) * P],
                                                ACT.Identity, scale=scale(t // NX, k),
                                                bias=0.0 if shift is None else shift(t // NX, k))
                last.then_inc(taken[1].sem, taken[1].one())

        @block.vector
        def _(dve):
            dve.wait_ge(squares.sem, squares.at(1))
            variance(m, dve, m.var[:, 0:tiles], m.sums[:, 0:tiles], 1.0 / D)
            fine_rstd(m, dve, m.var[:, 0:tiles], m.rstd[:, 0:tiles], m.tmp[:, 0:tiles])
            for t in range(tiles + 1):
                if t < tiles:
                    if t >= 2:
                        dve.wait_ge(turned.sem, turned.at(2 * (t - 2) + 2))
                    nc.vector.tensor_scalar(m.scratch[:, t % 2, :], m.x[:, t, :], m.rstd[:, t:t + 1], None, ALU.mult) \
                        .then_inc(normed.sem, normed.one())
                if t >= 1:
                    u = t - 1
                    dve.wait_ge(turned.sem, turned.at(2 * u + 1))
                    for k in range(4):
                        src = ps[(2 * u) % 4][:, k * P:(k + 1) * P]
                        dst = out[:, k, u * P:(u + 1) * P]
                        if shift is None:
                            last = nc.vector.tensor_scalar(dst, src, scale(u // NX, k), None, ALU.mult)
                        else:
                            last = nc.vector.tensor_scalar(dst, src, scale(u // NX, k), shift(u // NX, k), ALU.mult, ALU.add)
                    last.then_inc(taken[0].sem, taken[0].one())

        @block.tensor
        def _(pe):
            for t in range(tiles):
                pe.wait_ge(normed.sem, normed.at(t + 1))
                for half in range(2):
                    if t >= 2:
                        pe.wait_ge(taken[half].sem, taken[half].at(t - 1))
                    for k in range(4):
                        last = nc.tensor.transpose(ps[(2 * t + half) % 4][:, k * P:(k + 1) * P],
                                                   m.scratch[:, t % 2, (4 * half + k) * P:(4 * half + k + 1) * P], m.ident[:, :])
                    last.then_inc(turned.sem, turned.one())


class Gates:

    def __init__(self, m, n_tok, tmp):
        self.m, self.n, self.tmp = m, n_tok, tmp
        self.ready, self.exp, self.done = m.sig("gate_in_psum"), m.sig("gate_exp_ready"), m.sig("gate_done")

    def bank(self, g):
        return self.m.ps[4 + g % 4][:, 0:self.n]

    def matmuls(self, pe, g, panel, j, k_tiles=KD, width=512):
        if g >= 4:
            pe.wait_ge(self.done.sem, self.done.at(g - 3))
        for k in range(k_tiles):
            last = self.m.nc.tensor.matmul(self.bank(g), self.m.slot(panel)[:, k * width + j * P:k * width + (j + 1) * P],
                                           self.m.hT[:, k, 0:self.n], start=k == 0, stop=k == k_tiles - 1)
        last.then_inc(self.ready.sem, self.ready.one())

    def exponential(self, act, g):
        act.wait_ge(self.ready.sem, self.ready.at(g + 1))
        if g >= 2:
            act.wait_ge(self.done.sem, self.done.at(g - 1))
        self.m.nc.scalar.activation(self.tmp[:, g % 2, 0:self.n], self.bank(g), ACT.Exp, scale=-1.0) \
            .then_inc(self.exp.sem, self.exp.one())

    def finish(self, dve, g, out, silu):
        nc, chain, t = self.m.nc, self.m.sig("dve_chain"), self.tmp[:, g % 2, 0:self.n]
        dve.wait_ge(self.exp.sem, self.exp.at(g + 1))
        after(dve, nc.vector.tensor_scalar(t, t, 1.0, None, ALU.add), chain)
        if silu:
            after(dve, nc.vector.reciprocal(t, t), chain)
            last = nc.vector.tensor_tensor(out, self.bank(g), t, ALU.mult)
        else:
            last = nc.vector.reciprocal(out, t)
        last.then_inc(self.done.sem, self.done.one())


def rope(m, dve, out, src, t, heads):
    nc, chain = m.nc, m.sig("dve_chain")
    wide = [P, heads, 32]
    cos = m.cos[:, t, :].unsqueeze(1).broadcast_to(wide)
    sin = m.sin[:, t, :].unsqueeze(1).broadcast_to(wide)
    ta = m.scratch[:, 0, 0:heads * 32].rearrange("p (h c) -> p h c", h=heads)
    tb = m.scratch[:, 1, 0:heads * 32].rearrange("p (h c) -> p h c", h=heads)
    nc.vector.tensor_tensor(ta, src[:, :, 0, :], cos, ALU.mult)
    after(dve, nc.vector.tensor_tensor(tb, src[:, :, 1, :], sin, ALU.mult), chain)
    after(dve, nc.vector.tensor_tensor(out[:, :, 0, :], ta, tb, ALU.subtract), chain)
    nc.vector.tensor_tensor(ta, src[:, :, 0, :], sin, ALU.mult)
    after(dve, nc.vector.tensor_tensor(tb, src[:, :, 1, :], cos, ALU.mult), chain)
    return nc.vector.tensor_tensor(out[:, :, 1, :], ta, tb, ALU.add)


def attention(m, own, heads, streams, scale, score_parts, v_of, place, mask=None, sink=None):
    nc, ps = m.nc, m.ps
    probs = m.sb("probs", [P, 3, 512], own)
    probsT = m.sb("probsT", [P, 2, 4, N], own)
    neg_max, den, rden, esink = (m.sb(n, [P, 3], own) for n in ("neg_max", "den", "rden", "esink"))
    units = [(h, s, q) for h in range(heads) for s in range(streams) for q in range(NX)]
    U, LAG = len(units), 2
    keys = lambda s: range(0, NT) if s == 0 else range(NX, NT)

    with m.step() as block:
        scored, maxed, expd = m.sig("scores_in_psum"), m.sig("row_max_ready"), m.sig("probs_ready")
        normed, turned, copied = m.sig("probs_normalised"), m.sig("probsT_in_psum"), m.sig("probsT_copied")
        outed, taken = m.sig("attended_in_psum"), m.sig("attended_taken")

        @block.tensor
        def _(pe):
            for step in range(U + LAG + 2):
                if step < U:
                    u = step
                    h, s, q = units[u]
                    first = keys(s)[0] * P
                    if u >= 3:
                        pe.wait_ge(expd.sem, expd.at(u - 2))
                    parts = score_parts(h, NX * s + q)
                    opposite = 1 - q
                    with_mask = mask is not None and s == 0
                    for i, (lhsT, rhs) in enumerate(parts):
                        last = nc.tensor.matmul(ps[u % 3][:, first:512], lhsT, rhs[:, first:512], start=i == 0,
                                                stop=i == len(parts) - 1)
                    if with_mask:
                        last = nc.tensor.matmul(ps[u % 3][:, opposite * P:(opposite + 1) * P], m.ident[:, :], mask[:, q, :],
                                                start=False, stop=True, skip_group_check=True)
                    last.then_inc(scored.sem, scored.one())
                u = step - LAG
                if 0 <= u < U:
                    h, s, q = units[u]
                    pe.wait_ge(normed.sem, normed.at(u + 1))
                    if u >= 2:
                        pe.wait_ge(copied.sem, copied.at(u - 1))
                    for kt in keys(s):
                        last = nc.tensor.transpose(ps[3 + u % 2][:, kt * P:(kt + 1) * P],
                                                   probs[:, u % 3, kt * P:(kt + 1) * P], m.ident[:, :])
                    last.then_inc(turned.sem, turned.one())
                u = step - LAG - 1
                if 0 <= u < U and u % NX == NX - 1:
                    v = u // NX
                    h, s, q = units[u]
                    pe.wait_ge(copied.sem, copied.at(u + 1))
                    if v >= 2:
                        pe.wait_ge(taken.sem, taken.at(v - 1))
                    for kt in keys(s):
                        last = nc.tensor.matmul(ps[5 + v % 2][:, 0:N], v_of(h, kt), probsT[:, v % 2, kt, :],
                                                start=kt == keys(s)[0], stop=kt == NT - 1)
                    last.then_inc(outed.sem, outed.one())

        @block.scalar
        def _(act):
            for step in range(U + LAG):
                if step < U:
                    u = step
                    h, s, q = units[u]
                    first = keys(s)[0] * P
                    act.wait_ge(maxed.sem, maxed.at(u + 1))
                    if u >= 3:
                        act.wait_ge(turned.sem, turned.at(u - 2))
                    if sink is not None:
                        nc.scalar.activation(esink[:, u % 3:u % 3 + 1], sink[:, h:h + 1], ACT.Exp,
                                             bias=neg_max[:, u % 3:u % 3 + 1])
                    nc.scalar.activation(probs[:, u % 3, first:512], ps[u % 3][:, first:512], ACT.Exp, scale=scale,
                                         bias=neg_max[:, u % 3:u % 3 + 1], accum_out=den[:, u % 3:u % 3 + 1]) \
                        .then_inc(expd.sem, expd.one())
                u = step - LAG
                if 0 <= u < U:
                    h, s, q = units[u]
                    v = u // NX
                    act.wait_ge(turned.sem, turned.at(u + 1))
                    if v >= 2:
                        act.wait_ge(outed.sem, outed.at(v - 1))
                    first = keys(s)[0]
                    nc.scalar.activation(probsT[:, v % 2, first:NT, q * P:(q + 1) * P],
                                         ps[3 + u % 2][:, first * P:512].rearrange("p (k q) -> p k q", q=P), ACT.Copy) \
                        .then_inc(copied.sem, copied.one())

        @block.vector
        def _(dve):
            chain = m.sig("dve_chain")
            for step in range(U + LAG + 2):
                if step < U:
                    u = step
                    h, s, q = units[u]
                    first = keys(s)[0] * P
                    col = neg_max[:, u % 3:u % 3 + 1]
                    dve.wait_ge(scored.sem, scored.at(u + 1))
                    after(dve, nc.vector.tensor_reduce(col, ps[u % 3][:, first:512], AX, ALU.max), chain)
                    if sink is None:
                        last = nc.vector.tensor_scalar(col, col, -scale, None, ALU.mult)
                    else:
                        last = nc.vector.tensor_scalar(col, col, -scale, m.neg_sink[:, h:h + 1], ALU.mult, ALU.min)
                    last.then_inc(maxed.sem, maxed.one())
                u = step - 1
                if 0 <= u < U:
                    h, s, q = units[u]
                    first = keys(s)[0] * P
                    c = slice(u % 3, u % 3 + 1)
                    dve.wait_ge(expd.sem, expd.at(u + 1))
                    if sink is not None:
                        after(dve, nc.vector.tensor_tensor(den[:, c], den[:, c], esink[:, c], ALU.add), chain)
                    after(dve, nc.vector.reciprocal(rden[:, c], den[:, c]), chain)
                    nc.vector.tensor_scalar(probs[:, u % 3, first:512], probs[:, u % 3, first:512], rden[:, c], None,
                                            ALU.mult).then_inc(normed.sem, normed.one())
                u = step - LAG - 1
                if 0 <= u < U and u % NX == NX - 1:
                    v = u // NX
                    h, s, q = units[u]
                    dve.wait_ge(outed.sem, outed.at(v + 1))
                    rows, tile = place(h)
                    dst = m.gT[rows, tile, s * N:(s + 1) * N]
                    nc.vector.tensor_tensor(dst, ps[5 + v % 2][rows, 0:N], dst, ALU.mult).then_inc(taken.sem, taken.one())


def project_out(m, name, tiles, gated):
    nc, ps = m.nc, m.ps
    panels = m.take(2, name, name)
    bank = lambda t, n: ps[2 * t + n]
    with m.step() as block:
        ready, squares = m.sig("projected_in_psum"), m.sig("squares_summed")

        @block.sync
        def _(sp):
            for n, i in enumerate(panels):
                sp.wait_ge(ready.sem, ready.at((n + 1) * tiles))
                m.load_next(sp, i)

        @block.tensor
        def _(pe):
            for n, i in enumerate(panels):
                pe.wait_ge(*m.loaded(i))
                for t in range(tiles):
                    for k in range(KD):
                        last = nc.tensor.matmul(bank(t, n)[:, :], m.gT[:, k, t * P:(t + 1) * P],
                                                m.slot(i)[:, k * 512:(k + 1) * 512], start=k == 0, stop=k == KD - 1)
                    last.then_inc(ready.sem, ready.one())

        @block.scalar
        def _(act):
            if gated:
                for n in range(2):
                    for t in range(tiles):
                        act.wait_ge(ready.sem, ready.at(n * tiles + t + 1))
                        after(act, nc.scalar.activation(m.scratch[:, 0, 0:512], bank(t, n)[:, :], ACT.Square,
                                                        accum_out=m.sums[:, n * NT + t:n * NT + t + 1]), m.sig("act_chain"))
                nc.scalar.nop().then_inc(squares.sem, squares.one())
                rough_rstd(m, act, m.var[:, 0:tiles], m.rstd[:, 0:tiles])

        @block.vector
        def _(dve):
            chain = m.sig("dve_chain")
            if gated:
                dve.wait_ge(squares.sem, squares.at(1))
                after(dve, nc.vector.tensor_tensor(m.sums[:, 0:tiles], m.sums[:, 0:tiles], m.sums[:, NT:NT + tiles],
                                                   ALU.add), chain)
                variance(m, dve, m.var[:, 0:tiles], m.sums[:, 0:tiles], 1.0 / D)
                fine_rstd(m, dve, m.var[:, 0:tiles], m.rstd[:, 0:tiles], m.tmp[:, 0:tiles])
            else:
                dve.wait_ge(ready.sem, ready.at(2 * tiles))
            for t in range(tiles):
                for n in range(2):
                    part = m.x[:, t, n * 512:(n + 1) * 512]
                    if gated:
                        y = m.scratch[:, 1, n * 512:(n + 1) * 512]
                        after(dve, nc.vector.scalar_tensor_tensor(out=y, in0=bank(t, n)[:, :], scalar=m.rstd[:, t:t + 1],
                                                                  in1=m.gate[:, t // NX, n * 512:(n + 1) * 512],
                                                                  op0=ALU.mult, op1=ALU.mult), chain)
                        after(dve, nc.vector.tensor_tensor(part, part, y, ALU.add), chain)
                    else:
                        after(dve, nc.vector.tensor_tensor(part, part, bank(t, n)[:, :], ALU.add), chain)


def latent_layer(m, layer):
    nc, ps = m.nc, m.ps
    j = layer // 3
    streams = 2 if layer < DEPTH - 1 else 1
    tq = NX * streams
    nq = tq * P
    norm_to_channels(m, NT, m.hT, lambda s, k: m.scale1[:, s, k:k + 1], lambda s, k: m.shift[:, s, k:k + 1])
    with ExitStack() as own:
        m.gT = m.sb("gT", [P, KD, 512], own)
        qnT = m.sb("q_nopeT", [P, A_H, 512], own)
        qrT = m.sb("q_ropeT", [P, A_H // 2, 512], own)
        krT = m.sb("k_ropeT", [P, 512], own)
        v = m.sb("values", [P, NT, A_H * A_V], own)
        with ExitStack() as early:
            cq = m.sb("cq", [P, NT, A_QR], early)
            ckv = m.sb("ckv", [P, NT, A_KVR + A_ROPE], early)
            cqT = m.sb("cqT", [P, 4, 512], early)
            ckvT = m.sb("ckvT", [P, 2, 512], early)
            kr2 = m.sb("kr2", [P, NT, 2, A_ROPE], early)
            latent_inputs(m, layer, streams, cq, ckv)
            latent_norms(m, j, tq, cq, ckv, kr2, cqT, ckvT, krT)
            latent_qkv(m, layer, tq, cqT, ckvT, cq, qnT, qrT, v)
        knT = m.hT
        attention(m, own, A_H, streams, (A_NOPE + A_ROPE) ** -0.5,
                  lambda h, t: [(qnT[:, h, t * P:(t + 1) * P], knT[:, h, :]),
                                (qrT[h % 2 * 64:h % 2 * 64 + 64, h // 2, t * P:(t + 1) * P],
                                 krT[h % 2 * 64:h % 2 * 64 + 64, :])],
                  lambda h, kt: v[:, kt, h * A_V:(h + 1) * A_V],
                  lambda h: (slice(0, P), h))
        project_out(m, f"a_out{layer}", tq, True)


def latent_inputs(m, layer, streams, cq, ckv):
    nc, ps = m.nc, m.ps
    tq = NX * streams
    panels = m.take(4, f"a_cq{layer}", f"a_ckv{layer}", f"a_gate{layer}", f"a_gate{layer}")
    with m.step() as block:
        ready, read = m.sig("latent_in_psum"), m.sig("latent_read")
        gates = Gates(m, tq * P, m.scratch)
        groups = [(0, t) for t in range(tq)] + [(1, t) for t in range(NT)]
        width = (A_QR, A_KVR + A_ROPE)

        @block.sync
        def _(sp):
            for n in range(2):
                sp.wait_ge(ready.sem, ready.at(tq + n * NT))
                m.load_next(sp, panels[n])
            for n in range(2):
                sp.wait_ge(gates.ready.sem, gates.ready.at(4 * n + 4))
                m.load_next(sp, panels[2 + n])

        @block.tensor
        def _(pe):
            for g, (kind, t) in enumerate(groups):
                i, w = panels[kind], width[kind]
                if t == 0:
                    pe.wait_ge(*m.loaded(i))
                if g >= 4:
                    pe.wait_ge(read.sem, read.at(g - 3))
                for k in range(KD):
                    last = nc.tensor.matmul(ps[g % 4][:, 0:w], m.hT[:, k, t * P:(t + 1) * P],
                                            m.slot(i)[:, k * w:(k + 1) * w], start=k == 0, stop=k == KD - 1)
                last.then_inc(ready.sem, ready.one())
            for g in range(8):
                i = panels[2 + g // 4]
                if g % 4 == 0:
                    pe.wait_ge(*m.loaded(i))
                gates.matmuls(pe, g, i, g % 4)

        @block.scalar
        def _(act):
            for g, (kind, t) in enumerate(groups):
                act.wait_ge(ready.sem, ready.at(g + 1))
                src, c = ps[g % 4], (t + NT if kind == 0 else t)
                nc.scalar.activation((cq if kind == 0 else ckv)[:, t, :], src[:, 0:width[kind]], ACT.Copy)
                w = A_QR if kind == 0 else A_KVR
                after(act, nc.scalar.activation(m.junk[:, 0:w], src[:, 0:w], ACT.Square, accum_out=m.sums[:, c:c + 1]),
                      m.sig("act_chain"))
                nc.scalar.nop().then_inc(read.sem, read.one())
            for g in range(8):
                gates.exponential(act, g)

        @block.vector
        def _(dve):
            for g in range(8):
                gates.finish(dve, g, m.gT[:, g, 0:tq * P], True)


def latent_norms(m, j, tq, cq, ckv, kr2, cqT, ckvT, krT):
    nc, ps = m.nc, m.ps
    cols = NT + tq
    with m.step() as block:
        normed, turned, read = m.sig("latent_normed"), m.sig("latentT_in_psum"), m.sig("latentT_read")

        @block.vector
        def _(dve):
            chain = m.sig("dve_chain")
            after(dve, nc.vector.tensor_scalar(m.sums[:, 0:NT], m.sums[:, 0:NT], A_QR / A_KVR, None, ALU.mult), chain)
            variance(m, dve, m.var[:, 0:cols], m.sums[:, 0:cols], 1.0 / A_QR)
            fine_rstd(m, dve, m.var[:, 0:cols], m.rstd[:, 0:cols], m.tmp[:, 0:cols])
            for t in range(NT):
                lat = ckv[:, t, 0:A_KVR]
                kr = ckv[:, t, A_KVR:].rearrange("p (h x c) -> p h x c", h=1, x=2)
                nc.vector.tensor_scalar(lat, lat, m.rstd[:, t:t + 1], None, ALU.mult)
                if t < NX:
                    after(dve, rope(m, dve, kr2[:, t, 0:1, :].rearrange("p h (x c) -> p h x c", x=2), kr, t, 1), chain)
                    last = nc.vector.tensor_copy(kr2[:, t, 1, :], kr2[:, t, 0, :])
                else:
                    nc.vector.tensor_copy(kr2[:, t, 0, :], ckv[:, t, A_KVR:])
                    last = nc.vector.tensor_copy(kr2[:, t, 1, :], ckv[:, t, A_KVR:])
                if t < tq:
                    after(dve, last, chain)
                    last = nc.vector.tensor_scalar(cq[:, t, :], cq[:, t, :], m.rstd[:, NT + t:NT + t + 1], None, ALU.mult)
                after(dve, last, chain)
                nc.vector.nop().then_inc(normed.sem, normed.one())

        @block.tensor
        def _(pe):
            for t in range(NT):
                pe.wait_ge(normed.sem, normed.at(t + 1))
                if t >= 2:
                    pe.wait_ge(read.sem, read.at(t - 1))
                a, b = ps[2 * (t % 2)], ps[2 * (t % 2) + 1]
                for c in range(2):
                    nc.tensor.transpose(a[:, c * P:(c + 1) * P], ckv[:, t, c * P:(c + 1) * P], m.ident[:, :])
                last = nc.tensor.transpose(a[:, 2 * P:3 * P], kr2[:, t].rearrange("p a c -> p (a c)"), m.ident[:, :])
                if t < tq:
                    for c in range(4):
                        last = nc.tensor.transpose(b[:, c * P:(c + 1) * P], cq[:, t, c * P:(c + 1) * P], m.ident[:, :])
                last.then_inc(turned.sem, turned.one())

        @block.scalar
        def _(act):
            rough_rstd(m, act, m.var[:, 0:cols], m.rstd[:, 0:cols])
            for t in range(NT):
                act.wait_ge(turned.sem, turned.at(t + 1))
                a, b, tok = ps[2 * (t % 2)], ps[2 * (t % 2) + 1], slice(t * P, (t + 1) * P)
                for c in range(2):
                    nc.scalar.activation(ckvT[:, c, tok], a[:, c * P:(c + 1) * P], ACT.Copy,
                                         scale=m.vec("a_g_kv", 2 * j + c, 2 * j + c + 1))
                last = nc.scalar.activation(krT[:, tok], a[:, 2 * P:3 * P], ACT.Copy)
                if t < tq:
                    for c in range(4):
                        last = nc.scalar.activation(cqT[:, c, tok], b[:, c * P:(c + 1) * P], ACT.Copy,
                                                    scale=m.vec("a_g_q", 4 * j + c, 4 * j + c + 1))
                last.then_inc(read.sem, read.one())


def latent_qkv(m, layer, tq, cqT, ckvT, qr, qnT, qrT, v):
    nc, ps = m.nc, m.ps
    panels = m.take(3, f"a_q{layer}", f"a_q{layer}", f"a_kv{layer}")
    knT = m.hT
    wide = A_NOPE + A_ROPE
    with m.step() as block:
        a_ready, a_read = m.sig("heads_in_psum"), m.sig("heads_read")
        d_ready, d_read = m.sig("token_part_in_psum"), m.sig("token_part_read")

        @block.sync
        def _(sp):
            for n, count in enumerate((tq, 2 * tq, 2 * tq + 2 * NT)):
                sp.wait_ge(d_ready.sem, d_ready.at(count))
                m.load_next(sp, panels[n])

        @block.tensor
        def _(pe):
            a = d = 0
            for n in range(2):
                i = panels[n]
                w = m.slot(i)[:, 0:4 * 768].rearrange("p (k h c) -> p k h c", k=4, h=4)
                pe.wait_ge(*m.loaded(i))
                for h in range(4):
                    if a >= 4:
                        pe.wait_ge(a_read.sem, a_read.at(a - 3))
                    for k in range(4):
                        last = nc.tensor.matmul(ps[a % 4][:, 0:tq * P], w[:, k, h, 0:A_NOPE], cqT[:, k, 0:tq * P],
                                                start=k == 0, stop=k == 3)
                    last.then_inc(a_ready.sem, a_ready.one())
                    a += 1
                for t in range(tq):
                    if d >= 4:
                        pe.wait_ge(d_read.sem, d_read.at(d - 3))
                    for k in range(4):
                        last = nc.tensor.matmul(ps[4 + d % 4][:, 0:N].rearrange("p (h c) -> p h c", h=4),
                                                cqT[:, k, t * P:(t + 1) * P], w[:, k, :, A_NOPE:wide],
                                                start=k == 0, stop=k == 3)
                    last.then_inc(d_ready.sem, d_ready.one())
                    d += 1
            i = panels[2]
            w = m.slot(i)[:, :].rearrange("p (k h c) -> p k h c", k=2, h=A_H)
            pe.wait_ge(*m.loaded(i))
            for h in range(A_H):
                pe.wait_ge(a_read.sem, a_read.at(a - 3))
                for k in range(2):
                    last = nc.tensor.matmul(ps[a % 4][:, :], w[:, k, h, 0:A_NOPE], ckvT[:, k, :], start=k == 0, stop=k == 1)
                last.then_inc(a_ready.sem, a_ready.one())
                a += 1
            for t in range(NT):
                for half in range(2):
                    if d >= 4:
                        pe.wait_ge(d_read.sem, d_read.at(d - 3))
                    for k in range(2):
                        last = nc.tensor.matmul(ps[4 + d % 4][:, :].rearrange("p (h c) -> p h c", h=4),
                                                ckvT[:, k, t * P:(t + 1) * P], w[:, k, 4 * half:4 * half + 4, A_NOPE:],
                                                start=k == 0, stop=k == 1)
                    last.then_inc(d_ready.sem, d_ready.one())
                    d += 1
            for t in range(tq):
                pe.wait_ge(d_read.sem, d_read.at(d - 3))
                for c in range(4):
                    last = nc.tensor.transpose(ps[4 + d % 4][:, c * P:(c + 1) * P], qr[:, t, c * P:(c + 1) * P], m.ident[:, :])
                last.then_inc(d_ready.sem, d_ready.one())
                d += 1

        @block.scalar
        def _(act):
            for a in range(2 * A_H):
                act.wait_ge(a_ready.sem, a_ready.at(a + 1))
                if a < A_H:
                    last = nc.scalar.activation(qnT[:, a, 0:tq * P], ps[a % 4][:, 0:tq * P], ACT.Copy)
                else:
                    last = nc.scalar.activation(knT[:, a - A_H, :], ps[a % 4][:, :], ACT.Copy)
                last.then_inc(a_read.sem, a_read.one())

        @block.vector
        def _(dve):
            d = 0
            for n in range(2):
                for t in range(tq):
                    dve.wait_ge(d_ready.sem, d_ready.at(d + 1))
                    src = ps[4 + d % 4][:, 0:N].rearrange("p (h x c) -> p h x c", h=4, x=2)
                    dst = qr[:, t, n * N:(n + 1) * N].rearrange("p (h x c) -> p h x c", h=4, x=2)
                    if t < NX:
                        last = rope(m, dve, dst, src, t, 4)
                    else:
                        last = nc.vector.tensor_copy(dst, src)
                    last.then_inc(d_read.sem, d_read.one())
                    dve.wait_ge(d_read.sem, d_read.at(d + 1))
                    d += 1
            for t in range(NT):
                for half in range(2):
                    dve.wait_ge(d_ready.sem, d_ready.at(d + 1))
                    nc.vector.tensor_copy(v[:, t, half * 512:(half + 1) * 512], ps[4 + d % 4][:, :]) \
                        .then_inc(d_read.sem, d_read.one())
                    d += 1
            for t in range(tq):
                dve.wait_ge(d_ready.sem, d_ready.at(d + 1))
                nc.vector.tensor_copy(qrT[:, :, t * P:(t + 1) * P], ps[4 + d % 4][:, :].rearrange("p (c t) -> p c t", c=4)) \
                    .then_inc(d_read.sem, d_read.one())
                d += 1


def window_layer(m):
    norm_to_channels(m, NT, m.hT, lambda s, k: m.scale1[:, s, k:k + 1], lambda s, k: m.shift[:, s, k:k + 1])
    with ExitStack() as own:
        m.gT = m.sb("gT", [P, KD, 512], own)
        qT = m.hT
        kT = m.sb("kT", [P, B_KVH, 512], own)
        v2 = m.sb("v2", [P, NT, B_KVH, 2, B_HD], own)
        mask = m.sb("band", [P, NX, P], own)
        with ExitStack() as early:
            q = m.sb("q", [P, NT, D], early)
            k2 = m.sb("k2", [P, NT, B_KVH, 2, B_HD], early)
            window_inputs(m, q, k2, v2, mask)
            window_turn(m, q, k2, qT, kT)
        attention(m, own, B_H, 2, B_HD ** -0.5,
                  lambda h, t: [(qT[h % 2 * 64:h % 2 * 64 + 64, h // 2, t * P:(t + 1) * P],
                                 kT[h % 2 * 64:h % 2 * 64 + 64, h // 4, :])],
                  lambda h, kt: v2[:, kt, h // 4].rearrange("p a c -> p (a c)"),
                  lambda h: (slice(h % 2 * 64, h % 2 * 64 + 64), h // 2),
                  mask=mask, sink=m.rows[:, ROW["sink"][0]:ROW["sink"][1]])
        project_out(m, "b_out", NT, True)


def window_inputs(m, q, k2, v2, mask):
    nc, ps = m.nc, m.ps
    panels = m.take(5, *["b_in"] * 5)
    with ExitStack() as own, m.step() as block:
        gate_tmp = m.sb("gate_tmp", [P, 2, 512], own)
        ready, read = m.sig("latent_in_psum"), m.sig("latent_read")
        landed = m.sig("mask_landed")
        gates = Gates(m, 512, gate_tmp)
        groups = [(n, t) for n in range(3) for t in range(NT)]

        @block.sync
        def _(sp):
            sp.dma_start(mask[:], m.dram["band"]).then_inc(landed.sem, landed.sixteen())
            for n in range(3):
                sp.wait_ge(ready.sem, ready.at((n + 1) * NT))
                m.load_next(sp, panels[n])
            for n in range(2):
                sp.wait_ge(gates.ready.sem, gates.ready.at(4 * n + 4))
                m.load_next(sp, panels[3 + n])
            sp.wait_ge(landed.sem, landed.at(16))

        @block.tensor
        def _(pe):
            for g, (n, t) in enumerate(groups):
                i = panels[n]
                if t == 0:
                    pe.wait_ge(*m.loaded(i))
                if g >= 4:
                    pe.wait_ge(read.sem, read.at(g - 3))
                for k in range(KD):
                    last = nc.tensor.matmul(ps[g % 4][:, :], m.hT[:, k, t * P:(t + 1) * P],
                                            m.slot(i)[:, k * 512:(k + 1) * 512], start=k == 0, stop=k == KD - 1)
                last.then_inc(ready.sem, ready.one())
            for g in range(8):
                i = panels[3 + g // 4]
                if g % 4 == 0:
                    pe.wait_ge(*m.loaded(i))
                gates.matmuls(pe, g, i, g % 4)

        @block.scalar
        def _(act):
            for g in range(8):
                gates.exponential(act, g)

        @block.vector
        def _(dve):
            chain = m.sig("dve_chain")
            nc.vector.tensor_scalar(m.neg_sink[:], m.rows[:, ROW["sink"][0]:ROW["sink"][1]], -1.0, None, ALU.mult)
            for g, (n, t) in enumerate(groups):
                dve.wait_ge(ready.sem, ready.at(g + 1))
                bank = ps[g % 4]
                if n < 2:
                    heads, part = 8, bank[:, :]
                    dst = q[:, t, n * 512:(n + 1) * 512].rearrange("p (h x c) -> p h x c", h=8, x=2)
                else:
                    heads, part = B_KVH, bank[:, 0:N]
                    dst = k2[:, t, :, 0, :].rearrange("p h (x c) -> p h x c", x=2)
                src = part.rearrange("p (h x c) -> p h x c", h=heads, x=2)
                last = rope(m, dve, dst, src, t, heads) if t < NX else nc.vector.tensor_copy(dst, src)
                if n == 2:
                    after(dve, last, chain)
                    nc.vector.tensor_copy(k2[:, t, :, 1, :], k2[:, t, :, 0, :])
                    for a in range(2):
                        last = nc.vector.tensor_copy(v2[:, t, :, a, :], bank[:, N:512].rearrange("p (h c) -> p h c", h=B_KVH))
                last.then_inc(read.sem, read.one())
                dve.wait_ge(read.sem, read.at(g + 1))
            for g in range(8):
                gates.finish(dve, g, m.gT[:, g, :], True)


def window_turn(m, q, k2, qT, kT):
    nc, ps = m.nc, m.ps
    with m.step() as block:
        turned, read = m.sig("qT_in_psum"), m.sig("qT_read")
        groups = [(c, t) for t in range(NT) for c in range(3)]

        @block.tensor
        def _(pe):
            for g, (c, t) in enumerate(groups):
                if g >= 4:
                    pe.wait_ge(read.sem, read.at(g - 3))
                for b in range(4):
                    src = q[:, t, c * 512 + b * P:c * 512 + (b + 1) * P] if c < 2 else \
                        k2[:, t, b].rearrange("p a c -> p (a c)")
                    last = nc.tensor.transpose(ps[g % 4][:, b * P:(b + 1) * P], src, m.ident[:, :])
                last.then_inc(turned.sem, turned.one())

        @block.scalar
        def _(act):
            for g, (c, t) in enumerate(groups):
                act.wait_ge(turned.sem, turned.at(g + 1))
                dst = (qT[:, 4 * c:4 * c + 4, :] if c < 2 else kT)[:, :, t * P:(t + 1) * P]
                nc.scalar.activation(dst, ps[g % 4][:, :].rearrange("p (b t) -> p b t", b=4), ACT.Copy) \
                    .then_inc(read.sem, read.one())


def conv_layer(m):
    norm_to_channels(m, NT, m.hT, lambda s, k: m.scale1[:, s, k:k + 1], lambda s, k: m.shift[:, s, k:k + 1])
    with ExitStack() as own:
        m.gT = m.sb("gT", [P, KD, 512], own)
        u = m.sb("u", [P, NT, 3, D], own)
        conv_inputs(m, u)
        with ExitStack() as mid:
            dft = m.sb("dft", [P, NX, 6 * P], mid)
            idft = m.sb("idft", [P, 4, N], mid)
            zT = m.sb("zT", [C_EMB, N], mid)
            h1 = m.sb("ffn1", [C_FFN, N], mid)
            h2 = m.sb("ffn2", [C_FFN, N], mid)
            spec = m.sb("filter_spectrum", [P, 5, 512], mid)
            conv_ffn(m, mid, dft, idft, zT, h1, h2)
            decay, w3 = m.take(2, "c_decay", "c_w3")
            for order in range(2):
                for half in range(2):
                    conv_filters(m, order, half, dft, h2, spec, decay, w3)
                    conv_apply(m, order, half, dft, idft, spec, u)
        conv_gate(m, u)
        project_out(m, "c_out", NT, True)


def conv_inputs(m, u):
    nc, ps = m.nc, m.ps
    panels = m.take(8, *["c_in"] * 8)
    CH = 24
    with ExitStack() as own, m.step() as block:
        uc = m.sb("short", [P, 2, 512], own)
        ready, mid, conved = m.sig("heads_in_psum"), m.sig("centre_tap_ready"), m.sig("short_conv_ready")
        turned, read = m.sig("qT_in_psum"), m.sig("qT_read")
        gates = Gates(m, 512, m.scratch)

        @block.sync
        def _(sp):
            for n in range(6):
                sp.wait_ge(ready.sem, ready.at(4 * n + 4))
                m.load_next(sp, panels[n])
            for n in range(2):
                sp.wait_ge(gates.ready.sem, gates.ready.at(4 * n + 4))
                m.load_next(sp, panels[6 + n])

        @block.tensor
        def _(pe):
            for g in range(CH + 1):
                if g < CH:
                    i = panels[g // 4]
                    if g % 4 == 0:
                        pe.wait_ge(*m.loaded(i))
                    if g >= 2:
                        pe.wait_ge(conved.sem, conved.at(g - 1))
                    for k in range(KD):
                        last = nc.tensor.matmul(ps[g % 2][:, :], m.slot(i)[:, k * 512 + g % 4 * P:k * 512 + (g % 4 + 1) * P],
                                                m.hT[:, k, :], start=k == 0, stop=k == KD - 1)
                    last.then_inc(ready.sem, ready.one())
                if g >= 1:
                    c = g - 1
                    pe.wait_ge(conved.sem, conved.at(c + 1))
                    if c >= 2:
                        pe.wait_ge(read.sem, read.at(c - 1))
                    for t in range(NT):
                        last = nc.tensor.transpose(ps[2 + c % 2][:, t * P:(t + 1) * P], uc[:, c % 2, t * P:(t + 1) * P], m.ident[:, :])
                    last.then_inc(turned.sem, turned.one())
            for g in range(8):
                i = panels[6 + g // 4]
                if g % 4 == 0:
                    pe.wait_ge(*m.loaded(i))
                gates.matmuls(pe, g, i, g % 4)

        @block.scalar
        def _(act):
            for g in range(CH + 1):
                if g < CH:
                    act.wait_ge(ready.sem, ready.at(g + 1))
                    if g >= 2:
                        act.wait_ge(turned.sem, turned.at(g - 1))
                    nc.scalar.activation(uc[:, g % 2, :], ps[g % 2][:, :], ACT.Identity,
                                         scale=m.vec("conv_w", CH + g, CH + g + 1), bias=m.vec("conv_b", g, g + 1)) \
                        .then_inc(mid.sem, mid.one())
                if g >= 1:
                    c = g - 1
                    act.wait_ge(turned.sem, turned.at(c + 1))
                    nc.scalar.activation(u[:, :, c // 8, c % 8 * P:(c % 8 + 1) * P],
                                         ps[2 + c % 2][:, :].rearrange("p (t c) -> p t c", t=NT), ACT.Copy) \
                        .then_inc(read.sem, read.one())
            for g in range(8):
                gates.exponential(act, g)

        @block.vector
        def _(dve):
            for g in range(CH):
                src = ps[g % 2][:, :].rearrange("p (s n) -> p s n", s=2)
                dst = uc[:, g % 2, :].rearrange("p (s n) -> p s n", s=2)
                dve.wait_ge(mid.sem, mid.at(g + 1))
                after(dve, nc.vector.scalar_tensor_tensor(out=dst[:, :, 1:N], in0=src[:, :, 0:N - 1],
                                                          scalar=m.vec("conv_w", g, g + 1), in1=dst[:, :, 1:N],
                                                          op0=ALU.mult, op1=ALU.add), m.sig("dve_chain"))
                nc.vector.scalar_tensor_tensor(out=dst[:, :, 0:N - 1], in0=src[:, :, 1:N],
                                               scalar=m.vec("conv_w", 2 * CH + g, 2 * CH + g + 1), in1=dst[:, :, 0:N - 1],
                                               op0=ALU.mult, op1=ALU.add).then_inc(conved.sem, conved.one())
            for g in range(8):
                gates.finish(dve, g, m.gT[:, g, :], True)


ROUND = 1.5 * 2.0 ** 23
TWO_PI_A = 6.28125
TWO_PI_B = float(np.float32(int((2 * math.pi - TWO_PI_A) * 2 ** 20) / 2 ** 20))
TWO_PI_C = 2 * math.pi - TWO_PI_A - TWO_PI_B


def conv_ffn(m, own, dft, idft, zT, h1, h2):
    nc, ps = m.nc, m.ps
    with m.step() as block:
        landed, ready, reduced, sines = (m.sig(n) for n in ("dft_landed", "ffn_in_psum", "angle_reduced", "sine_ready"))
        turns = m.scratch[0:C_FFN, 0, 0:N]

        @block.sync
        def _(sp):
            for dst, src in ((zT, "zT"), (dft, "dft"), (idft, "idft")):
                sp.dma_start(dst[:], m.dram[src]).then_inc(landed.sem, landed.sixteen())
            sp.wait_ge(landed.sem, landed.at(48))

        @block.tensor
        def _(pe):
            pe.wait_ge(landed.sem, landed.at(48))
            nc.tensor.matmul(ps[0][0:C_FFN, 0:N], m.vec("f_w1")[0:C_EMB, :], zT[:, :], start=True, stop=True) \
                .then_inc(ready.sem, ready.one())
            pe.wait_ge(sines.sem, sines.at(1))
            nc.tensor.matmul(ps[1][0:C_FFN, 0:N], m.vec("f_w2")[0:C_FFN, :], h1[:, :], start=True, stop=True) \
                .then_inc(ready.sem, ready.one())

        @block.vector
        def _(dve):
            chain = m.sig("dve_chain")
            for i, (bias, h) in enumerate((("f_b1", h1), ("f_b2", h2))):
                dve.wait_ge(ready.sem, ready.at(i + 1))
                after(dve, nc.vector.tensor_scalar(h[:], ps[i][0:C_FFN, 0:N], m.vec(bias)[0:C_FFN, :],
                                                   m.vec("f_freq")[0:C_FFN, :], ALU.add, ALU.mult), chain)
                after(dve, nc.vector.tensor_scalar(turns, h[:], 1.0 / (2 * math.pi), ROUND, ALU.mult, ALU.add), chain)
                after(dve, nc.vector.tensor_scalar(turns, turns, ROUND, None, ALU.subtract), chain)
                for part in (TWO_PI_A, TWO_PI_B, TWO_PI_C):
                    after(dve, nc.vector.scalar_tensor_tensor(out=h[:], in0=turns, scalar=-part, in1=h[:],
                                                              op0=ALU.mult, op1=ALU.add), chain)
                nc.vector.tensor_scalar(h[:], h[:], 3.1415925, -3.1415925, ALU.min, ALU.max) \
                    .then_inc(reduced.sem, reduced.one())

        @block.scalar
        def _(act):
            for i, h in enumerate((h1, h2)):
                act.wait_ge(reduced.sem, reduced.at(i + 1))
                nc.scalar.activation(h[:], h[:], ACT.Sin).then_inc(sines.sem, sines.one())


def conv_filters(m, order, half, dft, h2, spec, decay, w3):
    nc, ps = m.nc, m.ps
    both = m.hT[:, 0:2 * NX, :].rearrange("p (t w) c -> p t w c", t=NX)
    cols = slice(half * 512, (half + 1) * 512)
    with m.step() as block:
        ready, made, spectral, copied = (m.sig(n) for n in ("filter_in_psum", "filter_ready", "spectrum_in_psum", "spectrum_copied"))
        paired = m.sig("filters_paired")
        w = m.slot(w3)[0:C_FFN, :].rearrange("p (w o c) -> p w o c", w=2, o=2)
        fall = m.slot(decay)[:, 0:2 * D].rearrange("p (t c) -> p t c", t=NX)
        bias = m.slot(decay)[0:1, 2 * D:4 * D].rearrange("p (o c) -> p o c", o=2)
        groups = [(t, way) for t in range(NX) for way in range(2)]
        tiles = [(0, 0), (1, 0), (4, 1), (3, 1), (5, 0)]

        @block.tensor
        def _(pe):
            pe.wait_ge(*m.loaded(w3))
            for g, (t, way) in enumerate(groups):
                nc.tensor.matmul(ps[g][:, :], h2[:, t * P:(t + 1) * P], w[:, way, order, cols],
                                 start=True, stop=True).then_inc(ready.sem, ready.one())
            pe.wait_ge(paired.sem, paired.at(1))
            for g in range(5):
                if g >= 4:
                    pe.wait_ge(copied.sem, copied.at(g - 3))
                col, way = tiles[g]
                for t in range(NX):
                    last = nc.tensor.matmul(ps[4 + g % 4][:, :], dft[:, t, col * P:(col + 1) * P],
                                            both[:, t, way, :], start=t == 0, stop=t == NX - 1)
                last.then_inc(spectral.sem, spectral.one())

        @block.vector
        def _(dve):
            chain = m.sig("dve_chain")
            dve.wait_ge(*m.loaded(decay))
            for g, (t, way) in enumerate(groups):
                dve.wait_ge(ready.sem, ready.at(g + 1))
                nc.vector.tensor_tensor(both[:, t, way, :], ps[g][:, :], fall[:, t, cols], ALU.mult).then_inc(made.sem, made.one())
            dve.wait_ge(made.sem, made.at(len(groups)))
            for t in range(NX):
                total, other = m.scratch[:, t, 0:512], both[:, t, 1, :]
                after(dve, nc.vector.tensor_tensor(total, both[:, t, 0, :], other, ALU.add), chain)
                after(dve, nc.vector.tensor_tensor(other, both[:, t, 0, :], other, ALU.subtract), chain)
                after(dve, nc.vector.tensor_copy(both[:, t, 0, :], total), chain)
            after(dve, nc.vector.tensor_tensor(both[0:1, 0, 0, :], both[0:1, 0, 0, :], bias[:, order, cols], ALU.add), chain)
            nc.vector.nop().then_inc(paired.sem, paired.one())

        @block.scalar
        def _(act):
            for g in range(5):
                act.wait_ge(spectral.sem, spectral.at(g + 1))
                nc.scalar.activation(spec[:, g, :], ps[4 + g % 4][:, :], ACT.Copy) \
                    .then_inc(copied.sem, copied.one())

        if order == 1 and half == 1:
            @block.sync
            def _(sp):
                sp.wait_ge(paired.sem, paired.at(1))
                m.load_next(sp, decay)
                sp.wait_ge(ready.sem, ready.at(len(groups)))
                m.load_next(sp, w3)


def conv_apply(m, order, half, dft, idft, spec, u):
    nc, ps = m.nc, m.ps
    cols = slice(half * 512, (half + 1) * 512)
    with m.step() as block:
        prod = m.hT[:].rearrange("p (a f) c -> p a f c", a=2)
        ta = m.scratch[:, 0, 0:512]
        tb = m.scratch[:, 1, 0:512]
        ready, read = m.sig("spectrum_in_psum"), m.sig("spectrum_used")
        back, taken = m.sig("convolved_in_psum"), m.sig("convolved_taken")
        units = [0, 1]
        recipe = [((0, 0), (2, 2), ALU.subtract), ((1, 1), (3, 3), ALU.subtract),
                  ((0, 2), (2, 4), ALU.add), ((1, 3), (3, 1), ALU.add)]

        @block.tensor
        def _(pe):
            for step in range(len(units) + 1):
                if step < len(units):
                    s = units[step]
                    if step >= 1:
                        pe.wait_ge(read.sem, read.at(4 * step))
                    for f in range(4):
                        for t in range(NX):
                            last = nc.tensor.matmul(ps[f][:, :], dft[:, t, f * P:(f + 1) * P],
                                                    u[:, NX * s + t, 0, cols], start=t == 0, stop=t == NX - 1)
                    last.then_inc(ready.sem, ready.one())
                if step >= 1:
                    v = step - 1
                    pe.wait_ge(read.sem, read.at(4 * v + 4))
                    for t in range(NX):
                        if v >= 2:
                            pe.wait_ge(taken.sem, taken.at(2 * (v - 2) + t + 1))
                        for f in range(4):
                            last = nc.tensor.matmul(ps[4 + 2 * (v % 2) + t][:, :], idft[:, f, t * P:(t + 1) * P],
                                                    prod[:, v % 2, f, :], start=f == 0, stop=f == 3)
                        last.then_inc(back.sem, back.one())

        @block.vector
        def _(dve):
            chain = m.sig("dve_chain")

            def take(v):
                s = units[v]
                for t in range(NX):
                    dve.wait_ge(back.sem, back.at(2 * v + t + 1))
                    nc.vector.tensor_tensor(u[:, NX * s + t, 0, cols], ps[4 + 2 * (v % 2) + t][:, :],
                                            u[:, NX * s + t, 1 + order, cols], ALU.mult).then_inc(taken.sem, taken.one())

            for v, s in enumerate(units):
                dve.wait_ge(ready.sem, ready.at(v + 1))
                if v >= 2:
                    dve.wait_ge(back.sem, back.at(2 * (v - 2) + 2))
                for f, ((ua, ka), (ub, kb), op) in enumerate(recipe):
                    nc.vector.tensor_tensor(ta, ps[ua][:, :], spec[:, ka, :], ALU.mult)
                    after(dve, nc.vector.tensor_tensor(tb, ps[ub][:, :], spec[:, kb, :], ALU.mult), chain)
                    nc.vector.tensor_tensor(prod[:, v % 2, f, :], ta, tb, op).then_inc(read.sem, read.one())
                    dve.wait_ge(read.sem, read.at(4 * v + f + 1))
                if v >= 1:
                    take(v - 1)
            take(len(units) - 1)


def conv_gate(m, u):
    nc, ps = m.nc, m.ps
    with m.step() as block:
        turned, read = m.sig("qT_in_psum"), m.sig("qT_read")
        groups = [(t, c) for t in range(NT) for c in range(2)]

        @block.tensor
        def _(pe):
            for g, (t, c) in enumerate(groups):
                if g >= 4:
                    pe.wait_ge(read.sem, read.at(g - 3))
                for b in range(4):
                    k = 4 * c + b
                    last = nc.tensor.transpose(ps[g % 4][:, b * P:(b + 1) * P], u[:, t, 0, k * P:(k + 1) * P], m.ident[:, :])
                last.then_inc(turned.sem, turned.one())

        @block.vector
        def _(dve):
            for g, (t, c) in enumerate(groups):
                dve.wait_ge(turned.sem, turned.at(g + 1))
                dst = m.gT[:, 4 * c:4 * c + 4, t * P:(t + 1) * P]
                nc.vector.tensor_tensor(dst, ps[g % 4][:, :].rearrange("p (b t) -> p b t", b=4), dst, ALU.mult) \
                    .then_inc(read.sem, read.one())


def second_mixer(m):
    hT = m.hT
    norm_to_channels(m, NX, hT, lambda s, k: m.vec("g_mix", k, k + 1), None)
    with ExitStack() as own:
        m.gT = hT[:, :, N:2 * N]
        go = m.sb("open_o", [P, M_H, N], own)
        ga = m.sb("open_a", [P, KD, N], own)
        gb = m.sb("open_b", [P, KD, N], own)
        up = m.sb("u_pool", [P, 4, POOL_PAD + N], own)
        qk = m.sb("qk_raw", [P, 2 * M_H, CONV_K - 1 + N], own)
        qkT = m.sb("qkT", [P, 2 * M_H, N], own)
        v = m.sb("v_mlstm", [P, NX, M_H * M_HD], own)
        zif = m.sb("z_if", [P, NX, 2 * M_H], own)
        poolT = m.sb("poolT", [P, 4, N], own)
        hmT = m.sb("hmT", [P, M_H, N], own)
        tri = m.sb("tri", [P, NX, N], own)
        causal = m.sb("causal", [P, NX, N], own)
        counts = m.sb("counts", [P, 4, N], own)
        fcum = m.sb("forget_sum", [P, NX, M_H], own)
        rbc = m.sb("log_input", [P, M_H, N], own)
        second_inputs(m, go, ga, gb, up, qk, v, zif, tri, causal, counts)
        second_convs(m, up, qk, qkT, poolT, counts)
        mlstm_gates(m, own, zif, tri, fcum, rbc)
        mlstm_heads(m, own, qkT, v, causal, fcum, rbc, go, hmT)
        second_merge(m, poolT, hmT, ga, gb)
        project_out(m, "s_out", NX, False)


def second_inputs(m, go, ga, gb, up, qk, v, zif, tri, causal, counts):
    nc, ps = m.nc, m.ps
    panels = m.take(9, *["s_in"] * 9)
    w_if = m.vec("w_if").rearrange("p (k c) -> p k c", k=KD)
    with m.step() as block:
        ready, read, landed = m.sig("latent_in_psum"), m.sig("latent_read"), m.sig("masks_landed")
        gates = Gates(m, N, m.scratch)
        groups = [(n, j) for n in range(3) for j in range(4)] + [(3, t) for t in range(NX)] + [(4, t) for t in range(NX)]
        out_of = [go, ga, ga, gb, gb]

        @block.sync
        def _(sp):
            for dst, src in ((tri, "tri"), (causal, "causal"), (counts, "counts")):
                sp.dma_start(dst[:], m.dram[src]).then_inc(landed.sem, landed.sixteen())
            for n, count in enumerate((4, 8, 12, 12 + NX)):
                sp.wait_ge(ready.sem, ready.at(count))
                m.load_next(sp, panels[n])
            for n in range(5):
                sp.wait_ge(gates.ready.sem, gates.ready.at(4 * n + 4))
                m.load_next(sp, panels[4 + n])
            sp.wait_ge(landed.sem, landed.at(48))

        @block.tensor
        def _(pe):
            for g, (n, j) in enumerate(groups):
                i = panels[min(n, 3)]
                if j == 0 and n < 4:
                    pe.wait_ge(*m.loaded(i))
                if g >= 4:
                    pe.wait_ge(read.sem, read.at(g - 3))
                for k in range(KD):
                    tok = m.hT[:, k, j * P:(j + 1) * P]
                    flags = dict(start=k == 0, stop=k == KD - 1)
                    if n < 3:
                        last = nc.tensor.matmul(ps[g % 4][:, 0:N], m.slot(i)[:, k * 512 + j * P:k * 512 + (j + 1) * P],
                                                m.hT[:, k, 0:N], **flags)
                    elif n == 3:
                        last = nc.tensor.matmul(ps[g % 4][:, :], tok, m.slot(i)[:, k * 512:(k + 1) * 512], **flags)
                    else:
                        last = nc.tensor.matmul(ps[g % 4][:, 0:2 * M_H], tok, w_if[:, k, :], **flags)
                last.then_inc(ready.sem, ready.one())
            for g in range(20):
                i = panels[4 + g // 4]
                if g % 4 == 0:
                    pe.wait_ge(*m.loaded(i))
                gates.matmuls(pe, g, i, g % 4)

        @block.scalar
        def _(act):
            for g, (n, j) in enumerate(groups):
                act.wait_ge(ready.sem, ready.at(g + 1))
                dst, src = ((up[:, j, POOL_PAD:], ps[g % 4][:, 0:N]), (qk[:, j, CONV_K - 1:], ps[g % 4][:, 0:N]),
                            (qk[:, M_H + j, CONV_K - 1:], ps[g % 4][:, 0:N]), (v[:, min(j, 1), :], ps[g % 4][:, :]),
                            (zif[:, min(j, 1), :], ps[g % 4][:, 0:2 * M_H]))[n]
                nc.scalar.activation(dst, src, ACT.Copy).then_inc(read.sem, read.one())
            for g in range(20):
                gates.exponential(act, g)

        @block.vector
        def _(dve):
            nc.vector.memset(up[:, :, 0:POOL_PAD], 0.0)
            nc.vector.memset(qk[:, :, 0:CONV_K - 1], 0.0)
            for g in range(20):
                which = out_of[g // 4]
                at = g % 4 + (4 if g // 4 in (2, 4) else 0)
                gates.finish(dve, g, which[:, at, :], False)


def second_convs(m, up, qk, qkT, poolT, counts):
    nc, ps = m.nc, m.ps
    (panel,) = m.take(1, "s_pool")
    with ExitStack() as own, m.step() as block:
        sums = [m.sb(f"window{i}", [P, POOL_PAD + N], own) for i in range(2)]
        expo = m.sb("silu_exp", [P, 2 * M_H, N], own)
        diffs = m.sb("pool_diff", [P, 4, N], own)
        conved, expd = m.sig("short_conv_ready"), m.sig("gate_exp_ready")
        diffed, ready = m.sig("pool_diff_ready"), m.sig("pooled_in_psum")

        @block.sync
        def _(sp):
            sp.wait_ge(ready.sem, ready.at(4))
            m.load_next(sp, panel)

        @block.vector
        def _(dve):
            chain = m.sig("dve_chain")
            for j in range(2 * M_H):
                name, h = ("conv_q", j) if j < M_H else ("conv_k", j - M_H)
                last = nc.vector.tensor_scalar(qkT[:, j, :], qk[:, j, 0:N], m.vec(name, h, h + 1), None, ALU.mult)
                for tap in range(1, CONV_K):
                    after(dve, last, chain)
                    last = nc.vector.scalar_tensor_tensor(out=qkT[:, j, :], in0=qk[:, j, tap:tap + N],
                                                          scalar=m.vec(name, tap * M_H + h, tap * M_H + h + 1),
                                                          in1=qkT[:, j, :], op0=ALU.mult, op1=ALU.add)
                last.then_inc(conved.sem, conved.one())
            for g, window in enumerate(POOL_WINDOWS):
                src, width = up[:, g, :], 1
                buf = 0
                while width < window:
                    dst = sums[buf]
                    after(dve, nc.vector.tensor_copy(dst[:, 0:width], src[:, 0:width]), chain)
                    after(dve, nc.vector.tensor_tensor(dst[:, width:], src[:, width:], src[:, 0:POOL_PAD + N - width], ALU.add), chain)
                    src, buf, width = dst[:, :], 1 - buf, 2 * width
                mean = sums[buf][:, 0:N]
                after(dve, nc.vector.tensor_tensor(mean, src[:, POOL_PAD:], counts[:, g, :], ALU.mult), chain)
                after(dve, nc.vector.tensor_tensor(diffs[:, g, :], mean, up[:, g, POOL_PAD:], ALU.subtract), chain)
                nc.vector.nop().then_inc(diffed.sem, diffed.one())
            dve.wait_ge(expd.sem, expd.at(1))
            after(dve, nc.vector.tensor_scalar(expo[:], expo[:], 1.0, None, ALU.add), chain)
            after(dve, nc.vector.reciprocal(expo[:], expo[:]), chain)
            nc.vector.tensor_tensor(qkT[:], qkT[:], expo[:], ALU.mult)

        @block.scalar
        def _(act):
            act.wait_ge(conved.sem, conved.at(2 * M_H))
            nc.scalar.activation(expo[:], qkT[:], ACT.Exp, scale=-1.0).then_inc(expd.sem, expd.one())
            for g in range(4):
                act.wait_ge(ready.sem, ready.at(g + 1))
                nc.scalar.activation(poolT[:, g, :], ps[g][:, 0:N], ACT.Copy, scale=m.vec("pool_scale", g, g + 1))

        @block.tensor
        def _(pe):
            pe.wait_ge(*m.loaded(panel))
            for g in range(4):
                pe.wait_ge(diffed.sem, diffed.at(g + 1))
                nc.tensor.matmul(ps[g][:, 0:N], m.slot(panel)[:, g * P:(g + 1) * P], diffs[:, g, :], start=True, stop=True) \
                    .then_inc(ready.sem, ready.one())


def mlstm_gates(m, own, zif, tri, fcum, rbc):
    nc, ps = m.nc, m.ps
    with ExitStack() as mine, m.step() as block:
        lf = m.sb("log_forget", [P, NX, M_H], mine)
        tmp = m.sb("log_tmp", [P, NX, M_H], mine)
        rT = m.sb("log_inputT", [M_H, N], mine)
        biased, softened, summed = m.sig("gates_biased"), m.sig("softplus_ready"), m.sig("log_forget_ready")
        cum, rin, rturn, rcopied, spread = (m.sig(n) for n in ("forget_sum_in_psum", "log_input_ready", "log_inputT_in_psum",
                                                              "log_inputT_copied", "log_input_spread"))
        i_pre, f_pre = zif[:, :, 0:M_H], zif[:, :, M_H:]

        @block.vector
        def _(dve):
            chain = m.sig("dve_chain")
            bias = m.rows[:, ROW["b_if"][0]:ROW["b_if"][1]].unsqueeze(1).broadcast_to([P, NX, 2 * M_H])
            after(dve, nc.vector.tensor_tensor(zif[:], zif[:], bias, ALU.add), chain)
            after(dve, nc.vector.tensor_scalar(tmp[:], f_pre, -1.0, None, ALU.mult), chain)
            nc.vector.tensor_tensor(tmp[:], tmp[:], f_pre, ALU.min).then_inc(biased.sem, biased.one())
            dve.wait_ge(softened.sem, softened.at(1))
            after(dve, nc.vector.tensor_scalar(lf[:], f_pre, 0.0, None, ALU.min), chain)
            nc.vector.tensor_tensor(lf[:], lf[:], tmp[:], ALU.subtract).then_inc(summed.sem, summed.one())
            dve.wait_ge(cum.sem, cum.at(1))
            after(dve, nc.vector.tensor_copy(fcum[:].rearrange("p t h -> p (t h)"), ps[0][:, 0:NX * M_H]), chain)
            nc.vector.tensor_tensor(tmp[:], i_pre, fcum[:], ALU.subtract).then_inc(rin.sem, rin.one())
            dve.wait_ge(rturn.sem, rturn.at(1))
            nc.vector.tensor_copy(rT[:], ps[1][0:M_H, 0:N]).then_inc(rcopied.sem, rcopied.one())
            dve.wait_ge(spread.sem, spread.at(1))
            for half in range(2):
                nc.vector.tensor_copy(rbc[:, 2 * half:2 * half + 2, :], ps[2 + half][:, :].rearrange("p (h s) -> p h s", h=2))

        @block.scalar
        def _(act):
            act.wait_ge(biased.sem, biased.at(1))
            after(act, nc.scalar.activation(tmp[:], tmp[:], ACT.Exp), m.sig("act_chain"))
            nc.scalar.activation(tmp[:], tmp[:], ACT.Ln, bias=1.0).then_inc(softened.sem, softened.one())

        @block.tensor
        def _(pe):
            pe.wait_ge(summed.sem, summed.at(1))
            for t in range(NX):
                for s in range(NX):
                    last = nc.tensor.matmul(ps[0][:, t * M_H:(t + 1) * M_H], tri[:, s, t * P:(t + 1) * P], lf[:, s, :],
                                            start=s == 0, stop=s == NX - 1)
            last.then_inc(cum.sem, cum.one())
            pe.wait_ge(rin.sem, rin.at(1))
            for t in range(NX):
                last = nc.tensor.transpose(ps[1][0:M_H, t * P:(t + 1) * P], tmp[:, t, :], m.ident[:, :])
            last.then_inc(rturn.sem, rturn.one())
            pe.wait_ge(rcopied.sem, rcopied.at(1))
            for h in range(M_H):
                last = nc.tensor.matmul(ps[2 + h // 2][:, h % 2 * N:(h % 2 + 1) * N], m.sel[0:M_H, h, :], rT[:, :],
                                        start=True, stop=True)
            last.then_inc(spread.sem, spread.one())


def mlstm_heads(m, own, qkT, v, causal, fcum, rbc, go, hmT):
    nc, ps = m.nc, m.ps
    units = [(t, h) for t in range(NX) for h in range(M_H)]
    U = len(units)
    with ExitStack() as mine, m.step() as block:
        masked = m.sb("masked_log", [P, 2, N], mine)
        weight = m.sb("weights", [P, 2, N], mine)
        swT = m.sb("scoresT", [P, 2, NX, P], mine)
        cols = m.sb("mlstm_cols", [P, 2, 8], mine)
        hm = m.sb("h_mlstm", [P, NX, M_H, M_HD], mine)
        stats = m.sb("head_stats", [P, 3, NX * M_H], mine)
        scored, argued, weighed = m.sig("scores_in_psum"), m.sig("row_max_ready"), m.sig("probs_ready")
        normed, turned, copied = m.sig("probs_normalised"), m.sig("probsT_in_psum"), m.sig("probsT_copied")
        outed, taken = m.sig("attended_in_psum"), m.sig("attended_taken")
        centred, back, finished = m.sig("heads_normalised"), m.sig("headsT_in_psum"), m.sig("headsT_read")
        col = lambda u, c: cols[:, u % 2, c:c + 1]
        MX, NEG, STAB, NQ, DEN, RDEN, POS = range(7)

        @block.tensor
        def _(pe):
            for step in range(U + 1):
                if step < U:
                    u = step
                    t, h = units[u]
                    if u >= 2:
                        pe.wait_ge(normed.sem, normed.at(u - 1))
                    nc.tensor.matmul(ps[u % 2][:, 0:N], qkT[:, h, t * P:(t + 1) * P], qkT[:, M_H + h, :], start=True, stop=True) \
                        .then_inc(scored.sem, scored.one())
                if step >= 1:
                    u = step - 1
                    t, h = units[u]
                    pe.wait_ge(normed.sem, normed.at(u + 1))
                    if u >= 2:
                        pe.wait_ge(copied.sem, copied.at(u - 1))
                    for s in range(NX):
                        last = nc.tensor.transpose(ps[2 + u % 2][:, s * P:(s + 1) * P], weight[:, u % 2, s * P:(s + 1) * P],
                                                   m.ident[:, :])
                    last.then_inc(turned.sem, turned.one())
                    pe.wait_ge(copied.sem, copied.at(u + 1))
                    if u >= 2:
                        pe.wait_ge(taken.sem, taken.at(u - 1))
                    for s in range(NX):
                        last = nc.tensor.matmul(ps[4 + u % 2][:, 0:M_HD], swT[:, u % 2, s, :], v[:, s, h * M_HD:(h + 1) * M_HD],
                                                start=s == 0, stop=s == NX - 1)
                    last.then_inc(outed.sem, outed.one())
            pe.wait_ge(centred.sem, centred.at(1))
            for h in range(M_H):
                if h >= 2:
                    pe.wait_ge(finished.sem, finished.at(h - 1))
                for t in range(NX):
                    last = nc.tensor.transpose(ps[6 + h % 2][:, t * P:(t + 1) * P], hm[:, t, h, :], m.ident[:, :])
                last.then_inc(back.sem, back.one())

        @block.scalar
        def _(act):
            for step in range(U + 1):
                if step < U:
                    u = step
                    act.wait_ge(argued.sem, argued.at(u + 1))
                    nc.scalar.activation(col(u, STAB), col(u, STAB), ACT.Exp, scale=-1.0)
                    if u >= 2:
                        act.wait_ge(turned.sem, turned.at(u - 1))
                    nc.scalar.activation(weight[:, u % 2, :], masked[:, u % 2, :], ACT.Exp, bias=col(u, NEG)) \
                        .then_inc(weighed.sem, weighed.one())
                if step >= 1:
                    u = step - 1
                    act.wait_ge(turned.sem, turned.at(u + 1))
                    if u >= 2:
                        act.wait_ge(outed.sem, outed.at(u - 1))
                    nc.scalar.activation(swT[:, u % 2].rearrange("p s t -> p (s t)"), ps[2 + u % 2][:, 0:N], ACT.Copy) \
                        .then_inc(copied.sem, copied.one())
            n = NX * M_H
            rough_rstd(m, act, stats[:, 1, 0:n], stats[:, 2, 0:n])

        @block.vector
        def _(dve):
            chain = m.sig("dve_chain")
            for step in range(U + 2):
                if step < U:
                    u = step
                    t, h = units[u]
                    if u >= 2:
                        dve.wait_ge(weighed.sem, weighed.at(u - 1))
                    after(dve, nc.vector.tensor_tensor(masked[:, u % 2, :], rbc[:, h, :], causal[:, t, :], ALU.add), chain)
                    after(dve, nc.vector.tensor_reduce(col(u, MX), masked[:, u % 2, :], AX, ALU.max), chain)
                    after(dve, nc.vector.tensor_scalar(col(u, POS), col(u, MX), 0.0, None, ALU.max), chain)
                    nc.vector.tensor_scalar(col(u, NEG), col(u, POS), -1.0, None, ALU.mult)
                    nc.vector.tensor_tensor(col(u, STAB), col(u, POS), fcum[:, t, h:h + 1], ALU.add) \
                        .then_inc(argued.sem, argued.one())
                if 1 <= step <= U:
                    u = step - 1
                    dve.wait_ge(weighed.sem, weighed.at(u + 1))
                    dve.wait_ge(scored.sem, scored.at(u + 1))
                    w = weight[:, u % 2, :]
                    after(dve, nc.vector.scalar_tensor_tensor(out=w, in0=ps[u % 2][:, 0:N], scalar=M_HD ** -0.5, in1=w,
                                                              op0=ALU.mult, op1=ALU.mult), chain)
                    after(dve, nc.vector.tensor_reduce(col(u, NQ), w, AX, ALU.add), chain)
                    after(dve, nc.vector.tensor_scalar(col(u, DEN), col(u, NQ), -1.0, None, ALU.mult), chain)
                    after(dve, nc.vector.tensor_tensor(col(u, DEN), col(u, DEN), col(u, NQ), ALU.max), chain)
                    after(dve, nc.vector.tensor_tensor(col(u, DEN), col(u, DEN), col(u, STAB), ALU.max), chain)
                    after(dve, nc.vector.reciprocal(col(u, RDEN), col(u, DEN)), chain)
                    after(dve, nc.vector.tensor_scalar(w, w, col(u, RDEN), None, ALU.mult), chain)
                    nc.vector.nop().then_inc(normed.sem, normed.one())
                if step >= 2:
                    u = step - 2
                    t, h = units[u]
                    dve.wait_ge(outed.sem, outed.at(u + 1))
                    nc.vector.tensor_copy(hm[:, t, h, :], ps[4 + u % 2][:, 0:M_HD]).then_inc(taken.sem, taken.one())
            dve.wait_ge(taken.sem, taken.at(U))
            all_h = hm[:].rearrange("p t h c -> p (t h) c")
            n = NX * M_H
            mean, var, rstd = stats[:, 0, :], stats[:, 1, :], stats[:, 2, :]
            wide = [P, n, M_HD]
            sq = m.scratch[:].rearrange("p a b -> p (a b)")[:, 0:n * M_HD].rearrange("p (n c) -> p n c", n=n)
            after(dve, nc.vector.tensor_reduce(mean, all_h, AX, ALU.add), chain)
            after(dve, nc.vector.tensor_scalar(mean, mean, 1.0 / M_HD, None, ALU.mult), chain)
            after(dve, nc.vector.tensor_tensor(all_h, all_h, mean.unsqueeze(2).broadcast_to(wide), ALU.subtract), chain)
            after(dve, nc.vector.tensor_tensor(sq, all_h, all_h, ALU.mult), chain)
            after(dve, nc.vector.tensor_reduce(var, sq, AX, ALU.add), chain)
            variance(m, dve, var, var, 1.0 / M_HD)
            fine_rstd(m, dve, var, rstd, m.tmp[:, 0:n])
            after(dve, nc.vector.tensor_tensor(all_h, all_h, rstd.unsqueeze(2).broadcast_to(wide), ALU.mult), chain)
            nc.vector.nop().then_inc(centred.sem, centred.one())
            for h in range(M_H):
                dve.wait_ge(back.sem, back.at(h + 1))
                nc.vector.scalar_tensor_tensor(out=hmT[:, h, :], in0=ps[6 + h % 2][:, 0:N], scalar=m.vec("g_head", h, h + 1),
                                               in1=go[:, h, :], op0=ALU.mult, op1=ALU.mult).then_inc(finished.sem, finished.one())


def second_merge(m, poolT, hmT, ga, gb):
    nc, ps = m.nc, m.ps
    panels = m.take(2, "s_br_a", "s_br_b")
    with m.step() as block:
        ready, used = m.sig("branch_in_psum"), m.sig("branch_used")
        groups = [(c, b) for b in range(2) for c in range(KD)]

        @block.sync
        def _(sp):
            for n in range(2):
                sp.wait_ge(ready.sem, ready.at((n + 1) * KD))
                m.load_next(sp, panels[n])

        @block.tensor
        def _(pe):
            for g, (c, b) in enumerate(groups):
                if c == 0:
                    pe.wait_ge(*m.loaded(panels[b]))
                if g >= 4:
                    pe.wait_ge(used.sem, used.at(g - 3))
                for k in range(4):
                    last = nc.tensor.matmul(ps[g % 4][:, 0:N], m.slot(panels[b])[:, k * D + c * P:k * D + (c + 1) * P],
                                            (poolT, hmT)[b][:, k, :], start=k == 0, stop=k == 3)
                last.then_inc(ready.sem, ready.one())

        @block.vector
        def _(dve):
            for g, (c, b) in enumerate(groups):
                dve.wait_ge(ready.sem, ready.at(g + 1))
                gate = (ga, gb)[b][:, c, :]
                dst = m.gT[:, c, :] if b == 0 else gate
                last = nc.vector.tensor_tensor(dst, ps[g % 4][:, 0:N], gate, ALU.mult)
                if b == 1:
                    after(dve, last, m.sig("dve_chain"))
                    last = nc.vector.tensor_tensor(m.gT[:, c, :], m.gT[:, c, :], gate, ALU.add)
                last.then_inc(used.sem, used.one())


def route(m, spread):
    nc, ps = m.nc, m.ps
    norm_to_channels(m, NX, m.hT, lambda s, k: m.vec("g_ffn", k, k + 1), None)
    w_route = m.vec("w_route").rearrange("p (k c) -> p k c", k=KD)
    with ExitStack() as own, m.step() as block:
        logits = m.sb("logits", [P, NX, N_ROUTE], own)
        glog = m.sb("group_logits", [P, NX, 8], own)
        elog = m.sb("group_experts", [P, NX, N_EXP], own)
        top = m.sb("top", [P, NX, 2, 8], own)
        where = m.sb("where", [P, NX, 2, 8], own, dt=U32)
        wheref = m.sb("wheref", [P, NX, 2, 8], own)
        onehot = m.sb("group_onehot", [P, NX, 8], own)
        c = m.sb("route_cols", [P, NX, 8], own)
        gates = m.sb("gates", [P, NX, N_EXP], own)
        gatesT = m.sb("gatesT", [N_EXP, N], own)
        sel = m.sb("selector", [N_EXP, N_EXP, P], own)
        landed, ready, argued, expd = m.sig("selector_landed"), m.sig("logits_in_psum"), m.sig("route_args_ready"), m.sig("route_exps_ready")
        gated, turned, copied, wide, taken = (m.sig(n) for n in ("gates_ready", "gatesT_in_psum", "gatesT_copied", "gate_rows_in_psum", "gate_rows_taken"))
        iota = m.rows[:, ROW["iota"][0]:ROW["iota"][1]]

        @block.sync
        def _(sp):
            for i in range(N_DENSE + RING, N_DENSE + MOE_RING):
                m.issue(sp, i)
            sp.dma_start(sel[:], m.dram["selector"]).then_inc(landed.sem, landed.sixteen())

        @block.tensor
        def _(pe):
            for t in range(NX):
                for k in range(KD):
                    last = nc.tensor.matmul(ps[t][:, 0:N_ROUTE], m.hT[:, k, t * P:(t + 1) * P], w_route[:, k, :],
                                            start=k == 0, stop=k == KD - 1)
                last.then_inc(ready.sem, ready.one())
            pe.wait_ge(gated.sem, gated.at(1))
            for t in range(NX):
                last = nc.tensor.transpose(ps[2][0:N_EXP, t * P:(t + 1) * P], gates[:, t, :], m.ident[:, :])
            last.then_inc(turned.sem, turned.one())
            pe.wait_ge(landed.sem, landed.at(16))
            pe.wait_ge(copied.sem, copied.at(1))
            for e in range(N_EXP):
                if e >= 4:
                    pe.wait_ge(taken.sem, taken.at(e - 3))
                nc.tensor.matmul(ps[4 + e % 4][:, 0:N], sel[:, e, :], gatesT[:, :], start=True, stop=True) \
                    .then_inc(wide.sem, wide.one())

        @block.scalar
        def _(act):
            act.wait_ge(argued.sem, argued.at(1))
            nc.scalar.activation(onehot[:], glog[:], ACT.Exp)
            nc.scalar.activation(c[:, :, 1:2], c[:, :, 0:1], ACT.Exp).then_inc(expd.sem, expd.one())
            for e in range(N_EXP):
                act.wait_ge(wide.sem, wide.at(e + 1))
                nc.scalar.activation(spread[:, e, :], ps[4 + e % 4][:, 0:N], ACT.Copy).then_inc(taken.sem, taken.one())

        @block.vector
        def _(dve):
            chain = m.sig("dve_chain")
            v = nc.vector
            bias = m.rows[:, ROW["b_route"][0]:ROW["b_route"][1]]
            dve.wait_ge(ready.sem, ready.at(NX))
            for t in range(NX):
                after(dve, v.tensor_tensor(logits[:, t, :], ps[t][:, 0:N_ROUTE], bias, ALU.add), chain)
            after(dve, v.memset(glog[:], MASKED), chain)
            after(dve, v.tensor_copy(glog[:, :, 0:N_GROUPS], logits[:, :, 0:N_GROUPS]), chain)
            for t in range(NX):
                after(dve, v.max(top[:, t, 0, :], glog[:, t, :]), chain)
                after(dve, v.max_index(where[:, t, 0, :], top[:, t, 0, :], glog[:, t, :]), chain)
                after(dve, v.tensor_copy(wheref[:, t, 0, :], where[:, t, 0, :]), chain)
                after(dve, v.tensor_scalar(onehot[:, t, 0:N_GROUPS], iota[:, 0:N_GROUPS], wheref[:, t, 0, 0:1], None, ALU.is_equal), chain)
                mine = onehot[:, t, 0:N_GROUPS].unsqueeze(2).broadcast_to([P, N_GROUPS, PER_GROUP])
                e3 = elog[:, t, :].rearrange("p (g e) -> p g e", g=N_GROUPS)
                after(dve, v.tensor_tensor(e3, logits[:, t, N_GROUPS:].rearrange("p (g e) -> p g e", g=N_GROUPS), mine, ALU.mult), chain)
                after(dve, v.tensor_scalar(onehot[:, t, 0:N_GROUPS], onehot[:, t, 0:N_GROUPS], -1.0, -MASKED, ALU.add, ALU.mult), chain)
                after(dve, v.tensor_tensor(e3, e3, mine, ALU.add), chain)
                after(dve, v.max(top[:, t, 1, :], elog[:, t, :]), chain)
                after(dve, v.max_index(where[:, t, 1, :], top[:, t, 1, :], elog[:, t, :]), chain)
                after(dve, v.tensor_copy(wheref[:, t, 1, :], where[:, t, 1, :]), chain)
                after(dve, v.tensor_scalar(glog[:, t, :], glog[:, t, :], top[:, t, 0, 0:1], None, ALU.subtract), chain)
                after(dve, v.tensor_tensor(c[:, t, 0:1], top[:, t, 1, 1:2], top[:, t, 1, 0:1], ALU.subtract), chain)
            v.nop().then_inc(argued.sem, argued.one())
            dve.wait_ge(expd.sem, expd.at(1))
            for t in range(NX):
                after(dve, v.tensor_reduce(c[:, t, 2:3], onehot[:, t, :], AX, ALU.add), chain)
                after(dve, v.tensor_scalar(c[:, t, 3:4], c[:, t, 1:2], 1.0, None, ALU.add), chain)
                after(dve, v.tensor_tensor(c[:, t, 3:4], c[:, t, 3:4], c[:, t, 2:3], ALU.mult), chain)
                after(dve, v.reciprocal(c[:, t, 4:5], c[:, t, 3:4]), chain)
                after(dve, v.tensor_tensor(c[:, t, 5:6], c[:, t, 4:5], c[:, t, 1:2], ALU.mult), chain)
                after(dve, v.tensor_scalar(gates[:, t, :], iota, wheref[:, t, 1, 0:1], c[:, t, 4:5], ALU.is_equal, ALU.mult), chain)
                after(dve, v.tensor_scalar(elog[:, t, :], iota, wheref[:, t, 1, 1:2], c[:, t, 5:6], ALU.is_equal, ALU.mult), chain)
                after(dve, v.tensor_tensor(gates[:, t, :], gates[:, t, :], elog[:, t, :], ALU.add), chain)
            v.nop().then_inc(gated.sem, gated.one())
            dve.wait_ge(turned.sem, turned.at(1))
            v.tensor_copy(gatesT[:], ps[2][0:N_EXP, 0:N]).then_inc(copied.sem, copied.one())


def experts(m):
    nc, ps = m.nc, m.ps
    with ExitStack() as own:
        spread = m.sb("gate_rows", [P, N_EXP, N], own)
        route(m, spread)
        with m.step() as block:
            ex = m.sb("expert_exp", [P, 2, N], own)
            hidT = m.sb("hiddenT", [P, 2, 4, N], own)
            zero = m.sb("zero", [P, 512], own)
            PAIRS = N_EXP // 2
            gate_in, up_in, expd, hidden = (m.sig(n) for n in ("expert_gate_in_psum", "expert_up_in_psum", "expert_exp_ready", "hidden_ready"))
            downed, summed, zeroed = m.sig("expert_down_done"), m.sig("experts_summed"), m.sig("zero_ready")
            slot_loaded = [m.sig(f"slot{s}_loaded") for s in range(MOE_RING)]
            first_load = [m.loaded(N_DENSE + s)[1] for s in range(MOE_RING)]
            xT = m.hT
            bank = lambda kind, c: ps[4 + 2 * (c % 2) + kind][:, 0:N]

            @block.sync
            def _(sp):
                def reload(pair, a):
                    for kind, (done, per_expert) in enumerate(((gate_in, 4), (up_in, 4), (downed, 1))):
                        s = 3 * a + kind
                        sp.wait_ge(done.sem, (pair - 1) * (2 * per_expert) + done.base + (a + 1) * per_expert)
                        sp.dma_start(m.slots[s][:], m.dram["panels"][bass.ds(pair * MOE_RING + N_DENSE + s, 1)]
                                     .rearrange("o p c -> (o p) c")).then_inc(slot_loaded[s].sem, 16)
                with sp.Fori(1, PAIRS) as pair:
                    for a in range(2):
                        reload(pair, a)

            @block.tensor
            def _(pe):
                pe.wait_ge(zeroed.sem, zeroed.at(1))
                for b in range(4):
                    nc.tensor.matmul(ps[b][:, :], zero[:, 0:P], zero[:, :], start=True, stop=False)
                def expert(pair, a, first):
                    for c in range(4):
                        if not (first and c < 2):
                            pe.wait_ge(hidden.sem, pair * 8 + hidden.base + 4 * a + c - 1)
                        for kind, ready in ((0, gate_in), (1, up_in)):
                            s = 3 * a + kind
                            if c == 0:
                                pe.wait_ge(slot_loaded[s].sem, pair * 16 + first_load[s])
                            for k in range(KD):
                                last = nc.tensor.matmul(bank(kind, c), m.slots[s][:, k * 512 + c * P:k * 512 + (c + 1) * P], xT[:, k, 0:N],
                                                        start=k == 0, stop=k == KD - 1)
                            last.then_inc(ready.sem, 1)
                    s = 3 * a + 2
                    pe.wait_ge(slot_loaded[s].sem, pair * 16 + first_load[s])
                    for c in range(4):
                        pe.wait_ge(hidden.sem, pair * 8 + hidden.base + 4 * a + c + 1)
                        for t in range(NX):
                            for n in range(2):
                                last = nc.tensor.matmul(ps[2 * t + n][:, :], hidT[:, a, c, t * P:(t + 1) * P],
                                                        m.slots[s][:, c * D + n * 512:c * D + (n + 1) * 512],
                                                        start=False, stop=False)
                    last.then_inc(downed.sem, 1)
                expert(0, 0, True)
                expert(0, 1, False)
                with pe.Fori(1, PAIRS) as pair:
                    for a in range(2):
                        expert(pair, a, False)
                for b in range(4):
                    last = nc.tensor.matmul(ps[b][:, :], zero[:, 0:P], zero[:, :], start=False, stop=True)
                last.then_inc(summed.sem, summed.one())

            @block.scalar
            def _(act):
                def expert(pair, a, first):
                    for c in range(4):
                        act.wait_ge(gate_in.sem, pair * 8 + gate_in.base + 4 * a + c + 1)
                        if not (first and c < 2):
                            act.wait_ge(hidden.sem, pair * 8 + hidden.base + 4 * a + c - 1)
                        nc.scalar.activation(ex[:, c % 2, :], bank(0, c), ACT.Exp, scale=-1.0).then_inc(expd.sem, 1)
                expert(0, 0, True)
                expert(0, 1, False)
                with act.Fori(1, PAIRS) as pair:
                    for a in range(2):
                        expert(pair, a, False)

            @block.vector
            def _(dve):
                nc.vector.memset(zero[:], 0.0).then_inc(zeroed.sem, zeroed.one())
                chain = m.sig("expert_chain")
                def expert(pair, a, first):
                    e = pair * 2 + a
                    row = spread[:, e, :] if first else spread[:, bass.ds(e, 1), :].rearrange("p o n -> p (o n)")
                    for c in range(4):
                        t = ex[:, c % 2, :]
                        h = hidT[:, a, c, :]
                        before = pair * (8 * 4) + chain.base + (4 * a + c) * 4
                        dve.wait_ge(expd.sem, pair * 8 + expd.base + 4 * a + c + 1)
                        nc.vector.tensor_scalar(t, t, 1.0, None, ALU.add).then_inc(chain.sem, 1)
                        dve.wait_ge(chain.sem, before + 1)
                        nc.vector.reciprocal(t, t).then_inc(chain.sem, 1)
                        dve.wait_ge(chain.sem, before + 2)
                        nc.vector.tensor_tensor(t, bank(0, c), t, ALU.mult).then_inc(chain.sem, 1)
                        dve.wait_ge(chain.sem, before + 3)
                        nc.vector.tensor_tensor(t, t, row, ALU.mult).then_inc(chain.sem, 1)
                        dve.wait_ge(chain.sem, before + 4)
                        dve.wait_ge(up_in.sem, pair * 8 + up_in.base + 4 * a + c + 1)
                        if not first:
                            dve.wait_ge(downed.sem, pair * 2 + downed.base + a - 1)
                        nc.vector.tensor_tensor(h, bank(1, c), t, ALU.mult).then_inc(hidden.sem, 1)
                expert(0, 0, True)
                expert(0, 1, True)
                with dve.Fori(1, PAIRS) as pair:
                    for a in range(2):
                        expert(pair, a, False)
                dve.wait_ge(summed.sem, summed.at(1))
                for t in range(NX):
                    for n in range(2):
                        part = m.x[:, t, n * 512:(n + 1) * 512]
                        nc.vector.tensor_tensor(part, part, ps[2 * t + n][:, :], ALU.add)


def finish(m):
    nc = m.nc
    with m.step() as block:
        g_final = m.sb("g_final", [P, D])
        squares, done, stored = m.sig("squares_summed"), m.sig("out_ready"), m.sig("out_stored")
        landed = m.sig("g_final_landed")

        @block.scalar
        def _(act):
            for t in range(NX):
                after(act, nc.scalar.activation(m.scratch[:, t, :], m.x[:, t, :], ACT.Square,
                                                accum_out=m.sums[:, t:t + 1]), m.sig("act_chain"))
            nc.scalar.nop().then_inc(squares.sem, squares.one())
            rough_rstd(m, act, m.var[:, 0:NX], m.rstd[:, 0:NX])

        @block.vector
        def _(dve):
            dve.wait_ge(squares.sem, squares.at(1))
            variance(m, dve, m.var[:, 0:NX], m.sums[:, 0:NX], 1.0 / D)
            fine_rstd(m, dve, m.var[:, 0:NX], m.rstd[:, 0:NX], m.tmp[:, 0:NX])
            dve.wait_ge(landed.sem, landed.at(16))
            for t in range(NX):
                nc.vector.scalar_tensor_tensor(out=m.scratch[:, t, :], in0=m.x[:, t, :], scalar=m.rstd[:, t:t + 1],
                                               in1=g_final[:],
                                               op0=ALU.mult, op1=ALU.mult).then_inc(done.sem, done.one())

        @block.sync
        def _(sp):
            sp.dma_start(g_final[:], m.dram["g_final"]).then_inc(landed.sem, landed.sixteen())
            for t in range(NX):
                sp.wait_ge(done.sem, done.at(t + 1))
                sp.dma_start(m.dram["out"][0, t * P:(t + 1) * P, :], m.scratch[:, t, :]).then_inc(stored.sem, stored.sixteen())
            sp.wait_ge(stored.sem, stored.at(16 * NX))


def build(nc, dram):
    with ExitStack() as stack:
        m = Core(nc, stack, dram)
        m.vecs = m.sb("vecs", [P, VEC["width"]])
        m.cst = m.sb("cst", [P, CST["width"]])
        m.rows = m.sb("rows", [P, ROW["width"]])
        m.x = m.sb("x_tok", [P, NT, D])
        m.hT = m.sb("hT", [P, KD, 512])
        m.scratch = m.sb("scratch", [P, 2, D])
        m.junk = m.sb("junk", [P, 512])
        m.gate = m.sb("gate_rows_all", [P, 2, D])
        m.scale1 = m.sb("scale1", [P, 2, KD])
        m.shift = m.sb("shift", [P, 2, KD])
        m.cond = m.sb("cond", [P, 2 * KD])
        m.neg_sink = m.sb("neg_sink", [P, B_H])
        m.sums, m.var, m.rstd, m.tmp = (m.sb(n, [P, 8]) for n in ("sums", "var", "rstd", "tmp8"))
        m.slots = [m.sb(f"slot{i}", [P, SLOT]) for i in range(RING)]
        cst = lambda name: m.cst[:, CST[name][0]:CST[name][1]]
        m.ident = cst("ident")
        m.cos = cst("cos").rearrange("p (t c) -> p t c", t=NX)
        m.sin = cst("sin").rearrange("p (t c) -> p t c", t=NX)
        m.sel = cst("sel").rearrange("p (h q) -> p h q", h=4)
        load_constants(m)
        for layer in range(DEPTH):
            modulation(m, layer)
            if layer % 3 == 0:
                latent_layer(m, layer)
            elif layer % 3 == 1:
                window_layer(m)
            else:
                conv_layer(m)
        second_mixer(m)
        m.slots += [m.sb(f"slot{i}", [P, SLOT]) for i in range(RING, MOE_RING)]
        experts(m)
        finish(m)


def by_channel(a):
    a = np.asarray(a)
    return np.moveaxis(a.reshape(-1, P), 0, 1)


def k_major(w, cols=None):
    w = np.asarray(w)
    return w.reshape(w.shape[0] // P, P, w.shape[1]).transpose(1, 0, 2).reshape(P, -1)


def pad(a, rows=P):
    a = np.asarray(a)
    return np.concatenate([a, np.zeros((rows - a.shape[0],) + a.shape[1:], a.dtype)], 0)


def constants():
    f = np.float32
    tok = np.arange(N)
    inv = ROPE_BASE ** (-np.arange(0, 32, 2) / 32.0)
    ang = np.concatenate([(tok // GRID_W)[:, None] * inv, (tok % GRID_W)[:, None] * inv], 1)
    by_tile = lambda a: a.reshape(NX, P, -1).transpose(1, 0, 2).reshape(P, -1)
    sel = np.zeros((P, 4, P))
    for h in range(4):
        sel[h, h] = 1
    cst = np.concatenate([np.eye(P), by_tile(np.cos(ang)), by_tile(np.sin(ang)), sel.reshape(P, -1)], 1)
    q, k = np.arange(P)[:, None], np.arange(P)[None, :]
    band = np.stack([np.where(k + P - q <= B_WINDOW, 0.0, MASKED), np.where(q + P - k <= B_WINDOW, 0.0, MASKED)], 1)
    n2 = 2 * N
    freq = np.arange(N)
    turn = 2 * np.pi * np.outer(tok, freq) / n2
    cos, sin, nyq = np.cos(turn), np.sin(turn), (-1.0) ** tok
    sin_n, cos_n = sin.copy(), cos[:, 0:P].copy()
    sin_n[:, 0], cos_n[:, 0] = nyq, nyq
    dft = np.concatenate([cos, sin_n, sin[:, 0:P], cos_n], 1)
    idft = np.concatenate([2 * cos.T / n2, 2 * sin.T / n2], 0)
    idft[0] /= 2
    idft[N] = nyq / n2
    t = np.linspace(0, 1, N)[:, None]
    w = 2 * np.pi / N * tok[:, None]
    bands = np.linspace(1e-4, C_BANDS - 1, C_BANDS)[None]
    z = np.concatenate([t, np.cos(bands * w), -np.sin(bands * w)], -1)
    decay = np.exp(-t * np.abs(np.linspace(C_MIN_DECAY, C_MAX_DECAY, D)))
    tri = (tok[:, None] <= tok[None, :]) * 1.0
    counts = np.stack([1.0 / np.minimum(tok + 1, wdw) for wdw in POOL_WINDOWS])
    selector = np.zeros((N_EXP, N_EXP, P))
    selector[np.arange(N_EXP), np.arange(N_EXP)] = 1
    out = dict(cst=cst, band=band, zT=z.T, decay=by_tile(decay), dft=by_tile(dft).reshape(P, NX, 6 * P),
               idft=idft.reshape(4, P, N).transpose(1, 0, 2), tri=by_tile(tri).reshape(P, NX, N),
               causal=by_tile(np.where(tri.T > 0, 0.0, MASKED)).reshape(P, NX, N),
               counts=np.broadcast_to(counts, (P, 4, N)), selector=selector)
    return {k: np.ascontiguousarray(a, f) for k, a in out.items()}


def lay_out(i):
    a = {k: np.asarray(v) for k, v in i.items()}
    cst = constants()
    panels = []

    def add(name, w):
        w = w.reshape(P, -1)
        assert w.shape[1] <= SLOT and panel_plan()[len(panels)][1] == w.shape[1], (name, w.shape)
        panels.append(w)

    for layer in range(DEPTH):
        for n in range(6):
            add("mod", k_major(a["w_mod"][layer][:, n * 512:(n + 1) * 512]))
        if layer % 3 == 0:
            j = layer // 3
            w = a["a_w_in"][j]
            at = A_QR + A_KVR + A_ROPE
            for lo, hi in ((0, A_QR), (A_QR, at), (at, at + 512), (at + 512, at + D)):
                add("a_in", k_major(w[:, lo:hi]))
            for n in range(2):
                add("a_q", k_major(a["a_w_q"][j][:, n * 768:(n + 1) * 768]))
            add("a_kv", k_major(a["a_w_kv"][j]))
            out = a["a_w_out"][j]
        elif layer % 3 == 1:
            for n in range(5):
                add("b_in", k_major(a["b_w_in"][0][:, n * 512:(n + 1) * 512]))
            out = a["b_w_out"][0]
        else:
            for n in range(8):
                add("c_in", k_major(a["c_w_in"][0][:, n * 512:(n + 1) * 512]))
            add("c_decay", np.concatenate([cst["decay"], pad(a["c_filt_bias"][0].reshape(1, -1))], 1))
            add("c_w3", pad(a["c_f_w3"][0]))
            out = a["c_w_out"][0]
        for n in range(2):
            add("out", k_major(out[:, n * 512:(n + 1) * 512]))
    w = a["w_in_2"][0]
    at_if = 5 * 512
    cols = [n * 512 for n in range(5)] + [at_if + 8 + n * 512 for n in range(4)]
    for c in cols:
        add("s_in", k_major(w[:, c:c + 512]))
    add("s_pool", a["w_pool_2"][0].transpose(1, 0, 2))
    add("s_br_a", k_major(a["w_br_a_2"][0]))
    add("s_br_b", k_major(a["w_br_b_2"][0]))
    for n in range(2):
        add("s_out", k_major(a["w_out_2"][0][:, n * 512:(n + 1) * 512]))
    assert len(panels) == N_DENSE
    all_panels = np.zeros((N_DENSE + 3 * N_EXP, P, SLOT), np.float32)
    for n, w_ in enumerate(panels):
        all_panels[n, :, :w_.shape[1]] = w_
    ex = all_panels[N_DENSE:].reshape(N_EXP, 3, P, SLOT)
    for kind, name in enumerate(("w_e_gate_2", "w_e_up_2", "w_e_down_2")):
        e = a[name][0]
        kt = e.shape[1] // P
        ex[:, kind] = e.reshape(N_EXP, kt, P, e.shape[2]).transpose(0, 2, 1, 3).reshape(N_EXP, P, SLOT)

    vecs = np.concatenate([
        by_channel(a["g_pre"]), by_channel(a["a_g_q"]), by_channel(a["a_g_kv"]), by_channel(a["c_conv_w"][0]),
        by_channel(a["c_conv_b"][0]), pad(a["c_f_b1"][0][:, None]), pad(a["c_f_freq"][0][:, None]),
        pad(a["c_f_b2"][0][:, None]), pad(a["c_f_w1"][0]), pad(a["c_f_w2"][0]), by_channel(a["g_mix_2"][0]),
        by_channel(a["g_ffn_2"][0]), by_channel(a["g_head_2"][0]), by_channel(a["pool_scale_2"][0]),
        by_channel(a["conv_q_2"][0]), by_channel(a["conv_k_2"][0]), by_channel(a["c"][0]), by_channel(a["c_ctx"]),
        k_major(w[:, at_if:at_if + 8]), k_major(np.concatenate([a["w_rg_2"][0], a["w_re_2"][0]], 1)),
    ], 1)
    assert vecs.shape[1] == VEC["width"]
    row = np.concatenate([a["b_sink"][0], a["b_rg_2"][0], a["b_re_2"][0], a["b_if_2"][0],
                          np.arange(N_EXP, dtype=np.float32)])
    mod_rows = np.concatenate([a["b_mod"], a["g_post"]], 1)
    return dict(
        panels=all_panels, vecs=vecs, g_final=np.broadcast_to(a["g_final_2"], (P, D)), rows=np.broadcast_to(row, (P, len(row))),
        tokens=np.concatenate([a["x"][0], a["ctx"][0]], 0),
        mod_rows=np.broadcast_to(mod_rows[:, None, :], (DEPTH, 2, 4 * D)),
        **{k: cst[k] for k in ("cst", "band", "zT", "dft", "idft", "tri", "causal", "counts", "selector")})


def kernel(**inputs):
    import concourse.bacc as bacc
    from concourse.bass_utils import run_bass_kernel_spmd

    arrays = {k: np.ascontiguousarray(v) for k, v in lay_out(inputs).items()}
    nc = bacc.Bacc("TRN2", target_bir_lowering=False, num_devices=1)
    dram = {k: nc.dram_tensor(k + "_dram", v.shape, F32, kind="ExternalInput").ap() for k, v in arrays.items()}
    dram["out"] = nc.dram_tensor("out_dram", (1, N, D), F32, kind="ExternalOutput").ap()
    build(nc, dram)
    r = run_bass_kernel_spmd(nc, [{k + "_dram": v for k, v in arrays.items()}], core_ids=[0])
    return r.results[0]["out_dram"]
```

```python
import math
from contextlib import ExitStack, contextmanager

import numpy as np

import concourse.bass as bass
from concourse import mybir

F32 = mybir.dt.float32
U32 = mybir.dt.uint32
ALU = mybir.AluOpType
ACT = mybir.ActivationFunctionType
AX = mybir.AxisListType.X

P = 128
D = 1024
KD = D // P
N = 256
NX = N // P
NT = 2 * NX
DEPTH = 4
EPS = 1e-6
NORM = 2 * NT
GRID_W = 64
ROPE_BASE = 10000.0
MASKED = -1e30

A_H, A_QR, A_KVR, A_NOPE, A_ROPE, A_V = 8, 512, 256, 128, 64, 128
B_H, B_KVH, B_HD, B_WINDOW = 16, 4, 64, 128
C_BANDS = 16
C_EMB = 1 + 2 * C_BANDS
C_FFN = 64
C_MIN_DECAY = math.log(1e-2) / 1.5
C_MAX_DECAY = math.log(1e-2) / 0.3

POOL_WINDOWS = (2, 4, 8, 16)
POOL_PAD = 16
M_H, M_HD = 4, 128
CONV_K = 4
N_GROUPS, PER_GROUP = 4, 8
N_EXP = N_GROUPS * PER_GROUP
D_EXP = 512
N_ROUTE = N_GROUPS + N_EXP

SLOT = 4096
RING = 4
SLOTS = 64
MOD_SLOTS = 3
MOE_RING = 6


def columns(fields):
    at, out = 0, {}
    for name, width in fields:
        out[name] = (at, at + width)
        at += width
    out["width"] = at
    return out


VEC = columns([
    ("g_pre", DEPTH * KD), ("a_g_q", 2 * 4), ("a_g_kv", 2 * 2), ("conv_w", 3 * 24), ("conv_b", 24),
    ("f_b1", 1), ("f_freq", 1), ("f_b2", 1), ("f_w1", C_FFN), ("f_w2", C_FFN),
    ("g_mix", KD), ("g_head", 4), ("pool_scale", 4), ("conv_q", 4 * 4), ("conv_k", 4 * 4),
    ("cond", 2 * KD), ("w_if", KD * 8), ("w_route", KD * N_ROUTE),
])
ROW = columns([("sink", B_H), ("b_route", N_ROUTE), ("b_if", 8), ("iota", SLOTS)])
CST = columns([("ident", P), ("cos", NX * 32), ("sin", NX * 32), ("sel", 4 * P),
               ("mod_sel", 2 * P), ("mod_fold", 2)])


def panel_plan():
    plan = []
    for layer in range(DEPTH):
        plan += [(f"mod{layer}.{n}", SLOT) for n in range(6)]
        if layer % 3 == 0:
            plan += [(f"a_cq{layer}", SLOT), (f"a_ckv{layer}", 8 * (A_KVR + A_ROPE))]
            plan += [(f"a_gate{layer}.{n}", SLOT) for n in range(2)]
            plan += [(f"a_q{layer}.{n}", 4 * 768) for n in range(2)]
            plan += [(f"a_kv{layer}", SLOT)]
            plan += [(f"a_out{layer}.{n}", SLOT) for n in range(2)]
        elif layer % 3 == 1:
            plan += [(f"b_in.{n}", SLOT) for n in range(5)]
            plan += [(f"b_out.{n}", SLOT) for n in range(2)]
        else:
            plan += [(f"c_in.{n}", SLOT) for n in range(8)]
            plan += [("c_decay", SLOT), ("c_w3", SLOT)]
            plan += [(f"c_out.{n}", SLOT) for n in range(2)]
    plan += [(f"s_in.{n}", SLOT) for n in range(9)]
    plan += [("s_pool", 512), ("s_br_a", SLOT), ("s_br_b", SLOT)]
    plan += [(f"s_out.{n}", SLOT) for n in range(2)]
    return plan


N_DENSE = len(panel_plan())


def slot_table():
    table, at = [], 0
    for name, _ in panel_plan():
        if name.startswith("mod") and int(name[-1]) >= 6 - MOD_SLOTS:
            table.append(MOE_RING + int(name[-1]) - 6 + MOD_SLOTS)
        else:
            table.append(at % RING)
            at += 1
    return table


SLOT_TABLE = slot_table()


def slot_of(i):
    return SLOT_TABLE[i] if i < N_DENSE else (i - N_DENSE) % MOE_RING


class Signal:

    def __init__(self, sem):
        self.sem, self.total, self.base = sem, 0, 0

    def one(self):
        self.total += 1
        return 1

    def sixteen(self):
        self.total += 16
        return 16

    def at(self, n):
        return self.base + n


class Core:

    def __init__(self, nc, stack, dram):
        self.nc, self.stack, self.dram = nc, stack, dram
        self.signals, self.names = {}, {}
        self.plan = panel_plan()
        self.next_panel = 0
        self.ps = [stack.enter_context(nc.psum_tensor(f"bank{i}", [P, 512], F32)) for i in range(8)]

    def sb(self, name, shape, stack=None, dt=F32):
        again = self.names[name] = self.names.get(name, 0) + 1
        name = name if again == 1 else f"{name}_{again}"
        return (stack or self.stack).enter_context(self.nc.sbuf_tensor(name, shape, dt))

    def sig(self, name):
        if name not in self.signals:
            self.signals[name] = Signal(self.stack.enter_context(self.nc.semaphore(name)))
        return self.signals[name]

    @contextmanager
    def step(self):
        for s in self.signals.values():
            s.base = s.total
        with self.nc.Block(no_gpsimd_drain=True) as block:
            yield block

    def slot(self, i):
        s = slot_of(i)
        return self.slots[s] if s < MOE_RING else self.mod_slots[s - MOE_RING]

    def loaded(self, i):
        s = slot_of(i)
        before = sum(1 for j in range(i + 1) if slot_of(j) == s)
        return self.sig(f"slot{s}_loaded").sem, 16 * before

    def issue(self, sp, i):
        width = self.plan[i][1] if i < N_DENSE else SLOT
        g = self.sig(f"slot{slot_of(i)}_loaded")
        sp.dma_start(self.slot(i)[:, 0:width], self.dram["panels"][i, :, 0:width]).then_inc(g.sem, g.sixteen())

    def followers(self, i):
        s = slot_of(i)
        return [j for j in range(i + 1, min(i + 1 + 2 * MOE_RING, N_DENSE + MOE_RING)) if slot_of(j) == s][:1]

    def take(self, n, *names):
        got = list(range(self.next_panel, self.next_panel + n))
        self.next_panel += n
        for i, name in zip(got, names):
            assert self.plan[i][0].startswith(name), (self.plan[i], name)
        return got

    def load_next(self, sp, i):
        for j in self.followers(i):
            self.issue(sp, j)

    def vec(self, name, a=0, b=None):
        lo, hi = VEC[name]
        return self.vecs[:, lo + a:(hi if b is None else lo + b)]


def after(eng, ins, signal):
    ins.then_inc(signal.sem, signal.one())
    eng.wait_ge(signal.sem, signal.total)


def variance(m, dve, v, sums, inv_n):
    m.nc.vector.tensor_scalar(v, sums, inv_n, EPS, ALU.mult, ALU.add) \
        .then_inc(m.sig("variance_ready").sem, m.sig("variance_ready").one())


def rough_rstd(m, act, v, y, nth=1):
    s, rough = m.sig("act_chain"), m.sig("rough_rstd_ready")
    act.wait_ge(m.sig("variance_ready").sem, m.sig("variance_ready").at(nth))
    after(act, m.nc.scalar.activation(y, v, ACT.Ln), s)
    m.nc.scalar.activation(y, y, ACT.Exp, scale=-0.5).then_inc(rough.sem, rough.one())


def fine_rstd(m, dve, v, y, tmp, nth=1):
    s = m.sig("dve_chain")
    dve.wait_ge(m.sig("rough_rstd_ready").sem, m.sig("rough_rstd_ready").at(nth))
    after(dve, m.nc.vector.tensor_tensor(tmp, y, y, ALU.mult), s)
    after(dve, m.nc.vector.tensor_tensor(tmp, tmp, v, ALU.mult), s)
    after(dve, m.nc.vector.tensor_scalar(tmp, tmp, -0.5, 1.5, ALU.mult, ALU.add), s)
    after(dve, m.nc.vector.tensor_tensor(y, y, tmp, ALU.mult), s)


def load_constants(m):
    nc = m.nc
    with m.step() as block:
        landed = m.sig("constants_landed")

        @block.sync
        def _(sp):
            for dst, src in ((m.vecs, "vecs"), (m.cst, "cst")):
                sp.dma_start(dst[:], m.dram[src]).then_inc(landed.sem, landed.sixteen())
            sp.dma_start(m.rows[:], m.dram["rows"]).then_inc(landed.sem, landed.sixteen())
            for i in range(6 - MOD_SLOTS):
                m.issue(sp, i)

        @block.scalar
        def _(act):
            act.wait_ge(landed.sem, landed.at(16 * 3))
            nc.scalar.activation(m.cond[:], m.vec("cond"), ACT.Exp, scale=-1.0) \
                .then_inc(m.sig("act_chain").sem, m.sig("act_chain").one())

        @block.vector
        def _(dve):
            s = m.sig("dve_chain")
            dve.wait_ge(m.sig("act_chain").sem, m.sig("act_chain").at(1))
            nc.vector.memset(m.cond_wide[:], 0.0)
            after(dve, nc.vector.tensor_scalar(m.cond[:], m.cond[:], 1.0, None, ALU.add), s)
            after(dve, nc.vector.reciprocal(m.cond[:], m.cond[:]), s)
            after(dve, nc.vector.tensor_tensor(m.cond_wide[:, :, 0:2], m.cond[:].rearrange("p (s k) -> p k s", s=2),
                                               m.vec("cond").rearrange("p (s k) -> p k s", s=2), ALU.mult), s)


def enter_layer(m, layer, projection=None):
    nc, ps = m.nc, m.ps
    out_panels = m.take(2, projection, projection) if projection else []
    panels = m.take(6, *[f"mod{layer}.{n}" for n in range(6)])
    ringed = 6 - MOD_SLOTS
    bank = lambda t, n: ps[2 * t + n]
    norm = slice(NORM, NORM + NT)
    with ExitStack() as own:
        m.mod_slots = [m.sb(f"mod_slot{i}", [P, SLOT], own) for i in range(MOD_SLOTS)]
        given = m.sb("mod_given", [P, 4 * D], own)
        row = m.hT[:].rearrange("p k t -> p (k t)")[:, 0:3 * D]
        with m.step() as block:
            landed, chunk, chunk_read = m.sig("mod_given_landed"), m.sig("mod_chunk_in_psum"), m.sig("mod_chunk_read")
            cols, gates = m.sig("mod_columns_in_psum"), m.sig("mod_gate_in_psum")
            ready, squares, added = m.sig("projected_in_psum"), m.sig("squares_summed"), m.sig("residual_added")
            tokens = m.sig("tokens_landed")

            @block.sync
            def _(sp):
                sp.dma_start(given[:], m.dram["mod_rows"][layer]).then_inc(landed.sem, landed.sixteen())
                for i in panels[ringed:]:
                    m.issue(sp, i)
                if projection:
                    for i in out_panels:
                        sp.wait_ge(ready.sem, ready.at(NT))
                        m.load_next(sp, i)
                else:
                    for t in range(NT):
                        sp.dma_start(m.x[:, t, :], m.dram["tokens"][t * P:(t + 1) * P, :]) \
                            .then_inc(tokens.sem, tokens.sixteen())
                    m.issue(sp, 6)
                for n, i in enumerate(panels[:ringed]):
                    sp.wait_ge(chunk.sem, chunk.at(n + 1))
                    m.load_next(sp, i)

            @block.tensor
            def _(pe):
                if projection:
                    for i in out_panels:
                        pe.wait_ge(*m.loaded(i))
                    for t in range(NT):
                        for n, i in enumerate(out_panels):
                            for k in range(KD):
                                last = nc.tensor.matmul(bank(t, n)[:, :], m.gT[:, k, t * P:(t + 1) * P],
                                                        m.slot(i)[:, k * 512:(k + 1) * 512], start=k == 0, stop=k == KD - 1)
                        last.then_inc(ready.sem, ready.one())

                def column_part(n):
                    i = panels[n]
                    pe.wait_ge(*m.loaded(i))
                    if n >= 4:
                        pe.wait_ge(chunk_read.sem, chunk_read.at(n - 3))
                    for k in range(KD):
                        g = k % 4
                        last = nc.tensor.matmul(ps[n % 4][32 * g:32 * (g + 1), :], m.cond_wide[:, k, :],
                                                m.slot(i)[:, k * 512:(k + 1) * 512], start=k < 4, stop=k >= 4)
                    last.then_inc(chunk.sem, chunk.one())

                if projection:
                    pe.wait_ge(added.sem, added.at(2))
                for n in range(4):
                    column_part(n)
                pe.wait_ge(chunk_read.sem, chunk_read.at(4))
                for n in range(4, 6):
                    column_part(n)
                for j in range(2 * KD):
                    last = nc.tensor.matmul(ps[2][:, 2 * j:2 * j + 2], row[:, j * P:(j + 1) * P], m.mod_fold,
                                            start=True, stop=True)
                last.then_inc(cols.sem, cols.one())
                for n in range(2):
                    pe.wait_ge(chunk_read.sem, chunk_read.at(5 + n))
                    for s in range(2):
                        nc.tensor.matmul(ps[4 + 2 * s + n][:, :], m.mod_sel[:, s, :],
                                         row[:, 2 * D + n * 512:2 * D + (n + 1) * 512], start=True, stop=True) \
                            .then_inc(gates.sem, gates.one())

            @block.vector
            def _(dve):
                chain = m.sig("dve_chain")
                if projection:
                    for t in range(NT):
                        one = slice(t, t + 1)
                        dve.wait_ge(squares.sem, squares.at(t + 1))
                        after(dve, nc.vector.tensor_tensor(m.sums[:, one], m.sums[:, one], m.sums[:, NT + t:NT + t + 1],
                                                           ALU.add), chain)
                        variance(m, dve, m.var[:, one], m.sums[:, one], 1.0 / D)
                        fine_rstd(m, dve, m.var[:, one], m.rstd[:, one], m.tmp[:, one], t + 1)
                        for n in range(2):
                            part = m.x[:, t, n * 512:(n + 1) * 512]
                            y = m.scratch[:, 1, n * 512:(n + 1) * 512]
                            after(dve, nc.vector.scalar_tensor_tensor(out=y, in0=bank(t, n)[:, :], scalar=m.rstd[:, one],
                                                                      in1=m.gate[:, t // NX, n * 512:(n + 1) * 512],
                                                                      op0=ALU.mult, op1=ALU.mult), chain)
                            last = nc.vector.tensor_tensor(part, part, y, ALU.add)
                            if n == 0:
                                after(dve, last, chain)
                        last.then_inc(added.sem, added.one())
                    dve.wait_ge(added.sem, added.at(NT))

                def add_given(n):
                    dve.wait_ge(chunk.sem, chunk.at(n + 1))
                    part = row[:, n * 512:(n + 1) * 512]
                    add = nc.vector.tensor_tensor(part, ps[n % 4][:, :], given[:, n * 512:(n + 1) * 512], ALU.add)
                    if n >= 4:
                        after(dve, add, chain)
                        add = nc.vector.tensor_tensor(part, part, given[:, 3 * D + (n - 4) * 512:3 * D + (n - 3) * 512],
                                                      ALU.mult)
                    add.then_inc(chunk_read.sem, chunk_read.one())

                dve.wait_ge(landed.sem, landed.at(16))
                for n in range(6):
                    add_given(n)
                dve.wait_ge(squares.sem, squares.at(NT + 1 if projection else 1))
                variance(m, dve, m.var[:, norm], m.sums[:, norm], 1.0 / D)
                fine_rstd(m, dve, m.var[:, norm], m.rstd[:, norm], m.tmp[:, norm], NT + 1 if projection else 1)
                dve.wait_ge(cols.sem, cols.at(1))
                both = ps[2][:, 0:4 * KD].rearrange("p (w k s) -> p w s k", w=2, s=2)
                nc.vector.tensor_copy(m.shift[:], both[:, 0])
                for s in range(2):
                    nc.vector.scalar_tensor_tensor(out=m.scale1[:, s, :], in0=both[:, 1, s, :], scalar=1.0,
                                                   in1=m.vec("g_pre", layer * KD, (layer + 1) * KD),
                                                   op0=ALU.add, op1=ALU.mult)

            @block.scalar
            def _(act):
                chain = m.sig("act_chain")

                def square_x(t):
                    after(act, nc.scalar.activation(m.scratch[:, 0, :], m.x[:, t, :], ACT.Square,
                                                    accum_out=m.sums[:, NORM + t:NORM + t + 1]), chain)

                for t in range(NT):
                    if projection:
                        act.wait_ge(ready.sem, ready.at(t + 1))
                        for n in range(2):
                            after(act, nc.scalar.activation(m.scratch[:, 0, 0:512], bank(t, n)[:, :], ACT.Square,
                                                            accum_out=m.sums[:, n * NT + t:n * NT + t + 1]), chain)
                        nc.scalar.nop().then_inc(squares.sem, squares.one())
                        rough_rstd(m, act, m.var[:, t:t + 1], m.rstd[:, t:t + 1], t + 1)
                        if t >= 1:
                            act.wait_ge(added.sem, added.at(t))
                            square_x(t - 1)
                    else:
                        act.wait_ge(tokens.sem, tokens.at(16 * NT))
                        square_x(t)
                if projection:
                    act.wait_ge(added.sem, added.at(NT))
                    square_x(NT - 1)
                nc.scalar.nop().then_inc(squares.sem, squares.one())
                rough_rstd(m, act, m.var[:, norm], m.rstd[:, norm], NT + 1 if projection else 1)
                for n in range(2):
                    for s in range(2):
                        act.wait_ge(gates.sem, gates.at(2 * n + s + 1))
                        nc.scalar.activation(m.gate[:, s, n * 512:(n + 1) * 512], ps[4 + 2 * s + n][:, :], ACT.Copy)


def norm_to_channels(m, tiles, out, scale, shift, by_token=None, stats=True):
    nc, ps = m.nc, m.ps
    cols = slice(NORM, NORM + tiles)
    normed_at = (lambda t: m.scratch[:, t % 2, :]) if by_token is None else (lambda t: by_token[0][:, t, :])
    with m.step() as block:
        squares, normed, turned = m.sig("squares_summed"), m.sig("normed_ready"), m.sig("turned_in_psum")
        taken = {0: m.sig("turned_taken_by_dve"), 1: m.sig("turned_taken_by_act")}

        @block.scalar
        def _(act):
            if stats:
                for t in range(tiles):
                    after(act, nc.scalar.activation(m.scratch[:, t % 2, :], m.x[:, t, :], ACT.Square,
                                                    accum_out=m.sums[:, NORM + t:NORM + t + 1]), m.sig("act_chain"))
                nc.scalar.nop().then_inc(squares.sem, squares.one())
                rough_rstd(m, act, m.var[:, cols], m.rstd[:, cols])
            for t in range(tiles):
                act.wait_ge(turned.sem, turned.at(2 * t + 2))
                if by_token is not None:
                    last = nc.scalar.activation(out[:, 4:8, t * P:(t + 1) * P],
                                                ps[(2 * t + 1) % 4][:, :].rearrange("p (k t) -> p k t", k=4), ACT.Copy)
                else:
                    for k in range(4, 8):
                        last = nc.scalar.activation(out[:, k, t * P:(t + 1) * P],
                                                    ps[(2 * t + 1) % 4][:, (k - 4) * P:(k - 3) * P],
                                                    ACT.Identity, scale=scale(t // NX, k),
                                                    bias=0.0 if shift is None else shift(t // NX, k))
                last.then_inc(taken[1].sem, taken[1].one())

        @block.vector
        def _(dve):
            if stats:
                dve.wait_ge(squares.sem, squares.at(1))
                variance(m, dve, m.var[:, cols], m.sums[:, cols], 1.0 / D)
                fine_rstd(m, dve, m.var[:, cols], m.rstd[:, cols], m.tmp[:, cols])
            for t in range(tiles + 1):
                if t < tiles:
                    if t >= 2:
                        dve.wait_ge(turned.sem, turned.at(2 * (t - 2) + 2))
                    if by_token is None:
                        last = nc.vector.tensor_scalar(normed_at(t), m.x[:, t, :], m.rstd[:, NORM + t:NORM + t + 1], None,
                                                       ALU.mult)
                    else:
                        last = nc.vector.scalar_tensor_tensor(out=normed_at(t), in0=m.x[:, t, :],
                                                              scalar=m.rstd[:, NORM + t:NORM + t + 1],
                                                              in1=by_token[1][:], op0=ALU.mult, op1=ALU.mult)
                    last.then_inc(normed.sem, normed.one())
                if t >= 1:
                    u = t - 1
                    dve.wait_ge(turned.sem, turned.at(2 * u + 1))
                    for k in range(4):
                        src = ps[(2 * u) % 4][:, k * P:(k + 1) * P]
                        dst = out[:, k, u * P:(u + 1) * P]
                        if by_token is not None:
                            last = nc.vector.tensor_copy(dst, src)
                        elif shift is None:
                            last = nc.vector.tensor_scalar(dst, src, scale(u // NX, k), None, ALU.mult)
                        else:
                            last = nc.vector.tensor_scalar(dst, src, scale(u // NX, k), shift(u // NX, k), ALU.mult, ALU.add)
                    last.then_inc(taken[0].sem, taken[0].one())

        @block.tensor
        def _(pe):
            for t in range(tiles):
                pe.wait_ge(normed.sem, normed.at(t + 1))
                for half in range(2):
                    if t >= 2:
                        pe.wait_ge(taken[half].sem, taken[half].at(t - 1))
                    for k in range(4):
                        last = nc.tensor.transpose(ps[(2 * t + half) % 4][:, k * P:(k + 1) * P],
                                                   normed_at(t)[:, (4 * half + k) * P:(4 * half + k + 1) * P], m.ident[:, :])
                    last.then_inc(turned.sem, turned.one())


class Gates:

    def __init__(self, m, n_tok, tmp):
        self.m, self.n, self.tmp = m, n_tok, tmp
        self.ready, self.exp, self.done = m.sig("gate_in_psum"), m.sig("gate_exp_ready"), m.sig("gate_done")

    def bank(self, g):
        return self.m.ps[4 + g % 4][:, 0:self.n]

    def matmuls(self, pe, g, panel, j, k_tiles=KD, width=512):
        if g >= 4:
            pe.wait_ge(self.done.sem, self.done.at(g - 3))
        for k in range(k_tiles):
            last = self.m.nc.tensor.matmul(self.bank(g), self.m.slot(panel)[:, k * width + j * P:k * width + (j + 1) * P],
                                           self.m.hT[:, k, 0:self.n], start=k == 0, stop=k == k_tiles - 1)
        last.then_inc(self.ready.sem, self.ready.one())

    def exponential(self, act, g):
        act.wait_ge(self.ready.sem, self.ready.at(g + 1))
        if g >= 2:
            act.wait_ge(self.done.sem, self.done.at(g - 1))
        self.m.nc.scalar.activation(self.tmp[:, g % 2, 0:self.n], self.bank(g), ACT.Exp, scale=-1.0) \
            .then_inc(self.exp.sem, self.exp.one())

    def finish(self, dve, g, out, silu):
        nc, chain, t = self.m.nc, self.m.sig("dve_chain"), self.tmp[:, g % 2, 0:self.n]
        dve.wait_ge(self.exp.sem, self.exp.at(g + 1))
        after(dve, nc.vector.tensor_scalar(t, t, 1.0, None, ALU.add), chain)
        if silu:
            after(dve, nc.vector.reciprocal(t, t), chain)
            last = nc.vector.tensor_tensor(out, self.bank(g), t, ALU.mult)
        else:
            last = nc.vector.reciprocal(out, t)
        last.then_inc(self.done.sem, self.done.one())


def rope(m, dve, out, src, t, heads):
    nc, chain = m.nc, m.sig("dve_chain")
    wide = [P, heads, 32]
    cos = m.cos[:, t, :].unsqueeze(1).broadcast_to(wide)
    sin = m.sin[:, t, :].unsqueeze(1).broadcast_to(wide)
    ta = m.scratch[:, 0, 0:heads * 32].rearrange("p (h c) -> p h c", h=heads)
    tb = m.scratch[:, 1, 0:heads * 32].rearrange("p (h c) -> p h c", h=heads)
    nc.vector.tensor_tensor(ta, src[:, :, 0, :], cos, ALU.mult)
    after(dve, nc.vector.tensor_tensor(tb, src[:, :, 1, :], sin, ALU.mult), chain)
    after(dve, nc.vector.tensor_tensor(out[:, :, 0, :], ta, tb, ALU.subtract), chain)
    nc.vector.tensor_tensor(ta, src[:, :, 0, :], sin, ALU.mult)
    after(dve, nc.vector.tensor_tensor(tb, src[:, :, 1, :], cos, ALU.mult), chain)
    return nc.vector.tensor_tensor(out[:, :, 1, :], ta, tb, ALU.add)


def attention(m, own, heads, streams, scale, score_parts, v_of, place, mask=None, sink=None):
    nc, ps = m.nc, m.ps
    BUFS, LAG = 4, 3
    probs = m.sb("probs", [P, BUFS, 512], own)
    probsT = m.sb("probsT", [P, 2, 4, N], own)
    neg_max, den, rden, esink = (m.sb(n, [P, BUFS], own) for n in ("neg_max", "den", "rden", "esink"))
    units = [(h, s, q) for h in range(heads) for s in range(streams) for q in range(NX)]
    U = len(units)
    keys = lambda s: range(0, NT) if s == 0 else range(NX, NT)

    with m.step() as block:
        scored, maxed, expd = m.sig("scores_in_psum"), m.sig("row_max_ready"), m.sig("probs_ready")
        normed, turned, copied = m.sig("probs_normalised"), m.sig("probsT_in_psum"), m.sig("probsT_copied")
        outed, taken = m.sig("attended_in_psum"), m.sig("attended_taken")

        @block.tensor
        def _(pe):
            for step in range(U + LAG + 2):
                if step < U:
                    u = step
                    h, s, q = units[u]
                    first = keys(s)[0] * P
                    if u >= BUFS:
                        pe.wait_ge(expd.sem, expd.at(u - BUFS + 1))
                    parts = score_parts(h, NX * s + q)
                    opposite = 1 - q
                    with_mask = mask is not None and s == 0
                    for i, (lhsT, rhs) in enumerate(parts):
                        last = nc.tensor.matmul(ps[u % BUFS][:, first:512], lhsT, rhs[:, first:512], start=i == 0,
                                                stop=i == len(parts) - 1)
                    if with_mask:
                        last = nc.tensor.matmul(ps[u % BUFS][:, opposite * P:(opposite + 1) * P], m.ident[:, :], mask[:, q, :],
                                                start=False, stop=True, skip_group_check=True)
                    last.then_inc(scored.sem, scored.one())
                u = step - LAG
                if 0 <= u < U:
                    h, s, q = units[u]
                    pe.wait_ge(normed.sem, normed.at(u + 1))
                    if u >= 2:
                        pe.wait_ge(copied.sem, copied.at(u - 1))
                    for kt in keys(s):
                        last = nc.tensor.transpose(ps[BUFS + u % 2][:, kt * P:(kt + 1) * P],
                                                   probs[:, u % BUFS, kt * P:(kt + 1) * P], m.ident[:, :])
                    last.then_inc(turned.sem, turned.one())
                u = step - LAG - 1
                if 0 <= u < U and u % NX == NX - 1:
                    v = u // NX
                    h, s, q = units[u]
                    pe.wait_ge(copied.sem, copied.at(u + 1))
                    if v >= 2:
                        pe.wait_ge(taken.sem, taken.at(v - 1))
                    for kt in keys(s):
                        last = nc.tensor.matmul(ps[BUFS + 2 + v % 2][:, 0:N], v_of(h, kt), probsT[:, v % 2, kt, :],
                                                start=kt == keys(s)[0], stop=kt == NT - 1)
                    last.then_inc(outed.sem, outed.one())

        @block.scalar
        def _(act):
            for step in range(U + LAG):
                if step < U:
                    u = step
                    h, s, q = units[u]
                    first = keys(s)[0] * P
                    act.wait_ge(maxed.sem, maxed.at(u + 1))
                    if u >= BUFS:
                        act.wait_ge(turned.sem, turned.at(u - BUFS + 1))
                    if sink is not None:
                        nc.scalar.activation(esink[:, u % BUFS:u % BUFS + 1], sink[:, h:h + 1], ACT.Exp,
                                             bias=neg_max[:, u % BUFS:u % BUFS + 1])
                    nc.scalar.activation(probs[:, u % BUFS, first:512], ps[u % BUFS][:, first:512], ACT.Exp, scale=scale,
                                         bias=neg_max[:, u % BUFS:u % BUFS + 1], accum_out=den[:, u % BUFS:u % BUFS + 1]) \
                        .then_inc(expd.sem, expd.one())
                u = step - LAG
                if 0 <= u < U:
                    h, s, q = units[u]
                    v = u // NX
                    act.wait_ge(turned.sem, turned.at(u + 1))
                    if v >= 2:
                        act.wait_ge(outed.sem, outed.at(v - 1))
                    first = keys(s)[0]
                    nc.scalar.activation(probsT[:, v % 2, first:NT, q * P:(q + 1) * P],
                                         ps[BUFS + u % 2][:, first * P:512].rearrange("p (k q) -> p k q", q=P), ACT.Copy) \
                        .then_inc(copied.sem, copied.one())

        @block.vector
        def _(dve):
            chain = m.sig("dve_chain")
            for step in range(U + LAG + 2):
                if step < U:
                    u = step
                    h, s, q = units[u]
                    first = keys(s)[0] * P
                    col = neg_max[:, u % BUFS:u % BUFS + 1]
                    dve.wait_ge(scored.sem, scored.at(u + 1))
                    after(dve, nc.vector.tensor_reduce(col, ps[u % BUFS][:, first:512], AX, ALU.max), chain)
                    if sink is None:
                        last = nc.vector.tensor_scalar(col, col, -scale, None, ALU.mult)
                    else:
                        last = nc.vector.tensor_scalar(col, col, -scale, m.neg_sink[:, h:h + 1], ALU.mult, ALU.min)
                    last.then_inc(maxed.sem, maxed.one())
                u = step - 1
                if 0 <= u < U:
                    h, s, q = units[u]
                    first = keys(s)[0] * P
                    c = slice(u % BUFS, u % BUFS + 1)
                    dve.wait_ge(expd.sem, expd.at(u + 1))
                    if sink is not None:
                        after(dve, nc.vector.tensor_tensor(den[:, c], den[:, c], esink[:, c], ALU.add), chain)
                    after(dve, nc.vector.reciprocal(rden[:, c], den[:, c]), chain)
                    nc.vector.tensor_scalar(probs[:, u % BUFS, first:512], probs[:, u % BUFS, first:512], rden[:, c], None,
                                            ALU.mult).then_inc(normed.sem, normed.one())
                u = step - LAG - 1
                if 0 <= u < U and u % NX == NX - 1:
                    v = u // NX
                    h, s, q = units[u]
                    dve.wait_ge(outed.sem, outed.at(v + 1))
                    rows, tile = place(h)
                    dst = m.gT[rows, tile, s * N:(s + 1) * N]
                    nc.vector.tensor_tensor(dst, ps[BUFS + 2 + v % 2][rows, 0:N], dst, ALU.mult).then_inc(taken.sem, taken.one())


def project_out(m, name, tiles, gated):
    nc, ps = m.nc, m.ps
    panels = m.take(2, name, name)
    bank = lambda t, n: ps[2 * t + n]
    with m.step() as block:
        ready, squares = m.sig("projected_in_psum"), m.sig("squares_summed")

        @block.sync
        def _(sp):
            for n, i in enumerate(panels):
                sp.wait_ge(ready.sem, ready.at((n + 1) * tiles))
                m.load_next(sp, i)

        @block.tensor
        def _(pe):
            for n, i in enumerate(panels):
                pe.wait_ge(*m.loaded(i))
                for t in range(tiles):
                    for k in range(KD):
                        last = nc.tensor.matmul(bank(t, n)[:, :], m.gT[:, k, t * P:(t + 1) * P],
                                                m.slot(i)[:, k * 512:(k + 1) * 512], start=k == 0, stop=k == KD - 1)
                    last.then_inc(ready.sem, ready.one())

        @block.scalar
        def _(act):
            if gated:
                for n in range(2):
                    for t in range(tiles):
                        act.wait_ge(ready.sem, ready.at(n * tiles + t + 1))
                        after(act, nc.scalar.activation(m.scratch[:, 0, 0:512], bank(t, n)[:, :], ACT.Square,
                                                        accum_out=m.sums[:, n * NT + t:n * NT + t + 1]), m.sig("act_chain"))
                nc.scalar.nop().then_inc(squares.sem, squares.one())
                rough_rstd(m, act, m.var[:, 0:tiles], m.rstd[:, 0:tiles])

        @block.vector
        def _(dve):
            chain = m.sig("dve_chain")
            if gated:
                dve.wait_ge(squares.sem, squares.at(1))
                after(dve, nc.vector.tensor_tensor(m.sums[:, 0:tiles], m.sums[:, 0:tiles], m.sums[:, NT:NT + tiles],
                                                   ALU.add), chain)
                variance(m, dve, m.var[:, 0:tiles], m.sums[:, 0:tiles], 1.0 / D)
                fine_rstd(m, dve, m.var[:, 0:tiles], m.rstd[:, 0:tiles], m.tmp[:, 0:tiles])
            else:
                dve.wait_ge(ready.sem, ready.at(2 * tiles))
            for t in range(tiles):
                for n in range(2):
                    part = m.x[:, t, n * 512:(n + 1) * 512]
                    if gated:
                        y = m.scratch[:, 1, n * 512:(n + 1) * 512]
                        after(dve, nc.vector.scalar_tensor_tensor(out=y, in0=bank(t, n)[:, :], scalar=m.rstd[:, t:t + 1],
                                                                  in1=m.gate[:, t // NX, n * 512:(n + 1) * 512],
                                                                  op0=ALU.mult, op1=ALU.mult), chain)
                        after(dve, nc.vector.tensor_tensor(part, part, y, ALU.add), chain)
                    else:
                        after(dve, nc.vector.tensor_tensor(part, part, bank(t, n)[:, :], ALU.add), chain)


def latent_layer(m, layer):
    nc, ps = m.nc, m.ps
    j = layer // 3
    streams = 2 if layer < DEPTH - 1 else 1
    tq = NX * streams
    nq = tq * P
    norm_to_channels(m, NT, m.hT, lambda s, k: m.scale1[:, s, k:k + 1], lambda s, k: m.shift[:, s, k:k + 1],
                     stats=False)
    with ExitStack() as own:
        qnT = m.sb("q_nopeT", [P, A_H, 512], own)
        qrT = m.sb("q_ropeT", [P, A_H // 2, 512], own)
        krT = m.sb("k_ropeT", [P, 2, 512], own)
        v = m.sb("values", [P, NT, A_H * A_V], own)
        with ExitStack() as early:
            cq = m.sb("cq", [P, NT, A_QR], early)
            ckv = m.sb("ckv", [P, NT, A_KVR + A_ROPE], early)
            cqT = m.sb("cqT", [P, 4, 512], early)
            ckvT = m.sb("ckvT", [P, 2, 512], early)
            kr2 = m.sb("kr2", [P, NT, 2, A_ROPE], early)
            latent_inputs(m, layer, streams, cq, ckv)
            latent_norms(m, j, tq, cq, ckv, kr2, cqT, ckvT, krT)
            latent_qkv(m, layer, tq, cqT, ckvT, cq, qnT, qrT, v)
        knT = m.hT
        attention(m, own, A_H, streams, (A_NOPE + A_ROPE) ** -0.5,
                  lambda h, t: [(qnT[:, h, t * P:(t + 1) * P], knT[:, h, :]),
                                (qrT[:, h // 2, t * P:(t + 1) * P], krT[:, h % 2, :])],
                  lambda h, kt: v[:, kt, h * A_V:(h + 1) * A_V],
                  lambda h: (slice(0, P), h))


def latent_inputs(m, layer, streams, cq, ckv):
    nc, ps = m.nc, m.ps
    tq = NX * streams
    panels = m.take(4, f"a_cq{layer}", f"a_ckv{layer}", f"a_gate{layer}", f"a_gate{layer}")
    with m.step() as block:
        ready, read = m.sig("latent_in_psum"), m.sig("latent_read")
        gates = Gates(m, tq * P, m.scratch)
        groups = [(0, t) for t in range(tq)] + [(1, t) for t in range(NT)]
        width = (A_QR, A_KVR + A_ROPE)

        @block.sync
        def _(sp):
            for n in range(2):
                sp.wait_ge(ready.sem, ready.at(tq + n * NT))
                m.load_next(sp, panels[n])
            for n in range(2):
                sp.wait_ge(gates.ready.sem, gates.ready.at(4 * n + 4))
                m.load_next(sp, panels[2 + n])

        @block.tensor
        def _(pe):
            for g, (kind, t) in enumerate(groups):
                i, w = panels[kind], width[kind]
                if t == 0:
                    pe.wait_ge(*m.loaded(i))
                if g >= 4:
                    pe.wait_ge(read.sem, read.at(g - 3))
                for k in range(KD):
                    last = nc.tensor.matmul(ps[g % 4][:, 0:w], m.hT[:, k, t * P:(t + 1) * P],
                                            m.slot(i)[:, k * w:(k + 1) * w], start=k == 0, stop=k == KD - 1)
                last.then_inc(ready.sem, ready.one())
            for g in range(8):
                i = panels[2 + g // 4]
                if g % 4 == 0:
                    pe.wait_ge(*m.loaded(i))
                gates.matmuls(pe, g, i, g % 4)

        @block.scalar
        def _(act):
            for g, (kind, t) in enumerate(groups):
                act.wait_ge(ready.sem, ready.at(g + 1))
                src, c = ps[g % 4], (t + NT if kind == 0 else t)
                nc.scalar.activation((cq if kind == 0 else ckv)[:, t, :], src[:, 0:width[kind]], ACT.Copy)
                w = A_QR if kind == 0 else A_KVR
                after(act, nc.scalar.activation(m.scratch[:, 0, 0:w], src[:, 0:w], ACT.Square, accum_out=m.sums[:, c:c + 1]),
                      m.sig("act_chain"))
                nc.scalar.nop().then_inc(read.sem, read.one())
            for g in range(8):
                gates.exponential(act, g)

        @block.vector
        def _(dve):
            for g in range(8):
                gates.finish(dve, g, m.gT[:, g, 0:tq * P], True)


def latent_norms(m, j, tq, cq, ckv, kr2, cqT, ckvT, krT):
    nc, ps = m.nc, m.ps
    cols = NT + tq
    with m.step() as block:
        normed, turned, read = m.sig("latent_normed"), m.sig("latentT_in_psum"), m.sig("latentT_read")

        @block.vector
        def _(dve):
            chain = m.sig("dve_chain")
            nc.vector.memset(krT[64:P, 0, :], 0.0)
            nc.vector.memset(krT[0:64, 1, :], 0.0)
            after(dve, nc.vector.tensor_scalar(m.sums[:, 0:NT], m.sums[:, 0:NT], A_QR / A_KVR, None, ALU.mult), chain)
            variance(m, dve, m.var[:, 0:cols], m.sums[:, 0:cols], 1.0 / A_QR)
            fine_rstd(m, dve, m.var[:, 0:cols], m.rstd[:, 0:cols], m.tmp[:, 0:cols])
            for t in range(NT):
                lat = ckv[:, t, 0:A_KVR]
                kr = ckv[:, t, A_KVR:].rearrange("p (h x c) -> p h x c", h=1, x=2)
                nc.vector.tensor_scalar(lat, lat, m.rstd[:, t:t + 1], None, ALU.mult)
                if t < NX:
                    after(dve, rope(m, dve, kr2[:, t, 0:1, :].rearrange("p h (x c) -> p h x c", x=2), kr, t, 1), chain)
                    last = nc.vector.tensor_copy(kr2[:, t, 1, :], kr2[:, t, 0, :])
                else:
                    nc.vector.tensor_copy(kr2[:, t, 0, :], ckv[:, t, A_KVR:])
                    last = nc.vector.tensor_copy(kr2[:, t, 1, :], ckv[:, t, A_KVR:])
                if t < tq:
                    after(dve, last, chain)
                    last = nc.vector.tensor_scalar(cq[:, t, :], cq[:, t, :], m.rstd[:, NT + t:NT + t + 1], None, ALU.mult)
                after(dve, last, chain)
                nc.vector.nop().then_inc(normed.sem, normed.one())

        @block.tensor
        def _(pe):
            for t in range(NT):
                pe.wait_ge(normed.sem, normed.at(t + 1))
                if t >= 2:
                    pe.wait_ge(read.sem, read.at(t - 1))
                a, b = ps[2 * (t % 2)], ps[2 * (t % 2) + 1]
                for c in range(2):
                    nc.tensor.transpose(a[:, c * P:(c + 1) * P], ckv[:, t, c * P:(c + 1) * P], m.ident[:, :])
                last = nc.tensor.transpose(a[:, 2 * P:3 * P], kr2[:, t].rearrange("p a c -> p (a c)"), m.ident[:, :])
                if t < tq:
                    for c in range(4):
                        last = nc.tensor.transpose(b[:, c * P:(c + 1) * P], cq[:, t, c * P:(c + 1) * P], m.ident[:, :])
                last.then_inc(turned.sem, turned.one())

        @block.scalar
        def _(act):
            rough_rstd(m, act, m.var[:, 0:cols], m.rstd[:, 0:cols])
            for t in range(NT):
                act.wait_ge(turned.sem, turned.at(t + 1))
                a, b, tok = ps[2 * (t % 2)], ps[2 * (t % 2) + 1], slice(t * P, (t + 1) * P)
                for c in range(2):
                    nc.scalar.activation(ckvT[:, c, tok], a[:, c * P:(c + 1) * P], ACT.Copy,
                                         scale=m.vec("a_g_kv", 2 * j + c, 2 * j + c + 1))
                for odd in range(2):
                    rows = slice(64 * odd, 64 * odd + 64)
                    last = nc.scalar.activation(krT[rows, odd, tok], a[rows, 2 * P:3 * P], ACT.Copy)
                if t < tq:
                    for c in range(4):
                        last = nc.scalar.activation(cqT[:, c, tok], b[:, c * P:(c + 1) * P], ACT.Copy,
                                                    scale=m.vec("a_g_q", 4 * j + c, 4 * j + c + 1))
                last.then_inc(read.sem, read.one())


def latent_qkv(m, layer, tq, cqT, ckvT, qr, qnT, qrT, v):
    nc, ps = m.nc, m.ps
    panels = m.take(3, f"a_q{layer}", f"a_q{layer}", f"a_kv{layer}")
    knT = m.hT
    wide = A_NOPE + A_ROPE
    with m.step() as block:
        a_ready, a_read = m.sig("heads_in_psum"), m.sig("heads_read")
        d_ready, d_read = m.sig("token_part_in_psum"), m.sig("token_part_read")

        @block.sync
        def _(sp):
            for n, count in enumerate((tq, 2 * tq, 2 * tq + 2 * NT)):
                sp.wait_ge(d_ready.sem, d_ready.at(count))
                m.load_next(sp, panels[n])

        @block.tensor
        def _(pe):
            a = d = 0
            for n in range(2):
                i = panels[n]
                w = m.slot(i)[:, 0:4 * 768].rearrange("p (k h c) -> p k h c", k=4, h=4)
                pe.wait_ge(*m.loaded(i))
                for h in range(4):
                    if a >= 4:
                        pe.wait_ge(a_read.sem, a_read.at(a - 3))
                    for k in range(4):
                        last = nc.tensor.matmul(ps[a % 4][:, 0:tq * P], w[:, k, h, 0:A_NOPE], cqT[:, k, 0:tq * P],
                                                start=k == 0, stop=k == 3)
                    last.then_inc(a_ready.sem, a_ready.one())
                    a += 1
                for t in range(tq):
                    if d >= 4:
                        pe.wait_ge(d_read.sem, d_read.at(d - 3))
                    for k in range(4):
                        last = nc.tensor.matmul(ps[4 + d % 4][:, 0:N].rearrange("p (h c) -> p h c", h=4),
                                                cqT[:, k, t * P:(t + 1) * P], w[:, k, :, A_NOPE:wide],
                                                start=k == 0, stop=k == 3)
                    last.then_inc(d_ready.sem, d_ready.one())
                    d += 1
            i = panels[2]
            w = m.slot(i)[:, :].rearrange("p (k h c) -> p k h c", k=2, h=A_H)
            pe.wait_ge(*m.loaded(i))
            for h in range(A_H):
                pe.wait_ge(a_read.sem, a_read.at(a - 3))
                for k in range(2):
                    last = nc.tensor.matmul(ps[a % 4][:, :], w[:, k, h, 0:A_NOPE], ckvT[:, k, :], start=k == 0, stop=k == 1)
                last.then_inc(a_ready.sem, a_ready.one())
                a += 1
            for t in range(NT):
                for half in range(2):
                    if d >= 4:
                        pe.wait_ge(d_read.sem, d_read.at(d - 3))
                    for k in range(2):
                        last = nc.tensor.matmul(ps[4 + d % 4][:, :].rearrange("p (h c) -> p h c", h=4),
                                                ckvT[:, k, t * P:(t + 1) * P], w[:, k, 4 * half:4 * half + 4, A_NOPE:],
                                                start=k == 0, stop=k == 1)
                    last.then_inc(d_ready.sem, d_ready.one())
                    d += 1
            for t in range(tq):
                pe.wait_ge(d_read.sem, d_read.at(d - 3))
                for c in range(4):
                    last = nc.tensor.transpose(ps[4 + d % 4][:, c * P:(c + 1) * P], qr[:, t, c * P:(c + 1) * P], m.ident[:, :])
                last.then_inc(d_ready.sem, d_ready.one())
                d += 1

        @block.scalar
        def _(act):
            for a in range(2 * A_H):
                act.wait_ge(a_ready.sem, a_ready.at(a + 1))
                if a < A_H:
                    last = nc.scalar.activation(qnT[:, a, 0:tq * P], ps[a % 4][:, 0:tq * P], ACT.Copy)
                else:
                    last = nc.scalar.activation(knT[:, a - A_H, :], ps[a % 4][:, :], ACT.Copy)
                last.then_inc(a_read.sem, a_read.one())

        @block.vector
        def _(dve):
            d = 0
            for n in range(2):
                for t in range(tq):
                    dve.wait_ge(d_ready.sem, d_ready.at(d + 1))
                    src = ps[4 + d % 4][:, 0:N].rearrange("p (h x c) -> p h x c", h=4, x=2)
                    dst = qr[:, t, n * N:(n + 1) * N].rearrange("p (h x c) -> p h x c", h=4, x=2)
                    if t < NX:
                        last = rope(m, dve, dst, src, t, 4)
                    else:
                        last = nc.vector.tensor_copy(dst, src)
                    last.then_inc(d_read.sem, d_read.one())
                    dve.wait_ge(d_read.sem, d_read.at(d + 1))
                    d += 1
            for t in range(NT):
                for half in range(2):
                    dve.wait_ge(d_ready.sem, d_ready.at(d + 1))
                    nc.vector.tensor_copy(v[:, t, half * 512:(half + 1) * 512], ps[4 + d % 4][:, :]) \
                        .then_inc(d_read.sem, d_read.one())
                    d += 1
            for t in range(tq):
                dve.wait_ge(d_ready.sem, d_ready.at(d + 1))
                nc.vector.tensor_copy(qrT[:, :, t * P:(t + 1) * P], ps[4 + d % 4][:, :].rearrange("p (c t) -> p c t", c=4)) \
                    .then_inc(d_read.sem, d_read.one())
                d += 1


def window_layer(m):
    norm_to_channels(m, NT, m.hT, lambda s, k: m.scale1[:, s, k:k + 1], lambda s, k: m.shift[:, s, k:k + 1],
                     stats=False)
    with ExitStack() as own:
        qT = m.hT
        kT = m.sb("kT", [P, 2, B_KVH, 512], own)
        v2 = m.sb("v2", [P, NT, B_KVH, 2, B_HD], own)
        mask = m.sb("band", [P, NX, P], own)
        with ExitStack() as early:
            q = m.sb("q", [P, NT, D], early)
            k2 = m.sb("k2", [P, NT, B_KVH, 2, B_HD], early)
            window_inputs(m, q, k2, v2, mask)
            window_turn(m, q, k2, qT, kT)
        attention(m, own, B_H, 2, B_HD ** -0.5,
                  lambda h, t: [(qT[:, h // 2, t * P:(t + 1) * P], kT[:, h % 2, h // 4, :])],
                  lambda h, kt: v2[:, kt, h // 4].rearrange("p a c -> p (a c)"),
                  lambda h: (slice(h % 2 * 64, h % 2 * 64 + 64), h // 2),
                  mask=mask, sink=m.rows[:, ROW["sink"][0]:ROW["sink"][1]])


def window_inputs(m, q, k2, v2, mask):
    nc, ps = m.nc, m.ps
    panels = m.take(5, *["b_in"] * 5)
    with ExitStack() as own, m.step() as block:
        gate_tmp = m.sb("gate_tmp", [P, 2, 512], own)
        ready, read = m.sig("latent_in_psum"), m.sig("latent_read")
        landed = m.sig("mask_landed")
        gates = Gates(m, 512, gate_tmp)
        groups = [(n, t) for n in range(3) for t in range(NT)]

        @block.sync
        def _(sp):
            sp.dma_start(mask[:], m.dram["band"]).then_inc(landed.sem, landed.sixteen())
            for n in range(3):
                sp.wait_ge(ready.sem, ready.at((n + 1) * NT))
                m.load_next(sp, panels[n])
            for n in range(2):
                sp.wait_ge(gates.ready.sem, gates.ready.at(4 * n + 4))
                m.load_next(sp, panels[3 + n])
            sp.wait_ge(landed.sem, landed.at(16))

        @block.tensor
        def _(pe):
            for g, (n, t) in enumerate(groups):
                i = panels[n]
                if t == 0:
                    pe.wait_ge(*m.loaded(i))
                if g >= 4:
                    pe.wait_ge(read.sem, read.at(g - 3))
                for k in range(KD):
                    last = nc.tensor.matmul(ps[g % 4][:, :], m.hT[:, k, t * P:(t + 1) * P],
                                            m.slot(i)[:, k * 512:(k + 1) * 512], start=k == 0, stop=k == KD - 1)
                last.then_inc(ready.sem, ready.one())
            for g in range(8):
                i = panels[3 + g // 4]
                if g % 4 == 0:
                    pe.wait_ge(*m.loaded(i))
                gates.matmuls(pe, g, i, g % 4)

        @block.scalar
        def _(act):
            for g in range(8):
                gates.exponential(act, g)

        @block.vector
        def _(dve):
            chain = m.sig("dve_chain")
            nc.vector.tensor_scalar(m.neg_sink[:], m.rows[:, ROW["sink"][0]:ROW["sink"][1]], -1.0, None, ALU.mult)
            for g, (n, t) in enumerate(groups):
                dve.wait_ge(ready.sem, ready.at(g + 1))
                bank = ps[g % 4]
                if n < 2:
                    heads, part = 8, bank[:, :]
                    dst = q[:, t, n * 512:(n + 1) * 512].rearrange("p (h x c) -> p h x c", h=8, x=2)
                else:
                    heads, part = B_KVH, bank[:, 0:N]
                    dst = k2[:, t, :, 0, :].rearrange("p h (x c) -> p h x c", x=2)
                src = part.rearrange("p (h x c) -> p h x c", h=heads, x=2)
                last = rope(m, dve, dst, src, t, heads) if t < NX else nc.vector.tensor_copy(dst, src)
                if n == 2:
                    after(dve, last, chain)
                    nc.vector.tensor_copy(k2[:, t, :, 1, :], k2[:, t, :, 0, :])
                    for a in range(2):
                        last = nc.vector.tensor_copy(v2[:, t, :, a, :], bank[:, N:512].rearrange("p (h c) -> p h c", h=B_KVH))
                last.then_inc(read.sem, read.one())
                dve.wait_ge(read.sem, read.at(g + 1))
            for g in range(8):
                gates.finish(dve, g, m.gT[:, g, :], True)


def window_turn(m, q, k2, qT, kT):
    nc, ps = m.nc, m.ps
    with m.step() as block:
        turned, read = m.sig("qT_in_psum"), m.sig("qT_read")
        groups = [(c, t) for t in range(NT) for c in range(3)]

        @block.tensor
        def _(pe):
            for g, (c, t) in enumerate(groups):
                if g >= 4:
                    pe.wait_ge(read.sem, read.at(g - 3))
                for b in range(4):
                    src = q[:, t, c * 512 + b * P:c * 512 + (b + 1) * P] if c < 2 else \
                        k2[:, t, b].rearrange("p a c -> p (a c)")
                    last = nc.tensor.transpose(ps[g % 4][:, b * P:(b + 1) * P], src, m.ident[:, :])
                last.then_inc(turned.sem, turned.one())

        @block.scalar
        def _(act):
            for g, (c, t) in enumerate(groups):
                act.wait_ge(turned.sem, turned.at(g + 1))
                src = ps[g % 4][:, :].rearrange("p (b t) -> p b t", b=4)
                if c < 2:
                    last = nc.scalar.activation(qT[:, 4 * c:4 * c + 4, t * P:(t + 1) * P], src, ACT.Copy)
                else:
                    for odd in range(2):
                        rows = slice(64 * odd, 64 * odd + 64)
                        last = nc.scalar.activation(kT[rows, odd, :, t * P:(t + 1) * P], src[rows], ACT.Copy)
                last.then_inc(read.sem, read.one())

        @block.vector
        def _(dve):
            nc.vector.memset(kT[64:P, 0], 0.0)
            nc.vector.memset(kT[0:64, 1], 0.0)


def conv_layer(m):
    norm_to_channels(m, NT, m.hT, lambda s, k: m.scale1[:, s, k:k + 1], lambda s, k: m.shift[:, s, k:k + 1],
                     stats=False)
    with ExitStack() as own:
        u = m.sb("u", [P, NT, 3, D], own)
        conv_inputs(m, u)
        with ExitStack() as mid:
            dft = m.sb("dft", [P, NX, 6 * P], mid)
            idft = m.sb("idft", [P, 4, N], mid)
            zT = m.sb("zT", [C_EMB, N], mid)
            h1 = m.sb("ffn1", [C_FFN, N], mid)
            h2 = m.sb("ffn2", [C_FFN, N], mid)
            spec = m.sb("filter_spectrum", [P, 5, 512], mid)
            conv_ffn(m, mid, dft, idft, zT, h1, h2)
            decay, w3 = m.take(2, "c_decay", "c_w3")
            for order in range(2):
                for half in range(2):
                    conv_filters(m, order, half, dft, h2, spec, decay, w3)
                    conv_apply(m, order, half, dft, idft, spec, u)
        conv_gate(m, u)


def conv_inputs(m, u):
    nc, ps = m.nc, m.ps
    panels = m.take(8, *["c_in"] * 8)
    CH = 24
    with ExitStack() as own, m.step() as block:
        uc = m.sb("short", [P, 2, 512], own)
        ready, mid, conved = m.sig("heads_in_psum"), m.sig("centre_tap_ready"), m.sig("short_conv_ready")
        turned, read = m.sig("qT_in_psum"), m.sig("qT_read")
        gates = Gates(m, 512, m.scratch)

        @block.sync
        def _(sp):
            for n in range(6):
                sp.wait_ge(ready.sem, ready.at(4 * n + 4))
                m.load_next(sp, panels[n])
            for n in range(2):
                sp.wait_ge(gates.ready.sem, gates.ready.at(4 * n + 4))
                m.load_next(sp, panels[6 + n])

        @block.tensor
        def _(pe):
            for g in range(CH + 1):
                if g < CH:
                    i = panels[g // 4]
                    if g % 4 == 0:
                        pe.wait_ge(*m.loaded(i))
                    if g >= 2:
                        pe.wait_ge(conved.sem, conved.at(g - 1))
                    for k in range(KD):
                        last = nc.tensor.matmul(ps[g % 2][:, :], m.slot(i)[:, k * 512 + g % 4 * P:k * 512 + (g % 4 + 1) * P],
                                                m.hT[:, k, :], start=k == 0, stop=k == KD - 1)
                    last.then_inc(ready.sem, ready.one())
                if g >= 1:
                    c = g - 1
                    pe.wait_ge(conved.sem, conved.at(c + 1))
                    if c >= 2:
                        pe.wait_ge(read.sem, read.at(c - 1))
                    for t in range(NT):
                        last = nc.tensor.transpose(ps[2 + c % 2][:, t * P:(t + 1) * P], uc[:, c % 2, t * P:(t + 1) * P], m.ident[:, :])
                    last.then_inc(turned.sem, turned.one())
            for g in range(8):
                i = panels[6 + g // 4]
                if g % 4 == 0:
                    pe.wait_ge(*m.loaded(i))
                gates.matmuls(pe, g, i, g % 4)

        @block.scalar
        def _(act):
            for g in range(CH + 1):
                if g < CH:
                    act.wait_ge(ready.sem, ready.at(g + 1))
                    if g >= 2:
                        act.wait_ge(turned.sem, turned.at(g - 1))
                    nc.scalar.activation(uc[:, g % 2, :], ps[g % 2][:, :], ACT.Identity,
                                         scale=m.vec("conv_w", CH + g, CH + g + 1), bias=m.vec("conv_b", g, g + 1)) \
                        .then_inc(mid.sem, mid.one())
                if g >= 1:
                    c = g - 1
                    act.wait_ge(turned.sem, turned.at(c + 1))
                    nc.scalar.activation(u[:, :, c // 8, c % 8 * P:(c % 8 + 1) * P],
                                         ps[2 + c % 2][:, :].rearrange("p (t c) -> p t c", t=NT), ACT.Copy) \
                        .then_inc(read.sem, read.one())
            for g in range(8):
                gates.exponential(act, g)

        @block.vector
        def _(dve):
            for g in range(CH):
                src = ps[g % 2][:, :].rearrange("p (s n) -> p s n", s=2)
                dst = uc[:, g % 2, :].rearrange("p (s n) -> p s n", s=2)
                dve.wait_ge(mid.sem, mid.at(g + 1))
                after(dve, nc.vector.scalar_tensor_tensor(out=dst[:, :, 1:N], in0=src[:, :, 0:N - 1],
                                                          scalar=m.vec("conv_w", g, g + 1), in1=dst[:, :, 1:N],
                                                          op0=ALU.mult, op1=ALU.add), m.sig("dve_chain"))
                nc.vector.scalar_tensor_tensor(out=dst[:, :, 0:N - 1], in0=src[:, :, 1:N],
                                               scalar=m.vec("conv_w", 2 * CH + g, 2 * CH + g + 1), in1=dst[:, :, 0:N - 1],
                                               op0=ALU.mult, op1=ALU.add).then_inc(conved.sem, conved.one())
            for g in range(8):
                gates.finish(dve, g, m.gT[:, g, :], True)


ROUND = 1.5 * 2.0 ** 23
TWO_PI_A = 6.28125
TWO_PI_B = float(np.float32(int((2 * math.pi - TWO_PI_A) * 2 ** 20) / 2 ** 20))
TWO_PI_C = 2 * math.pi - TWO_PI_A - TWO_PI_B


def conv_ffn(m, own, dft, idft, zT, h1, h2):
    nc, ps = m.nc, m.ps
    with m.step() as block:
        landed, ready, reduced, sines = (m.sig(n) for n in ("dft_landed", "ffn_in_psum", "angle_reduced", "sine_ready"))
        turns = m.scratch[0:C_FFN, 0, 0:N]

        @block.sync
        def _(sp):
            for dst, src in ((zT, "zT"), (dft, "dft"), (idft, "idft")):
                sp.dma_start(dst[:], m.dram[src]).then_inc(landed.sem, landed.sixteen())
            sp.wait_ge(landed.sem, landed.at(48))

        @block.tensor
        def _(pe):
            pe.wait_ge(landed.sem, landed.at(48))
            nc.tensor.matmul(ps[0][0:C_FFN, 0:N], m.vec("f_w1")[0:C_EMB, :], zT[:, :], start=True, stop=True) \
                .then_inc(ready.sem, ready.one())
            pe.wait_ge(sines.sem, sines.at(1))
            nc.tensor.matmul(ps[1][0:C_FFN, 0:N], m.vec("f_w2")[0:C_FFN, :], h1[:, :], start=True, stop=True) \
                .then_inc(ready.sem, ready.one())

        @block.vector
        def _(dve):
            chain = m.sig("dve_chain")
            for i, (bias, h) in enumerate((("f_b1", h1), ("f_b2", h2))):
                dve.wait_ge(ready.sem, ready.at(i + 1))
                after(dve, nc.vector.tensor_scalar(h[:], ps[i][0:C_FFN, 0:N], m.vec(bias)[0:C_FFN, :],
                                                   m.vec("f_freq")[0:C_FFN, :], ALU.add, ALU.mult), chain)
                after(dve, nc.vector.tensor_scalar(turns, h[:], 1.0 / (2 * math.pi), ROUND, ALU.mult, ALU.add), chain)
                after(dve, nc.vector.tensor_scalar(turns, turns, ROUND, None, ALU.subtract), chain)
                for part in (TWO_PI_A, TWO_PI_B, TWO_PI_C):
                    after(dve, nc.vector.scalar_tensor_tensor(out=h[:], in0=turns, scalar=-part, in1=h[:],
                                                              op0=ALU.mult, op1=ALU.add), chain)
                nc.vector.tensor_scalar(h[:], h[:], 3.1415925, -3.1415925, ALU.min, ALU.max) \
                    .then_inc(reduced.sem, reduced.one())

        @block.scalar
        def _(act):
            for i, h in enumerate((h1, h2)):
                act.wait_ge(reduced.sem, reduced.at(i + 1))
                nc.scalar.activation(h[:], h[:], ACT.Sin).then_inc(sines.sem, sines.one())


def conv_filters(m, order, half, dft, h2, spec, decay, w3):
    nc, ps = m.nc, m.ps
    both = m.hT[:, 0:2 * NX, :].rearrange("p (t w) c -> p t w c", t=NX)
    cols = slice(half * 512, (half + 1) * 512)
    with m.step() as block:
        ready, made, spectral, copied = (m.sig(n) for n in ("filter_in_psum", "filter_ready", "spectrum_in_psum", "spectrum_copied"))
        paired = m.sig("filters_paired")
        w = m.slot(w3)[0:C_FFN, :].rearrange("p (w o c) -> p w o c", w=2, o=2)
        fall = m.slot(decay)[:, 0:2 * D].rearrange("p (t c) -> p t c", t=NX)
        bias = m.slot(decay)[0:1, 2 * D:4 * D].rearrange("p (o c) -> p o c", o=2)
        groups = [(t, way) for t in range(NX) for way in range(2)]
        tiles = [(0, 0), (1, 0), (4, 1), (3, 1), (5, 0)]

        @block.tensor
        def _(pe):
            pe.wait_ge(*m.loaded(w3))
            for g, (t, way) in enumerate(groups):
                nc.tensor.matmul(ps[g][:, :], h2[:, t * P:(t + 1) * P], w[:, way, order, cols],
                                 start=True, stop=True).then_inc(ready.sem, ready.one())
            pe.wait_ge(paired.sem, paired.at(1))
            for g in range(5):
                if g >= 4:
                    pe.wait_ge(copied.sem, copied.at(g - 3))
                col, way = tiles[g]
                for t in range(NX):
                    last = nc.tensor.matmul(ps[4 + g % 4][:, :], dft[:, t, col * P:(col + 1) * P],
                                            both[:, t, way, :], start=t == 0, stop=t == NX - 1)
                last.then_inc(spectral.sem, spectral.one())

        @block.vector
        def _(dve):
            chain = m.sig("dve_chain")
            dve.wait_ge(*m.loaded(decay))
            for g, (t, way) in enumerate(groups):
                dve.wait_ge(ready.sem, ready.at(g + 1))
                nc.vector.tensor_tensor(both[:, t, way, :], ps[g][:, :], fall[:, t, cols], ALU.mult).then_inc(made.sem, made.one())
            dve.wait_ge(made.sem, made.at(len(groups)))
            for t in range(NX):
                total, other = m.scratch[:, t, 0:512], both[:, t, 1, :]
                after(dve, nc.vector.tensor_tensor(total, both[:, t, 0, :], other, ALU.add), chain)
                after(dve, nc.vector.tensor_tensor(other, both[:, t, 0, :], other, ALU.subtract), chain)
                after(dve, nc.vector.tensor_copy(both[:, t, 0, :], total), chain)
            after(dve, nc.vector.tensor_tensor(both[0:1, 0, 0, :], both[0:1, 0, 0, :], bias[:, order, cols], ALU.add), chain)
            nc.vector.nop().then_inc(paired.sem, paired.one())

        @block.scalar
        def _(act):
            for g in range(5):
                act.wait_ge(spectral.sem, spectral.at(g + 1))
                nc.scalar.activation(spec[:, g, :], ps[4 + g % 4][:, :], ACT.Copy) \
                    .then_inc(copied.sem, copied.one())

        if order == 1 and half == 1:
            @block.sync
            def _(sp):
                sp.wait_ge(paired.sem, paired.at(1))
                m.load_next(sp, decay)
                sp.wait_ge(ready.sem, ready.at(len(groups)))
                m.load_next(sp, w3)


def conv_apply(m, order, half, dft, idft, spec, u):
    nc, ps = m.nc, m.ps
    cols = slice(half * 512, (half + 1) * 512)
    with m.step() as block:
        prod = m.hT[:].rearrange("p (a f) c -> p a f c", a=2)
        ta = m.scratch[:, 0, 0:512]
        tb = m.scratch[:, 1, 0:512]
        ready, read = m.sig("spectrum_in_psum"), m.sig("spectrum_used")
        back, taken = m.sig("convolved_in_psum"), m.sig("convolved_taken")
        units = [0, 1]
        recipe = [((0, 0), (2, 2), ALU.subtract), ((1, 1), (3, 3), ALU.subtract),
                  ((0, 2), (2, 4), ALU.add), ((1, 3), (3, 1), ALU.add)]

        @block.tensor
        def _(pe):
            for step in range(len(units) + 1):
                if step < len(units):
                    s = units[step]
                    if step >= 1:
                        pe.wait_ge(read.sem, read.at(4 * step))
                    for f in range(4):
                        for t in range(NX):
                            last = nc.tensor.matmul(ps[f][:, :], dft[:, t, f * P:(f + 1) * P],
                                                    u[:, NX * s + t, 0, cols], start=t == 0, stop=t == NX - 1)
                    last.then_inc(ready.sem, ready.one())
                if step >= 1:
                    v = step - 1
                    pe.wait_ge(read.sem, read.at(4 * v + 4))
                    for t in range(NX):
                        if v >= 2:
                            pe.wait_ge(taken.sem, taken.at(2 * (v - 2) + t + 1))
                        for f in range(4):
                            last = nc.tensor.matmul(ps[4 + 2 * (v % 2) + t][:, :], idft[:, f, t * P:(t + 1) * P],
                                                    prod[:, v % 2, f, :], start=f == 0, stop=f == 3)
                        last.then_inc(back.sem, back.one())

        @block.vector
        def _(dve):
            chain = m.sig("dve_chain")

            def take(v):
                s = units[v]
                for t in range(NX):
                    dve.wait_ge(back.sem, back.at(2 * v + t + 1))
                    nc.vector.tensor_tensor(u[:, NX * s + t, 0, cols], ps[4 + 2 * (v % 2) + t][:, :],
                                            u[:, NX * s + t, 1 + order, cols], ALU.mult).then_inc(taken.sem, taken.one())

            for v, s in enumerate(units):
                dve.wait_ge(ready.sem, ready.at(v + 1))
                if v >= 2:
                    dve.wait_ge(back.sem, back.at(2 * (v - 2) + 2))
                for f, ((ua, ka), (ub, kb), op) in enumerate(recipe):
                    nc.vector.tensor_tensor(ta, ps[ua][:, :], spec[:, ka, :], ALU.mult)
                    after(dve, nc.vector.tensor_tensor(tb, ps[ub][:, :], spec[:, kb, :], ALU.mult), chain)
                    nc.vector.tensor_tensor(prod[:, v % 2, f, :], ta, tb, op).then_inc(read.sem, read.one())
                    dve.wait_ge(read.sem, read.at(4 * v + f + 1))
                if v >= 1:
                    take(v - 1)
            take(len(units) - 1)


def conv_gate(m, u):
    nc, ps = m.nc, m.ps
    with m.step() as block:
        turned, read = m.sig("qT_in_psum"), m.sig("qT_read")
        groups = [(t, c) for t in range(NT) for c in range(2)]

        @block.tensor
        def _(pe):
            for g, (t, c) in enumerate(groups):
                if g >= 4:
                    pe.wait_ge(read.sem, read.at(g - 3))
                for b in range(4):
                    k = 4 * c + b
                    last = nc.tensor.transpose(ps[g % 4][:, b * P:(b + 1) * P], u[:, t, 0, k * P:(k + 1) * P], m.ident[:, :])
                last.then_inc(turned.sem, turned.one())

        @block.vector
        def _(dve):
            for g, (t, c) in enumerate(groups):
                dve.wait_ge(turned.sem, turned.at(g + 1))
                dst = m.gT[:, 4 * c:4 * c + 4, t * P:(t + 1) * P]
                nc.vector.tensor_tensor(dst, ps[g % 4][:, :].rearrange("p (b t) -> p b t", b=4), dst, ALU.mult) \
                    .then_inc(read.sem, read.one())


def second_mixer(m):
    hT = m.hT
    norm_to_channels(m, NX, hT, lambda s, k: m.vec("g_mix", k, k + 1), None)
    with ExitStack() as own:
        m.gT = hT[:, :, N:2 * N]
        go = m.sb("open_o", [P, M_H, N], own)
        ga = m.sb("open_a", [P, KD, N], own)
        gb = m.sb("open_b", [P, KD, N], own)
        up = m.sb("u_pool", [P, 4, POOL_PAD + N], own)
        qk = m.sb("qk_raw", [P, 2 * M_H, CONV_K - 1 + N], own)
        qkT = m.sb("qkT", [P, 2 * M_H, N], own)
        v = m.sb("v_mlstm", [P, NX, M_H * M_HD], own)
        zif = m.sb("z_if", [P, NX, 2 * M_H], own)
        poolT = m.sb("poolT", [P, 4, N], own)
        hmT = m.sb("hmT", [P, M_H, N], own)
        tri = m.sb("tri", [P, NX, N], own)
        causal = m.sb("causal", [P, NX, N], own)
        counts = m.sb("counts", [P, 4, N], own)
        fcum = m.sb("forget_sum", [P, NX, M_H], own)
        rbc = m.sb("log_input", [P, M_H, N], own)
        second_inputs(m, go, ga, gb, up, qk, v, zif, tri, causal, counts)
        second_convs(m, up, qk, qkT, poolT, counts)
        mlstm_gates(m, own, zif, tri, fcum, rbc)
        mlstm_heads(m, own, qkT, v, causal, fcum, rbc, go, hmT)
        second_merge(m, poolT, hmT, ga, gb)
        project_out(m, "s_out", NX, False)


def second_inputs(m, go, ga, gb, up, qk, v, zif, tri, causal, counts):
    nc, ps = m.nc, m.ps
    panels = m.take(9, *["s_in"] * 9)
    w_if = m.vec("w_if").rearrange("p (k c) -> p k c", k=KD)
    with m.step() as block:
        ready, read, landed = m.sig("latent_in_psum"), m.sig("latent_read"), m.sig("masks_landed")
        gates = Gates(m, N, m.scratch)
        groups = [(n, j) for n in range(3) for j in range(4)] + [(3, t) for t in range(NX)] + [(4, t) for t in range(NX)]
        out_of = [go, ga, ga, gb, gb]

        @block.sync
        def _(sp):
            for dst, src in ((tri, "tri"), (causal, "causal"), (counts, "counts")):
                sp.dma_start(dst[:], m.dram[src]).then_inc(landed.sem, landed.sixteen())
            for n, count in enumerate((4, 8, 12, 12 + NX)):
                sp.wait_ge(ready.sem, ready.at(count))
                m.load_next(sp, panels[n])
            for n in range(5):
                sp.wait_ge(gates.ready.sem, gates.ready.at(4 * n + 4))
                m.load_next(sp, panels[4 + n])
            sp.wait_ge(landed.sem, landed.at(48))

        @block.tensor
        def _(pe):
            for g, (n, j) in enumerate(groups):
                i = panels[min(n, 3)]
                if j == 0 and n < 4:
                    pe.wait_ge(*m.loaded(i))
                if g >= 4:
                    pe.wait_ge(read.sem, read.at(g - 3))
                for k in range(KD):
                    tok = m.hT[:, k, j * P:(j + 1) * P]
                    flags = dict(start=k == 0, stop=k == KD - 1)
                    if n < 3:
                        last = nc.tensor.matmul(ps[g % 4][:, 0:N], m.slot(i)[:, k * 512 + j * P:k * 512 + (j + 1) * P],
                                                m.hT[:, k, 0:N], **flags)
                    elif n == 3:
                        last = nc.tensor.matmul(ps[g % 4][:, :], tok, m.slot(i)[:, k * 512:(k + 1) * 512], **flags)
                    else:
                        last = nc.tensor.matmul(ps[g % 4][:, 0:2 * M_H], tok, w_if[:, k, :], **flags)
                last.then_inc(ready.sem, ready.one())
            for g in range(20):
                i = panels[4 + g // 4]
                if g % 4 == 0:
                    pe.wait_ge(*m.loaded(i))
                gates.matmuls(pe, g, i, g % 4)

        @block.scalar
        def _(act):
            for g, (n, j) in enumerate(groups):
                act.wait_ge(ready.sem, ready.at(g + 1))
                dst, src = ((up[:, j, POOL_PAD:], ps[g % 4][:, 0:N]), (qk[:, j, CONV_K - 1:], ps[g % 4][:, 0:N]),
                            (qk[:, M_H + j, CONV_K - 1:], ps[g % 4][:, 0:N]), (v[:, min(j, 1), :], ps[g % 4][:, :]),
                            (zif[:, min(j, 1), :], ps[g % 4][:, 0:2 * M_H]))[n]
                nc.scalar.activation(dst, src, ACT.Copy).then_inc(read.sem, read.one())
            for g in range(20):
                gates.exponential(act, g)

        @block.vector
        def _(dve):
            nc.vector.memset(up[:, :, 0:POOL_PAD], 0.0)
            nc.vector.memset(qk[:, :, 0:CONV_K - 1], 0.0)
            for g in range(20):
                which = out_of[g // 4]
                at = g % 4 + (4 if g // 4 in (2, 4) else 0)
                gates.finish(dve, g, which[:, at, :], False)


def second_convs(m, up, qk, qkT, poolT, counts):
    nc, ps = m.nc, m.ps
    (panel,) = m.take(1, "s_pool")
    with ExitStack() as own, m.step() as block:
        sums = [m.sb(f"window{i}", [P, POOL_PAD + N], own) for i in range(2)]
        expo = m.sb("silu_exp", [P, 2 * M_H, N], own)
        diffs = m.sb("pool_diff", [P, 4, N], own)
        conved, expd = m.sig("short_conv_ready"), m.sig("gate_exp_ready")
        diffed, ready = m.sig("pool_diff_ready"), m.sig("pooled_in_psum")

        @block.sync
        def _(sp):
            sp.wait_ge(ready.sem, ready.at(4))
            m.load_next(sp, panel)

        @block.vector
        def _(dve):
            chain = m.sig("dve_chain")
            for j in range(2 * M_H):
                name, h = ("conv_q", j) if j < M_H else ("conv_k", j - M_H)
                last = nc.vector.tensor_scalar(qkT[:, j, :], qk[:, j, 0:N], m.vec(name, h, h + 1), None, ALU.mult)
                for tap in range(1, CONV_K):
                    after(dve, last, chain)
                    last = nc.vector.scalar_tensor_tensor(out=qkT[:, j, :], in0=qk[:, j, tap:tap + N],
                                                          scalar=m.vec(name, tap * M_H + h, tap * M_H + h + 1),
                                                          in1=qkT[:, j, :], op0=ALU.mult, op1=ALU.add)
                last.then_inc(conved.sem, conved.one())
            for g, window in enumerate(POOL_WINDOWS):
                src, width = up[:, g, :], 1
                buf = 0
                while width < window:
                    dst = sums[buf]
                    after(dve, nc.vector.tensor_copy(dst[:, 0:width], src[:, 0:width]), chain)
                    after(dve, nc.vector.tensor_tensor(dst[:, width:], src[:, width:], src[:, 0:POOL_PAD + N - width], ALU.add), chain)
                    src, buf, width = dst[:, :], 1 - buf, 2 * width
                mean = sums[buf][:, 0:N]
                after(dve, nc.vector.tensor_tensor(mean, src[:, POOL_PAD:], counts[:, g, :], ALU.mult), chain)
                after(dve, nc.vector.tensor_tensor(diffs[:, g, :], mean, up[:, g, POOL_PAD:], ALU.subtract), chain)
                nc.vector.nop().then_inc(diffed.sem, diffed.one())
            dve.wait_ge(expd.sem, expd.at(1))
            after(dve, nc.vector.tensor_scalar(expo[:], expo[:], 1.0, None, ALU.add), chain)
            after(dve, nc.vector.reciprocal(expo[:], expo[:]), chain)
            nc.vector.tensor_tensor(qkT[:], qkT[:], expo[:], ALU.mult)

        @block.scalar
        def _(act):
            act.wait_ge(conved.sem, conved.at(2 * M_H))
            nc.scalar.activation(expo[:], qkT[:], ACT.Exp, scale=-1.0).then_inc(expd.sem, expd.one())
            for g in range(4):
                act.wait_ge(ready.sem, ready.at(g + 1))
                nc.scalar.activation(poolT[:, g, :], ps[g][:, 0:N], ACT.Copy, scale=m.vec("pool_scale", g, g + 1))

        @block.tensor
        def _(pe):
            pe.wait_ge(*m.loaded(panel))
            for g in range(4):
                pe.wait_ge(diffed.sem, diffed.at(g + 1))
                nc.tensor.matmul(ps[g][:, 0:N], m.slot(panel)[:, g * P:(g + 1) * P], diffs[:, g, :], start=True, stop=True) \
                    .then_inc(ready.sem, ready.one())


def mlstm_gates(m, own, zif, tri, fcum, rbc):
    nc, ps = m.nc, m.ps
    with ExitStack() as mine, m.step() as block:
        lf = m.sb("log_forget", [P, NX, M_H], mine)
        tmp = m.sb("log_tmp", [P, NX, M_H], mine)
        rT = m.sb("log_inputT", [M_H, N], mine)
        biased, softened, summed = m.sig("gates_biased"), m.sig("softplus_ready"), m.sig("log_forget_ready")
        cum, rin, rturn, rcopied, spread = (m.sig(n) for n in ("forget_sum_in_psum", "log_input_ready", "log_inputT_in_psum",
                                                              "log_inputT_copied", "log_input_spread"))
        i_pre, f_pre = zif[:, :, 0:M_H], zif[:, :, M_H:]

        @block.vector
        def _(dve):
            chain = m.sig("dve_chain")
            bias = m.rows[:, ROW["b_if"][0]:ROW["b_if"][1]].unsqueeze(1).broadcast_to([P, NX, 2 * M_H])
            after(dve, nc.vector.tensor_tensor(zif[:], zif[:], bias, ALU.add), chain)
            after(dve, nc.vector.tensor_scalar(tmp[:], f_pre, -1.0, None, ALU.mult), chain)
            nc.vector.tensor_tensor(tmp[:], tmp[:], f_pre, ALU.min).then_inc(biased.sem, biased.one())
            dve.wait_ge(softened.sem, softened.at(1))
            after(dve, nc.vector.tensor_scalar(lf[:], f_pre, 0.0, None, ALU.min), chain)
            nc.vector.tensor_tensor(lf[:], lf[:], tmp[:], ALU.subtract).then_inc(summed.sem, summed.one())
            dve.wait_ge(cum.sem, cum.at(1))
            after(dve, nc.vector.tensor_copy(fcum[:].rearrange("p t h -> p (t h)"), ps[0][:, 0:NX * M_H]), chain)
            nc.vector.tensor_tensor(tmp[:], i_pre, fcum[:], ALU.subtract).then_inc(rin.sem, rin.one())
            dve.wait_ge(rturn.sem, rturn.at(1))
            nc.vector.tensor_copy(rT[:], ps[1][0:M_H, 0:N]).then_inc(rcopied.sem, rcopied.one())
            dve.wait_ge(spread.sem, spread.at(1))
            for half in range(2):
                nc.vector.tensor_copy(rbc[:, 2 * half:2 * half + 2, :], ps[2 + half][:, :].rearrange("p (h s) -> p h s", h=2))

        @block.scalar
        def _(act):
            act.wait_ge(biased.sem, biased.at(1))
            after(act, nc.scalar.activation(tmp[:], tmp[:], ACT.Exp), m.sig("act_chain"))
            nc.scalar.activation(tmp[:], tmp[:], ACT.Ln, bias=1.0).then_inc(softened.sem, softened.one())

        @block.tensor
        def _(pe):
            pe.wait_ge(summed.sem, summed.at(1))
            for t in range(NX):
                for s in range(NX):
                    last = nc.tensor.matmul(ps[0][:, t * M_H:(t + 1) * M_H], tri[:, s, t * P:(t + 1) * P], lf[:, s, :],
                                            start=s == 0, stop=s == NX - 1)
            last.then_inc(cum.sem, cum.one())
            pe.wait_ge(rin.sem, rin.at(1))
            for t in range(NX):
                last = nc.tensor.transpose(ps[1][0:M_H, t * P:(t + 1) * P], tmp[:, t, :], m.ident[:, :])
            last.then_inc(rturn.sem, rturn.one())
            pe.wait_ge(rcopied.sem, rcopied.at(1))
            for h in range(M_H):
                last = nc.tensor.matmul(ps[2 + h // 2][:, h % 2 * N:(h % 2 + 1) * N], m.sel[0:M_H, h, :], rT[:, :],
                                        start=True, stop=True)
            last.then_inc(spread.sem, spread.one())


def mlstm_heads(m, own, qkT, v, causal, fcum, rbc, go, hmT):
    nc, ps = m.nc, m.ps
    units = [(t, h) for t in range(NX) for h in range(M_H)]
    U = len(units)
    with ExitStack() as mine, m.step() as block:
        masked = m.sb("masked_log", [P, 2, N], mine)
        weight = m.sb("weights", [P, 2, N], mine)
        swT = m.sb("scoresT", [P, 2, NX, P], mine)
        cols = m.sb("mlstm_cols", [P, 2, 8], mine)
        hm = m.sb("h_mlstm", [P, NX, M_H, M_HD], mine)
        stats = m.sb("head_stats", [P, 3, NX * M_H], mine)
        scored, argued, weighed = m.sig("scores_in_psum"), m.sig("row_max_ready"), m.sig("probs_ready")
        normed, turned, copied = m.sig("probs_normalised"), m.sig("probsT_in_psum"), m.sig("probsT_copied")
        outed, taken = m.sig("attended_in_psum"), m.sig("attended_taken")
        centred, back, finished = m.sig("heads_normalised"), m.sig("headsT_in_psum"), m.sig("headsT_read")
        col = lambda u, c: cols[:, u % 2, c:c + 1]
        MX, NEG, STAB, NQ, DEN, RDEN, POS = range(7)

        @block.tensor
        def _(pe):
            for step in range(U + 1):
                if step < U:
                    u = step
                    t, h = units[u]
                    if u >= 2:
                        pe.wait_ge(normed.sem, normed.at(u - 1))
                    nc.tensor.matmul(ps[u % 2][:, 0:N], qkT[:, h, t * P:(t + 1) * P], qkT[:, M_H + h, :], start=True, stop=True) \
                        .then_inc(scored.sem, scored.one())
                if step >= 1:
                    u = step - 1
                    t, h = units[u]
                    pe.wait_ge(normed.sem, normed.at(u + 1))
                    if u >= 2:
                        pe.wait_ge(copied.sem, copied.at(u - 1))
                    for s in range(NX):
                        last = nc.tensor.transpose(ps[2 + u % 2][:, s * P:(s + 1) * P], weight[:, u % 2, s * P:(s + 1) * P],
                                                   m.ident[:, :])
                    last.then_inc(turned.sem, turned.one())
                    pe.wait_ge(copied.sem, copied.at(u + 1))
                    if u >= 2:
                        pe.wait_ge(taken.sem, taken.at(u - 1))
                    for s in range(NX):
                        last = nc.tensor.matmul(ps[4 + u % 2][:, 0:M_HD], swT[:, u % 2, s, :], v[:, s, h * M_HD:(h + 1) * M_HD],
                                                start=s == 0, stop=s == NX - 1)
                    last.then_inc(outed.sem, outed.one())
            pe.wait_ge(centred.sem, centred.at(1))
            for h in range(M_H):
                if h >= 2:
                    pe.wait_ge(finished.sem, finished.at(h - 1))
                for t in range(NX):
                    last = nc.tensor.transpose(ps[6 + h % 2][:, t * P:(t + 1) * P], hm[:, t, h, :], m.ident[:, :])
                last.then_inc(back.sem, back.one())

        @block.scalar
        def _(act):
            for step in range(U + 1):
                if step < U:
                    u = step
                    act.wait_ge(argued.sem, argued.at(u + 1))
                    nc.scalar.activation(col(u, STAB), col(u, STAB), ACT.Exp, scale=-1.0)
                    if u >= 2:
                        act.wait_ge(turned.sem, turned.at(u - 1))
                    nc.scalar.activation(weight[:, u % 2, :], masked[:, u % 2, :], ACT.Exp, bias=col(u, NEG)) \
                        .then_inc(weighed.sem, weighed.one())
                if step >= 1:
                    u = step - 1
                    act.wait_ge(turned.sem, turned.at(u + 1))
                    if u >= 2:
                        act.wait_ge(outed.sem, outed.at(u - 1))
                    nc.scalar.activation(swT[:, u % 2].rearrange("p s t -> p (s t)"), ps[2 + u % 2][:, 0:N], ACT.Copy) \
                        .then_inc(copied.sem, copied.one())
            n = NX * M_H
            rough_rstd(m, act, stats[:, 1, 0:n], stats[:, 2, 0:n])

        @block.vector
        def _(dve):
            chain = m.sig("dve_chain")
            for step in range(U + 2):
                if step < U:
                    u = step
                    t, h = units[u]
                    if u >= 2:
                        dve.wait_ge(weighed.sem, weighed.at(u - 1))
                    after(dve, nc.vector.tensor_tensor(masked[:, u % 2, :], rbc[:, h, :], causal[:, t, :], ALU.add), chain)
                    after(dve, nc.vector.tensor_reduce(col(u, MX), masked[:, u % 2, :], AX, ALU.max), chain)
                    after(dve, nc.vector.tensor_scalar(col(u, POS), col(u, MX), 0.0, None, ALU.max), chain)
                    nc.vector.tensor_scalar(col(u, NEG), col(u, POS), -1.0, None, ALU.mult)
                    nc.vector.tensor_tensor(col(u, STAB), col(u, POS), fcum[:, t, h:h + 1], ALU.add) \
                        .then_inc(argued.sem, argued.one())
                if 1 <= step <= U:
                    u = step - 1
                    dve.wait_ge(weighed.sem, weighed.at(u + 1))
                    dve.wait_ge(scored.sem, scored.at(u + 1))
                    w = weight[:, u % 2, :]
                    after(dve, nc.vector.scalar_tensor_tensor(out=w, in0=ps[u % 2][:, 0:N], scalar=M_HD ** -0.5, in1=w,
                                                              op0=ALU.mult, op1=ALU.mult), chain)
                    after(dve, nc.vector.tensor_reduce(col(u, NQ), w, AX, ALU.add), chain)
                    after(dve, nc.vector.tensor_scalar(col(u, DEN), col(u, NQ), -1.0, None, ALU.mult), chain)
                    after(dve, nc.vector.tensor_tensor(col(u, DEN), col(u, DEN), col(u, NQ), ALU.max), chain)
                    after(dve, nc.vector.tensor_tensor(col(u, DEN), col(u, DEN), col(u, STAB), ALU.max), chain)
                    after(dve, nc.vector.reciprocal(col(u, RDEN), col(u, DEN)), chain)
                    after(dve, nc.vector.tensor_scalar(w, w, col(u, RDEN), None, ALU.mult), chain)
                    nc.vector.nop().then_inc(normed.sem, normed.one())
                if step >= 2:
                    u = step - 2
                    t, h = units[u]
                    dve.wait_ge(outed.sem, outed.at(u + 1))
                    nc.vector.tensor_copy(hm[:, t, h, :], ps[4 + u % 2][:, 0:M_HD]).then_inc(taken.sem, taken.one())
            dve.wait_ge(taken.sem, taken.at(U))
            all_h = hm[:].rearrange("p t h c -> p (t h) c")
            n = NX * M_H
            mean, var, rstd = stats[:, 0, :], stats[:, 1, :], stats[:, 2, :]
            wide = [P, n, M_HD]
            sq = m.scratch[:].rearrange("p a b -> p (a b)")[:, 0:n * M_HD].rearrange("p (n c) -> p n c", n=n)
            after(dve, nc.vector.tensor_reduce(mean, all_h, AX, ALU.add), chain)
            after(dve, nc.vector.tensor_scalar(mean, mean, 1.0 / M_HD, None, ALU.mult), chain)
            after(dve, nc.vector.tensor_tensor(all_h, all_h, mean.unsqueeze(2).broadcast_to(wide), ALU.subtract), chain)
            after(dve, nc.vector.tensor_tensor(sq, all_h, all_h, ALU.mult), chain)
            after(dve, nc.vector.tensor_reduce(var, sq, AX, ALU.add), chain)
            variance(m, dve, var, var, 1.0 / M_HD)
            fine_rstd(m, dve, var, rstd, m.tmp[:, 0:n])
            after(dve, nc.vector.tensor_tensor(all_h, all_h, rstd.unsqueeze(2).broadcast_to(wide), ALU.mult), chain)
            nc.vector.nop().then_inc(centred.sem, centred.one())
            for h in range(M_H):
                dve.wait_ge(back.sem, back.at(h + 1))
                nc.vector.scalar_tensor_tensor(out=hmT[:, h, :], in0=ps[6 + h % 2][:, 0:N], scalar=m.vec("g_head", h, h + 1),
                                               in1=go[:, h, :], op0=ALU.mult, op1=ALU.mult).then_inc(finished.sem, finished.one())


def second_merge(m, poolT, hmT, ga, gb):
    nc, ps = m.nc, m.ps
    panels = m.take(2, "s_br_a", "s_br_b")
    with m.step() as block:
        ready, used = m.sig("branch_in_psum"), m.sig("branch_used")
        groups = [(c, b) for b in range(2) for c in range(KD)]

        @block.sync
        def _(sp):
            for n in range(2):
                sp.wait_ge(ready.sem, ready.at((n + 1) * KD))
                m.load_next(sp, panels[n])

        @block.tensor
        def _(pe):
            for g, (c, b) in enumerate(groups):
                if c == 0:
                    pe.wait_ge(*m.loaded(panels[b]))
                if g >= 4:
                    pe.wait_ge(used.sem, used.at(g - 3))
                for k in range(4):
                    last = nc.tensor.matmul(ps[g % 4][:, 0:N], m.slot(panels[b])[:, k * D + c * P:k * D + (c + 1) * P],
                                            (poolT, hmT)[b][:, k, :], start=k == 0, stop=k == 3)
                last.then_inc(ready.sem, ready.one())

        @block.vector
        def _(dve):
            for g, (c, b) in enumerate(groups):
                dve.wait_ge(ready.sem, ready.at(g + 1))
                gate = (ga, gb)[b][:, c, :]
                dst = m.gT[:, c, :] if b == 0 else gate
                last = nc.vector.tensor_tensor(dst, ps[g % 4][:, 0:N], gate, ALU.mult)
                if b == 1:
                    after(dve, last, m.sig("dve_chain"))
                    last = nc.vector.tensor_tensor(m.gT[:, c, :], m.gT[:, c, :], gate, ALU.add)
                last.then_inc(used.sem, used.one())


def route(m, own, h):
    nc, ps = m.nc, m.ps
    m.gates = m.sb("gates", [P, NX, N_EXP], own)
    m.place = m.sb("place", [P, NX, N_EXP], own)
    m.longest = m.sb("longest_list", [P, 1], own, dt=mybir.dt.int32)
    with ExitStack() as mine:
        g_row = m.sb("g_ffn", [P, D], mine)
        with m.step() as block:
            landed = m.sig("constants_landed")

            @block.sync
            def _(sp):
                sp.dma_start(g_row[:], m.dram["g_ffn"]).then_inc(landed.sem, landed.sixteen())
                for i in range(N_DENSE + RING, N_DENSE + MOE_RING):
                    m.issue(sp, i)
                sp.wait_ge(landed.sem, landed.at(16))

        norm_to_channels(m, NX, m.hT, None, None, by_token=(h, g_row))
    w_route = m.vec("w_route").rearrange("p (k c) -> p k c", k=KD)
    with ExitStack() as mine, m.step() as block:
        logits = m.sb("logits", [P, NX, N_ROUTE], mine)
        glog = m.sb("group_logits", [P, NX, 8], mine)
        elog = m.sb("group_experts", [P, NX, N_EXP], mine)
        top = m.sb("top", [P, NX, 2, 8], mine)
        where = m.sb("where", [P, NX, 2, 8], mine, dt=U32)
        wheref = m.sb("wheref", [P, NX, 2, 8], mine)
        onehot = m.sb("group_onehot", [P, NX, 8], mine)
        c = m.sb("route_cols", [P, NX, 8], mine)
        chosen = m.sb("chosen", [P, NX, N_EXP], mine)
        tri = m.sb("tri", [P, NX, N], mine)
        ones = m.sb("ones", [P, P], mine)
        count = m.sb("list_length", [P, 1], mine)
        gates, place = m.gates, m.place
        landed, ready, argued, expd = m.sig("masks_landed"), m.sig("logits_in_psum"), m.sig("route_args_ready"), m.sig("route_exps_ready")
        picked, ranked = m.sig("chosen_ready"), m.sig("places_in_psum")
        iota = m.rows[:, ROW["iota"][0]:ROW["iota"][0] + N_EXP]

        @block.sync
        def _(sp):
            sp.dma_start(tri[:], m.dram["tri"]).then_inc(landed.sem, landed.sixteen())

        @block.tensor
        def _(pe):
            for t in range(NX):
                for k in range(KD):
                    last = nc.tensor.matmul(ps[t][:, 0:N_ROUTE], m.hT[:, k, t * P:(t + 1) * P], w_route[:, k, :],
                                            start=k == 0, stop=k == KD - 1)
                last.then_inc(ready.sem, ready.one())
            pe.wait_ge(landed.sem, landed.at(16))
            pe.wait_ge(picked.sem, picked.at(1))
            for t in range(NX):
                for s in range(NX):
                    nc.tensor.matmul(ps[2][:, t * N_EXP:(t + 1) * N_EXP], tri[:, s, t * P:(t + 1) * P], chosen[:, s, :],
                                     start=s == 0, stop=s == NX - 1)
            for s in range(NX):
                last = nc.tensor.matmul(ps[3][:, 0:N_EXP], ones[:, :], chosen[:, s, :], start=s == 0, stop=s == NX - 1)
            last.then_inc(ranked.sem, ranked.one())

        @block.scalar
        def _(act):
            act.wait_ge(argued.sem, argued.at(1))
            nc.scalar.activation(onehot[:], glog[:], ACT.Exp)
            nc.scalar.activation(c[:, :, 1:2], c[:, :, 0:1], ACT.Exp).then_inc(expd.sem, expd.one())

        @block.vector
        def _(dve):
            chain = m.sig("dve_chain")
            v = nc.vector
            bias = m.rows[:, ROW["b_route"][0]:ROW["b_route"][1]]
            v.memset(ones[:], 1.0)
            dve.wait_ge(ready.sem, ready.at(NX))
            for t in range(NX):
                after(dve, v.tensor_tensor(logits[:, t, :], ps[t][:, 0:N_ROUTE], bias, ALU.add), chain)
            after(dve, v.memset(glog[:], MASKED), chain)
            after(dve, v.tensor_copy(glog[:, :, 0:N_GROUPS], logits[:, :, 0:N_GROUPS]), chain)
            for t in range(NX):
                after(dve, v.max(top[:, t, 0, :], glog[:, t, :]), chain)
                after(dve, v.max_index(where[:, t, 0, :], top[:, t, 0, :], glog[:, t, :]), chain)
                after(dve, v.tensor_copy(wheref[:, t, 0, :], where[:, t, 0, :]), chain)
                after(dve, v.tensor_scalar(onehot[:, t, 0:N_GROUPS], iota[:, 0:N_GROUPS], wheref[:, t, 0, 0:1], None, ALU.is_equal), chain)
                mine_ = onehot[:, t, 0:N_GROUPS].unsqueeze(2).broadcast_to([P, N_GROUPS, PER_GROUP])
                e3 = elog[:, t, :].rearrange("p (g e) -> p g e", g=N_GROUPS)
                after(dve, v.tensor_tensor(e3, logits[:, t, N_GROUPS:].rearrange("p (g e) -> p g e", g=N_GROUPS), mine_, ALU.mult), chain)
                after(dve, v.tensor_scalar(onehot[:, t, 0:N_GROUPS], onehot[:, t, 0:N_GROUPS], -1.0, -MASKED, ALU.add, ALU.mult), chain)
                after(dve, v.tensor_tensor(e3, e3, mine_, ALU.add), chain)
                after(dve, v.max(top[:, t, 1, :], elog[:, t, :]), chain)
                after(dve, v.max_index(where[:, t, 1, :], top[:, t, 1, :], elog[:, t, :]), chain)
                after(dve, v.tensor_copy(wheref[:, t, 1, :], where[:, t, 1, :]), chain)
                after(dve, v.tensor_scalar(glog[:, t, :], glog[:, t, :], top[:, t, 0, 0:1], None, ALU.subtract), chain)
                after(dve, v.tensor_tensor(c[:, t, 0:1], top[:, t, 1, 1:2], top[:, t, 1, 0:1], ALU.subtract), chain)
            v.nop().then_inc(argued.sem, argued.one())
            for t in range(NX):
                after(dve, v.tensor_scalar(chosen[:, t, :], iota, wheref[:, t, 1, 0:1], None, ALU.is_equal), chain)
                after(dve, v.scalar_tensor_tensor(out=chosen[:, t, :], in0=iota, scalar=wheref[:, t, 1, 1:2],
                                                  in1=chosen[:, t, :], op0=ALU.is_equal, op1=ALU.add), chain)
            v.nop().then_inc(picked.sem, picked.one())
            dve.wait_ge(expd.sem, expd.at(1))
            for t in range(NX):
                after(dve, v.tensor_reduce(c[:, t, 2:3], onehot[:, t, :], AX, ALU.add), chain)
                after(dve, v.tensor_scalar(c[:, t, 3:4], c[:, t, 1:2], 1.0, None, ALU.add), chain)
                after(dve, v.tensor_tensor(c[:, t, 3:4], c[:, t, 3:4], c[:, t, 2:3], ALU.mult), chain)
                after(dve, v.reciprocal(c[:, t, 4:5], c[:, t, 3:4]), chain)
                after(dve, v.tensor_tensor(c[:, t, 5:6], c[:, t, 4:5], c[:, t, 1:2], ALU.mult), chain)
                after(dve, v.tensor_scalar(gates[:, t, :], iota, wheref[:, t, 1, 0:1], c[:, t, 4:5], ALU.is_equal, ALU.mult), chain)
                after(dve, v.tensor_scalar(elog[:, t, :], iota, wheref[:, t, 1, 1:2], c[:, t, 5:6], ALU.is_equal, ALU.mult), chain)
                after(dve, v.tensor_tensor(gates[:, t, :], gates[:, t, :], elog[:, t, :], ALU.add), chain)
            dve.wait_ge(ranked.sem, ranked.at(1))
            upto = ps[2][:, 0:NX * N_EXP].rearrange("p (t e) -> p t e", t=NX)
            after(dve, v.tensor_tensor(place[:], upto, chosen[:], ALU.mult), chain)
            after(dve, v.tensor_scalar(place[:], place[:], -1.0, None, ALU.add), chain)
            after(dve, v.tensor_reduce(count[:], ps[3][:, 0:N_EXP], AX, ALU.max), chain)
            v.tensor_copy(m.longest[:], count[:])


def experts(m):
    with ExitStack() as own:
        h = m.sb("h_tok", [P, NX, D], own)
        route(m, own, h)
        with ExitStack() as mine:
            expert_lists(m, mine, h)
        with ExitStack() as mine:
            expert_overflow(m, mine)


def expert_lists(m, own, h):
    nc, ps = m.nc, m.ps
    PAIRS = N_EXP // 2
    F = D_EXP
    pick = m.sb("pick", [P, NX, 2, SLOTS], own)
    give = m.sb("give", [P, NX, 2, SLOTS], own)
    xs = m.sb("picked_tokens", [P, KD, 2 * SLOTS], own)
    hid = m.sb("hidden", [2 * SLOTS, F], own)
    hidT = m.sb("hiddenT", [P, F // P, 2 * SLOTS], own)
    giveT = m.sb("giveT", [P, N], own)
    ys = m.sb("expert_out", [P, 2, 512], own)
    zero = m.sb("zero", [P, 512], own)
    iota = m.rows[:, ROW["iota"][0]:ROW["iota"][1]].unsqueeze(1).unsqueeze(1).broadcast_to([P, NX, 2, SLOTS])
    with m.step() as block:
        picking, picked, xs_ready = m.sig("pick_ready"), m.sig("picked_in_psum"), m.sig("picked_copied")
        mid, expd, hidden = m.sig("expert_mid_in_psum"), m.sig("gate_exp_ready"), m.sig("hidden_ready")
        giving, turned, copied = m.sig("give_ready"), m.sig("hiddenT_in_psum"), m.sig("hiddenT_copied")
        downed, ys_ready = m.sig("expert_out_in_psum"), m.sig("expert_out_copied")
        summed, zeroed = m.sig("experts_summed"), m.sig("zero_ready")
        slot_loaded = [m.sig(f"slot{s}_loaded") for s in range(MOE_RING)]
        first_load = [m.loaded(N_DENSE + s)[1] for s in range(MOE_RING)]
        xbank = lambda k: ps[4 + k // 4][:, k % 4 * P:(k % 4 + 1) * P]

        @block.sync
        def _(sp):
            def reload(pair, s):
                sp.dma_start(m.slots[s][:], m.dram["panels"][bass.ds(pair * MOE_RING + N_DENSE + s, 1)]
                             .rearrange("o p c -> (o p) c")).then_inc(slot_loaded[s].sem, 16)
            with sp.Fori(1, PAIRS) as pair:
                for kind in range(2):
                    sp.wait_ge(mid.sem, pair * 2 + mid.base + kind - 1)
                    reload(pair, kind)
                    reload(pair, 3 + kind)
                sp.wait_ge(downed.sem, pair + downed.base)
                reload(pair, 2)
                reload(pair, 5)

        @block.tensor
        def _(pe):
            def gather(pair):
                pe.wait_ge(picking.sem, pair + picking.base + 1)
                for k in range(KD):
                    for t in range(NX):
                        last = nc.tensor.matmul(xbank(k), h[:, t, k * P:(k + 1) * P],
                                                pick[:, t].rearrange("p a s -> p (a s)"), start=t == 0, stop=t == NX - 1)
                last.then_inc(picked.sem, 1)

            def first_half(pair):
                pe.wait_ge(xs_ready.sem, pair + xs_ready.base + 1)
                for kind in range(2):
                    for a in range(2):
                        pe.wait_ge(slot_loaded[3 * a + kind].sem, pair * 16 + first_load[3 * a + kind])
                    for k in range(KD):
                        for a in range(2):
                            last = nc.tensor.matmul(ps[6 + kind][a * SLOTS:(a + 1) * SLOTS, :],
                                                    xs[:, k, a * SLOTS:(a + 1) * SLOTS],
                                                    m.slots[3 * a + kind][:, k * F:(k + 1) * F], start=k == 0, stop=k == KD - 1)
                    last.then_inc(mid.sem, 1)

            def combine(pair):
                pe.wait_ge(ys_ready.sem, pair + ys_ready.base + 1)
                for t in range(NX):
                    for n in range(2):
                        last = nc.tensor.matmul(ps[2 * t + n][:, :], giveT[:, t * P:(t + 1) * P], ys[:, n, :],
                                                start=False, stop=False)
                return last

            def second_half(pair, more):
                pe.wait_ge(hidden.sem, pair + hidden.base + 1)
                for c in range(F // P):
                    nc.tensor.transpose(ps[6][:, c * P:(c + 1) * P], hid[:, c * P:(c + 1) * P], m.ident[:, :])
                pe.wait_ge(giving.sem, pair + giving.base + 1)
                for t in range(NX):
                    last = nc.tensor.transpose(ps[7][:, t * P:(t + 1) * P], give[:, t].rearrange("p a s -> p (a s)"),
                                               m.ident[:, :])
                last.then_inc(turned.sem, 1)
                pe.wait_ge(copied.sem, pair + copied.base + 1)
                if more:
                    pe.wait_ge(xs_ready.sem, pair + xs_ready.base + 2)
                for a in range(2):
                    pe.wait_ge(slot_loaded[3 * a + 2].sem, pair * 16 + first_load[3 * a + 2])
                for c in range(F // P):
                    for n in range(2):
                        for a in range(2):
                            last = nc.tensor.matmul(ps[4 + n][a * SLOTS:(a + 1) * SLOTS, :], hidT[:, c, a * SLOTS:(a + 1) * SLOTS],
                                                    m.slots[3 * a + 2][:, c * D + n * 512:c * D + (n + 1) * 512],
                                                    start=c == 0, stop=c == F // P - 1)
                last.then_inc(downed.sem, 1)

            pe.wait_ge(zeroed.sem, zeroed.at(1))
            for b in range(4):
                nc.tensor.matmul(ps[b][:, :], zero[:, 0:P], zero[:, :], start=True, stop=False)
            gather(0)
            first_half(0)
            gather(1)
            second_half(0, True)
            with pe.Fori(1, PAIRS - 1) as pair:
                first_half(pair)
                combine(pair - 1)
                gather(pair + 1)
                second_half(pair, True)
            first_half(PAIRS - 1)
            combine(PAIRS - 2)
            second_half(PAIRS - 1, False)
            combine(PAIRS - 1)
            for b in range(4):
                last = nc.tensor.matmul(ps[b][:, :], zero[:, 0:P], zero[:, :], start=False, stop=True)
            last.then_inc(summed.sem, summed.one())

        @block.scalar
        def _(act):
            def take_picked(pair):
                act.wait_ge(picked.sem, pair + picked.base + 1)
                for half in range(2):
                    last = nc.scalar.activation(xs[:, 4 * half:4 * half + 4, :].rearrange("p k s -> p (k s)"),
                                                ps[4 + half][:, :], ACT.Copy)
                last.then_inc(xs_ready.sem, 1)

            def body(pair, more):
                act.wait_ge(mid.sem, pair * 2 + mid.base + 1)
                nc.scalar.activation(hid[:], ps[6][:, :], ACT.Exp, scale=-1.0).then_inc(expd.sem, 1)
                if more:
                    take_picked(pair + 1)
                act.wait_ge(turned.sem, pair + turned.base + 1)
                nc.scalar.activation(hidT[:].rearrange("p c s -> p (c s)"), ps[6][:, :], ACT.Copy)
                nc.scalar.activation(giveT[:], ps[7][:, 0:N], ACT.Copy).then_inc(copied.sem, 1)
                act.wait_ge(downed.sem, pair + downed.base + 1)
                for n in range(2):
                    last = nc.scalar.activation(ys[:, n, :], ps[4 + n][:, :], ACT.Copy)
                last.then_inc(ys_ready.sem, 1)

            take_picked(0)
            body(0, True)
            with act.Fori(1, PAIRS - 1) as pair:
                body(pair, True)
            body(PAIRS - 1, False)

        @block.vector
        def _(dve):
            nc.vector.memset(zero[:], 0.0).then_inc(zeroed.sem, zeroed.one())
            chain = m.sig("expert_chain")
            PER_PAIR = 4

            def of_pair(col, pair, static):
                e = col[:, :, 2 * pair:2 * pair + 2] if static else col[:, :, bass.ds(pair * 2, 2)]
                return e.unsqueeze(3).broadcast_to([P, NX, 2, SLOTS])

            def build_pick(pair, static):
                nc.vector.tensor_tensor(pick[:], iota, of_pair(m.place, pair, static), ALU.is_equal).then_inc(picking.sem, 1)

            def body(pair, static, first, more):
                at = [0]

                def link(ins):
                    at[0] += 1
                    ins.then_inc(chain.sem, 1)
                    dve.wait_ge(chain.sem, pair * PER_PAIR + chain.base + at[0])

                if more:
                    dve.wait_ge(picked.sem, pair + picked.base + 1)
                    build_pick(pair + 1, static)
                if not first:
                    dve.wait_ge(turned.sem, pair + turned.base)
                link(nc.vector.tensor_tensor(give[:], iota, of_pair(m.place, pair, static), ALU.is_equal))
                nc.vector.tensor_tensor(give[:], give[:], of_pair(m.gates, pair, static), ALU.mult).then_inc(giving.sem, 1)
                dve.wait_ge(expd.sem, pair + expd.base + 1)
                link(nc.vector.tensor_scalar(hid[:], hid[:], 1.0, None, ALU.add))
                link(nc.vector.reciprocal(hid[:], hid[:]))
                link(nc.vector.tensor_tensor(hid[:], ps[6][:, :], hid[:], ALU.mult))
                dve.wait_ge(mid.sem, pair * 2 + mid.base + 2)
                nc.vector.tensor_tensor(hid[:], hid[:], ps[7][:, :], ALU.mult).then_inc(hidden.sem, 1)
                assert at[0] == PER_PAIR

            build_pick(0, True)
            body(0, True, True, True)
            with dve.Fori(1, PAIRS - 1) as pair:
                body(pair, False, False, True)
            body(PAIRS - 1, True, False, False)
            dve.wait_ge(summed.sem, summed.at(1))
            for t in range(NX):
                for n in range(2):
                    part = m.x[:, t, n * 512:(n + 1) * 512]
                    nc.vector.tensor_tensor(part, part, ps[2 * t + n][:, :], ALU.add)


def expert_overflow(m, own):
    nc, ps = m.nc, m.ps
    spread = m.sb("gate_rows", [P, N_EXP, N], own)
    left = m.sb("gates_left", [P, NX, N_EXP], own)
    leftT = m.sb("gates_leftT", [N_EXP, N], own)
    sel = m.slots[4][0:N_EXP, :].rearrange("k (e p) -> k e p", e=N_EXP)
    ex = m.sb("expert_exp", [P, 2, N], own)
    hidT = m.sb("hiddenT", [P, 4, N], own)
    zero = m.sb("zero", [P, 512], own)
    names = ("landed", "loaded", "left_ready", "leftT_in_psum", "leftT_copied", "row_in_psum", "row_taken", "gate_in",
             "exp_ready", "hidden_ready", "down_done", "summed", "chain")
    with m.step() as block:
        (landed, loaded, left_ready, turned, copied, wide, taken, mid, expd, hidden, downed, summed,
         chain) = (m.sig("overflow_" + n).sem for n in names)
        xT = m.hT
        bank = lambda kind, c: ps[4 + 2 * (c % 2) + kind][:, 0:N]

        def overflows(eng):
            return eng.value_load(m.longest[0:1, 0:1], min_val=0, max_val=2 * N) > SLOTS

        @block.sync
        def _(sp):
            with sp.If(overflows(sp)):
                sp.dma_start(sel, m.dram["selector"]).then_inc(landed, 16)

                def load(e):
                    for s in range(3):
                        sp.dma_start(m.slots[s][:], m.dram["panels"][bass.ds(e * 3 + N_DENSE + s, 1)]
                                     .rearrange("o p c -> (o p) c")).then_inc(loaded, 16)
                load(0)
                with sp.Fori(1, N_EXP) as e:
                    sp.wait_ge(downed, e)
                    load(e)

        @block.tensor
        def _(pe):
            with pe.If(overflows(pe)):
                pe.wait_ge(left_ready, 1)
                for t in range(NX):
                    last = nc.tensor.transpose(ps[2][0:N_EXP, t * P:(t + 1) * P], left[:, t, :], m.ident[:, :])
                last.then_inc(turned, 1)
                pe.wait_ge(landed, 16)
                pe.wait_ge(copied, 1)
                for e in range(N_EXP):
                    if e >= 4:
                        pe.wait_ge(taken, e - 3)
                    nc.tensor.matmul(ps[4 + e % 4][:, 0:N], sel[:, e, :], leftT[:, :], start=True, stop=True).then_inc(wide, 1)
                pe.wait_ge(taken, N_EXP)
                for b in range(4):
                    nc.tensor.matmul(ps[b][:, :], zero[:, 0:P], zero[:, :], start=True, stop=False)
                with pe.Fori(0, N_EXP) as e:
                    pe.wait_ge(loaded, e * 48 + 48)
                    for c in range(4):
                        if c >= 2:
                            pe.wait_ge(hidden, e * 4 + c - 1)
                        for kind in range(2):
                            for k in range(KD):
                                last = nc.tensor.matmul(bank(kind, c), m.slots[kind][:, k * 512 + c * P:k * 512 + (c + 1) * P],
                                                        xT[:, k, 0:N], start=k == 0, stop=k == KD - 1)
                        last.then_inc(mid, 1)
                    pe.wait_ge(hidden, e * 4 + 4)
                    for c in range(4):
                        for t in range(NX):
                            for n in range(2):
                                last = nc.tensor.matmul(ps[2 * t + n][:, :], hidT[:, c, t * P:(t + 1) * P],
                                                        m.slots[2][:, c * D + n * 512:c * D + (n + 1) * 512],
                                                        start=False, stop=False)
                    last.then_inc(downed, 1)
                for b in range(4):
                    last = nc.tensor.matmul(ps[b][:, :], zero[:, 0:P], zero[:, :], start=False, stop=True)
                last.then_inc(summed, 1)

        @block.scalar
        def _(act):
            with act.If(overflows(act)):
                for e in range(N_EXP):
                    act.wait_ge(wide, e + 1)
                    nc.scalar.activation(spread[:, e, :], ps[4 + e % 4][:, 0:N], ACT.Copy).then_inc(taken, 1)
                with act.Fori(0, N_EXP) as e:
                    for c in range(4):
                        act.wait_ge(mid, e * 4 + c + 1)
                        nc.scalar.activation(ex[:, c % 2, :], bank(0, c), ACT.Exp, scale=-1.0).then_inc(expd, 1)

        @block.vector
        def _(dve):
            with dve.If(overflows(dve)):
                nc.vector.memset(zero[:], 0.0).then_inc(chain, 1)
                nc.vector.tensor_scalar(left[:], m.place[:], float(SLOTS), None, ALU.is_ge).then_inc(chain, 1)
                dve.wait_ge(chain, 2)
                nc.vector.tensor_tensor(left[:], left[:], m.gates[:], ALU.mult).then_inc(left_ready, 1)
                dve.wait_ge(turned, 1)
                nc.vector.tensor_copy(leftT[:], ps[2][0:N_EXP, 0:N]).then_inc(copied, 1)
                dve.wait_ge(taken, N_EXP)
                with dve.Fori(0, N_EXP) as e:
                    for c in range(4):
                        t = ex[:, c % 2, :]
                        before = e * 16 + 4 * c + 2
                        dve.wait_ge(expd, e * 4 + c + 1)
                        nc.vector.tensor_scalar(t, t, 1.0, None, ALU.add).then_inc(chain, 1)
                        dve.wait_ge(chain, before + 1)
                        nc.vector.reciprocal(t, t).then_inc(chain, 1)
                        dve.wait_ge(chain, before + 2)
                        nc.vector.tensor_tensor(t, bank(0, c), t, ALU.mult).then_inc(chain, 1)
                        dve.wait_ge(chain, before + 3)
                        row = spread[:, bass.ds(e, 1), :].rearrange("p o n -> p (o n)")
                        nc.vector.tensor_tensor(t, t, row, ALU.mult).then_inc(chain, 1)
                        dve.wait_ge(chain, before + 4)
                        nc.vector.tensor_tensor(hidT[:, c, :], bank(1, c), t, ALU.mult).then_inc(hidden, 1)
                dve.wait_ge(summed, 1)
                for t in range(NX):
                    for n in range(2):
                        part = m.x[:, t, n * 512:(n + 1) * 512]
                        nc.vector.tensor_tensor(part, part, ps[2 * t + n][:, :], ALU.add)


def finish(m):
    nc = m.nc
    with m.step() as block:
        g_final = m.sb("g_final", [P, D])
        squares, done, stored = m.sig("squares_summed"), m.sig("out_ready"), m.sig("out_stored")
        landed = m.sig("g_final_landed")

        @block.scalar
        def _(act):
            for t in range(NX):
                after(act, nc.scalar.activation(m.scratch[:, t, :], m.x[:, t, :], ACT.Square,
                                                accum_out=m.sums[:, t:t + 1]), m.sig("act_chain"))
            nc.scalar.nop().then_inc(squares.sem, squares.one())
            rough_rstd(m, act, m.var[:, 0:NX], m.rstd[:, 0:NX])

        @block.vector
        def _(dve):
            dve.wait_ge(squares.sem, squares.at(1))
            variance(m, dve, m.var[:, 0:NX], m.sums[:, 0:NX], 1.0 / D)
            fine_rstd(m, dve, m.var[:, 0:NX], m.rstd[:, 0:NX], m.tmp[:, 0:NX])
            dve.wait_ge(landed.sem, landed.at(16))
            for t in range(NX):
                nc.vector.scalar_tensor_tensor(out=m.scratch[:, t, :], in0=m.x[:, t, :], scalar=m.rstd[:, t:t + 1],
                                               in1=g_final[:],
                                               op0=ALU.mult, op1=ALU.mult).then_inc(done.sem, done.one())

        @block.sync
        def _(sp):
            sp.dma_start(g_final[:], m.dram["g_final"]).then_inc(landed.sem, landed.sixteen())
            for t in range(NX):
                sp.wait_ge(done.sem, done.at(t + 1))
                sp.dma_start(m.dram["out"][0, t * P:(t + 1) * P, :], m.scratch[:, t, :]).then_inc(stored.sem, stored.sixteen())
            sp.wait_ge(stored.sem, stored.at(16 * NX))


def build(nc, dram):
    with ExitStack() as stack:
        m = Core(nc, stack, dram)
        m.vecs = m.sb("vecs", [P, VEC["width"]])
        m.cst = m.sb("cst", [P, CST["width"]])
        m.rows = m.sb("rows", [P, ROW["width"]])
        m.x = m.sb("x_tok", [P, NT, D])
        m.hT = m.sb("hT", [P, KD, 512])
        m.scratch = m.sb("scratch", [P, 2, D])
        m.gate = m.sb("gate_rows_all", [P, 2, D])
        m.scale1 = m.sb("scale1", [P, 2, KD])
        m.shift = m.sb("shift", [P, 2, KD])
        m.cond = m.sb("cond", [P, 2 * KD])
        m.cond_wide = m.sb("cond_wide", [P, KD, 32])
        m.neg_sink = m.sb("neg_sink", [P, B_H])
        m.sums, m.var, m.rstd, m.tmp = (m.sb(n, [P, NORM + NT]) for n in ("sums", "var", "rstd", "tmp8"))
        m.slots = [m.sb(f"slot{i}", [P, SLOT]) for i in range(RING)]
        cst = lambda name: m.cst[:, CST[name][0]:CST[name][1]]
        m.ident = cst("ident")
        m.cos = cst("cos").rearrange("p (t c) -> p t c", t=NX)
        m.sin = cst("sin").rearrange("p (t c) -> p t c", t=NX)
        m.sel = cst("sel").rearrange("p (h q) -> p h q", h=4)
        m.mod_sel = cst("mod_sel").rearrange("p (s q) -> p s q", s=2)
        m.mod_fold = cst("mod_fold")
        load_constants(m)
        outs = {0: "a_out0", 1: "b_out", 2: "c_out"}
        with ExitStack() as layers:
            m.gT = m.sb("gT", [P, KD, 512], layers)
            for layer in range(DEPTH):
                enter_layer(m, layer, outs[layer - 1] if layer else None)
                if layer % 3 == 0:
                    latent_layer(m, layer)
                elif layer % 3 == 1:
                    window_layer(m)
                else:
                    conv_layer(m)
            project_out(m, "a_out3", NX, True)
        second_mixer(m)
        m.slots += [m.sb(f"slot{i}", [P, SLOT]) for i in range(RING, MOE_RING)]
        experts(m)
        finish(m)


def by_channel(a):
    a = np.asarray(a)
    return np.moveaxis(a.reshape(-1, P), 0, 1)


def k_major(w, cols=None):
    w = np.asarray(w)
    return w.reshape(w.shape[0] // P, P, w.shape[1]).transpose(1, 0, 2).reshape(P, -1)


def pad(a, rows=P):
    a = np.asarray(a)
    return np.concatenate([a, np.zeros((rows - a.shape[0],) + a.shape[1:], a.dtype)], 0)


def constants():
    f = np.float32
    tok = np.arange(N)
    inv = ROPE_BASE ** (-np.arange(0, 32, 2) / 32.0)
    ang = np.concatenate([(tok // GRID_W)[:, None] * inv, (tok % GRID_W)[:, None] * inv], 1)
    by_tile = lambda a: a.reshape(NX, P, -1).transpose(1, 0, 2).reshape(P, -1)
    mod_sel = np.zeros((P, 2, P))
    for s in range(2):
        mod_sel[s::32, s] = 1
    sel = np.zeros((P, 4, P))
    for h in range(4):
        sel[h, h] = 1
    cst = np.concatenate([np.eye(P), by_tile(np.cos(ang)), by_tile(np.sin(ang)), sel.reshape(P, -1),
                          mod_sel.reshape(P, -1), mod_sel[:, :, 0]], 1)
    q, k = np.arange(P)[:, None], np.arange(P)[None, :]
    band = np.stack([np.where(k + P - q <= B_WINDOW, 0.0, MASKED), np.where(q + P - k <= B_WINDOW, 0.0, MASKED)], 1)
    n2 = 2 * N
    freq = np.arange(N)
    turn = 2 * np.pi * np.outer(tok, freq) / n2
    cos, sin, nyq = np.cos(turn), np.sin(turn), (-1.0) ** tok
    sin_n, cos_n = sin.copy(), cos[:, 0:P].copy()
    sin_n[:, 0], cos_n[:, 0] = nyq, nyq
    dft = np.concatenate([cos, sin_n, sin[:, 0:P], cos_n], 1)
    idft = np.concatenate([2 * cos.T / n2, 2 * sin.T / n2], 0)
    idft[0] /= 2
    idft[N] = nyq / n2
    t = np.linspace(0, 1, N)[:, None]
    w = 2 * np.pi / N * tok[:, None]
    bands = np.linspace(1e-4, C_BANDS - 1, C_BANDS)[None]
    z = np.concatenate([t, np.cos(bands * w), -np.sin(bands * w)], -1)
    decay = np.exp(-t * np.abs(np.linspace(C_MIN_DECAY, C_MAX_DECAY, D)))
    tri = (tok[:, None] <= tok[None, :]) * 1.0
    counts = np.stack([1.0 / np.minimum(tok + 1, wdw) for wdw in POOL_WINDOWS])
    selector = np.zeros((N_EXP, N_EXP, P))
    selector[np.arange(N_EXP), np.arange(N_EXP)] = 1
    out = dict(cst=cst, band=band, zT=z.T, decay=by_tile(decay), dft=by_tile(dft).reshape(P, NX, 6 * P),
               idft=idft.reshape(4, P, N).transpose(1, 0, 2), tri=by_tile(tri).reshape(P, NX, N),
               causal=by_tile(np.where(tri.T > 0, 0.0, MASKED)).reshape(P, NX, N),
               counts=np.broadcast_to(counts, (P, 4, N)), selector=selector)
    return {k: np.ascontiguousarray(a, f) for k, a in out.items()}


def lay_out(i):
    a = {k: np.asarray(v) for k, v in i.items()}
    cst = constants()
    panels = []

    def add(name, w):
        w = w.reshape(P, -1)
        assert w.shape[1] <= SLOT and panel_plan()[len(panels)][1] == w.shape[1], (name, w.shape)
        panels.append(w)

    for layer in range(DEPTH):
        for n in range(6):
            add("mod", k_major(a["w_mod"][layer][:, n * 512:(n + 1) * 512]))
        if layer % 3 == 0:
            j = layer // 3
            w = a["a_w_in"][j]
            at = A_QR + A_KVR + A_ROPE
            for lo, hi in ((0, A_QR), (A_QR, at), (at, at + 512), (at + 512, at + D)):
                add("a_in", k_major(w[:, lo:hi]))
            for n in range(2):
                add("a_q", k_major(a["a_w_q"][j][:, n * 768:(n + 1) * 768]))
            add("a_kv", k_major(a["a_w_kv"][j]))
            out = a["a_w_out"][j]
        elif layer % 3 == 1:
            for n in range(5):
                add("b_in", k_major(a["b_w_in"][0][:, n * 512:(n + 1) * 512]))
            out = a["b_w_out"][0]
        else:
            for n in range(8):
                add("c_in", k_major(a["c_w_in"][0][:, n * 512:(n + 1) * 512]))
            add("c_decay", np.concatenate([cst["decay"], pad(a["c_filt_bias"][0].reshape(1, -1))], 1))
            add("c_w3", pad(a["c_f_w3"][0]))
            out = a["c_w_out"][0]
        for n in range(2):
            add("out", k_major(out[:, n * 512:(n + 1) * 512]))
    w = a["w_in_2"][0]
    at_if = 5 * 512
    cols = [n * 512 for n in range(5)] + [at_if + 8 + n * 512 for n in range(4)]
    for c in cols:
        add("s_in", k_major(w[:, c:c + 512]))
    add("s_pool", a["w_pool_2"][0].transpose(1, 0, 2))
    add("s_br_a", k_major(a["w_br_a_2"][0]))
    add("s_br_b", k_major(a["w_br_b_2"][0]))
    for n in range(2):
        add("s_out", k_major(a["w_out_2"][0][:, n * 512:(n + 1) * 512]))
    assert len(panels) == N_DENSE
    all_panels = np.zeros((N_DENSE + 3 * N_EXP, P, SLOT), np.float32)
    for n, w_ in enumerate(panels):
        all_panels[n, :, :w_.shape[1]] = w_
    ex = all_panels[N_DENSE:].reshape(N_EXP, 3, P, SLOT)
    for kind, name in enumerate(("w_e_gate_2", "w_e_up_2", "w_e_down_2")):
        e = a[name][0]
        kt = e.shape[1] // P
        ex[:, kind] = e.reshape(N_EXP, kt, P, e.shape[2]).transpose(0, 2, 1, 3).reshape(N_EXP, P, SLOT)

    vecs = np.concatenate([
        by_channel(a["g_pre"]), by_channel(a["a_g_q"]), by_channel(a["a_g_kv"]), by_channel(a["c_conv_w"][0]),
        by_channel(a["c_conv_b"][0]), pad(a["c_f_b1"][0][:, None]), pad(a["c_f_freq"][0][:, None]),
        pad(a["c_f_b2"][0][:, None]), pad(a["c_f_w1"][0]), pad(a["c_f_w2"][0]), by_channel(a["g_mix_2"][0]),
        by_channel(a["g_head_2"][0]), by_channel(a["pool_scale_2"][0]),
        by_channel(a["conv_q_2"][0]), by_channel(a["conv_k_2"][0]), by_channel(a["c"][0]), by_channel(a["c_ctx"]),
        k_major(w[:, at_if:at_if + 8]), k_major(np.concatenate([a["w_rg_2"][0], a["w_re_2"][0]], 1)),
    ], 1)
    assert vecs.shape[1] == VEC["width"]
    row = np.concatenate([a["b_sink"][0], a["b_rg_2"][0], a["b_re_2"][0], a["b_if_2"][0],
                          np.arange(SLOTS, dtype=np.float32)])
    mod_rows = np.zeros((DEPTH, P, 4 * D), np.float32)
    mod_rows[:, 0:2, 0:3 * D] = a["b_mod"][:, None]
    mod_rows[:, :, 3 * D:] = a["g_post"][:, None]
    return dict(
        panels=all_panels, vecs=vecs, g_final=np.broadcast_to(a["g_final_2"], (P, D)), g_ffn=np.broadcast_to(a["g_ffn_2"][0], (P, D)), rows=np.broadcast_to(row, (P, len(row))),
        tokens=np.concatenate([a["x"][0], a["ctx"][0]], 0),
        mod_rows=mod_rows,
        **{k: cst[k] for k in ("cst", "band", "zT", "dft", "idft", "tri", "causal", "counts", "selector")})


def kernel(**inputs):
    import concourse.bacc as bacc
    from concourse.bass_utils import run_bass_kernel_spmd

    arrays = {k: np.ascontiguousarray(v) for k, v in lay_out(inputs).items()}
    nc = bacc.Bacc("TRN2", target_bir_lowering=False, num_devices=1)
    dram = {k: nc.dram_tensor(k + "_dram", v.shape, F32, kind="ExternalInput").ap() for k, v in arrays.items()}
    dram["out"] = nc.dram_tensor("out_dram", (1, N, D), F32, kind="ExternalOutput").ap()
    build(nc, dram)
    r = run_bass_kernel_spmd(nc, [{k + "_dram": v for k, v in arrays.items()}], core_ids=[0])
    return r.results[0]["out_dram"]
```

```python
import math
from contextlib import ExitStack, contextmanager

import numpy as np

import concourse.bass as bass
from concourse import mybir

F32 = mybir.dt.float32
U32 = mybir.dt.uint32
ALU = mybir.AluOpType
ACT = mybir.ActivationFunctionType
AX = mybir.AxisListType.X

P = 128
D = 1024
KD = D // P
N = 256
NX = N // P
NT = 2 * NX
DEPTH = 4
EPS = 1e-6
NORM = 2 * NT
GRID_W = 64
ROPE_BASE = 10000.0
MASKED = -1e30

A_H, A_QR, A_KVR, A_NOPE, A_ROPE, A_V = 8, 512, 256, 128, 64, 128
B_H, B_KVH, B_HD, B_WINDOW = 16, 4, 64, 128
C_BANDS = 16
C_EMB = 1 + 2 * C_BANDS
C_FFN = 64
C_MIN_DECAY = math.log(1e-2) / 1.5
C_MAX_DECAY = math.log(1e-2) / 0.3

POOL_WINDOWS = (2, 4, 8, 16)
POOL_PAD = 16
M_H, M_HD = 4, 128
CONV_K = 4
N_GROUPS, PER_GROUP = 4, 8
N_EXP = N_GROUPS * PER_GROUP
D_EXP = 512
N_ROUTE = N_GROUPS + N_EXP

SLOT = 4096
RING = 4
SLOTS = 64
MOD_SLOTS = 3
MOE_RING = 6


def columns(fields):
    at, out = 0, {}
    for name, width in fields:
        out[name] = (at, at + width)
        at += width
    out["width"] = at
    return out


VEC = columns([
    ("g_pre", DEPTH * KD), ("a_g_q", 2 * 4), ("a_g_kv", 2 * 2), ("conv_w", 3 * 24), ("conv_b", 24),
    ("f_b1", 1), ("f_freq", 1), ("f_b2", 1), ("f_w1", C_FFN), ("f_w2", C_FFN),
    ("g_mix", KD), ("g_head", 4), ("pool_scale", 4), ("conv_q", 4 * 4), ("conv_k", 4 * 4),
    ("cond", 2 * KD), ("w_if", KD * 8), ("w_route", KD * N_ROUTE),
])
ROW = columns([("sink", B_H), ("b_route", N_ROUTE), ("b_if", 8), ("iota", SLOTS)])
CST = columns([("ident", P), ("cos", NX * 32), ("sin", NX * 32), ("sel", 4 * P), ("mod_sel", 2 * P)])


def panel_plan():
    plan = []
    for layer in range(DEPTH):
        plan += [(f"mod{layer}.{n}", SLOT) for n in range(6)]
        if layer % 3 == 0:
            plan += [(f"a_cq{layer}", SLOT), (f"a_ckv{layer}", 8 * (A_KVR + A_ROPE))]
            plan += [(f"a_gate{layer}.{n}", SLOT) for n in range(2)]
            plan += [(f"a_q{layer}.{n}", 4 * 768) for n in range(2)]
            plan += [(f"a_kv{layer}", SLOT)]
            plan += [(f"a_out{layer}.{n}", SLOT) for n in range(2)]
        elif layer % 3 == 1:
            plan += [(f"b_in.{n}", SLOT) for n in range(5)]
            plan += [(f"b_out.{n}", SLOT) for n in range(2)]
        else:
            plan += [(f"c_in.{n}", SLOT) for n in range(8)]
            plan += [("c_decay", SLOT), ("c_w3", SLOT)]
            plan += [(f"c_out.{n}", SLOT) for n in range(2)]
    plan += [(f"s_in.{n}", SLOT) for n in range(5)]
    plan += [("s_pool", 512)]
    plan += [(f"s_gates.{n}", SLOT) for n in range(4)]
    plan += [("s_br_a", SLOT), ("s_br_b", SLOT)]
    plan += [(f"s_out.{n}", SLOT) for n in range(2)]
    return plan


N_DENSE = len(panel_plan())


def slot_table():
    table, at = [], 0
    for name, _ in panel_plan():
        if name.startswith("mod") and int(name[-1]) >= 6 - MOD_SLOTS:
            table.append(MOE_RING + int(name[-1]) - 6 + MOD_SLOTS)
        else:
            table.append(at % RING)
            at += 1
    return table


SLOT_TABLE = slot_table()


def slot_of(i):
    return SLOT_TABLE[i] if i < N_DENSE else (i - N_DENSE) % MOE_RING


class Signal:

    def __init__(self, sem):
        self.sem, self.total, self.base = sem, 0, 0

    def one(self):
        self.total += 1
        return 1

    def sixteen(self):
        self.total += 16
        return 16

    def at(self, n):
        return self.base + n


class Core:

    def __init__(self, nc, stack, dram):
        self.nc, self.stack, self.dram = nc, stack, dram
        self.signals, self.names = {}, {}
        self.plan = panel_plan()
        self.next_panel = 0
        self.ps = [stack.enter_context(nc.psum_tensor(f"bank{i}", [P, 512], F32)) for i in range(8)]

    def sb(self, name, shape, stack=None, dt=F32):
        again = self.names[name] = self.names.get(name, 0) + 1
        name = name if again == 1 else f"{name}_{again}"
        return (stack or self.stack).enter_context(self.nc.sbuf_tensor(name, shape, dt))

    def sig(self, name):
        if name not in self.signals:
            self.signals[name] = Signal(self.stack.enter_context(self.nc.semaphore(name)))
        return self.signals[name]

    @contextmanager
    def step(self):
        for s in self.signals.values():
            s.base = s.total
        with self.nc.Block(no_gpsimd_drain=True) as block:
            yield block

    def slot(self, i):
        s = slot_of(i)
        return self.slots[s] if s < MOE_RING else self.mod_slots[s - MOE_RING]

    def loaded(self, i):
        s = slot_of(i)
        before = sum(1 for j in range(i + 1) if slot_of(j) == s)
        return self.sig(f"slot{s}_loaded").sem, 16 * before

    def issue(self, sp, i):
        width = self.plan[i][1] if i < N_DENSE else SLOT
        g = self.sig(f"slot{slot_of(i)}_loaded")
        sp.dma_start(self.slot(i)[:, 0:width], self.dram["panels"][i, :, 0:width]).then_inc(g.sem, g.sixteen())

    def followers(self, i):
        s = slot_of(i)
        return [j for j in range(i + 1, min(i + 1 + 2 * MOE_RING, N_DENSE + MOE_RING)) if slot_of(j) == s][:1]

    def take(self, n, *names):
        got = list(range(self.next_panel, self.next_panel + n))
        self.next_panel += n
        for i, name in zip(got, names):
            assert self.plan[i][0].startswith(name), (self.plan[i], name)
        return got

    def load_next(self, sp, i):
        for j in self.followers(i):
            self.issue(sp, j)

    def vec(self, name, a=0, b=None):
        lo, hi = VEC[name]
        return self.vecs[:, lo + a:(hi if b is None else lo + b)]


def after(eng, ins, signal):
    ins.then_inc(signal.sem, signal.one())
    eng.wait_ge(signal.sem, signal.total)


def variance(m, dve, v, sums, inv_n):
    m.nc.vector.tensor_scalar(v, sums, inv_n, EPS, ALU.mult, ALU.add) \
        .then_inc(m.sig("variance_ready").sem, m.sig("variance_ready").one())


def rough_rstd(m, act, v, y, nth=1):
    s, rough = m.sig("act_chain"), m.sig("rough_rstd_ready")
    act.wait_ge(m.sig("variance_ready").sem, m.sig("variance_ready").at(nth))
    after(act, m.nc.scalar.activation(y, v, ACT.Ln), s)
    m.nc.scalar.activation(y, y, ACT.Exp, scale=-0.5).then_inc(rough.sem, rough.one())


def fine_rstd(m, dve, v, y, tmp, nth=1):
    s = m.sig("dve_chain")
    dve.wait_ge(m.sig("rough_rstd_ready").sem, m.sig("rough_rstd_ready").at(nth))
    after(dve, m.nc.vector.tensor_tensor(tmp, y, y, ALU.mult), s)
    after(dve, m.nc.vector.tensor_tensor(tmp, tmp, v, ALU.mult), s)
    after(dve, m.nc.vector.tensor_scalar(tmp, tmp, -0.5, 1.5, ALU.mult, ALU.add), s)
    after(dve, m.nc.vector.tensor_tensor(y, y, tmp, ALU.mult), s)


def load_constants(m):
    nc = m.nc
    with m.step() as block:
        landed = m.sig("constants_landed")

        @block.sync
        def _(sp):
            for dst, src in ((m.vecs, "vecs"), (m.cst, "cst")):
                sp.dma_start(dst[:], m.dram[src]).then_inc(landed.sem, landed.sixteen())
            sp.dma_start(m.rows[:], m.dram["rows"]).then_inc(landed.sem, landed.sixteen())
            for i in range(6 - MOD_SLOTS):
                m.issue(sp, i)

        @block.scalar
        def _(act):
            act.wait_ge(landed.sem, landed.at(16 * 3))
            nc.scalar.activation(m.cond[:], m.vec("cond"), ACT.Exp, scale=-1.0) \
                .then_inc(m.sig("act_chain").sem, m.sig("act_chain").one())

        @block.vector
        def _(dve):
            s = m.sig("dve_chain")
            dve.wait_ge(m.sig("act_chain").sem, m.sig("act_chain").at(1))
            nc.vector.memset(m.cond_wide[:], 0.0)
            after(dve, nc.vector.tensor_scalar(m.cond[:], m.cond[:], 1.0, None, ALU.add), s)
            after(dve, nc.vector.reciprocal(m.cond[:], m.cond[:]), s)
            after(dve, nc.vector.tensor_tensor(m.cond_wide[:, :, 0:2], m.cond[:].rearrange("p (s k) -> p k s", s=2),
                                               m.vec("cond").rearrange("p (s k) -> p k s", s=2), ALU.mult), s)


def enter_layer(m, layer, projection=None):
    nc, ps = m.nc, m.ps
    out_panels = m.take(2, projection, projection) if projection else []
    panels = m.take(6, *[f"mod{layer}.{n}" for n in range(6)])
    ringed = 6 - MOD_SLOTS
    bank = lambda t, n: ps[2 * t + n]
    turned_bank = lambda j: (2, 3, 0, 1)[j // 4]
    norm = slice(NORM, NORM + NT)
    with ExitStack() as own:
        m.mod_slots = [m.sb(f"mod_slot{i}", [P, SLOT], own) for i in range(MOD_SLOTS)]
        given = m.sb("mod_given", [P, 4 * D], own)
        row = m.hT[:].rearrange("p k t -> p (k t)")[:, 0:3 * D]
        with m.step() as block:
            landed, chunk, chunk_read = m.sig("mod_given_landed"), m.sig("mod_chunk_in_psum"), m.sig("mod_chunk_read")
            cols, gates = m.sig("mod_columns_in_psum"), m.sig("mod_gate_in_psum")
            ready, squares, added = m.sig("projected_in_psum"), m.sig("squares_summed"), m.sig("residual_added")
            tokens = m.sig("tokens_landed")

            @block.sync
            def _(sp):
                sp.dma_start(given[:], m.dram["mod_rows"][layer]).then_inc(landed.sem, landed.sixteen())
                for i in panels[ringed:]:
                    m.issue(sp, i)
                if projection:
                    for i in out_panels:
                        sp.wait_ge(ready.sem, ready.at(NT))
                        m.load_next(sp, i)
                else:
                    for t in range(NT):
                        sp.dma_start(m.x[:, t, :], m.dram["tokens"][t * P:(t + 1) * P, :]) \
                            .then_inc(tokens.sem, tokens.sixteen())
                    m.issue(sp, 6)
                for n, i in enumerate(panels[:ringed]):
                    sp.wait_ge(chunk.sem, chunk.at(n + 1))
                    m.load_next(sp, i)

            @block.tensor
            def _(pe):
                if projection:
                    for i in out_panels:
                        pe.wait_ge(*m.loaded(i))
                    for t in range(NT):
                        for n, i in enumerate(out_panels):
                            for k in range(KD):
                                last = nc.tensor.matmul(bank(t, n)[:, :], m.gT[:, k, t * P:(t + 1) * P],
                                                        m.slot(i)[:, k * 512:(k + 1) * 512], start=k == 0, stop=k == KD - 1)
                        last.then_inc(ready.sem, ready.one())

                def column_part(n):
                    i = panels[n]
                    pe.wait_ge(*m.loaded(i))
                    if n >= 4:
                        pe.wait_ge(chunk_read.sem, chunk_read.at(n - 3))
                    for k in range(KD):
                        g = k % 4
                        last = nc.tensor.matmul(ps[n % 4][32 * g:32 * (g + 1), :], m.cond_wide[:, k, :],
                                                m.slot(i)[:, k * 512:(k + 1) * 512], start=k < 4, stop=k >= 4)
                    last.then_inc(chunk.sem, chunk.one())

                if projection:
                    pe.wait_ge(added.sem, added.at(2))
                for n in range(4):
                    column_part(n)
                for n in range(4, 6):
                    column_part(n)

                def turn_columns(which):
                    for k in range(KD):
                        j = which * KD + k
                        last = nc.tensor.transpose(ps[turned_bank(j)][:, j % 4 * P:(j % 4 + 1) * P],
                                                   row[:, j * P:(j + 1) * P], m.ident[:, :])
                    last.then_inc(cols.sem, cols.one())

                pe.wait_ge(chunk_read.sem, chunk_read.at(4))
                turn_columns(0)
                for n in range(2):
                    pe.wait_ge(chunk_read.sem, chunk_read.at(5 + n))
                    for s in range(2):
                        nc.tensor.matmul(ps[4 + 2 * s + n][:, :], m.mod_sel[:, s, :],
                                         row[:, 2 * D + n * 512:2 * D + (n + 1) * 512], start=True, stop=True) \
                            .then_inc(gates.sem, gates.one())
                turn_columns(1)

            @block.vector
            def _(dve):
                chain = m.sig("dve_chain")
                if projection:
                    for t in range(NT):
                        one = slice(t, t + 1)
                        dve.wait_ge(squares.sem, squares.at(t + 1))
                        after(dve, nc.vector.tensor_tensor(m.sums[:, one], m.sums[:, one], m.sums[:, NT + t:NT + t + 1],
                                                           ALU.add), chain)
                        variance(m, dve, m.var[:, one], m.sums[:, one], 1.0 / D)
                        fine_rstd(m, dve, m.var[:, one], m.rstd[:, one], m.tmp[:, one], t + 1)
                        for n in range(2):
                            part = m.x[:, t, n * 512:(n + 1) * 512]
                            y = m.scratch[:, 1, n * 512:(n + 1) * 512]
                            after(dve, nc.vector.scalar_tensor_tensor(out=y, in0=bank(t, n)[:, :], scalar=m.rstd[:, one],
                                                                      in1=m.gate[:, t // NX, n * 512:(n + 1) * 512],
                                                                      op0=ALU.mult, op1=ALU.mult), chain)
                            last = nc.vector.tensor_tensor(part, part, y, ALU.add)
                            if n == 0:
                                after(dve, last, chain)
                        last.then_inc(added.sem, added.one())
                    dve.wait_ge(added.sem, added.at(NT))

                def add_given(n):
                    dve.wait_ge(chunk.sem, chunk.at(n + 1))
                    part = row[:, n * 512:(n + 1) * 512]
                    add = nc.vector.tensor_tensor(part, ps[n % 4][:, :], given[:, n * 512:(n + 1) * 512], ALU.add)
                    if n >= 4:
                        after(dve, add, chain)
                        add = nc.vector.tensor_tensor(part, part, given[:, 3 * D + (n - 4) * 512:3 * D + (n - 3) * 512],
                                                      ALU.mult)
                    add.then_inc(chunk_read.sem, chunk_read.one())

                dve.wait_ge(landed.sem, landed.at(16))
                for n in range(6):
                    add_given(n)
                dve.wait_ge(squares.sem, squares.at(NT + 1 if projection else 1))
                variance(m, dve, m.var[:, norm], m.sums[:, norm], 1.0 / D)
                fine_rstd(m, dve, m.var[:, norm], m.rstd[:, norm], m.tmp[:, norm], NT + 1 if projection else 1)
                for which in range(2):
                    dve.wait_ge(cols.sem, cols.at(which + 1))
                    for half in range(2):
                        j = which * KD + 4 * half
                        parts = ps[turned_bank(j)][:, :].rearrange("p (k g r) -> p r k g", k=4, g=4)[:, 0:2]
                        last = nc.vector.tensor_reduce((m.shift if which == 0 else m.scale1)[:, :, 4 * half:4 * half + 4],
                                                       parts, AX, ALU.add)
                        last.then_inc(chain.sem, chain.one())
                dve.wait_ge(chain.sem, chain.total)
                for s in range(2):
                    nc.vector.scalar_tensor_tensor(out=m.scale1[:, s, :], in0=m.scale1[:, s, :], scalar=1.0,
                                                   in1=m.vec("g_pre", layer * KD, (layer + 1) * KD),
                                                   op0=ALU.add, op1=ALU.mult)

            @block.scalar
            def _(act):
                chain = m.sig("act_chain")

                def square_x(t):
                    after(act, nc.scalar.activation(m.scratch[:, 0, :], m.x[:, t, :], ACT.Square,
                                                    accum_out=m.sums[:, NORM + t:NORM + t + 1]), chain)

                for t in range(NT):
                    if projection:
                        act.wait_ge(ready.sem, ready.at(t + 1))
                        for n in range(2):
                            after(act, nc.scalar.activation(m.scratch[:, 0, 0:512], bank(t, n)[:, :], ACT.Square,
                                                            accum_out=m.sums[:, n * NT + t:n * NT + t + 1]), chain)
                        nc.scalar.nop().then_inc(squares.sem, squares.one())
                        rough_rstd(m, act, m.var[:, t:t + 1], m.rstd[:, t:t + 1], t + 1)
                        if t >= 1:
                            act.wait_ge(added.sem, added.at(t))
                            square_x(t - 1)
                    else:
                        act.wait_ge(tokens.sem, tokens.at(16 * NT))
                        square_x(t)
                if projection:
                    act.wait_ge(added.sem, added.at(NT))
                    square_x(NT - 1)
                nc.scalar.nop().then_inc(squares.sem, squares.one())
                rough_rstd(m, act, m.var[:, norm], m.rstd[:, norm], NT + 1 if projection else 1)
                for n in range(2):
                    for s in range(2):
                        act.wait_ge(gates.sem, gates.at(2 * n + s + 1))
                        nc.scalar.activation(m.gate[:, s, n * 512:(n + 1) * 512], ps[4 + 2 * s + n][:, :], ACT.Copy)


def norm_to_channels(m, tiles, out, scale, shift, by_token=None):
    nc, ps = m.nc, m.ps
    normed_at = (lambda t: m.scratch[:, t % 2, :]) if by_token is None else (lambda t: by_token[0][:, t, :])
    with m.step() as block:
        normed, turned = m.sig("normed_ready"), m.sig("turned_in_psum")
        taken = {0: m.sig("turned_taken_by_dve"), 1: m.sig("turned_taken_by_act")}

        @block.scalar
        def _(act):
            for t in range(tiles):
                act.wait_ge(turned.sem, turned.at(2 * t + 2))
                if by_token is not None:
                    last = nc.scalar.activation(out[:, 4:8, t * P:(t + 1) * P],
                                                ps[(2 * t + 1) % 4][:, :].rearrange("p (k t) -> p k t", k=4), ACT.Copy)
                else:
                    for k in range(4, 8):
                        last = nc.scalar.activation(out[:, k, t * P:(t + 1) * P],
                                                    ps[(2 * t + 1) % 4][:, (k - 4) * P:(k - 3) * P],
                                                    ACT.Identity, scale=scale(t // NX, k),
                                                    bias=0.0 if shift is None else shift(t // NX, k))
                last.then_inc(taken[1].sem, taken[1].one())

        @block.vector
        def _(dve):
            for t in range(tiles + 1):
                if t < tiles:
                    if t >= 2:
                        dve.wait_ge(turned.sem, turned.at(2 * (t - 2) + 2))
                    if by_token is None:
                        last = nc.vector.tensor_scalar(normed_at(t), m.x[:, t, :], m.rstd[:, NORM + t:NORM + t + 1], None,
                                                       ALU.mult)
                    else:
                        last = nc.vector.scalar_tensor_tensor(out=normed_at(t), in0=m.x[:, t, :],
                                                              scalar=m.rstd[:, NORM + t:NORM + t + 1],
                                                              in1=by_token[1][:], op0=ALU.mult, op1=ALU.mult)
                    last.then_inc(normed.sem, normed.one())
                if t >= 1:
                    u = t - 1
                    dve.wait_ge(turned.sem, turned.at(2 * u + 1))
                    for k in range(4):
                        src = ps[(2 * u) % 4][:, k * P:(k + 1) * P]
                        dst = out[:, k, u * P:(u + 1) * P]
                        if by_token is not None:
                            last = nc.vector.tensor_copy(dst, src)
                        elif shift is None:
                            last = nc.vector.tensor_scalar(dst, src, scale(u // NX, k), None, ALU.mult)
                        else:
                            last = nc.vector.tensor_scalar(dst, src, scale(u // NX, k), shift(u // NX, k), ALU.mult, ALU.add)
                    last.then_inc(taken[0].sem, taken[0].one())

        @block.tensor
        def _(pe):
            for t in range(tiles):
                pe.wait_ge(normed.sem, normed.at(t + 1))
                for half in range(2):
                    if t >= 2:
                        pe.wait_ge(taken[half].sem, taken[half].at(t - 1))
                    for k in range(4):
                        last = nc.tensor.transpose(ps[(2 * t + half) % 4][:, k * P:(k + 1) * P],
                                                   normed_at(t)[:, (4 * half + k) * P:(4 * half + k + 1) * P], m.ident[:, :])
                    last.then_inc(turned.sem, turned.one())


class Gates:

    def __init__(self, m, n_tok, tmp, banks=(4, 5, 6, 7)):
        self.m, self.n, self.tmp, self.banks = m, n_tok, tmp, banks
        self.ready, self.exp, self.done = m.sig("gate_in_psum"), m.sig("gate_exp_ready"), m.sig("gate_done")

    def bank(self, g):
        return self.m.ps[self.banks[g % len(self.banks)]][:, 0:self.n]

    def matmuls(self, pe, g, panel, j, k_tiles=KD, width=512):
        if g >= len(self.banks):
            pe.wait_ge(self.done.sem, self.done.at(g - len(self.banks) + 1))
        for k in range(k_tiles):
            last = self.m.nc.tensor.matmul(self.bank(g), self.m.slot(panel)[:, k * width + j * P:k * width + (j + 1) * P],
                                           self.m.hT[:, k, 0:self.n], start=k == 0, stop=k == k_tiles - 1)
        last.then_inc(self.ready.sem, self.ready.one())

    def exponential(self, act, g):
        act.wait_ge(self.ready.sem, self.ready.at(g + 1))
        if g >= 2:
            act.wait_ge(self.done.sem, self.done.at(g - 1))
        self.m.nc.scalar.activation(self.tmp[:, g % 2, 0:self.n], self.bank(g), ACT.Exp, scale=-1.0) \
            .then_inc(self.exp.sem, self.exp.one())

    def finish(self, dve, g, out, silu):
        nc, chain, t = self.m.nc, self.m.sig("dve_chain"), self.tmp[:, g % 2, 0:self.n]
        dve.wait_ge(self.exp.sem, self.exp.at(g + 1))
        after(dve, nc.vector.tensor_scalar(t, t, 1.0, None, ALU.add), chain)
        if silu:
            after(dve, nc.vector.reciprocal(t, t), chain)
            last = nc.vector.tensor_tensor(out, self.bank(g), t, ALU.mult)
        else:
            last = nc.vector.reciprocal(out, t)
        last.then_inc(self.done.sem, self.done.one())


def rope(m, dve, out, src, t, heads):
    nc, chain = m.nc, m.sig("dve_chain")
    wide = [P, heads, 32]
    cos = m.cos[:, t, :].unsqueeze(1).broadcast_to(wide)
    sin = m.sin[:, t, :].unsqueeze(1).broadcast_to(wide)
    ta = m.scratch[:, 0, 512:512 + heads * 32].rearrange("p (h c) -> p h c", h=heads)
    tb = m.scratch[:, 1, 512:512 + heads * 32].rearrange("p (h c) -> p h c", h=heads)
    nc.vector.tensor_tensor(ta, src[:, :, 0, :], cos, ALU.mult)
    after(dve, nc.vector.tensor_tensor(tb, src[:, :, 1, :], sin, ALU.mult), chain)
    after(dve, nc.vector.tensor_tensor(out[:, :, 0, :], ta, tb, ALU.subtract), chain)
    nc.vector.tensor_tensor(ta, src[:, :, 0, :], sin, ALU.mult)
    after(dve, nc.vector.tensor_tensor(tb, src[:, :, 1, :], cos, ALU.mult), chain)
    return nc.vector.tensor_tensor(out[:, :, 1, :], ta, tb, ALU.add)


def attention(m, own, heads, streams, scale, score_parts, v_of, together=1, mask=None, sink=None):
    nc, ps = m.nc, m.ps
    BUFS = 3
    probs = m.sb("probs", [P, BUFS, NX, 512], own)
    probsT = m.sb("probsT", [P, 2 * together, 4, N], own)
    neg_max, den, rden, esink = (m.sb(n, [P, BUFS, NX], own) for n in ("neg_max", "den", "rden", "esink"))
    units = [(h + i, s) for h in range(0, heads, together) for s in range(streams) for i in range(together)]
    rows = P // together
    U, LAG = len(units), 2
    keys = lambda s: range(0, NT) if s == 0 else range(NX, NT)
    scores = lambda u, q: ps[2 * (u % 2) + q]
    at = lambda u, q: NX * u + q + 1

    with m.step() as block:
        scored, maxed, expd = m.sig("scores_in_psum"), m.sig("row_max_ready"), m.sig("probs_ready")
        normed, turned, copied = m.sig("probs_normalised"), m.sig("probsT_in_psum"), m.sig("probsT_copied")
        outed, taken = m.sig("attended_in_psum"), m.sig("attended_taken")

        @block.tensor
        def _(pe):
            for step in range(U + LAG + 1):
                if step < U:
                    u = step
                    h, s = units[u]
                    first = keys(s)[0] * P
                    for q in range(NX):
                        if u >= 2:
                            pe.wait_ge(expd.sem, expd.at(at(u - 2, q)))
                        parts = score_parts(h, NX * s + q)
                        for i, (lhsT, rhs) in enumerate(parts):
                            last = nc.tensor.matmul(scores(u, q)[:, first:512], lhsT, rhs[:, first:512], start=i == 0,
                                                    stop=i == len(parts) - 1)
                        if mask is not None and s == 0:
                            last = nc.tensor.matmul(scores(u, q)[:, (1 - q) * P:(2 - q) * P], m.ident[:, :], mask[:, q, :],
                                                    start=False, stop=True, skip_group_check=True)
                        last.then_inc(scored.sem, scored.one())
                u = step - LAG
                if 0 <= u < U:
                    h, s = units[u]
                    for q in range(NX):
                        pe.wait_ge(normed.sem, normed.at(at(u, q)))
                        if u >= 1:
                            pe.wait_ge(copied.sem, copied.at(at(u - 1, q)))
                        for kt in keys(s):
                            last = nc.tensor.transpose(ps[4 + q][:, kt * P:(kt + 1) * P],
                                                       probs[:, u % BUFS, q, kt * P:(kt + 1) * P], m.ident[:, :])
                        last.then_inc(turned.sem, turned.one())
                u = step - LAG - 1
                if 0 <= u < U and u % together == together - 1:
                    w = u // together
                    pe.wait_ge(copied.sem, copied.at(at(u, NX - 1)))
                    if w >= 2:
                        pe.wait_ge(taken.sem, taken.at(w - 1))
                    for kt in keys(units[u][1]):
                        for i in range(together):
                            u_i = together * w + i
                            h, s = units[u_i]
                            last = nc.tensor.matmul(ps[6 + w % 2][rows * i:rows * (i + 1), 0:N], v_of(h, kt),
                                                    probsT[:, u_i % (2 * together), kt, :],
                                                    start=kt == keys(s)[0], stop=kt == NT - 1)
                    last.then_inc(outed.sem, outed.one())

        @block.scalar
        def _(act):
            for step in range(U + LAG):
                if step < U:
                    u = step
                    h, s = units[u]
                    b, first = u % BUFS, keys(s)[0] * P
                    act.wait_ge(maxed.sem, maxed.at(u + 1))
                    if u >= BUFS:
                        act.wait_ge(turned.sem, turned.at(at(u - BUFS, NX - 1)))
                    for q in range(NX):
                        bias = neg_max[:, b, q:q + 1]
                        if sink is not None:
                            nc.scalar.activation(esink[:, b, q:q + 1], sink[:, h:h + 1], ACT.Exp, bias=bias)
                        nc.scalar.activation(probs[:, b, q, first:512], scores(u, q)[:, first:512], ACT.Exp, scale=scale,
                                             bias=bias, accum_out=den[:, b, q:q + 1]).then_inc(expd.sem, expd.one())
                u = step - LAG
                if 0 <= u < U:
                    h, s = units[u]
                    first = keys(s)[0]
                    for q in range(NX):
                        act.wait_ge(turned.sem, turned.at(at(u, q)))
                        if u >= 2 * together:
                            act.wait_ge(outed.sem, outed.at(u // together - 1))
                        nc.scalar.activation(probsT[:, u % (2 * together), first:NT, q * P:(q + 1) * P],
                                             ps[4 + q][:, first * P:512].rearrange("p (k q) -> p k q", q=P), ACT.Copy) \
                            .then_inc(copied.sem, copied.one())

        @block.vector
        def _(dve):
            chain = m.sig("dve_chain")
            for step in range(U + LAG + 1):
                if step < U:
                    u = step
                    h, s = units[u]
                    b, first = u % BUFS, keys(s)[0] * P
                    for q in range(NX):
                        dve.wait_ge(scored.sem, scored.at(at(u, q)))
                        last = nc.vector.tensor_reduce(neg_max[:, b, q:q + 1], scores(u, q)[:, first:512], AX, ALU.max)
                        last.then_inc(chain.sem, chain.one())
                    dve.wait_ge(chain.sem, chain.total)
                    if sink is None:
                        last = nc.vector.tensor_scalar(neg_max[:, b, :], neg_max[:, b, :], -scale, None, ALU.mult)
                    else:
                        last = nc.vector.tensor_scalar(neg_max[:, b, :], neg_max[:, b, :], -scale, m.neg_sink[:, h:h + 1],
                                                       ALU.mult, ALU.min)
                    last.then_inc(maxed.sem, maxed.one())
                u = step - 1
                if 0 <= u < U:
                    h, s = units[u]
                    b, first = u % BUFS, keys(s)[0] * P
                    dve.wait_ge(expd.sem, expd.at(at(u, NX - 1)))
                    if sink is not None:
                        after(dve, nc.vector.tensor_tensor(den[:, b, :], den[:, b, :], esink[:, b, :], ALU.add), chain)
                    after(dve, nc.vector.reciprocal(rden[:, b, :], den[:, b, :]), chain)
                    for q in range(NX):
                        nc.vector.tensor_scalar(probs[:, b, q, first:512], probs[:, b, q, first:512], rden[:, b, q:q + 1],
                                                None, ALU.mult).then_inc(normed.sem, normed.one())
                u = step - LAG - 1
                if 0 <= u < U and u % together == together - 1:
                    h, s = units[u]
                    w = u // together
                    dve.wait_ge(outed.sem, outed.at(w + 1))
                    dst = m.gT[:, h // together, s * N:(s + 1) * N]
                    nc.vector.tensor_tensor(dst, ps[6 + w % 2][:, 0:N], dst, ALU.mult).then_inc(taken.sem, taken.one())


def project_out(m, name, tiles, gated):
    nc, ps = m.nc, m.ps
    panels = m.take(2, name, name)
    bank = lambda t, n: ps[2 * t + n]
    norm = slice(NORM, NORM + tiles)
    with m.step() as block:
        ready, squares, added = m.sig("projected_in_psum"), m.sig("squares_summed"), m.sig("residual_added")

        @block.sync
        def _(sp):
            for i in panels:
                sp.wait_ge(ready.sem, ready.at(tiles))
                m.load_next(sp, i)

        @block.tensor
        def _(pe):
            for i in panels:
                pe.wait_ge(*m.loaded(i))
            for t in range(tiles):
                for n, i in enumerate(panels):
                    for k in range(KD):
                        last = nc.tensor.matmul(bank(t, n)[:, :], m.gT[:, k, t * P:(t + 1) * P],
                                                m.slot(i)[:, k * 512:(k + 1) * 512], start=k == 0, stop=k == KD - 1)
                last.then_inc(ready.sem, ready.one())

        @block.scalar
        def _(act):
            chain = m.sig("act_chain")
            for t in range(tiles):
                if gated:
                    act.wait_ge(ready.sem, ready.at(t + 1))
                    for n in range(2):
                        after(act, nc.scalar.activation(m.scratch[:, 0, 0:512], bank(t, n)[:, :], ACT.Square,
                                                        accum_out=m.sums[:, n * NT + t:n * NT + t + 1]), chain)
                    nc.scalar.nop().then_inc(squares.sem, squares.one())
                    rough_rstd(m, act, m.var[:, t:t + 1], m.rstd[:, t:t + 1], t + 1)
            for t in range(tiles):
                act.wait_ge(added.sem, added.at(t + 1))
                after(act, nc.scalar.activation(m.scratch[:, 0, :], m.x[:, t, :], ACT.Square,
                                                accum_out=m.sums[:, NORM + t:NORM + t + 1]), chain)
            nc.scalar.nop().then_inc(squares.sem, squares.one())
            rough_rstd(m, act, m.var[:, norm], m.rstd[:, norm], tiles + 1 if gated else 1)

        @block.vector
        def _(dve):
            chain = m.sig("dve_chain")
            for t in range(tiles):
                one = slice(t, t + 1)
                if gated:
                    dve.wait_ge(squares.sem, squares.at(t + 1))
                    after(dve, nc.vector.tensor_tensor(m.sums[:, one], m.sums[:, one], m.sums[:, NT + t:NT + t + 1],
                                                       ALU.add), chain)
                    variance(m, dve, m.var[:, one], m.sums[:, one], 1.0 / D)
                    fine_rstd(m, dve, m.var[:, one], m.rstd[:, one], m.tmp[:, one], t + 1)
                else:
                    dve.wait_ge(ready.sem, ready.at(t + 1))
                for n in range(2):
                    part = m.x[:, t, n * 512:(n + 1) * 512]
                    if gated:
                        y = m.scratch[:, 1, n * 512:(n + 1) * 512]
                        after(dve, nc.vector.scalar_tensor_tensor(out=y, in0=bank(t, n)[:, :], scalar=m.rstd[:, one],
                                                                  in1=m.gate[:, t // NX, n * 512:(n + 1) * 512],
                                                                  op0=ALU.mult, op1=ALU.mult), chain)
                        last = nc.vector.tensor_tensor(part, part, y, ALU.add)
                    else:
                        last = nc.vector.tensor_tensor(part, part, bank(t, n)[:, :], ALU.add)
                    if n == 0:
                        after(dve, last, chain)
                last.then_inc(added.sem, added.one())
            dve.wait_ge(squares.sem, squares.at(tiles + 1 if gated else 1))
            variance(m, dve, m.var[:, norm], m.sums[:, norm], 1.0 / D)
            fine_rstd(m, dve, m.var[:, norm], m.rstd[:, norm], m.tmp[:, norm], tiles + 1 if gated else 1)


def latent_layer(m, layer):
    nc, ps = m.nc, m.ps
    j = layer // 3
    streams = 2 if layer < DEPTH - 1 else 1
    tq = NX * streams
    nq = tq * P
    norm_to_channels(m, NT, m.hT, lambda s, k: m.scale1[:, s, k:k + 1], lambda s, k: m.shift[:, s, k:k + 1])
    with ExitStack() as own:
        qnT = m.sb("q_nopeT", [P, A_H, 512], own)
        qrT = m.sb("q_ropeT", [P, A_H // 2, 512], own)
        krT = m.sb("k_ropeT", [P, 2, 512], own)
        v = m.sb("values", [P, NT, A_H * A_V], own)
        with ExitStack() as early:
            cq = m.sb("cq", [P, NT, A_QR], early)
            ckv = m.sb("ckv", [P, NT, A_KVR + A_ROPE], early)
            cqT = m.sb("cqT", [P, 4, 512], early)
            ckvT = m.sb("ckvT", [P, 2, 512], early)
            kr2 = m.sb("kr2", [P, NT, 2, A_ROPE], early)
            latent_inputs(m, layer, streams, cq, ckv, kr2, cqT, ckvT, krT)
            latent_qkv(m, layer, tq, cqT, ckvT, cq, qnT, qrT, v)
        knT = m.hT
        attention(m, own, A_H, streams, (A_NOPE + A_ROPE) ** -0.5,
                  lambda h, t: [(qnT[:, h, t * P:(t + 1) * P], knT[:, h, :]),
                                (qrT[:, h // 2, t * P:(t + 1) * P], krT[:, h % 2, :])],
                  lambda h, kt: v[:, kt, h * A_V:(h + 1) * A_V])


def latent_inputs(m, layer, streams, cq, ckv, kr2, cqT, ckvT, krT):
    nc, ps = m.nc, m.ps
    j = layer // 3
    tq = NX * streams
    cols = NT + tq
    panels = m.take(4, f"a_cq{layer}", f"a_ckv{layer}", f"a_gate{layer}", f"a_gate{layer}")
    TURN_AFTER = 3
    with m.step() as block:
        ready, read = m.sig("latent_in_psum"), m.sig("latent_read")
        normed, turned, turned_read = m.sig("latent_normed"), m.sig("latentT_in_psum"), m.sig("latentT_read")
        gates = Gates(m, tq * P, m.scratch)
        groups = [(0, t) for t in range(tq)] + [(1, t) for t in range(NT)]
        width = (A_QR, A_KVR + A_ROPE)

        @block.sync
        def _(sp):
            for n in range(2):
                sp.wait_ge(ready.sem, ready.at(tq + n * NT))
                m.load_next(sp, panels[n])
            for n in range(2):
                sp.wait_ge(gates.ready.sem, gates.ready.at(4 * n + 4))
                m.load_next(sp, panels[2 + n])

        @block.tensor
        def _(pe):
            for g, (kind, t) in enumerate(groups):
                i, w = panels[kind], width[kind]
                if t == 0:
                    pe.wait_ge(*m.loaded(i))
                if g >= 4:
                    pe.wait_ge(read.sem, read.at(g - 3))
                for k in range(KD):
                    last = nc.tensor.matmul(ps[g % 4][:, 0:w], m.hT[:, k, t * P:(t + 1) * P],
                                            m.slot(i)[:, k * w:(k + 1) * w], start=k == 0, stop=k == KD - 1)
                last.then_inc(ready.sem, ready.one())
            for g in range(8):
                i = panels[2 + g // 4]
                if g % 4 == 0:
                    pe.wait_ge(*m.loaded(i))
                gates.matmuls(pe, g, i, g % 4)
                t = g - TURN_AFTER
                if 0 <= t < NT:
                    pe.wait_ge(normed.sem, normed.at(t + 1))
                    if t == 0:
                        pe.wait_ge(read.sem, read.at(len(groups)))
                    if t >= 2:
                        pe.wait_ge(turned_read.sem, turned_read.at(t - 1))
                    a, b = ps[2 * (t % 2)], ps[2 * (t % 2) + 1]
                    for c in range(2):
                        nc.tensor.transpose(a[:, c * P:(c + 1) * P], ckv[:, t, c * P:(c + 1) * P], m.ident[:, :])
                    last = nc.tensor.transpose(a[:, 2 * P:3 * P], kr2[:, t].rearrange("p a c -> p (a c)"), m.ident[:, :])
                    if t < tq:
                        for c in range(4):
                            last = nc.tensor.transpose(b[:, c * P:(c + 1) * P], cq[:, t, c * P:(c + 1) * P], m.ident[:, :])
                    last.then_inc(turned.sem, turned.one())

        @block.scalar
        def _(act):
            for g, (kind, t) in enumerate(groups):
                act.wait_ge(ready.sem, ready.at(g + 1))
                src, c = ps[g % 4], (t + NT if kind == 0 else t)
                nc.scalar.activation((cq if kind == 0 else ckv)[:, t, :], src[:, 0:width[kind]], ACT.Copy)
                w = A_QR if kind == 0 else A_KVR
                after(act, nc.scalar.activation(m.scratch[:, 0, 0:w], src[:, 0:w], ACT.Square, accum_out=m.sums[:, c:c + 1]),
                      m.sig("act_chain"))
                nc.scalar.nop().then_inc(read.sem, read.one())
            rough_rstd(m, act, m.var[:, 0:cols], m.rstd[:, 0:cols])
            for g in range(8):
                gates.exponential(act, g)
                t = g - TURN_AFTER
                if 0 <= t < NT:
                    act.wait_ge(turned.sem, turned.at(t + 1))
                    a, b, tok = ps[2 * (t % 2)], ps[2 * (t % 2) + 1], slice(t * P, (t + 1) * P)
                    for c in range(2):
                        nc.scalar.activation(ckvT[:, c, tok], a[:, c * P:(c + 1) * P], ACT.Copy,
                                             scale=m.vec("a_g_kv", 2 * j + c, 2 * j + c + 1))
                    for odd in range(2):
                        rows = slice(64 * odd, 64 * odd + 64)
                        last = nc.scalar.activation(krT[rows, odd, tok], a[rows, 2 * P:3 * P], ACT.Copy)
                    if t < tq:
                        for c in range(4):
                            last = nc.scalar.activation(cqT[:, c, tok], b[:, c * P:(c + 1) * P], ACT.Copy,
                                                        scale=m.vec("a_g_q", 4 * j + c, 4 * j + c + 1))
                    last.then_inc(turned_read.sem, turned_read.one())

        @block.vector
        def _(dve):
            chain = m.sig("dve_chain")
            nc.vector.memset(krT[64:P, 0, :], 0.0)
            nc.vector.memset(krT[0:64, 1, :], 0.0)
            dve.wait_ge(read.sem, read.at(len(groups)))
            after(dve, nc.vector.tensor_scalar(m.sums[:, 0:NT], m.sums[:, 0:NT], A_QR / A_KVR, None, ALU.mult), chain)
            variance(m, dve, m.var[:, 0:cols], m.sums[:, 0:cols], 1.0 / A_QR)
            fine_rstd(m, dve, m.var[:, 0:cols], m.rstd[:, 0:cols], m.tmp[:, 0:cols])
            for g in range(8):
                if g < NT:
                    t = g
                    lat = ckv[:, t, 0:A_KVR]
                    kr = ckv[:, t, A_KVR:].rearrange("p (h x c) -> p h x c", h=1, x=2)
                    nc.vector.tensor_scalar(lat, lat, m.rstd[:, t:t + 1], None, ALU.mult)
                    if t < NX:
                        after(dve, rope(m, dve, kr2[:, t, 0:1, :].rearrange("p h (x c) -> p h x c", x=2), kr, t, 1), chain)
                        last = nc.vector.tensor_copy(kr2[:, t, 1, :], kr2[:, t, 0, :])
                    else:
                        nc.vector.tensor_copy(kr2[:, t, 0, :], ckv[:, t, A_KVR:])
                        last = nc.vector.tensor_copy(kr2[:, t, 1, :], ckv[:, t, A_KVR:])
                    if t < tq:
                        after(dve, last, chain)
                        last = nc.vector.tensor_scalar(cq[:, t, :], cq[:, t, :], m.rstd[:, NT + t:NT + t + 1], None, ALU.mult)
                    last.then_inc(normed.sem, normed.one())
                    dve.wait_ge(normed.sem, normed.at(t + 1))
                gates.finish(dve, g, m.gT[:, g, 0:tq * P], True)


def latent_qkv(m, layer, tq, cqT, ckvT, qr, qnT, qrT, v):
    nc, ps = m.nc, m.ps
    panels = m.take(3, f"a_q{layer}", f"a_q{layer}", f"a_kv{layer}")
    knT = m.hT
    wide = A_NOPE + A_ROPE
    with m.step() as block:
        a_ready, a_read = m.sig("heads_in_psum"), m.sig("heads_read")
        d_ready, d_read = m.sig("token_part_in_psum"), m.sig("token_part_read")

        @block.sync
        def _(sp):
            for n, count in enumerate((tq, 2 * tq, 2 * tq + 2 * NT)):
                sp.wait_ge(d_ready.sem, d_ready.at(count))
                m.load_next(sp, panels[n])

        @block.tensor
        def _(pe):
            a = d = 0
            for n in range(2):
                i = panels[n]
                w = m.slot(i)[:, 0:4 * 768].rearrange("p (k h c) -> p k h c", k=4, h=4)
                pe.wait_ge(*m.loaded(i))
                for h in range(4):
                    if a >= 4:
                        pe.wait_ge(a_read.sem, a_read.at(a - 3))
                    for k in range(4):
                        last = nc.tensor.matmul(ps[a % 4][:, 0:tq * P], w[:, k, h, 0:A_NOPE], cqT[:, k, 0:tq * P],
                                                start=k == 0, stop=k == 3)
                    last.then_inc(a_ready.sem, a_ready.one())
                    a += 1
                for t in range(tq):
                    if d >= 4:
                        pe.wait_ge(d_read.sem, d_read.at(d - 3))
                    for k in range(4):
                        last = nc.tensor.matmul(ps[4 + d % 4][:, 0:N].rearrange("p (h c) -> p h c", h=4),
                                                cqT[:, k, t * P:(t + 1) * P], w[:, k, :, A_NOPE:wide],
                                                start=k == 0, stop=k == 3)
                    last.then_inc(d_ready.sem, d_ready.one())
                    d += 1
            i = panels[2]
            w = m.slot(i)[:, :].rearrange("p (k h c) -> p k h c", k=2, h=A_H)
            pe.wait_ge(*m.loaded(i))
            for h in range(A_H):
                pe.wait_ge(a_read.sem, a_read.at(a - 3))
                for k in range(2):
                    last = nc.tensor.matmul(ps[a % 4][:, :], w[:, k, h, 0:A_NOPE], ckvT[:, k, :], start=k == 0, stop=k == 1)
                last.then_inc(a_ready.sem, a_ready.one())
                a += 1
            for t in range(NT):
                for half in range(2):
                    if d >= 4:
                        pe.wait_ge(d_read.sem, d_read.at(d - 3))
                    for k in range(2):
                        last = nc.tensor.matmul(ps[4 + d % 4][:, :].rearrange("p (h c) -> p h c", h=4),
                                                ckvT[:, k, t * P:(t + 1) * P], w[:, k, 4 * half:4 * half + 4, A_NOPE:],
                                                start=k == 0, stop=k == 1)
                    last.then_inc(d_ready.sem, d_ready.one())
                    d += 1
            for t in range(tq):
                pe.wait_ge(d_read.sem, d_read.at(d - 3))
                for c in range(4):
                    last = nc.tensor.transpose(ps[4 + d % 4][:, c * P:(c + 1) * P], qr[:, t, c * P:(c + 1) * P], m.ident[:, :])
                last.then_inc(d_ready.sem, d_ready.one())
                d += 1

        @block.scalar
        def _(act):
            for a in range(2 * A_H):
                act.wait_ge(a_ready.sem, a_ready.at(a + 1))
                if a < A_H:
                    last = nc.scalar.activation(qnT[:, a, 0:tq * P], ps[a % 4][:, 0:tq * P], ACT.Copy)
                else:
                    last = nc.scalar.activation(knT[:, a - A_H, :], ps[a % 4][:, :], ACT.Copy)
                last.then_inc(a_read.sem, a_read.one())

        @block.vector
        def _(dve):
            d = 0
            for n in range(2):
                for t in range(tq):
                    dve.wait_ge(d_ready.sem, d_ready.at(d + 1))
                    src = ps[4 + d % 4][:, 0:N].rearrange("p (h x c) -> p h x c", h=4, x=2)
                    dst = qr[:, t, n * N:(n + 1) * N].rearrange("p (h x c) -> p h x c", h=4, x=2)
                    if t < NX:
                        last = rope(m, dve, dst, src, t, 4)
                    else:
                        last = nc.vector.tensor_copy(dst, src)
                    last.then_inc(d_read.sem, d_read.one())
                    dve.wait_ge(d_read.sem, d_read.at(d + 1))
                    d += 1
            for t in range(NT):
                for half in range(2):
                    dve.wait_ge(d_ready.sem, d_ready.at(d + 1))
                    nc.vector.tensor_copy(v[:, t, half * 512:(half + 1) * 512], ps[4 + d % 4][:, :]) \
                        .then_inc(d_read.sem, d_read.one())
                    d += 1
            for t in range(tq):
                dve.wait_ge(d_ready.sem, d_ready.at(d + 1))
                nc.vector.tensor_copy(qrT[:, :, t * P:(t + 1) * P], ps[4 + d % 4][:, :].rearrange("p (c t) -> p c t", c=4)) \
                    .then_inc(d_read.sem, d_read.one())
                d += 1


def window_layer(m):
    norm_to_channels(m, NT, m.hT, lambda s, k: m.scale1[:, s, k:k + 1], lambda s, k: m.shift[:, s, k:k + 1])
    with ExitStack() as own:
        qT = m.hT
        kT = m.sb("kT", [P, 2, B_KVH, 512], own)
        v = m.sb("values", [P, NT, B_KVH, B_HD], own)
        mask = m.sb("band", [P, NX, P], own)
        with ExitStack() as early:
            q = m.sb("q", [P, NT, D], early)
            k2 = m.sb("k2", [P, NT, B_KVH, 2, B_HD], early)
            window_inputs(m, q, k2, v, mask)
            window_turn(m, q, k2, qT, kT)
        attention(m, own, B_H, 2, B_HD ** -0.5,
                  lambda h, t: [(qT[:, h // 2, t * P:(t + 1) * P], kT[:, h % 2, h // 4, :])],
                  lambda h, kt: v[:, kt, h // 4, :], together=2,
                  mask=mask, sink=m.rows[:, ROW["sink"][0]:ROW["sink"][1]])


def window_inputs(m, q, k2, v, mask):
    nc, ps = m.nc, m.ps
    panels = m.take(5, *["b_in"] * 5)
    with ExitStack() as own, m.step() as block:
        gate_tmp = m.sb("gate_tmp", [P, 2, 512], own)
        ready, read = m.sig("latent_in_psum"), m.sig("latent_read")
        landed = m.sig("mask_landed")
        gates = Gates(m, 512, gate_tmp)
        groups = [(n, t) for n in range(3) for t in range(NT)]

        @block.sync
        def _(sp):
            sp.dma_start(mask[:], m.dram["band"]).then_inc(landed.sem, landed.sixteen())
            for n in range(3):
                sp.wait_ge(ready.sem, ready.at((n + 1) * NT))
                m.load_next(sp, panels[n])
            for n in range(2):
                sp.wait_ge(gates.ready.sem, gates.ready.at(4 * n + 4))
                m.load_next(sp, panels[3 + n])
            sp.wait_ge(landed.sem, landed.at(16))

        @block.tensor
        def _(pe):
            for g, (n, t) in enumerate(groups):
                i = panels[n]
                if t == 0:
                    pe.wait_ge(*m.loaded(i))
                if g >= 4:
                    pe.wait_ge(read.sem, read.at(g - 3))
                for k in range(KD):
                    last = nc.tensor.matmul(ps[g % 4][:, :], m.hT[:, k, t * P:(t + 1) * P],
                                            m.slot(i)[:, k * 512:(k + 1) * 512], start=k == 0, stop=k == KD - 1)
                last.then_inc(ready.sem, ready.one())
            for g in range(8):
                i = panels[3 + g // 4]
                if g % 4 == 0:
                    pe.wait_ge(*m.loaded(i))
                gates.matmuls(pe, g, i, g % 4)

        @block.scalar
        def _(act):
            for g in range(8):
                gates.exponential(act, g)

        @block.vector
        def _(dve):
            chain = m.sig("dve_chain")
            nc.vector.tensor_scalar(m.neg_sink[:], m.rows[:, ROW["sink"][0]:ROW["sink"][1]], -1.0, None, ALU.mult)
            for g, (n, t) in enumerate(groups):
                dve.wait_ge(ready.sem, ready.at(g + 1))
                bank = ps[g % 4]
                if n < 2:
                    heads, part = 8, bank[:, :]
                    dst = q[:, t, n * 512:(n + 1) * 512].rearrange("p (h x c) -> p h x c", h=8, x=2)
                else:
                    heads, part = B_KVH, bank[:, 0:N]
                    dst = k2[:, t, :, 0, :].rearrange("p h (x c) -> p h x c", x=2)
                src = part.rearrange("p (h x c) -> p h x c", h=heads, x=2)
                last = rope(m, dve, dst, src, t, heads) if t < NX else nc.vector.tensor_copy(dst, src)
                if n == 2:
                    after(dve, last, chain)
                    nc.vector.tensor_copy(k2[:, t, :, 1, :], k2[:, t, :, 0, :])
                    last = nc.vector.tensor_copy(v[:, t], bank[:, N:512].rearrange("p (h c) -> p h c", h=B_KVH))
                last.then_inc(read.sem, read.one())
                dve.wait_ge(read.sem, read.at(g + 1))
            for g in range(8):
                gates.finish(dve, g, m.gT[:, g, :], True)


def window_turn(m, q, k2, qT, kT):
    nc, ps = m.nc, m.ps
    with m.step() as block:
        turned, read = m.sig("qT_in_psum"), m.sig("qT_read")
        groups = [(c, t) for t in range(NT) for c in range(3)]

        @block.tensor
        def _(pe):
            for g, (c, t) in enumerate(groups):
                if g >= 4:
                    pe.wait_ge(read.sem, read.at(g - 3))
                for b in range(4):
                    src = q[:, t, c * 512 + b * P:c * 512 + (b + 1) * P] if c < 2 else \
                        k2[:, t, b].rearrange("p a c -> p (a c)")
                    last = nc.tensor.transpose(ps[g % 4][:, b * P:(b + 1) * P], src, m.ident[:, :])
                last.then_inc(turned.sem, turned.one())

        @block.scalar
        def _(act):
            for g, (c, t) in enumerate(groups):
                act.wait_ge(turned.sem, turned.at(g + 1))
                src = ps[g % 4][:, :].rearrange("p (b t) -> p b t", b=4)
                if c < 2:
                    last = nc.scalar.activation(qT[:, 4 * c:4 * c + 4, t * P:(t + 1) * P], src, ACT.Copy)
                else:
                    for odd in range(2):
                        rows = slice(64 * odd, 64 * odd + 64)
                        last = nc.scalar.activation(kT[rows, odd, :, t * P:(t + 1) * P], src[rows], ACT.Copy)
                last.then_inc(read.sem, read.one())

        @block.vector
        def _(dve):
            nc.vector.memset(kT[64:P, 0], 0.0)
            nc.vector.memset(kT[0:64, 1], 0.0)


def conv_layer(m):
    norm_to_channels(m, NT, m.hT, lambda s, k: m.scale1[:, s, k:k + 1], lambda s, k: m.shift[:, s, k:k + 1])
    with ExitStack() as own:
        u = m.sb("u", [P, NT, 3, D], own)
        with ExitStack() as mid:
            dft = m.sb("dft", [P, NX, 6 * P], mid)
            idft = m.sb("idft", [P, 4, N], mid)
            zT = m.sb("zT", [C_EMB, N], mid)
            h1 = m.sb("ffn1", [C_FFN, N], mid)
            h2 = m.sb("ffn2", [C_FFN, N], mid)
            conv_inputs(m, u, FilterUnits(m, dft, idft, zT, h1, h2))
            spec = m.sb("filter_spectrum", [P, 5, 512], mid)
            decay, w3 = m.take(2, "c_decay", "c_w3")
            filters = Filters(m, h2, decay, w3)
            rounds = [(order, half) for order in range(2) for half in range(2)]
            conv_first_filters(m, filters)
            for (order, half), following in zip(rounds, rounds[1:] + [None]):
                conv_round(m, order, half, dft, idft, spec, u, filters, following)
        conv_gate(m, u)


ROUND = 1.5 * 2.0 ** 23
TWO_PI_A = 6.28125
TWO_PI_B = float(np.float32(int((2 * math.pi - TWO_PI_A) * 2 ** 20) / 2 ** 20))
TWO_PI_C = 2 * math.pi - TWO_PI_A - TWO_PI_B


class FilterUnits:

    def __init__(self, m, dft, idft, zT, h1, h2):
        self.m, self.dft, self.idft, self.zT, self.h = m, dft, idft, zT, (h1, h2)
        self.landed, self.ready, self.reduced, self.sines = (m.sig(n) for n in (
            "dft_landed", "ffn_in_psum", "angle_reduced", "sine_ready"))

    def load(self, sp):
        for dst, src in ((self.zT, "zT"), (self.dft, "dft"), (self.idft, "idft")):
            sp.dma_start(dst[:], self.m.dram[src]).then_inc(self.landed.sem, self.landed.sixteen())

    def product(self, pe, i):
        if i == 0:
            pe.wait_ge(self.landed.sem, self.landed.at(48))
            w, x = self.m.vec("f_w1")[0:C_EMB, :], self.zT[:, :]
        else:
            pe.wait_ge(self.sines.sem, self.sines.at(1))
            w, x = self.m.vec("f_w2")[0:C_FFN, :], self.h[0][:, :]
        self.m.nc.tensor.matmul(self.m.ps[4 + i][0:C_FFN, 0:N], w, x, start=True, stop=True) \
            .then_inc(self.ready.sem, self.ready.one())

    def reduce_angle(self, dve, i):
        v, chain, h = self.m.nc.vector, self.m.sig("dve_chain"), self.h[i]
        turns = self.m.scratch[0:C_FFN, 0, 0:N]
        dve.wait_ge(self.ready.sem, self.ready.at(i + 1))
        after(dve, v.tensor_scalar(h[:], self.m.ps[4 + i][0:C_FFN, 0:N], self.m.vec(("f_b1", "f_b2")[i])[0:C_FFN, :],
                                   self.m.vec("f_freq")[0:C_FFN, :], ALU.add, ALU.mult), chain)
        after(dve, v.tensor_scalar(turns, h[:], 1.0 / (2 * math.pi), ROUND, ALU.mult, ALU.add), chain)
        after(dve, v.tensor_scalar(turns, turns, ROUND, None, ALU.subtract), chain)
        for part in (TWO_PI_A, TWO_PI_B, TWO_PI_C):
            after(dve, v.scalar_tensor_tensor(out=h[:], in0=turns, scalar=-part, in1=h[:],
                                              op0=ALU.mult, op1=ALU.add), chain)
        v.tensor_scalar(h[:], h[:], 3.1415925, -3.1415925, ALU.min, ALU.max).then_inc(self.reduced.sem, self.reduced.one())

    def sine(self, act, i):
        act.wait_ge(self.reduced.sem, self.reduced.at(i + 1))
        self.m.nc.scalar.activation(self.h[i][:], self.h[i][:], ACT.Sin).then_inc(self.sines.sem, self.sines.one())


def conv_inputs(m, u, filter_units):
    nc, ps = m.nc, m.ps
    panels = m.take(8, *["c_in"] * 8)
    CH = 24
    with ExitStack() as own, m.step() as block:
        uc = m.sb("short", [P, 2, 512], own)
        ready, mid, conved = m.sig("heads_in_psum"), m.sig("centre_tap_ready"), m.sig("short_conv_ready")
        turned, read = m.sig("qT_in_psum"), m.sig("qT_read")
        gates = Gates(m, 512, m.scratch)
        FFN_AT = (5, 12)

        @block.sync
        def _(sp):
            filter_units.load(sp)
            for n in range(6):
                sp.wait_ge(ready.sem, ready.at(4 * n + 4))
                m.load_next(sp, panels[n])
            for n in range(2):
                sp.wait_ge(gates.ready.sem, gates.ready.at(4 * n + 4))
                m.load_next(sp, panels[6 + n])
            sp.wait_ge(filter_units.landed.sem, filter_units.landed.at(48))

        @block.tensor
        def _(pe):
            for g in range(CH + 1):
                if g < CH:
                    i = panels[g // 4]
                    if g % 4 == 0:
                        pe.wait_ge(*m.loaded(i))
                    if g >= 2:
                        pe.wait_ge(conved.sem, conved.at(g - 1))
                    for k in range(KD):
                        last = nc.tensor.matmul(ps[g % 2][:, :], m.slot(i)[:, k * 512 + g % 4 * P:k * 512 + (g % 4 + 1) * P],
                                                m.hT[:, k, :], start=k == 0, stop=k == KD - 1)
                    last.then_inc(ready.sem, ready.one())
                if g in FFN_AT:
                    filter_units.product(pe, FFN_AT.index(g))
                if g >= 1:
                    c = g - 1
                    pe.wait_ge(conved.sem, conved.at(c + 1))
                    if c >= 2:
                        pe.wait_ge(read.sem, read.at(c - 1))
                    for t in range(NT):
                        last = nc.tensor.transpose(ps[2 + c % 2][:, t * P:(t + 1) * P], uc[:, c % 2, t * P:(t + 1) * P], m.ident[:, :])
                    last.then_inc(turned.sem, turned.one())
            pe.wait_ge(filter_units.reduced.sem, filter_units.reduced.at(2))
            for g in range(8):
                i = panels[6 + g // 4]
                if g % 4 == 0:
                    pe.wait_ge(*m.loaded(i))
                gates.matmuls(pe, g, i, g % 4)

        @block.scalar
        def _(act):
            for g in range(CH + 1):
                if g < CH:
                    act.wait_ge(ready.sem, ready.at(g + 1))
                    if g >= 2:
                        act.wait_ge(turned.sem, turned.at(g - 1))
                    nc.scalar.activation(uc[:, g % 2, :], ps[g % 2][:, :], ACT.Identity,
                                         scale=m.vec("conv_w", CH + g, CH + g + 1), bias=m.vec("conv_b", g, g + 1)) \
                        .then_inc(mid.sem, mid.one())
                if g >= 1:
                    c = g - 1
                    act.wait_ge(turned.sem, turned.at(c + 1))
                    nc.scalar.activation(u[:, :, c // 8, c % 8 * P:(c % 8 + 1) * P],
                                         ps[2 + c % 2][:, :].rearrange("p (t c) -> p t c", t=NT), ACT.Copy) \
                        .then_inc(read.sem, read.one())
                if g - 2 in FFN_AT:
                    filter_units.sine(act, FFN_AT.index(g - 2))
            for g in range(8):
                gates.exponential(act, g)

        @block.vector
        def _(dve):
            for g in range(CH):
                src = ps[g % 2][:, :].rearrange("p (s n) -> p s n", s=2)
                dst = uc[:, g % 2, :].rearrange("p (s n) -> p s n", s=2)
                dve.wait_ge(mid.sem, mid.at(g + 1))
                after(dve, nc.vector.scalar_tensor_tensor(out=dst[:, :, 1:N], in0=src[:, :, 0:N - 1],
                                                          scalar=m.vec("conv_w", g, g + 1), in1=dst[:, :, 1:N],
                                                          op0=ALU.mult, op1=ALU.add), m.sig("dve_chain"))
                nc.vector.scalar_tensor_tensor(out=dst[:, :, 0:N - 1], in0=src[:, :, 1:N],
                                               scalar=m.vec("conv_w", 2 * CH + g, 2 * CH + g + 1), in1=dst[:, :, 0:N - 1],
                                               op0=ALU.mult, op1=ALU.add).then_inc(conved.sem, conved.one())
                if g in FFN_AT:
                    filter_units.reduce_angle(dve, FFN_AT.index(g))
            for g in range(8):
                gates.finish(dve, g, m.gT[:, g, :], True)


class Filters:

    def __init__(self, m, h2, decay, w3):
        self.m, self.h2, self.decay, self.w3 = m, h2, decay, w3
        self.w = m.slot(w3)[0:C_FFN, :].rearrange("p (w o c) -> p w o c", w=2, o=2)
        self.fall = m.slot(decay)[:, 0:2 * D].rearrange("p (t c) -> p t c", t=NX)
        self.bias = m.slot(decay)[0:1, 2 * D:4 * D].rearrange("p (o c) -> p o c", o=2)
        self.both = m.hT[:, 0:2 * NX, :].rearrange("p (t w) c -> p t w c", t=NX)
        self.groups = [(t, way) for t in range(NX) for way in range(2)]
        self.ready, self.made, self.paired = m.sig("filter_in_psum"), m.sig("filter_ready"), m.sig("filters_paired")

    def products(self, pe, order, half):
        pe.wait_ge(*self.m.loaded(self.w3))
        for g, (t, way) in enumerate(self.groups):
            self.m.nc.tensor.matmul(self.m.ps[4 + g][:, :], self.h2[:, t * P:(t + 1) * P],
                                    self.w[:, way, order, half * 512:(half + 1) * 512],
                                    start=True, stop=True).then_inc(self.ready.sem, self.ready.one())

    def pair(self, dve, order, half):
        v, chain, both, cols = self.m.nc.vector, self.m.sig("dve_chain"), self.both, slice(half * 512, (half + 1) * 512)
        dve.wait_ge(*self.m.loaded(self.decay))
        for g, (t, way) in enumerate(self.groups):
            dve.wait_ge(self.ready.sem, self.ready.at(g + 1))
            v.tensor_tensor(both[:, t, way, :], self.m.ps[4 + g][:, :], self.fall[:, t, cols], ALU.mult) \
                .then_inc(self.made.sem, self.made.one())
        dve.wait_ge(self.made.sem, self.made.at(len(self.groups)))
        for t in range(NX):
            total, other = self.m.scratch[:, t, 0:512], both[:, t, 1, :]
            after(dve, v.tensor_tensor(total, both[:, t, 0, :], other, ALU.add), chain)
            after(dve, v.tensor_tensor(other, both[:, t, 0, :], other, ALU.subtract), chain)
            after(dve, v.tensor_copy(both[:, t, 0, :], total), chain)
        v.tensor_tensor(both[0:1, 0, 0, :], both[0:1, 0, 0, :], self.bias[:, order, cols], ALU.add) \
            .then_inc(self.paired.sem, self.paired.one())


def conv_first_filters(m, filters):
    with m.step() as block:
        @block.tensor
        def _(pe):
            filters.products(pe, 0, 0)

        @block.vector
        def _(dve):
            filters.pair(dve, 0, 0)
            dve.wait_ge(filters.paired.sem, filters.paired.at(1))


def conv_round(m, order, half, dft, idft, spec, u, filters, following):
    nc, ps = m.nc, m.ps
    cols = slice(half * 512, (half + 1) * 512)
    with m.step() as block:
        prod = m.hT[:].rearrange("p (a f) c -> p a f c", a=2)
        ta = m.scratch[:, 0, 0:512]
        tb = m.scratch[:, 1, 0:512]
        spectral, copied = m.sig("filter_spectrum_in_psum"), m.sig("filter_spectrum_copied")
        ready, read = m.sig("spectrum_in_psum"), m.sig("spectrum_used")
        back, taken = m.sig("convolved_in_psum"), m.sig("convolved_taken")
        tiles = [(0, 0), (1, 0), (4, 1), (3, 1), (5, 0)]
        recipe = [((0, 0), (2, 2), ALU.subtract), ((1, 1), (3, 3), ALU.subtract),
                  ((0, 2), (2, 4), ALU.add), ((1, 3), (3, 1), ALU.add)]

        @block.tensor
        def _(pe):
            for g, (col, way) in enumerate(tiles):
                if g >= 4:
                    pe.wait_ge(copied.sem, copied.at(g - 3))
                for t in range(NX):
                    last = nc.tensor.matmul(ps[4 + g % 4][:, :], dft[:, t, col * P:(col + 1) * P],
                                            filters.both[:, t, way, :], start=t == 0, stop=t == NX - 1)
                last.then_inc(spectral.sem, spectral.one())
            for s in range(2):
                if s == 1:
                    pe.wait_ge(copied.sem, copied.at(len(tiles)))
                for f in range(4):
                    for t in range(NX):
                        last = nc.tensor.matmul(ps[4 * s + f][:, :], dft[:, t, f * P:(f + 1) * P],
                                                u[:, NX * s + t, 0, cols], start=t == 0, stop=t == NX - 1)
                last.then_inc(ready.sem, ready.one())
            for s in range(2):
                pe.wait_ge(read.sem, read.at(4 * s + 4))
                if s == 1 and following:
                    filters.products(pe, *following)
                for t in range(NX):
                    for f in range(4):
                        last = nc.tensor.matmul(ps[2 * s + t][:, :], idft[:, f, t * P:(t + 1) * P],
                                                prod[:, s, f, :], start=f == 0, stop=f == 3)
                    last.then_inc(back.sem, back.one())

        @block.vector
        def _(dve):
            chain = m.sig("dve_chain")

            def take(s):
                for t in range(NX):
                    dve.wait_ge(back.sem, back.at(2 * s + t + 1))
                    nc.vector.tensor_tensor(u[:, NX * s + t, 0, cols], ps[2 * s + t][:, :],
                                            u[:, NX * s + t, 1 + order, cols], ALU.mult).then_inc(taken.sem, taken.one())

            dve.wait_ge(copied.sem, copied.at(len(tiles)))
            for s in range(2):
                dve.wait_ge(ready.sem, ready.at(s + 1))
                for f, ((ua, ka), (ub, kb), op) in enumerate(recipe):
                    nc.vector.tensor_tensor(ta, ps[4 * s + ua][:, :], spec[:, ka, :], ALU.mult)
                    after(dve, nc.vector.tensor_tensor(tb, ps[4 * s + ub][:, :], spec[:, kb, :], ALU.mult), chain)
                    nc.vector.tensor_tensor(prod[:, s, f, :], ta, tb, op).then_inc(read.sem, read.one())
                    dve.wait_ge(read.sem, read.at(4 * s + f + 1))
            take(0)
            if following:
                filters.pair(dve, *following)
                dve.wait_ge(filters.paired.sem, filters.paired.at(1))
            take(1)

        @block.scalar
        def _(act):
            for g in range(len(tiles)):
                act.wait_ge(spectral.sem, spectral.at(g + 1))
                nc.scalar.activation(spec[:, g, :], ps[4 + g % 4][:, :], ACT.Copy) \
                    .then_inc(copied.sem, copied.one())

        if following == (1, 1):
            @block.sync
            def _(sp):
                sp.wait_ge(filters.ready.sem, filters.ready.at(4))
                m.load_next(sp, filters.w3)
                sp.wait_ge(filters.paired.sem, filters.paired.at(1))
                m.load_next(sp, filters.decay)


def conv_gate(m, u):
    nc, ps = m.nc, m.ps
    with m.step() as block:
        turned, read = m.sig("qT_in_psum"), m.sig("qT_read")
        groups = [(t, c) for t in range(NT) for c in range(2)]

        @block.tensor
        def _(pe):
            for g, (t, c) in enumerate(groups):
                if g >= 4:
                    pe.wait_ge(read.sem, read.at(g - 3))
                for b in range(4):
                    k = 4 * c + b
                    last = nc.tensor.transpose(ps[g % 4][:, b * P:(b + 1) * P], u[:, t, 0, k * P:(k + 1) * P], m.ident[:, :])
                last.then_inc(turned.sem, turned.one())

        @block.vector
        def _(dve):
            for g, (t, c) in enumerate(groups):
                dve.wait_ge(turned.sem, turned.at(g + 1))
                dst = m.gT[:, 4 * c:4 * c + 4, t * P:(t + 1) * P]
                nc.vector.tensor_tensor(dst, ps[g % 4][:, :].rearrange("p (b t) -> p b t", b=4), dst, ALU.mult) \
                    .then_inc(read.sem, read.one())


def second_mixer(m):
    hT = m.hT
    norm_to_channels(m, NX, hT, lambda s, k: m.vec("g_mix", k, k + 1), None)
    with ExitStack() as own:
        m.gT = hT[:, :, N:2 * N]
        go = m.sb("open_o", [P, M_H, N], own)
        ga = m.sb("open_a", [P, KD, N], own)
        gb = m.sb("open_b", [P, KD, N], own)
        up = m.sb("u_pool", [P, 4, POOL_PAD + N], own)
        qk = m.sb("qk_raw", [P, 2 * M_H, CONV_K - 1 + N], own)
        qkT = m.sb("qkT", [P, 2 * M_H, N], own)
        v = m.sb("v_mlstm", [P, NX, M_H * M_HD], own)
        zif = m.sb("z_if", [P, NX, 2 * M_H], own)
        poolT = m.sb("poolT", [P, 4, N], own)
        hmT = m.sb("hmT", [P, M_H, N], own)
        tri = m.sb("tri", [P, NX, N], own)
        causal = m.sb("causal", [P, NX, N], own)
        counts = m.sb("counts", [P, 4, N], own)
        fcum = m.sb("forget_sum", [P, NX, M_H], own)
        rbc = m.sb("log_input", [P, M_H, N], own)
        second_inputs(m, own, go, up, qk, qkT, v, zif, tri, causal, counts, poolT, fcum, rbc)
        mlstm_heads(m, own, qkT, v, causal, fcum, rbc, go, hmT, ga, gb, poolT)
        second_merge(m, hmT, ga, gb)
        project_out(m, "s_out", NX, False)


def second_inputs(m, own, go, up, qk, qkT, v, zif, tri, causal, counts, poolT, fcum, rbc):
    nc, ps = m.nc, m.ps
    panels = m.take(6, *["s_in"] * 5, "s_pool")
    w_if = m.vec("w_if").rearrange("p (k c) -> p k c", k=KD)
    with ExitStack() as mine, m.step() as block:
        sums = [m.sb(f"window{i}", [P, POOL_PAD + N], mine) for i in range(2)]
        expo = m.sb("silu_exp", [P, 2 * M_H, N], mine)
        diffs = m.sb("pool_diff", [P, 4, N], mine)
        lf = m.sb("log_forget", [P, NX, M_H], mine)
        tmp = m.sb("log_tmp", [P, NX, M_H], mine)
        rT = m.sb("log_inputT", [M_H, N], mine)
        ready, read, landed = m.sig("latent_in_psum"), m.sig("latent_read"), m.sig("masks_landed")
        biased, softened, summed = m.sig("gates_biased"), m.sig("softplus_ready"), m.sig("log_forget_ready")
        cum, rin, rturn, rcopied, spread, spread_read = (m.sig(n) for n in (
            "forget_sum_in_psum", "log_input_ready", "log_inputT_in_psum", "log_inputT_copied", "log_input_spread",
            "log_input_read"))
        conved, expd = m.sig("short_conv_ready"), m.sig("silu_exp_ready")
        diffed, pooled = m.sig("pool_diff_ready"), m.sig("pooled_in_psum")
        gates = Gates(m, N, m.scratch)
        i_pre, f_pre = zif[:, :, 0:M_H], zif[:, :, M_H:]
        groups = [("if", t) for t in range(NX)] + [(n, j) for n in range(3) for j in range(4)] + [(3, t) for t in range(NX)]
        done_at = lambda n: NX + 4 * min(n + 1, 3) + (NX if n == 3 else 0)

        @block.sync
        def _(sp):
            for dst, src in ((tri, "tri"), (counts, "counts"), (causal, "causal")):
                sp.dma_start(dst[:], m.dram[src]).then_inc(landed.sem, landed.sixteen())
            for n in range(4):
                sp.wait_ge(ready.sem, ready.at(done_at(n)))
                m.load_next(sp, panels[n])
            sp.wait_ge(gates.ready.sem, gates.ready.at(4))
            m.load_next(sp, panels[4])
            sp.wait_ge(pooled.sem, pooled.at(4))
            m.load_next(sp, panels[5])

        @block.tensor
        def _(pe):
            for g, (n, j) in enumerate(groups):
                if n != "if" and (j == 0):
                    pe.wait_ge(*m.loaded(panels[n]))
                if g >= 4:
                    pe.wait_ge(read.sem, read.at(g - 3))
                for k in range(KD):
                    tok = m.hT[:, k, j * P:(j + 1) * P]
                    flags = dict(start=k == 0, stop=k == KD - 1)
                    if n == "if":
                        last = nc.tensor.matmul(ps[g % 4][:, 0:2 * M_H], tok, w_if[:, k, :], **flags)
                    elif n < 3:
                        last = nc.tensor.matmul(ps[g % 4][:, 0:N], m.slot(panels[n])[:, k * 512 + j * P:k * 512 + (j + 1) * P],
                                                m.hT[:, k, 0:N], **flags)
                    else:
                        last = nc.tensor.matmul(ps[g % 4][:, :], tok, m.slot(panels[n])[:, k * 512:(k + 1) * 512], **flags)
                last.then_inc(ready.sem, ready.one())
                if (n, j) == (0, 3):
                    pe.wait_ge(landed.sem, landed.at(48))
                    pe.wait_ge(summed.sem, summed.at(1))
                    for t in range(NX):
                        for s_ in range(NX):
                            last = nc.tensor.matmul(ps[4][:, t * M_H:(t + 1) * M_H], tri[:, s_, t * P:(t + 1) * P],
                                                    lf[:, s_, :], start=s_ == 0, stop=s_ == NX - 1)
                    last.then_inc(cum.sem, cum.one())
                if (n, j) == (1, 3):
                    pe.wait_ge(rin.sem, rin.at(1))
                    for t in range(NX):
                        last = nc.tensor.transpose(ps[5][0:M_H, t * P:(t + 1) * P], tmp[:, t, :], m.ident[:, :])
                    last.then_inc(rturn.sem, rturn.one())
                if (n, j) == (2, 3):
                    pe.wait_ge(rcopied.sem, rcopied.at(1))
                    for h in range(M_H):
                        last = nc.tensor.matmul(ps[6 + h // 2][:, h % 2 * N:(h % 2 + 1) * N], m.sel[0:M_H, h, :], rT[:, :],
                                                start=True, stop=True)
                    last.then_inc(spread.sem, spread.one())
            pe.wait_ge(*m.loaded(panels[4]))
            pe.wait_ge(spread_read.sem, spread_read.at(1))
            for g in range(4):
                gates.matmuls(pe, g, panels[4], g)
            pe.wait_ge(*m.loaded(panels[5]))
            pe.wait_ge(read.sem, read.at(len(groups)))
            for g in range(4):
                pe.wait_ge(diffed.sem, diffed.at(g + 1))
                nc.tensor.matmul(ps[g][:, 0:N], m.slot(panels[5])[:, g * P:(g + 1) * P], diffs[:, g, :], start=True, stop=True) \
                    .then_inc(pooled.sem, pooled.one())

        @block.scalar
        def _(act):
            for g, (n, j) in enumerate(groups):
                act.wait_ge(ready.sem, ready.at(g + 1))
                if n == "if":
                    dst, src = zif[:, j, :], ps[g % 4][:, 0:2 * M_H]
                elif n == 0:
                    dst, src = up[:, j, POOL_PAD:], ps[g % 4][:, 0:N]
                elif n < 3:
                    dst, src = qk[:, (n - 1) * M_H + j, CONV_K - 1:], ps[g % 4][:, 0:N]
                else:
                    dst, src = v[:, j, :], ps[g % 4][:, :]
                nc.scalar.activation(dst, src, ACT.Copy).then_inc(read.sem, read.one())
                if (n, j) == ("if", NX - 1):
                    act.wait_ge(biased.sem, biased.at(1))
                    after(act, nc.scalar.activation(tmp[:], tmp[:], ACT.Exp), m.sig("act_chain"))
                    nc.scalar.activation(tmp[:], tmp[:], ACT.Ln, bias=1.0).then_inc(softened.sem, softened.one())
            act.wait_ge(conved.sem, conved.at(2 * M_H))
            nc.scalar.activation(expo[:], qkT[:], ACT.Exp, scale=-1.0).then_inc(expd.sem, expd.one())
            for g in range(4):
                gates.exponential(act, g)
            for g in range(4):
                act.wait_ge(pooled.sem, pooled.at(g + 1))
                nc.scalar.activation(poolT[:, g, :], ps[g][:, 0:N], ACT.Copy, scale=m.vec("pool_scale", g, g + 1))

        @block.vector
        def _(dve):
            chain = m.sig("dve_chain")
            after(dve, nc.vector.memset(up[:, :, 0:POOL_PAD], 0.0), chain)
            after(dve, nc.vector.memset(qk[:, :, 0:CONV_K - 1], 0.0), chain)
            bias = m.rows[:, ROW["b_if"][0]:ROW["b_if"][1]].unsqueeze(1).broadcast_to([P, NX, 2 * M_H])
            dve.wait_ge(read.sem, read.at(NX))
            after(dve, nc.vector.tensor_tensor(zif[:], zif[:], bias, ALU.add), chain)
            after(dve, nc.vector.tensor_scalar(tmp[:], f_pre, -1.0, None, ALU.mult), chain)
            nc.vector.tensor_tensor(tmp[:], tmp[:], f_pre, ALU.min).then_inc(biased.sem, biased.one())
            dve.wait_ge(softened.sem, softened.at(1))
            after(dve, nc.vector.tensor_scalar(lf[:], f_pre, 0.0, None, ALU.min), chain)
            nc.vector.tensor_tensor(lf[:], lf[:], tmp[:], ALU.subtract).then_inc(summed.sem, summed.one())

            dve.wait_ge(cum.sem, cum.at(1))
            after(dve, nc.vector.tensor_copy(fcum[:].rearrange("p t h -> p (t h)"), ps[4][:, 0:NX * M_H]), chain)
            nc.vector.tensor_tensor(tmp[:], i_pre, fcum[:], ALU.subtract).then_inc(rin.sem, rin.one())

            for g, window in enumerate(POOL_WINDOWS):
                src, width = up[:, g, :], 1
                buf = 0
                dve.wait_ge(read.sem, read.at(NX + g + 1))
                while width < window:
                    dst = sums[buf]
                    after(dve, nc.vector.tensor_copy(dst[:, 0:width], src[:, 0:width]), chain)
                    after(dve, nc.vector.tensor_tensor(dst[:, width:], src[:, width:], src[:, 0:POOL_PAD + N - width], ALU.add), chain)
                    src, buf, width = dst[:, :], 1 - buf, 2 * width
                mean = sums[buf][:, 0:N]
                after(dve, nc.vector.tensor_tensor(mean, src[:, POOL_PAD:], counts[:, g, :], ALU.mult), chain)
                after(dve, nc.vector.tensor_tensor(diffs[:, g, :], mean, up[:, g, POOL_PAD:], ALU.subtract), chain)
                nc.vector.nop().then_inc(diffed.sem, diffed.one())

            dve.wait_ge(rturn.sem, rturn.at(1))
            nc.vector.tensor_copy(rT[:], ps[5][0:M_H, 0:N]).then_inc(rcopied.sem, rcopied.one())
            for j in range(2 * M_H):
                dve.wait_ge(read.sem, read.at(NX + 4 + j + 1))
                name, h = ("conv_q", j) if j < M_H else ("conv_k", j - M_H)
                last = nc.vector.tensor_scalar(qkT[:, j, :], qk[:, j, 0:N], m.vec(name, h, h + 1), None, ALU.mult)
                for tap in range(1, CONV_K):
                    after(dve, last, chain)
                    last = nc.vector.scalar_tensor_tensor(out=qkT[:, j, :], in0=qk[:, j, tap:tap + N],
                                                          scalar=m.vec(name, tap * M_H + h, tap * M_H + h + 1),
                                                          in1=qkT[:, j, :], op0=ALU.mult, op1=ALU.add)
                last.then_inc(conved.sem, conved.one())
            dve.wait_ge(spread.sem, spread.at(1))
            for half in range(2):
                last = nc.vector.tensor_copy(rbc[:, 2 * half:2 * half + 2, :],
                                             ps[6 + half][:, :].rearrange("p (h s) -> p h s", h=2))
            last.then_inc(spread_read.sem, spread_read.one())
            dve.wait_ge(expd.sem, expd.at(1))
            after(dve, nc.vector.tensor_scalar(expo[:], expo[:], 1.0, None, ALU.add), chain)
            after(dve, nc.vector.reciprocal(expo[:], expo[:]), chain)
            nc.vector.tensor_tensor(qkT[:], qkT[:], expo[:], ALU.mult)
            for g in range(4):
                gates.finish(dve, g, go[:, g, :], False)


def mlstm_heads(m, own, qkT, v, causal, fcum, rbc, go, hmT, ga, gb, poolT):
    nc, ps = m.nc, m.ps
    panels = m.take(5, *["s_gates"] * 4, "s_br_a")
    units = [(t, h) for t in range(NX) for h in range(M_H)]
    U = len(units)
    gate_tiles = [(out, j) for out in (ga, gb) for j in range(KD)]
    PER_UNIT = len(gate_tiles) // U
    with ExitStack() as mine, m.step() as block:
        masked = m.sb("masked_log", [P, 2, N], mine)
        weight = m.sb("weights", [P, 2, N], mine)
        swT = m.sb("scoresT", [P, 2, NX, P], mine)
        cols = m.sb("mlstm_cols", [P, 2, 8], mine)
        hm = m.sb("h_mlstm", [P, NX, M_H, M_HD], mine)
        stats = m.sb("head_stats", [P, 3, NX * M_H], mine)
        scored, argued, weighed = m.sig("scores_in_psum"), m.sig("row_max_ready"), m.sig("probs_ready")
        normed, turned, copied = m.sig("probs_normalised"), m.sig("probsT_in_psum"), m.sig("probsT_copied")
        outed, taken = m.sig("attended_in_psum"), m.sig("attended_taken")
        centred, back, finished = m.sig("heads_normalised"), m.sig("headsT_in_psum"), m.sig("headsT_read")
        gates = Gates(m, N, m.scratch, (6, 7))
        branch = m.sig("branch_a_in_psum")
        col = lambda u, c: cols[:, u % 2, c:c + 1]
        MX, NEG, STAB, NQ, DEN, RDEN = range(6)

        @block.sync
        def _(sp):
            for n in range(4):
                sp.wait_ge(gates.ready.sem, gates.ready.at(4 * n + 4))
                m.load_next(sp, panels[n])
            sp.wait_ge(branch.sem, branch.at(KD))
            m.load_next(sp, panels[4])

        @block.tensor
        def _(pe):
            def gate_products(u):
                for g in range(PER_UNIT * u, PER_UNIT * (u + 1)):
                    if g % 4 == 0:
                        pe.wait_ge(*m.loaded(panels[g // 4]))
                    gates.matmuls(pe, g, panels[g // 4], g % 4)

            for step in range(U + 1):
                if step < U:
                    u = step
                    t, h = units[u]
                    if u >= 2:
                        pe.wait_ge(normed.sem, normed.at(u - 1))
                    nc.tensor.matmul(ps[u % 2][:, 0:N], qkT[:, h, t * P:(t + 1) * P], qkT[:, M_H + h, :], start=True, stop=True) \
                        .then_inc(scored.sem, scored.one())
                    gate_products(u)
                if step >= 1:
                    u = step - 1
                    t, h = units[u]
                    pe.wait_ge(normed.sem, normed.at(u + 1))
                    if u >= 2:
                        pe.wait_ge(copied.sem, copied.at(u - 1))
                    for s in range(NX):
                        last = nc.tensor.transpose(ps[2 + u % 2][:, s * P:(s + 1) * P], weight[:, u % 2, s * P:(s + 1) * P],
                                                   m.ident[:, :])
                    last.then_inc(turned.sem, turned.one())
                    pe.wait_ge(copied.sem, copied.at(u + 1))
                    if u >= 2:
                        pe.wait_ge(taken.sem, taken.at(u - 1))
                    for s in range(NX):
                        last = nc.tensor.matmul(ps[4 + u % 2][:, 0:M_HD], swT[:, u % 2, s, :], v[:, s, h * M_HD:(h + 1) * M_HD],
                                                start=s == 0, stop=s == NX - 1)
                    last.then_inc(outed.sem, outed.one())
            pe.wait_ge(*m.loaded(panels[4]))
            for c in range(KD):
                for k in range(4):
                    last = nc.tensor.matmul(ps[c // 2][:, c % 2 * N:(c % 2 + 1) * N],
                                            m.slot(panels[4])[:, k * D + c * P:k * D + (c + 1) * P],
                                            poolT[:, k, :], start=k == 0, stop=k == 3)
                last.then_inc(branch.sem, branch.one())
            pe.wait_ge(gates.done.sem, gates.done.at(len(gate_tiles)))
            pe.wait_ge(centred.sem, centred.at(1))
            for h in range(M_H):
                if h >= 2:
                    pe.wait_ge(finished.sem, finished.at(h - 1))
                for t in range(NX):
                    last = nc.tensor.transpose(ps[6 + h % 2][:, t * P:(t + 1) * P], hm[:, t, h, :], m.ident[:, :])
                last.then_inc(back.sem, back.one())

        @block.scalar
        def _(act):
            def take_head(u):
                t, h = units[u]
                act.wait_ge(outed.sem, outed.at(u + 1))
                nc.scalar.activation(hm[:, t, h, :], ps[4 + u % 2][:, 0:M_HD], ACT.Copy).then_inc(taken.sem, taken.one())

            for step in range(U + 1):
                if step < U:
                    u = step
                    act.wait_ge(argued.sem, argued.at(u + 1))
                    nc.scalar.activation(col(u, STAB), col(u, STAB), ACT.Exp, scale=-1.0)
                    if u >= 2:
                        act.wait_ge(turned.sem, turned.at(u - 1))
                    nc.scalar.activation(weight[:, u % 2, :], masked[:, u % 2, :], ACT.Exp, bias=col(u, NEG)) \
                        .then_inc(weighed.sem, weighed.one())
                    for g in range(PER_UNIT * u, PER_UNIT * (u + 1)):
                        gates.exponential(act, g)
                if step >= 1:
                    u = step - 1
                    act.wait_ge(turned.sem, turned.at(u + 1))
                    if u >= 2:
                        act.wait_ge(outed.sem, outed.at(u - 1))
                    nc.scalar.activation(swT[:, u % 2].rearrange("p s t -> p (s t)"), ps[2 + u % 2][:, 0:N], ACT.Copy) \
                        .then_inc(copied.sem, copied.one())
                if step >= 2:
                    take_head(step - 2)
            take_head(U - 1)
            n = NX * M_H
            rough_rstd(m, act, stats[:, 1, 0:n], stats[:, 2, 0:n])

        @block.vector
        def _(dve):
            chain = m.sig("dve_chain")
            for step in range(U + 1):
                if step < U:
                    u = step
                    t, h = units[u]
                    if u >= 2:
                        dve.wait_ge(weighed.sem, weighed.at(u - 1))
                    after(dve, nc.vector.tensor_tensor(masked[:, u % 2, :], rbc[:, h, :], causal[:, t, :], ALU.add), chain)
                    after(dve, nc.vector.tensor_reduce(col(u, MX), masked[:, u % 2, :], AX, ALU.max), chain)
                    after(dve, nc.vector.tensor_scalar(col(u, NEG), col(u, MX), -1.0, 0.0, ALU.mult, ALU.min), chain)
                    nc.vector.tensor_tensor(col(u, STAB), fcum[:, t, h:h + 1], col(u, NEG), ALU.subtract) \
                        .then_inc(argued.sem, argued.one())
                if 1 <= step <= U:
                    u = step - 1
                    dve.wait_ge(weighed.sem, weighed.at(u + 1))
                    dve.wait_ge(scored.sem, scored.at(u + 1))
                    w = weight[:, u % 2, :]
                    after(dve, nc.vector.scalar_tensor_tensor(out=w, in0=ps[u % 2][:, 0:N], scalar=M_HD ** -0.5, in1=w,
                                                              op0=ALU.mult, op1=ALU.mult), chain)
                    after(dve, nc.vector.tensor_reduce(col(u, NQ), w, AX, ALU.add), chain)
                    after(dve, nc.vector.scalar_tensor_tensor(out=col(u, DEN), in0=col(u, NQ), scalar=-1.0, in1=col(u, NQ),
                                                              op0=ALU.mult, op1=ALU.max), chain)
                    after(dve, nc.vector.tensor_tensor(col(u, DEN), col(u, DEN), col(u, STAB), ALU.max), chain)
                    after(dve, nc.vector.reciprocal(col(u, RDEN), col(u, DEN)), chain)
                    nc.vector.tensor_scalar(w, w, col(u, RDEN), None, ALU.mult).then_inc(normed.sem, normed.one())
                    for g in range(PER_UNIT * (step - 1), PER_UNIT * step):
                        out, j = gate_tiles[g]
                        gates.finish(dve, g, out[:, j, :], False)
            dve.wait_ge(taken.sem, taken.at(U))
            all_h = hm[:].rearrange("p t h c -> p (t h) c")
            n = NX * M_H
            mean, var, rstd = stats[:, 0, :], stats[:, 1, :], stats[:, 2, :]
            wide = [P, n, M_HD]
            sq = m.scratch[:].rearrange("p a b -> p (a b)")[:, 0:n * M_HD].rearrange("p (n c) -> p n c", n=n)
            after(dve, nc.vector.tensor_reduce(mean, all_h, AX, ALU.add), chain)
            after(dve, nc.vector.tensor_scalar(mean, mean, 1.0 / M_HD, None, ALU.mult), chain)
            after(dve, nc.vector.tensor_tensor(all_h, all_h, mean.unsqueeze(2).broadcast_to(wide), ALU.subtract), chain)
            after(dve, nc.vector.tensor_tensor(sq, all_h, all_h, ALU.mult), chain)
            after(dve, nc.vector.tensor_reduce(var, sq, AX, ALU.add), chain)
            variance(m, dve, var, var, 1.0 / M_HD)
            fine_rstd(m, dve, var, rstd, m.tmp[:, 0:n])
            after(dve, nc.vector.tensor_tensor(all_h, all_h, rstd.unsqueeze(2).broadcast_to(wide), ALU.mult), chain)
            nc.vector.nop().then_inc(centred.sem, centred.one())
            for h in range(M_H):
                dve.wait_ge(back.sem, back.at(h + 1))
                nc.vector.scalar_tensor_tensor(out=hmT[:, h, :], in0=ps[6 + h % 2][:, 0:N], scalar=m.vec("g_head", h, h + 1),
                                               in1=go[:, h, :], op0=ALU.mult, op1=ALU.mult).then_inc(finished.sem, finished.one())


def second_merge(m, hmT, ga, gb):
    nc, ps = m.nc, m.ps
    (panel,) = m.take(1, "s_br_b")
    with m.step() as block:
        ready, used = m.sig("branch_in_psum"), m.sig("branch_used")

        @block.sync
        def _(sp):
            sp.wait_ge(ready.sem, ready.at(KD))
            m.load_next(sp, panel)

        @block.tensor
        def _(pe):
            pe.wait_ge(*m.loaded(panel))
            for c in range(KD):
                if c >= 4:
                    pe.wait_ge(used.sem, used.at(c - 3))
                for k in range(4):
                    last = nc.tensor.matmul(ps[4 + c % 4][:, 0:N], m.slot(panel)[:, k * D + c * P:k * D + (c + 1) * P],
                                            hmT[:, k, :], start=k == 0, stop=k == 3)
                last.then_inc(ready.sem, ready.one())

        @block.vector
        def _(dve):
            chain = m.sig("dve_chain")
            for c in range(0, KD, 2):
                pair = slice(c, c + 2)
                nc.vector.tensor_tensor(m.gT[:, pair, :], ps[c // 2][:, :].rearrange("p (c n) -> p c n", c=2),
                                        ga[:, pair, :], ALU.mult).then_inc(chain.sem, chain.one())
            dve.wait_ge(chain.sem, chain.total)
            for c in range(KD):
                dve.wait_ge(ready.sem, ready.at(c + 1))
                after(dve, nc.vector.tensor_tensor(gb[:, c, :], ps[4 + c % 4][:, 0:N], gb[:, c, :], ALU.mult), chain)
                nc.vector.tensor_tensor(m.gT[:, c, :], m.gT[:, c, :], gb[:, c, :], ALU.add).then_inc(used.sem, used.one())


def route(m, own, h):
    nc, ps = m.nc, m.ps
    m.gates = m.sb("gates", [P, NX, N_EXP], own)
    m.place = m.sb("place", [P, NX, N_EXP], own)
    m.longest = m.sb("longest_list", [P, 1], own, dt=mybir.dt.int32)
    with ExitStack() as mine:
        g_row = m.sb("g_ffn", [P, D], mine)
        with m.step() as block:
            landed = m.sig("constants_landed")

            @block.sync
            def _(sp):
                sp.dma_start(g_row[:], m.dram["g_ffn"]).then_inc(landed.sem, landed.sixteen())
                for i in range(N_DENSE + RING, N_DENSE + MOE_RING):
                    m.issue(sp, i)
                sp.wait_ge(landed.sem, landed.at(16))

        norm_to_channels(m, NX, m.hT, None, None, by_token=(h, g_row))
    w_route = m.vec("w_route").rearrange("p (k c) -> p k c", k=KD)
    with ExitStack() as mine, m.step() as block:
        logits = m.sb("logits", [P, NX, N_ROUTE], mine)
        glog = m.sb("group_logits", [P, NX, 8], mine)
        elog = m.sb("group_experts", [P, NX, N_EXP], mine)
        top = m.sb("top", [P, NX, 2, 8], mine)
        where = m.sb("where", [P, NX, 2, 8], mine, dt=U32)
        wheref = m.sb("wheref", [P, NX, 2, 8], mine)
        onehot = m.sb("group_onehot", [P, NX, 8], mine)
        c = m.sb("route_cols", [P, NX, 8], mine)
        chosen = m.sb("chosen", [P, NX, N_EXP], mine)
        tri = m.sb("tri", [P, NX, N], mine)
        ones = m.sb("ones", [P, P], mine)
        count = m.sb("list_length", [P, 1], mine)
        gates, place = m.gates, m.place
        landed, ready, argued, expd = m.sig("masks_landed"), m.sig("logits_in_psum"), m.sig("route_args_ready"), m.sig("route_exps_ready")
        picked, ranked = m.sig("chosen_ready"), m.sig("places_in_psum")
        iota = m.rows[:, ROW["iota"][0]:ROW["iota"][0] + N_EXP]

        @block.sync
        def _(sp):
            sp.dma_start(tri[:], m.dram["tri"]).then_inc(landed.sem, landed.sixteen())

        @block.tensor
        def _(pe):
            for t in range(NX):
                for k in range(KD):
                    last = nc.tensor.matmul(ps[t][:, 0:N_ROUTE], m.hT[:, k, t * P:(t + 1) * P], w_route[:, k, :],
                                            start=k == 0, stop=k == KD - 1)
                last.then_inc(ready.sem, ready.one())
            pe.wait_ge(landed.sem, landed.at(16))
            pe.wait_ge(picked.sem, picked.at(1))
            for t in range(NX):
                for s in range(NX):
                    nc.tensor.matmul(ps[2][:, t * N_EXP:(t + 1) * N_EXP], tri[:, s, t * P:(t + 1) * P], chosen[:, s, :],
                                     start=s == 0, stop=s == NX - 1)
            for s in range(NX):
                last = nc.tensor.matmul(ps[3][:, 0:N_EXP], ones[:, :], chosen[:, s, :], start=s == 0, stop=s == NX - 1)
            last.then_inc(ranked.sem, ranked.one())

        @block.scalar
        def _(act):
            act.wait_ge(argued.sem, argued.at(1))
            nc.scalar.activation(onehot[:], glog[:], ACT.Exp)
            nc.scalar.activation(c[:, :, 1:2], c[:, :, 0:1], ACT.Exp).then_inc(expd.sem, expd.one())

        @block.vector
        def _(dve):
            chain = m.sig("dve_chain")
            v = nc.vector
            bias = m.rows[:, ROW["b_route"][0]:ROW["b_route"][1]]
            v.memset(ones[:], 1.0)
            dve.wait_ge(ready.sem, ready.at(NX))
            for t in range(NX):
                after(dve, v.tensor_tensor(logits[:, t, :], ps[t][:, 0:N_ROUTE], bias, ALU.add), chain)
            after(dve, v.memset(glog[:], MASKED), chain)
            after(dve, v.tensor_copy(glog[:, :, 0:N_GROUPS], logits[:, :, 0:N_GROUPS]), chain)
            for t in range(NX):
                after(dve, v.max(top[:, t, 0, :], glog[:, t, :]), chain)
                after(dve, v.max_index(where[:, t, 0, :], top[:, t, 0, :], glog[:, t, :]), chain)
                after(dve, v.tensor_copy(wheref[:, t, 0, :], where[:, t, 0, :]), chain)
                after(dve, v.tensor_scalar(onehot[:, t, 0:N_GROUPS], iota[:, 0:N_GROUPS], wheref[:, t, 0, 0:1], None, ALU.is_equal), chain)
                mine_ = onehot[:, t, 0:N_GROUPS].unsqueeze(2).broadcast_to([P, N_GROUPS, PER_GROUP])
                e3 = elog[:, t, :].rearrange("p (g e) -> p g e", g=N_GROUPS)
                after(dve, v.tensor_tensor(e3, logits[:, t, N_GROUPS:].rearrange("p (g e) -> p g e", g=N_GROUPS), mine_, ALU.mult), chain)
                after(dve, v.tensor_scalar(onehot[:, t, 0:N_GROUPS], onehot[:, t, 0:N_GROUPS], -1.0, -MASKED, ALU.add, ALU.mult), chain)
                after(dve, v.tensor_tensor(e3, e3, mine_, ALU.add), chain)
                after(dve, v.max(top[:, t, 1, :], elog[:, t, :]), chain)
                after(dve, v.max_index(where[:, t, 1, :], top[:, t, 1, :], elog[:, t, :]), chain)
                after(dve, v.tensor_copy(wheref[:, t, 1, :], where[:, t, 1, :]), chain)
                after(dve, v.tensor_scalar(glog[:, t, :], glog[:, t, :], top[:, t, 0, 0:1], None, ALU.subtract), chain)
                after(dve, v.tensor_tensor(c[:, t, 0:1], top[:, t, 1, 1:2], top[:, t, 1, 0:1], ALU.subtract), chain)
            v.nop().then_inc(argued.sem, argued.one())
            for t in range(NX):
                after(dve, v.tensor_scalar(chosen[:, t, :], iota, wheref[:, t, 1, 0:1], None, ALU.is_equal), chain)
                after(dve, v.scalar_tensor_tensor(out=chosen[:, t, :], in0=iota, scalar=wheref[:, t, 1, 1:2],
                                                  in1=chosen[:, t, :], op0=ALU.is_equal, op1=ALU.add), chain)
            v.nop().then_inc(picked.sem, picked.one())
            dve.wait_ge(expd.sem, expd.at(1))
            for t in range(NX):
                after(dve, v.tensor_reduce(c[:, t, 2:3], onehot[:, t, :], AX, ALU.add), chain)
                after(dve, v.tensor_scalar(c[:, t, 3:4], c[:, t, 1:2], 1.0, None, ALU.add), chain)
                after(dve, v.tensor_tensor(c[:, t, 3:4], c[:, t, 3:4], c[:, t, 2:3], ALU.mult), chain)
                after(dve, v.reciprocal(c[:, t, 4:5], c[:, t, 3:4]), chain)
                after(dve, v.tensor_tensor(c[:, t, 5:6], c[:, t, 4:5], c[:, t, 1:2], ALU.mult), chain)
                after(dve, v.tensor_scalar(gates[:, t, :], iota, wheref[:, t, 1, 0:1], c[:, t, 4:5], ALU.is_equal, ALU.mult), chain)
                after(dve, v.tensor_scalar(elog[:, t, :], iota, wheref[:, t, 1, 1:2], c[:, t, 5:6], ALU.is_equal, ALU.mult), chain)
                after(dve, v.tensor_tensor(gates[:, t, :], gates[:, t, :], elog[:, t, :], ALU.add), chain)
            dve.wait_ge(ranked.sem, ranked.at(1))
            upto = ps[2][:, 0:NX * N_EXP].rearrange("p (t e) -> p t e", t=NX)
            after(dve, v.tensor_tensor(place[:], upto, chosen[:], ALU.mult), chain)
            after(dve, v.tensor_scalar(place[:], place[:], -1.0, None, ALU.add), chain)
            after(dve, v.tensor_reduce(count[:], ps[3][:, 0:N_EXP], AX, ALU.max), chain)
            v.tensor_copy(m.longest[:], count[:])


def experts(m):
    with ExitStack() as own:
        h = m.sb("h_tok", [P, NX, D], own)
        route(m, own, h)
        with ExitStack() as mine:
            expert_lists(m, mine, h)
        with ExitStack() as mine:
            expert_overflow(m, mine)


def expert_lists(m, own, h):
    nc, ps = m.nc, m.ps
    PAIRS = N_EXP // 2
    F = D_EXP
    pick = m.sb("pick", [P, NX, 2, SLOTS], own)
    give = m.sb("give", [P, NX, 2, SLOTS], own)
    xs = m.sb("picked_tokens", [P, KD, 2 * SLOTS], own)
    hid = m.sb("hidden", [2 * SLOTS, F], own)
    hidT = m.sb("hiddenT", [P, F // P, 2 * SLOTS], own)
    giveT = m.sb("giveT", [P, N], own)
    ys = m.sb("expert_out", [P, 2, 512], own)
    zero = m.sb("zero", [P, 512], own)
    iota = m.rows[:, ROW["iota"][0]:ROW["iota"][1]].unsqueeze(1).unsqueeze(1).broadcast_to([P, NX, 2, SLOTS])
    with m.step() as block:
        picking, picked, xs_ready = m.sig("pick_ready"), m.sig("picked_in_psum"), m.sig("picked_copied")
        mid, expd, hidden = m.sig("expert_mid_in_psum"), m.sig("gate_exp_ready"), m.sig("hidden_ready")
        giving, turned, copied = m.sig("give_ready"), m.sig("hiddenT_in_psum"), m.sig("hiddenT_copied")
        downed, ys_ready = m.sig("expert_out_in_psum"), m.sig("expert_out_copied")
        summed, zeroed = m.sig("experts_summed"), m.sig("zero_ready")
        slot_loaded = [m.sig(f"slot{s}_loaded") for s in range(MOE_RING)]
        first_load = [m.loaded(N_DENSE + s)[1] for s in range(MOE_RING)]
        xbank = lambda k: ps[4 + k // 4][:, k % 4 * P:(k % 4 + 1) * P]

        @block.sync
        def _(sp):
            def reload(pair, s):
                sp.dma_start(m.slots[s][:], m.dram["panels"][bass.ds(pair * MOE_RING + N_DENSE + s, 1)]
                             .rearrange("o p c -> (o p) c")).then_inc(slot_loaded[s].sem, 16)
            with sp.Fori(1, PAIRS) as pair:
                for kind in range(2):
                    sp.wait_ge(mid.sem, pair * 2 + mid.base + kind - 1)
                    reload(pair, kind)
                    reload(pair, 3 + kind)
                sp.wait_ge(downed.sem, pair + downed.base)
                reload(pair, 2)
                reload(pair, 5)

        @block.tensor
        def _(pe):
            def gather(pair):
                pe.wait_ge(picking.sem, pair + picking.base + 1)
                for k in range(KD):
                    for t in range(NX):
                        last = nc.tensor.matmul(xbank(k), h[:, t, k * P:(k + 1) * P],
                                                pick[:, t].rearrange("p a s -> p (a s)"), start=t == 0, stop=t == NX - 1)
                last.then_inc(picked.sem, 1)

            def first_half(pair):
                pe.wait_ge(xs_ready.sem, pair + xs_ready.base + 1)
                for kind in range(2):
                    for a in range(2):
                        pe.wait_ge(slot_loaded[3 * a + kind].sem, pair * 16 + first_load[3 * a + kind])
                    for k in range(KD):
                        for a in range(2):
                            last = nc.tensor.matmul(ps[6 + kind][a * SLOTS:(a + 1) * SLOTS, :],
                                                    xs[:, k, a * SLOTS:(a + 1) * SLOTS],
                                                    m.slots[3 * a + kind][:, k * F:(k + 1) * F], start=k == 0, stop=k == KD - 1)
                    last.then_inc(mid.sem, 1)

            def combine(pair):
                pe.wait_ge(ys_ready.sem, pair + ys_ready.base + 1)
                for t in range(NX):
                    for n in range(2):
                        last = nc.tensor.matmul(ps[2 * t + n][:, :], giveT[:, t * P:(t + 1) * P], ys[:, n, :],
                                                start=False, stop=False)
                return last

            def second_half(pair, more):
                pe.wait_ge(hidden.sem, pair + hidden.base + 1)
                for c in range(F // P):
                    nc.tensor.transpose(ps[6][:, c * P:(c + 1) * P], hid[:, c * P:(c + 1) * P], m.ident[:, :])
                pe.wait_ge(giving.sem, pair + giving.base + 1)
                for t in range(NX):
                    last = nc.tensor.transpose(ps[7][:, t * P:(t + 1) * P], give[:, t].rearrange("p a s -> p (a s)"),
                                               m.ident[:, :])
                last.then_inc(turned.sem, 1)
                pe.wait_ge(copied.sem, pair + copied.base + 1)
                if more:
                    pe.wait_ge(xs_ready.sem, pair + xs_ready.base + 2)
                for a in range(2):
                    pe.wait_ge(slot_loaded[3 * a + 2].sem, pair * 16 + first_load[3 * a + 2])
                for c in range(F // P):
                    for n in range(2):
                        for a in range(2):
                            last = nc.tensor.matmul(ps[4 + n][a * SLOTS:(a + 1) * SLOTS, :], hidT[:, c, a * SLOTS:(a + 1) * SLOTS],
                                                    m.slots[3 * a + 2][:, c * D + n * 512:c * D + (n + 1) * 512],
                                                    start=c == 0, stop=c == F // P - 1)
                last.then_inc(downed.sem, 1)

            pe.wait_ge(zeroed.sem, zeroed.at(1))
            for b in range(4):
                nc.tensor.matmul(ps[b][:, :], zero[:, 0:P], zero[:, :], start=True, stop=False)
            gather(0)
            first_half(0)
            gather(1)
            second_half(0, True)
            with pe.Fori(1, PAIRS - 1) as pair:
                first_half(pair)
                combine(pair - 1)
                gather(pair + 1)
                second_half(pair, True)
            first_half(PAIRS - 1)
            combine(PAIRS - 2)
            second_half(PAIRS - 1, False)
            combine(PAIRS - 1)
            for b in range(4):
                last = nc.tensor.matmul(ps[b][:, :], zero[:, 0:P], zero[:, :], start=False, stop=True)
            last.then_inc(summed.sem, summed.one())

        @block.scalar
        def _(act):
            def take_picked(pair):
                act.wait_ge(picked.sem, pair + picked.base + 1)
                for half in range(2):
                    last = nc.scalar.activation(xs[:, 4 * half:4 * half + 4, :].rearrange("p k s -> p (k s)"),
                                                ps[4 + half][:, :], ACT.Copy)
                last.then_inc(xs_ready.sem, 1)

            def body(pair, more):
                act.wait_ge(mid.sem, pair * 2 + mid.base + 1)
                nc.scalar.activation(hid[:], ps[6][:, :], ACT.Exp, scale=-1.0).then_inc(expd.sem, 1)
                if more:
                    take_picked(pair + 1)
                act.wait_ge(turned.sem, pair + turned.base + 1)
                nc.scalar.activation(hidT[:].rearrange("p c s -> p (c s)"), ps[6][:, :], ACT.Copy)
                nc.scalar.activation(giveT[:], ps[7][:, 0:N], ACT.Copy).then_inc(copied.sem, 1)
                act.wait_ge(downed.sem, pair + downed.base + 1)
                for n in range(2):
                    last = nc.scalar.activation(ys[:, n, :], ps[4 + n][:, :], ACT.Copy)
                last.then_inc(ys_ready.sem, 1)

            take_picked(0)
            body(0, True)
            with act.Fori(1, PAIRS - 1) as pair:
                body(pair, True)
            body(PAIRS - 1, False)

        @block.vector
        def _(dve):
            nc.vector.memset(zero[:], 0.0).then_inc(zeroed.sem, zeroed.one())
            chain = m.sig("expert_chain")
            PER_PAIR = 4

            def of_pair(col, pair, static):
                e = col[:, :, 2 * pair:2 * pair + 2] if static else col[:, :, bass.ds(pair * 2, 2)]
                return e.unsqueeze(3).broadcast_to([P, NX, 2, SLOTS])

            def build_pick(pair, static):
                nc.vector.tensor_tensor(pick[:], iota, of_pair(m.place, pair, static), ALU.is_equal).then_inc(picking.sem, 1)

            def body(pair, static, first, more):
                at = [0]

                def link(ins):
                    at[0] += 1
                    ins.then_inc(chain.sem, 1)
                    dve.wait_ge(chain.sem, pair * PER_PAIR + chain.base + at[0])

                if more:
                    dve.wait_ge(picked.sem, pair + picked.base + 1)
                    build_pick(pair + 1, static)
                if not first:
                    dve.wait_ge(turned.sem, pair + turned.base)
                link(nc.vector.tensor_tensor(give[:], iota, of_pair(m.place, pair, static), ALU.is_equal))
                nc.vector.tensor_tensor(give[:], give[:], of_pair(m.gates, pair, static), ALU.mult).then_inc(giving.sem, 1)
                dve.wait_ge(expd.sem, pair + expd.base + 1)
                link(nc.vector.tensor_scalar(hid[:], hid[:], 1.0, None, ALU.add))
                link(nc.vector.reciprocal(hid[:], hid[:]))
                link(nc.vector.tensor_tensor(hid[:], ps[6][:, :], hid[:], ALU.mult))
                dve.wait_ge(mid.sem, pair * 2 + mid.base + 2)
                nc.vector.tensor_tensor(hid[:], hid[:], ps[7][:, :], ALU.mult).then_inc(hidden.sem, 1)
                assert at[0] == PER_PAIR

            build_pick(0, True)
            body(0, True, True, True)
            with dve.Fori(1, PAIRS - 1) as pair:
                body(pair, False, False, True)
            body(PAIRS - 1, True, False, False)
            dve.wait_ge(summed.sem, summed.at(1))
            for t in range(NX):
                for n in range(2):
                    part = m.x[:, t, n * 512:(n + 1) * 512]
                    nc.vector.tensor_tensor(part, part, ps[2 * t + n][:, :], ALU.add)


def expert_overflow(m, own):
    nc, ps = m.nc, m.ps
    spread = m.sb("gate_rows", [P, N_EXP, N], own)
    left = m.sb("gates_left", [P, NX, N_EXP], own)
    leftT = m.sb("gates_leftT", [N_EXP, N], own)
    sel = m.slots[4][0:N_EXP, :].rearrange("k (e p) -> k e p", e=N_EXP)
    ex = m.sb("expert_exp", [P, 2, N], own)
    hidT = m.sb("hiddenT", [P, 4, N], own)
    zero = m.sb("zero", [P, 512], own)
    names = ("landed", "loaded", "left_ready", "leftT_in_psum", "leftT_copied", "row_in_psum", "row_taken", "gate_in",
             "exp_ready", "hidden_ready", "down_done", "summed", "chain")
    with m.step() as block:
        (landed, loaded, left_ready, turned, copied, wide, taken, mid, expd, hidden, downed, summed,
         chain) = (m.sig("overflow_" + n).sem for n in names)
        xT = m.hT
        bank = lambda kind, c: ps[4 + 2 * (c % 2) + kind][:, 0:N]

        def overflows(eng):
            return eng.value_load(m.longest[0:1, 0:1], min_val=0, max_val=2 * N) > SLOTS

        @block.sync
        def _(sp):
            with sp.If(overflows(sp)):
                sp.dma_start(sel, m.dram["selector"]).then_inc(landed, 16)

                def load(e):
                    for s in range(3):
                        sp.dma_start(m.slots[s][:], m.dram["panels"][bass.ds(e * 3 + N_DENSE + s, 1)]
                                     .rearrange("o p c -> (o p) c")).then_inc(loaded, 16)
                load(0)
                with sp.Fori(1, N_EXP) as e:
                    sp.wait_ge(downed, e)
                    load(e)

        @block.tensor
        def _(pe):
            with pe.If(overflows(pe)):
                pe.wait_ge(left_ready, 1)
                for t in range(NX):
                    last = nc.tensor.transpose(ps[2][0:N_EXP, t * P:(t + 1) * P], left[:, t, :], m.ident[:, :])
                last.then_inc(turned, 1)
                pe.wait_ge(landed, 16)
                pe.wait_ge(copied, 1)
                for e in range(N_EXP):
                    if e >= 4:
                        pe.wait_ge(taken, e - 3)
                    nc.tensor.matmul(ps[4 + e % 4][:, 0:N], sel[:, e, :], leftT[:, :], start=True, stop=True).then_inc(wide, 1)
                pe.wait_ge(taken, N_EXP)
                for b in range(4):
                    nc.tensor.matmul(ps[b][:, :], zero[:, 0:P], zero[:, :], start=True, stop=False)
                with pe.Fori(0, N_EXP) as e:
                    pe.wait_ge(loaded, e * 48 + 48)
                    for c in range(4):
                        if c >= 2:
                            pe.wait_ge(hidden, e * 4 + c - 1)
                        for kind in range(2):
                            for k in range(KD):
                                last = nc.tensor.matmul(bank(kind, c), m.slots[kind][:, k * 512 + c * P:k * 512 + (c + 1) * P],
                                                        xT[:, k, 0:N], start=k == 0, stop=k == KD - 1)
                        last.then_inc(mid, 1)
                    pe.wait_ge(hidden, e * 4 + 4)
                    for c in range(4):
                        for t in range(NX):
                            for n in range(2):
                                last = nc.tensor.matmul(ps[2 * t + n][:, :], hidT[:, c, t * P:(t + 1) * P],
                                                        m.slots[2][:, c * D + n * 512:c * D + (n + 1) * 512],
                                                        start=False, stop=False)
                    last.then_inc(downed, 1)
                for b in range(4):
                    last = nc.tensor.matmul(ps[b][:, :], zero[:, 0:P], zero[:, :], start=False, stop=True)
                last.then_inc(summed, 1)

        @block.scalar
        def _(act):
            with act.If(overflows(act)):
                for e in range(N_EXP):
                    act.wait_ge(wide, e + 1)
                    nc.scalar.activation(spread[:, e, :], ps[4 + e % 4][:, 0:N], ACT.Copy).then_inc(taken, 1)
                with act.Fori(0, N_EXP) as e:
                    for c in range(4):
                        act.wait_ge(mid, e * 4 + c + 1)
                        nc.scalar.activation(ex[:, c % 2, :], bank(0, c), ACT.Exp, scale=-1.0).then_inc(expd, 1)

        @block.vector
        def _(dve):
            with dve.If(overflows(dve)):
                nc.vector.memset(zero[:], 0.0).then_inc(chain, 1)
                nc.vector.tensor_scalar(left[:], m.place[:], float(SLOTS), None, ALU.is_ge).then_inc(chain, 1)
                dve.wait_ge(chain, 2)
                nc.vector.tensor_tensor(left[:], left[:], m.gates[:], ALU.mult).then_inc(left_ready, 1)
                dve.wait_ge(turned, 1)
                nc.vector.tensor_copy(leftT[:], ps[2][0:N_EXP, 0:N]).then_inc(copied, 1)
                dve.wait_ge(taken, N_EXP)
                with dve.Fori(0, N_EXP) as e:
                    for c in range(4):
                        t = ex[:, c % 2, :]
                        before = e * 16 + 4 * c + 2
                        dve.wait_ge(expd, e * 4 + c + 1)
                        nc.vector.tensor_scalar(t, t, 1.0, None, ALU.add).then_inc(chain, 1)
                        dve.wait_ge(chain, before + 1)
                        nc.vector.reciprocal(t, t).then_inc(chain, 1)
                        dve.wait_ge(chain, before + 2)
                        nc.vector.tensor_tensor(t, bank(0, c), t, ALU.mult).then_inc(chain, 1)
                        dve.wait_ge(chain, before + 3)
                        row = spread[:, bass.ds(e, 1), :].rearrange("p o n -> p (o n)")
                        nc.vector.tensor_tensor(t, t, row, ALU.mult).then_inc(chain, 1)
                        dve.wait_ge(chain, before + 4)
                        nc.vector.tensor_tensor(hidT[:, c, :], bank(1, c), t, ALU.mult).then_inc(hidden, 1)
                dve.wait_ge(summed, 1)
                for t in range(NX):
                    for n in range(2):
                        part = m.x[:, t, n * 512:(n + 1) * 512]
                        nc.vector.tensor_tensor(part, part, ps[2 * t + n][:, :], ALU.add)


def finish(m):
    nc = m.nc
    with m.step() as block:
        g_final = m.sb("g_final", [P, D])
        squares, done, stored = m.sig("squares_summed"), m.sig("out_ready"), m.sig("out_stored")
        landed = m.sig("g_final_landed")

        @block.scalar
        def _(act):
            for t in range(NX):
                after(act, nc.scalar.activation(m.scratch[:, t, :], m.x[:, t, :], ACT.Square,
                                                accum_out=m.sums[:, t:t + 1]), m.sig("act_chain"))
            nc.scalar.nop().then_inc(squares.sem, squares.one())
            rough_rstd(m, act, m.var[:, 0:NX], m.rstd[:, 0:NX])

        @block.vector
        def _(dve):
            dve.wait_ge(squares.sem, squares.at(1))
            variance(m, dve, m.var[:, 0:NX], m.sums[:, 0:NX], 1.0 / D)
            fine_rstd(m, dve, m.var[:, 0:NX], m.rstd[:, 0:NX], m.tmp[:, 0:NX])
            dve.wait_ge(landed.sem, landed.at(16))
            for t in range(NX):
                nc.vector.scalar_tensor_tensor(out=m.scratch[:, t, :], in0=m.x[:, t, :], scalar=m.rstd[:, t:t + 1],
                                               in1=g_final[:],
                                               op0=ALU.mult, op1=ALU.mult).then_inc(done.sem, done.one())

        @block.sync
        def _(sp):
            sp.dma_start(g_final[:], m.dram["g_final"]).then_inc(landed.sem, landed.sixteen())
            for t in range(NX):
                sp.wait_ge(done.sem, done.at(t + 1))
                sp.dma_start(m.dram["out"][0, t * P:(t + 1) * P, :], m.scratch[:, t, :]).then_inc(stored.sem, stored.sixteen())
            sp.wait_ge(stored.sem, stored.at(16 * NX))


def build(nc, dram):
    with ExitStack() as stack:
        m = Core(nc, stack, dram)
        m.vecs = m.sb("vecs", [P, VEC["width"]])
        m.cst = m.sb("cst", [P, CST["width"]])
        m.rows = m.sb("rows", [P, ROW["width"]])
        m.x = m.sb("x_tok", [P, NT, D])
        m.hT = m.sb("hT", [P, KD, 512])
        m.scratch = m.sb("scratch", [P, 2, D])
        m.gate = m.sb("gate_rows_all", [P, 2, D])
        m.scale1 = m.sb("scale1", [P, 2, KD])
        m.shift = m.sb("shift", [P, 2, KD])
        m.cond = m.sb("cond", [P, 2 * KD])
        m.cond_wide = m.sb("cond_wide", [P, KD, 32])
        m.neg_sink = m.sb("neg_sink", [P, B_H])
        m.sums, m.var, m.rstd, m.tmp = (m.sb(n, [P, NORM + NT]) for n in ("sums", "var", "rstd", "tmp8"))
        m.slots = [m.sb(f"slot{i}", [P, SLOT]) for i in range(RING)]
        cst = lambda name: m.cst[:, CST[name][0]:CST[name][1]]
        m.ident = cst("ident")
        m.cos = cst("cos").rearrange("p (t c) -> p t c", t=NX)
        m.sin = cst("sin").rearrange("p (t c) -> p t c", t=NX)
        m.sel = cst("sel").rearrange("p (h q) -> p h q", h=4)
        m.mod_sel = cst("mod_sel").rearrange("p (s q) -> p s q", s=2)
        load_constants(m)
        outs = {0: "a_out0", 1: "b_out", 2: "c_out"}
        with ExitStack() as layers:
            m.gT = m.sb("gT", [P, KD, 512], layers)
            for layer in range(DEPTH):
                enter_layer(m, layer, outs[layer - 1] if layer else None)
                if layer % 3 == 0:
                    latent_layer(m, layer)
                elif layer % 3 == 1:
                    window_layer(m)
                else:
                    conv_layer(m)
            project_out(m, "a_out3", NX, True)
        second_mixer(m)
        m.slots += [m.sb(f"slot{i}", [P, SLOT]) for i in range(RING, MOE_RING)]
        experts(m)
        finish(m)


def by_channel(a):
    a = np.asarray(a)
    return np.moveaxis(a.reshape(-1, P), 0, 1)


def k_major(w, cols=None):
    w = np.asarray(w)
    return w.reshape(w.shape[0] // P, P, w.shape[1]).transpose(1, 0, 2).reshape(P, -1)


def pad(a, rows=P):
    a = np.asarray(a)
    return np.concatenate([a, np.zeros((rows - a.shape[0],) + a.shape[1:], a.dtype)], 0)


def constants():
    f = np.float32
    tok = np.arange(N)
    inv = ROPE_BASE ** (-np.arange(0, 32, 2) / 32.0)
    ang = np.concatenate([(tok // GRID_W)[:, None] * inv, (tok % GRID_W)[:, None] * inv], 1)
    by_tile = lambda a: a.reshape(NX, P, -1).transpose(1, 0, 2).reshape(P, -1)
    mod_sel = np.zeros((P, 2, P))
    for s in range(2):
        mod_sel[s::32, s] = 1
    sel = np.zeros((P, 4, P))
    for h in range(4):
        sel[h, h] = 1
    cst = np.concatenate([np.eye(P), by_tile(np.cos(ang)), by_tile(np.sin(ang)), sel.reshape(P, -1),
                          mod_sel.reshape(P, -1)], 1)
    q, k = np.arange(P)[:, None], np.arange(P)[None, :]
    band = np.stack([np.where(k + P - q <= B_WINDOW, 0.0, MASKED), np.where(q + P - k <= B_WINDOW, 0.0, MASKED)], 1)
    n2 = 2 * N
    freq = np.arange(N)
    turn = 2 * np.pi * np.outer(tok, freq) / n2
    cos, sin, nyq = np.cos(turn), np.sin(turn), (-1.0) ** tok
    sin_n, cos_n = sin.copy(), cos[:, 0:P].copy()
    sin_n[:, 0], cos_n[:, 0] = nyq, nyq
    dft = np.concatenate([cos, sin_n, sin[:, 0:P], cos_n], 1)
    idft = np.concatenate([2 * cos.T / n2, 2 * sin.T / n2], 0)
    idft[0] /= 2
    idft[N] = nyq / n2
    t = np.linspace(0, 1, N)[:, None]
    w = 2 * np.pi / N * tok[:, None]
    bands = np.linspace(1e-4, C_BANDS - 1, C_BANDS)[None]
    z = np.concatenate([t, np.cos(bands * w), -np.sin(bands * w)], -1)
    decay = np.exp(-t * np.abs(np.linspace(C_MIN_DECAY, C_MAX_DECAY, D)))
    tri = (tok[:, None] <= tok[None, :]) * 1.0
    counts = np.stack([1.0 / np.minimum(tok + 1, wdw) for wdw in POOL_WINDOWS])
    selector = np.zeros((N_EXP, N_EXP, P))
    selector[np.arange(N_EXP), np.arange(N_EXP)] = 1
    out = dict(cst=cst, band=band, zT=z.T, decay=by_tile(decay), dft=by_tile(dft).reshape(P, NX, 6 * P),
               idft=idft.reshape(4, P, N).transpose(1, 0, 2), tri=by_tile(tri).reshape(P, NX, N),
               causal=by_tile(np.where(tri.T > 0, 0.0, MASKED)).reshape(P, NX, N),
               counts=np.broadcast_to(counts, (P, 4, N)), selector=selector)
    return {k: np.ascontiguousarray(a, f) for k, a in out.items()}


def lay_out(i):
    a = {k: np.asarray(v) for k, v in i.items()}
    cst = constants()
    panels = []

    def add(name, w):
        w = w.reshape(P, -1)
        assert w.shape[1] <= SLOT and panel_plan()[len(panels)][1] == w.shape[1], (name, w.shape)
        panels.append(w)

    for layer in range(DEPTH):
        for n in range(6):
            add("mod", k_major(a["w_mod"][layer][:, n * 512:(n + 1) * 512]))
        if layer % 3 == 0:
            j = layer // 3
            w = a["a_w_in"][j]
            at = A_QR + A_KVR + A_ROPE
            for lo, hi in ((0, A_QR), (A_QR, at), (at, at + 512), (at + 512, at + D)):
                add("a_in", k_major(w[:, lo:hi]))
            for n in range(2):
                add("a_q", k_major(a["a_w_q"][j][:, n * 768:(n + 1) * 768]))
            add("a_kv", k_major(a["a_w_kv"][j]))
            out = a["a_w_out"][j]
        elif layer % 3 == 1:
            for n in range(5):
                add("b_in", k_major(a["b_w_in"][0][:, n * 512:(n + 1) * 512]))
            out = a["b_w_out"][0]
        else:
            for n in range(8):
                add("c_in", k_major(a["c_w_in"][0][:, n * 512:(n + 1) * 512]))
            add("c_decay", np.concatenate([cst["decay"], pad(a["c_filt_bias"][0].reshape(1, -1))], 1))
            add("c_w3", pad(a["c_f_w3"][0]))
            out = a["c_w_out"][0]
        for n in range(2):
            add("out", k_major(out[:, n * 512:(n + 1) * 512]))
    w = a["w_in_2"][0]
    at_if = 5 * 512
    cols = [n * 512 for n in range(5)] + [at_if + 8 + n * 512 for n in range(4)]
    for n, c in enumerate(cols):
        if n == 5:
            add("s_pool", a["w_pool_2"][0].transpose(1, 0, 2))
        add("s_in", k_major(w[:, c:c + 512]))
    add("s_br_a", k_major(a["w_br_a_2"][0]))
    add("s_br_b", k_major(a["w_br_b_2"][0]))
    for n in range(2):
        add("s_out", k_major(a["w_out_2"][0][:, n * 512:(n + 1) * 512]))
    assert len(panels) == N_DENSE
    all_panels = np.zeros((N_DENSE + 3 * N_EXP, P, SLOT), np.float32)
    for n, w_ in enumerate(panels):
        all_panels[n, :, :w_.shape[1]] = w_
    ex = all_panels[N_DENSE:].reshape(N_EXP, 3, P, SLOT)
    for kind, name in enumerate(("w_e_gate_2", "w_e_up_2", "w_e_down_2")):
        e = a[name][0]
        kt = e.shape[1] // P
        ex[:, kind] = e.reshape(N_EXP, kt, P, e.shape[2]).transpose(0, 2, 1, 3).reshape(N_EXP, P, SLOT)

    vecs = np.concatenate([
        by_channel(a["g_pre"]), by_channel(a["a_g_q"]), by_channel(a["a_g_kv"]), by_channel(a["c_conv_w"][0]),
        by_channel(a["c_conv_b"][0]), pad(a["c_f_b1"][0][:, None]), pad(a["c_f_freq"][0][:, None]),
        pad(a["c_f_b2"][0][:, None]), pad(a["c_f_w1"][0]), pad(a["c_f_w2"][0]), by_channel(a["g_mix_2"][0]),
        by_channel(a["g_head_2"][0]), by_channel(a["pool_scale_2"][0]),
        by_channel(a["conv_q_2"][0]), by_channel(a["conv_k_2"][0]), by_channel(a["c"][0]), by_channel(a["c_ctx"]),
        k_major(w[:, at_if:at_if + 8]), k_major(np.concatenate([a["w_rg_2"][0], a["w_re_2"][0]], 1)),
    ], 1)
    assert vecs.shape[1] == VEC["width"]
    row = np.concatenate([a["b_sink"][0], a["b_rg_2"][0], a["b_re_2"][0], a["b_if_2"][0],
                          np.arange(SLOTS, dtype=np.float32)])
    mod_rows = np.zeros((DEPTH, P, 4 * D), np.float32)
    mod_rows[:, 0:2, 0:3 * D] = a["b_mod"][:, None]
    mod_rows[:, :, 3 * D:] = a["g_post"][:, None]
    return dict(
        panels=all_panels, vecs=vecs, g_final=np.broadcast_to(a["g_final_2"], (P, D)), g_ffn=np.broadcast_to(a["g_ffn_2"][0], (P, D)), rows=np.broadcast_to(row, (P, len(row))),
        tokens=np.concatenate([a["x"][0], a["ctx"][0]], 0),
        mod_rows=mod_rows,
        **{k: cst[k] for k in ("cst", "band", "zT", "dft", "idft", "tri", "causal", "counts", "selector")})


def kernel(**inputs):
    import concourse.bacc as bacc
    from concourse.bass_utils import run_bass_kernel_spmd

    arrays = {k: np.ascontiguousarray(v) for k, v in lay_out(inputs).items()}
    nc = bacc.Bacc("TRN2", target_bir_lowering=False, num_devices=1)
    dram = {k: nc.dram_tensor(k + "_dram", v.shape, F32, kind="ExternalInput").ap() for k, v in arrays.items()}
    dram["out"] = nc.dram_tensor("out_dram", (1, N, D), F32, kind="ExternalOutput").ap()
    build(nc, dram)
    r = run_bass_kernel_spmd(nc, [{k + "_dram": v for k, v in arrays.items()}], core_ids=[0])
    return r.results[0]["out_dram"]
```
